# Optimizing a Trainium2 kernel written in Bass

```python
import math
import jax, jax.numpy as jnp
from jax import lax
import numpy as np

D_MODEL = 1024
BATCH = 1
SEQ = 1024
DEPTH = 1

HEAD_DIM = 64
MLSTM_WIDTH = D_MODEL // 4
MLSTM_HEADS = MLSTM_WIDTH // HEAD_DIM
MLSTM_CHUNK = 64
CONV_WIDTH = 4
S5_WIDTH = D_MODEL // 4
S5_GROUP_CH = 16
S5_GROUPS = S5_WIDTH // S5_GROUP_CH
S5_STATE = 64
S5_DT_MIN = 1e-3
S5_DT_MAX = 1e-1
ATTN_WIDTH = D_MODEL - MLSTM_WIDTH - S5_WIDTH
ATTN_HEADS = ATTN_WIDTH // HEAD_DIM
ATTN_BLOCK = 128
DILATED_PATTERNS = ((128, 1), (512, 4), (2048, 16))
REL_BUCKETS = 32
REL_MAX_EXACT = 16
REL_MAX_DIST = 2048
MEM_TOKENS = 256
MEM_HEADS = 4
MEM_HEAD_DIM = D_MODEL // MEM_HEADS
MOE_GROUPS = 4
EXPERTS_PER_GROUP = 8
N_EXPERTS = MOE_GROUPS * EXPERTS_PER_GROUP
TOP_K = 2
D_EXPERT = D_MODEL // 2
MOE_BLOCK = 128

IN_WIDTH = 2 * MLSTM_WIDTH + 2 * MLSTM_HEADS + S5_WIDTH + 3 * ATTN_WIDTH
RMS_EPS = 1e-6
NEG_INF = -1e30

kernel_name = 'hybrid_mlstm_s5_dilated_hmoe_block'

f32 = jnp.float32

def rms_norm(x, gain):
    xf = x.astype(f32)
    y = xf * lax.rsqrt(jnp.mean(xf * xf, axis=-1, keepdims=True) + RMS_EPS)
    return (y * gain.astype(f32)).astype(x.dtype)

def causal_depthwise_conv(x, w, b):
    k_w, c = w.shape
    y = lax.conv_general_dilated(x, w[:, None, :].astype(x.dtype), window_strides=(1,),
                                 padding=[(k_w - 1, 0)],
                                 dimension_numbers=('NWC', 'WIO', 'NWC'),
                                 feature_group_count=c)
    return y + b.astype(x.dtype)

def mlstm_chunkwise(q, k, v, log_i, log_f):
    B, H, S, Dh = q.shape
    L = MLSTM_CHUNK
    nc = S // L
    q = q.reshape(B, H, nc, L, Dh)
    k = k.reshape(B, H, nc, L, Dh)
    v = v.reshape(B, H, nc, L, Dh)
    log_i = log_i.reshape(B, H, nc, L)
    b = jnp.cumsum(log_f.reshape(B, H, nc, L), axis=-1)
    g = b[..., -1]
    a = g[..., None] - b + log_i

    def step(carry, xs):
        c_st, n_st, m_st = carry
        g_c, a_c, k_c, v_c = xs
        m_new = jnp.maximum(g_c + m_st, jnp.max(a_c, axis=-1))
        decay = jnp.exp(g_c + m_st - m_new)
        w = jnp.exp(a_c - m_new[..., None])
        c_new = decay[..., None, None] * c_st + jnp.einsum('bhl,bhld,bhle->bhde', w, k_c, v_c)
        n_new = decay[..., None] * n_st + jnp.einsum('bhl,bhld->bhd', w, k_c)
        return (c_new, n_new, m_new), (c_st, n_st, m_st)

    init = (jnp.zeros((B, H, Dh, Dh), f32), jnp.zeros((B, H, Dh), f32), jnp.zeros((B, H), f32))
    xs = (jnp.moveaxis(g, 2, 0), jnp.moveaxis(a, 2, 0), jnp.moveaxis(k, 2, 0), jnp.moveaxis(v, 2, 0))
    _, (c_prev, n_prev, m_prev) = lax.scan(step, init, xs)
    c_prev = jnp.moveaxis(c_prev, 0, 2)
    n_prev = jnp.moveaxis(n_prev, 0, 2)
    m_prev = jnp.moveaxis(m_prev, 0, 2)

    causal = np.tril(np.ones((L, L), dtype=bool))
    d_mat = jnp.where(causal, b[..., :, None] - b[..., None, :] + log_i[..., None, :], -jnp.inf)
    m_inter = b + m_prev[..., None]
    m_t = jnp.maximum(m_inter, jnp.max(d_mat, axis=-1))
    w_intra = jnp.exp(d_mat - m_t[..., None]) * jnp.einsum('bhcld,bhcsd->bhcls', q, k)
    inter = jnp.exp(m_inter - m_t)
    num = inter[..., None] * jnp.einsum('bhcld,bhcde->bhcle', q, c_prev) \
        + jnp.einsum('bhcls,bhcse->bhcle', w_intra, v)
    den = inter * jnp.einsum('bhcld,bhcd->bhcl', q, n_prev) + jnp.sum(w_intra, axis=-1)
    h = num / jnp.maximum(jnp.abs(den), jnp.exp(-m_t))[..., None]
    return h.reshape(B, H, S, Dh)

def mlstm_mixer(u, o_pre, i_pre, f_pre, conv_w, conv_b, wq, wk, wv, gate_bias, norm_gain, skip):
    B, S, W = u.shape
    H, Dh = MLSTM_HEADS, HEAD_DIM
    c = jax.nn.silu(causal_depthwise_conv(u, conv_w, conv_b))
    ch = c.reshape(B, S, H, Dh).astype(f32)
    uh = u.reshape(B, S, H, Dh).astype(f32)
    q = jnp.einsum('bshd,hde->bhse', ch, wq.astype(f32)) * (Dh ** -0.5)
    k = jnp.einsum('bshd,hde->bhse', ch, wk.astype(f32))
    v = jnp.einsum('bshd,hde->bhse', uh, wv.astype(f32))
    gb = gate_bias.astype(f32)
    log_i = jnp.transpose(i_pre.astype(f32) + gb[:H], (0, 2, 1))
    log_f = jnp.transpose(jax.nn.log_sigmoid(f_pre.astype(f32) + gb[H:]), (0, 2, 1))
    h = jnp.transpose(mlstm_chunkwise(q, k, v, log_i, log_f), (0, 2, 1, 3))
    h = h * lax.rsqrt(jnp.mean(h * h, axis=-1, keepdims=True) + RMS_EPS)
    h = h.reshape(B, S, W) * norm_gain.astype(f32) + skip.astype(f32) * c.astype(f32)
    return (jax.nn.sigmoid(o_pre.astype(f32)) * h).astype(u.dtype)

def s5_mixer(u, a_re, a_im, log_dt, b_re, b_im, c_re, c_im, d_skip, w_glu, b_glu):
    B, S, W = u.shape
    G, Hc, P = S5_GROUPS, S5_GROUP_CH, S5_STATE
    uf = u.astype(f32).reshape(B, S, G, Hc)
    a_re = a_re.astype(f32)
    a_im = a_im.astype(f32)
    dt = jnp.exp(log_dt.astype(f32))[:, None]
    mag = jnp.exp(a_re * dt)
    ab_re = mag * jnp.cos(a_im * dt)
    ab_im = mag * jnp.sin(a_im * dt)
    den = a_re * a_re + a_im * a_im
    xr, yi = ab_re - 1.0, ab_im
    coef_re = (xr * a_re + yi * a_im) / den
    coef_im = (yi * a_re - xr * a_im) / den
    b_re = b_re.astype(f32)
    b_im = b_im.astype(f32)
    bb_re = coef_re[..., None] * b_re - coef_im[..., None] * b_im
    bb_im = coef_re[..., None] * b_im + coef_im[..., None] * b_re
    bu_re = jnp.einsum('bsgh,gph->bsgp', uf, bb_re)
    bu_im = jnp.einsum('bsgh,gph->bsgp', uf, bb_im)
    a_seq_re = jnp.broadcast_to(ab_re, (1, S, G, P))
    a_seq_im = jnp.broadcast_to(ab_im, (1, S, G, P))

    def combine(e1, e2):
        a1r, a1i, b1r, b1i = e1
        a2r, a2i, b2r, b2i = e2
        return (a2r * a1r - a2i * a1i, a2r * a1i + a2i * a1r,
                a2r * b1r - a2i * b1i + b2r, a2r * b1i + a2i * b1r + b2i)

    _, _, st_re, st_im = lax.associative_scan(combine, (a_seq_re, a_seq_im, bu_re, bu_im), axis=1)
    y = jnp.einsum('bsgp,ghp->bsgh', st_re, c_re.astype(f32)) \
        - jnp.einsum('bsgp,ghp->bsgh', st_im, c_im.astype(f32)) \
        + d_skip.astype(f32) * uf
    z = jax.nn.gelu(y.reshape(B, S, W))
    out = z * jax.nn.sigmoid(z @ w_glu.astype(f32) + b_glu.astype(f32))
    return out.astype(u.dtype)

def t5_bucket(dist):
    exact = dist < REL_MAX_EXACT
    large = REL_MAX_EXACT + (np.log(np.maximum(dist, 1) / REL_MAX_EXACT)
                             / np.log(REL_MAX_DIST / REL_MAX_EXACT)
                             * (REL_BUCKETS - REL_MAX_EXACT)).astype(np.int32)
    large = np.minimum(large, REL_BUCKETS - 1)
    return np.where(exact, dist, large).astype(np.int32)

def dilated_bias_mask(window, dil, n_blocks, rel_table):
    n_back = window // dil
    i = np.arange(ATTN_BLOCK)[:, None]
    j = np.arange(2 * ATTN_BLOCK)[None, :]
    off = ATTN_BLOCK + i - j
    band = (off >= 0) & (off <= n_back)
    bucket = t5_bucket(np.clip(off, 0, None) * dil)
    bias = jnp.transpose(rel_table.astype(f32)[bucket], (2, 0, 1))
    key_valid = (np.arange(n_blocks)[:, None] > 0) | (j >= ATTN_BLOCK)
    mask = band[None, None, None, None] & key_valid[None, :, None, None, None, :]
    return bias, mask

def prev_block(x):
    return jnp.concatenate([jnp.zeros_like(x[:, :1]), x[:, :-1]], axis=1)

def dilated_attention(q, k, v, rel_table):
    B, S, H, Dh = q.shape
    q = q.astype(f32) * (Dh ** -0.5)
    k = k.astype(f32)
    v = v.astype(f32)
    outs, lses = [], []
    for window, dil in DILATED_PATTERNS:
        span = ATTN_BLOCK * dil
        s_pad = -(-S // span) * span
        nb = s_pad // span
        pad_w = ((0, 0), (0, s_pad - S), (0, 0), (0, 0))
        qb = jnp.pad(q, pad_w).reshape(B, nb, ATTN_BLOCK, dil, H, Dh)
        kb = jnp.pad(k, pad_w).reshape(B, nb, ATTN_BLOCK, dil, H, Dh)
        vb = jnp.pad(v, pad_w).reshape(B, nb, ATTN_BLOCK, dil, H, Dh)
        kw = jnp.concatenate([prev_block(kb), kb], axis=2)
        vw = jnp.concatenate([prev_block(vb), vb], axis=2)
        bias, mask = dilated_bias_mask(window, dil, nb, rel_table)
        s = jnp.einsum('bnirhe,bnjrhe->bnrhij', qb, kw) + bias
        s = jnp.where(mask, s, NEG_INF)
        m = jnp.max(s, axis=-1, keepdims=True)
        p = jnp.exp(s - m)
        l = jnp.sum(p, axis=-1, keepdims=True)
        o = jnp.einsum('bnrhij,bnjrhe->bnirhe', p / l, vw)
        lse = jnp.transpose((m + jnp.log(l))[..., 0], (0, 1, 4, 2, 3))
        outs.append(o.reshape(B, s_pad, H, Dh)[:, :S])
        lses.append(lse.reshape(B, s_pad, H)[:, :S])
    w = jax.nn.softmax(jnp.stack(lses), axis=0)
    return jnp.sum(w[..., None] * jnp.stack(outs), axis=0)

def memory_cross_attention(xn, memn, w_q, w_kv, w_o):
    B, S, D = xn.shape
    M = memn.shape[1]
    q = (xn @ w_q).reshape(B, S, MEM_HEADS, MEM_HEAD_DIM)
    k, v = jnp.split(memn @ w_kv, 2, axis=-1)
    k = k.reshape(B, M, MEM_HEADS, MEM_HEAD_DIM)
    v = v.reshape(B, M, MEM_HEADS, MEM_HEAD_DIM)
    s = jnp.einsum('bshe,bmhe->bhsm', q, k).astype(f32) * (MEM_HEAD_DIM ** -0.5)
    p = jax.nn.softmax(s, axis=-1).astype(v.dtype)
    o = jnp.einsum('bhsm,bmhe->bshe', p, v).reshape(B, S, D)
    return o @ w_o

def hier_moe(xn, w_group, b_group, w_expert, b_expert, w_gu, w_down):
    B, S, D = xn.shape
    T = B * S
    xt = xn.reshape(T, D)
    g_prob = jax.nn.softmax((xt @ w_group).astype(f32) + b_group.astype(f32), axis=-1)
    g_p, g_i = lax.top_k(g_prob, 1)
    e_logits = ((xt @ w_expert).astype(f32) + b_expert.astype(f32)).reshape(T, MOE_GROUPS, EXPERTS_PER_GROUP)
    e_logits = jnp.take_along_axis(e_logits, g_i[:, :, None], axis=1)[:, 0]
    e_p, e_i = lax.top_k(jax.nn.softmax(e_logits, axis=-1), TOP_K)
    gates = g_p * e_p / jnp.sum(e_p, axis=-1, keepdims=True)
    eid = (g_i * EXPERTS_PER_GROUP + e_i).reshape(-1)
    gate = gates.reshape(-1).astype(xt.dtype)
    tok = jnp.repeat(jnp.arange(T, dtype=jnp.int32), TOP_K)
    n_assign = T * TOP_K
    order = jnp.argsort(eid)
    eid_s, tok_s, gate_s = eid[order], tok[order], gate[order]
    counts = jnp.bincount(eid, length=N_EXPERTS)
    starts = jnp.cumsum(counts) - counts
    padded = (counts + MOE_BLOCK - 1) // MOE_BLOCK * MOE_BLOCK
    p_ends = jnp.cumsum(padded)
    p_starts = p_ends - padded
    dest = p_starts[eid_s] + jnp.arange(n_assign, dtype=jnp.int32) - starts[eid_s]
    n_blocks = -(-n_assign // MOE_BLOCK) + N_EXPERTS
    n_rows = n_blocks * MOE_BLOCK
    row_tok = jnp.full((n_rows,), T, jnp.int32).at[dest].set(tok_s)
    row_gate = jnp.zeros((n_rows,), xt.dtype).at[dest].set(gate_s)
    block_e = jnp.minimum(jnp.searchsorted(p_ends, jnp.arange(n_blocks) * MOE_BLOCK, side='right'),
                          N_EXPERTS - 1)
    x_rows = jnp.concatenate([xt, jnp.zeros((1, D), xt.dtype)], axis=0)[row_tok]
    x_rows = x_rows.reshape(n_blocks, MOE_BLOCK, D)

    def expert_block(args):
        xb, e = args
        a, b = jnp.split(xb @ w_gu[e], 2, axis=-1)
        return (jax.nn.silu(a) * b) @ w_down[e]

    y_rows = lax.map(expert_block, (x_rows, block_e)).reshape(n_rows, D)
    out = jnp.zeros((T + 1, D), xt.dtype).at[row_tok].add(y_rows * row_gate[:, None])[:T]
    return out.reshape(B, S, D)

def setup_inputs(seed: int = 0) -> dict:
    key = jax.random.key(seed)
    ks = iter(jax.random.split(key, 48))

    def nrm(shape, scale):
        return jax.random.normal(next(ks), shape, f32) * scale

    def gain(shape):
        return 1.0 + nrm(shape, 0.02)

    L, D = DEPTH, D_MODEL
    H, G, P, Hc = MLSTM_HEADS, S5_GROUPS, S5_STATE, S5_GROUP_CH
    n_idx = jnp.arange(P, dtype=f32)
    gate_bias = jnp.concatenate([nrm((L, H), 0.1),
                                 jnp.linspace(3.0, 6.0, H, dtype=f32)[None] + nrm((L, H), 0.1)], axis=-1)
    return {
        'x': nrm((BATCH, SEQ, D), 1.0),
        'mem': nrm((BATCH, MEM_TOKENS, D), 1.0),
        'rel_bias': nrm((REL_BUCKETS, ATTN_HEADS), 0.5),
        'norm_mix': gain((L, D)),
        'w_in': nrm((L, D, IN_WIDTH), D ** -0.5),
        'mlstm_conv_w': nrm((L, CONV_WIDTH, MLSTM_WIDTH), CONV_WIDTH ** -0.5),
        'mlstm_conv_b': nrm((L, MLSTM_WIDTH), 0.02),
        'mlstm_wq': nrm((L, H, HEAD_DIM, HEAD_DIM), HEAD_DIM ** -0.5),
        'mlstm_wk': nrm((L, H, HEAD_DIM, HEAD_DIM), HEAD_DIM ** -0.5),
        'mlstm_wv': nrm((L, H, HEAD_DIM, HEAD_DIM), HEAD_DIM ** -0.5),
        'mlstm_gate_bias': gate_bias,
        'mlstm_norm': gain((L, MLSTM_WIDTH)),
        'mlstm_skip': gain((L, MLSTM_WIDTH)),
        's5_a_re': -0.5 + nrm((L, G, P), 0.01),
        's5_a_im': math.pi * n_idx[None, None, :] + nrm((L, G, P), 0.01),
        's5_log_dt': jax.random.uniform(next(ks), (L, G), f32, math.log(S5_DT_MIN), math.log(S5_DT_MAX)),
        's5_b_re': nrm((L, G, P, Hc), (2.0 * Hc) ** -0.5),
        's5_b_im': nrm((L, G, P, Hc), (2.0 * Hc) ** -0.5),
        's5_c_re': nrm((L, G, Hc, P), (2.0 * P) ** -0.5),
        's5_c_im': nrm((L, G, Hc, P), (2.0 * P) ** -0.5),
        's5_d': nrm((L, G, Hc), 1.0),
        's5_w_glu': nrm((L, S5_WIDTH, S5_WIDTH), S5_WIDTH ** -0.5),
        's5_b_glu': nrm((L, S5_WIDTH), 0.02),
        's5_out_norm': gain((L, S5_WIDTH)),
        'attn_out_norm': gain((L, ATTN_WIDTH)),
        'w_out': nrm((L, D, D), D ** -0.5),
        'norm_xattn': gain((L, D)),
        'norm_mem': gain((L, D)),
        'xattn_w_q': nrm((L, D, D), D ** -0.5),
        'xattn_w_kv': nrm((L, D, 2 * D), D ** -0.5),
        'xattn_w_o': nrm((L, D, D), D ** -0.5),
        'norm_ffn': gain((L, D)),
        'router_w_group': nrm((L, D, MOE_GROUPS), D ** -0.5),
        'router_b_group': nrm((L, MOE_GROUPS), 0.01),
        'router_w_expert': nrm((L, D, N_EXPERTS), D ** -0.5),
        'router_b_expert': nrm((L, N_EXPERTS), 0.01),
        'expert_w_gu': nrm((L, N_EXPERTS, D, 2 * D_EXPERT), D ** -0.5),
        'expert_w_down': nrm((L, N_EXPERTS, D_EXPERT, D), D_EXPERT ** -0.5),
        'final_norm': gain((D,)),
    }

def reference(x, mem, rel_bias, norm_mix, w_in, mlstm_conv_w, mlstm_conv_b, mlstm_wq, mlstm_wk,
              mlstm_wv, mlstm_gate_bias, mlstm_norm, mlstm_skip, s5_a_re, s5_a_im, s5_log_dt,
              s5_b_re, s5_b_im, s5_c_re, s5_c_im, s5_d, s5_w_glu, s5_b_glu, s5_out_norm,
              attn_out_norm, w_out, norm_xattn, norm_mem, xattn_w_q, xattn_w_kv, xattn_w_o,
              norm_ffn, router_w_group, router_b_group, router_w_expert, router_b_expert,
              expert_w_gu, expert_w_down, final_norm):
    B, S, D = x.shape
    sizes = [MLSTM_WIDTH, MLSTM_WIDTH, MLSTM_HEADS, MLSTM_HEADS, S5_WIDTH,
             ATTN_WIDTH, ATTN_WIDTH, ATTN_WIDTH]
    split_at = [int(s) for s in np.cumsum(sizes)[:-1]]
    for l in range(DEPTH):
        proj = rms_norm(x, norm_mix[l]) @ w_in[l]
        m_u, m_o, m_i, m_f, s_u, a_q, a_k, a_v = jnp.split(proj, split_at, axis=-1)
        y_m = mlstm_mixer(m_u, m_o, m_i, m_f, mlstm_conv_w[l], mlstm_conv_b[l], mlstm_wq[l],
                          mlstm_wk[l], mlstm_wv[l], mlstm_gate_bias[l], mlstm_norm[l], mlstm_skip[l])
        y_s = s5_mixer(s_u, s5_a_re[l], s5_a_im[l], s5_log_dt[l], s5_b_re[l], s5_b_im[l],
                       s5_c_re[l], s5_c_im[l], s5_d[l], s5_w_glu[l], s5_b_glu[l])
        y_s = rms_norm(y_s, s5_out_norm[l])
        y_a = dilated_attention(a_q.reshape(B, S, ATTN_HEADS, HEAD_DIM),
                                a_k.reshape(B, S, ATTN_HEADS, HEAD_DIM),
                                a_v.reshape(B, S, ATTN_HEADS, HEAD_DIM), rel_bias)
        y_a = rms_norm(y_a.reshape(B, S, ATTN_WIDTH).astype(x.dtype), attn_out_norm[l])
        x = x + jnp.concatenate([y_m, y_s, y_a], axis=-1) @ w_out[l]
        x = x + memory_cross_attention(rms_norm(x, norm_xattn[l]), rms_norm(mem, norm_mem[l]),
                                       xattn_w_q[l], xattn_w_kv[l], xattn_w_o[l])
        x = x + hier_moe(rms_norm(x, norm_ffn[l]), router_w_group[l], router_b_group[l],
                         router_w_expert[l], router_b_expert[l], expert_w_gu[l], expert_w_down[l])
    return rms_norm(x, final_norm)


_drawn_inputs = setup_inputs


def setup_inputs(seed=0):
    import zlib

    import numpy as np

    out = dict(_drawn_inputs(seed))
    spreads = {}
    factors = {'mlstm_conv_b': 3.753,
     'mlstm_norm': 5.572,
     'mlstm_skip': 7.97,
     's5_a_re': 64.0,
     's5_b_glu': 5.503,
     's5_out_norm': 4.014,
     'attn_out_norm': 2.67,
     'norm_xattn': 8.0,
     'norm_mem': 8.0,
     'router_b_group': 42.56,
     'router_b_expert': 31.424,
     'final_norm': 7.416,
     'norm_ffn': 8.0}
    for name, (base, spread) in spreads.items():
        noise = np.random.default_rng([zlib.crc32(name.encode()), seed]).standard_normal(out[name].shape)
        drawn = base * np.exp(spread * noise) if base else spread * noise
        out[name] = __import__('jax').numpy.asarray(drawn.astype(out[name].dtype))
    for name, factor in factors.items():
        out[name] = (out[name] * factor).astype(out[name].dtype)
    return out
```

```python
from contextlib import ExitStack


import numpy as np

import concourse.bass as bass
from concourse import mybir

F32 = mybir.dt.float32
U32 = mybir.dt.uint32
I32 = mybir.dt.int32
ALU = mybir.AluOpType
ACT = mybir.ActivationFunctionType
AX_X = mybir.AxisListType.X

P = 128
S = 1024
D = 1024
KT = D // P
TT = S // P
HALF = 512
EPS = 1e-6
DH = 64

M_W = 256
M_H = 4
L = 64
NC = S // L
S5_G = 16
S5_C = 16
S5_L = 8
A_W = 512
A_H = 8
MEM = 256
X_H = 4
X_DH = 256

COL_UO = 0
COL_GATE = 2 * M_W
COL_S = COL_GATE + 2 * M_H
COL_Q = COL_S + 256
COL_K = COL_Q + A_W
COL_V = COL_K + A_W

SLOT = KT * HALF
SLOTS = 6
NEG = -1.0e30

VECS = {}
_at = 0
for _name, _n in (("conv_w", 8), ("conv_b", 2), ("m_gain", 2), ("m_skip", 2), ("s_gain", 2), ("a_gain", 4),
                  ("gate_b", 1), ("a_re", 8), ("a_im", 8), ("log_dt", 8), ("sign", 1)):
    VECS[_name] = (_at, _at + _n)
    _at += _n
VEC_N = _at


class Norm:

    def __init__(self, k, name, n, source, gain, dest, banks, ring, stat, wait_source, keep=None):
        self.k, self.n, self.source, self.gain, self.dest = k, n, source, gain, dest
        self.banks, self.ring, self.stat, self.wait_source, self.keep = banks, ring, stat, wait_source, keep
        self.squared = k.sem(name + "_squared")
        self.variance = k.sem(name + "_variance")
        self.root = k.sem(name + "_root")
        self.inverse = k.sem(name + "_inverse")
        self.scaled = k.sem(name + "_scaled")
        self.turned = k.sem(name + "_turned")
        self.evac_act = k.sem(name + "_evac_act")
        self.evac_dve = k.sem(name + "_evac_dve")

    def scalar(self, act):
        for i in range(self.n + 2):
            if i < self.n:
                self.wait_source(act, i)
                if i >= 2:
                    act.wait_ge(self.turned, 2 * (i - 1))
                    if self.keep is not None:
                        act.wait_ge(self.keep[(i - 2) % 2], 16 * ((i - 2) // 2 + 1))
                act.activation(self.ring[:, i % 2, :], self.source(i), ACT.Square,
                               accum_out=self.stat[:, i, 0:1]).then_inc(self.squared, 1)
            if 1 <= i <= self.n:
                t = i - 1
                act.wait_ge(self.variance, t + 1)
                act.activation(self.stat[:, t, 2:3], self.stat[:, t, 1:2], ACT.Sqrt).then_inc(self.root, 1)
            if i >= 2:
                t = i - 2
                act.wait_ge(self.turned, 2 * t + 1)
                act.activation(self.dest(t, 0), self.banks[(2 * t) % 4][:, :].rearrange("p (a b) -> p a b", a=4),
                               ACT.Copy).then_inc(self.evac_act, 1)

    def vector(self, dve):
        for i in range(self.n + 2):
            if i < self.n:
                dve.wait_ge(self.squared, i + 1)
                dve.tensor_scalar(self.stat[:, i, 1:2], self.stat[:, i, 0:1], 1.0 / D, EPS, ALU.mult,
                                  ALU.add).then_inc(self.variance, 1)
            if 1 <= i <= self.n:
                t = i - 1
                dve.wait_ge(self.root, t + 1)
                dve.reciprocal(self.stat[:, t, 3:4], self.stat[:, t, 2:3]).then_inc(self.inverse, 1)
                dve.wait_ge(self.inverse, t + 1)
                dve.scalar_tensor_tensor(out=self.ring[:, t % 2, :], in0=self.source(t),
                                         scalar=self.stat[:, t, 3:4], in1=self.gain,
                                         op0=ALU.mult, op1=ALU.mult).then_inc(self.scaled, 1)
            if i >= 2:
                t = i - 2
                dve.wait_ge(self.turned, 2 * t + 2)
                dve.tensor_copy(self.dest(t, 1), self.banks[(2 * t + 1) % 4][:, :].rearrange(
                    "p (a b) -> p a b", a=4)).then_inc(self.evac_dve, 1)

    def tensor(self, pe):
        for t in range(self.n):
            pe.wait_ge(self.scaled, t + 1)
            for h in range(2):
                if t >= 2:
                    pe.wait_ge((self.evac_act, self.evac_dve)[h], t - 1)
                bank = self.banks[(2 * t + h) % 4]
                for a in range(4):
                    c = 4 * h + a
                    last = pe.transpose(bank[:, a * P:(a + 1) * P], self.ring[:, t % 2, c * P:(c + 1) * P],
                                        self.k.ident[:, :])
                last.then_inc(self.turned, 1)


def load_chunk(k, queue, i):
    source, n = k.chunks[i]
    queue.dma_start(k.chunk(i, n), source.rearrange("(k p) n -> p k n", p=P)).then_inc(k.chunk_in[i], 16)


def in_projection(k):
    with k.stage() as st:
        xs, ring, gain = k.yT[:, 0:4, :], k.yT[:, 4:6, :], k.yT[:, 6, :]
        v_out = k.yT[:, 7, :].rearrange("p (a b) -> p a b", a=2)
        stat = st.sbuf("mix_stat", [P, TT, 4])
        tb = [st.psum(f"turn{i}", [P, HALF]) for i in range(4)]
        gb = [st.psum(f"gemm{i}", [P, HALF]) for i in range(4)]
        const_in = st.sem("const_in")
        gain_in = st.sem("mix_gain_in")
        x_in = [st.sem(f"x_in{i}") for i in range(4)]
        product = st.sem("product")
        out_act = st.sem("out_act")
        out_dve = st.sem("out_dve")
        v_stored = [st.sem(f"v_stored{i}") for i in range(2)]

        def wait_x(eng, t):
            eng.wait_ge(x_in[t % 4], 16 * (t // 4 + 1))

        norm = Norm(st, "mix", TT, lambda t: xs[:, t % 4, :], gain,
                    lambda t, h: k.xnT[:, 4 * h:4 * h + 4, t * P:(t + 1) * P], tb, ring, stat, wait_x)

        groups = []
        for m in range(4):
            dest = k.uP[:, m, 3:] if m < 2 else k.oT[:, m - 2, :]
            for h in range(2):
                groups.append((lambda c, m=m: k.chunk(0, HALF)[:, c, m * P:(m + 1) * P],
                               lambda c, h=h: k.xnT[:, c, h * HALF:(h + 1) * HALF],
                               (P, HALF), dest[:, h * HALF:(h + 1) * HALF], 1.0, 0))
        for h in range(2):
            groups.append((lambda c: k.chunk(1, 264)[:, c, 0:8],
                           lambda c, h=h: k.xnT[:, c, h * HALF:(h + 1) * HALF],
                           (8, HALF), k.gateT[:, h * HALF:(h + 1) * HALF], 1.0, 1))
        for s in range(S5_L):
            groups.append((lambda c, s=s: k.xnT[:, c, s::S5_L], lambda c: k.chunk(1, 264)[:, c, 8:264],
                           (P, 256), k.s_in[:, :, s, :], 1.0, 1))
        for i, dst, scale in ((2, k.qT, DH ** -0.5), (3, k.kT, 1.0)):
            for m in range(4):
                for h in range(2):
                    groups.append((lambda c, m=m, i=i: k.chunk(i, HALF)[:, c, m * P:(m + 1) * P],
                                   lambda c, h=h: k.xnT[:, c, h * HALF:(h + 1) * HALF],
                                   (P, HALF), dst[:, m, h * HALF:(h + 1) * HALF], scale, i))
        v_first = len(groups)
        for t in range(TT):
            groups.append((lambda c, t=t: k.xnT[:, c, t * P:(t + 1) * P], lambda c: k.chunk(4, HALF)[:, c, :],
                           (P, HALF), v_out[:, t % 2, :], 1.0, 4))

        def psum_of(g):
            rows, cols = groups[g][2]
            view = gb[g % 4][0:rows, 0:cols]
            return view.rearrange("p (a b) -> p a b", b=S5_C) if cols == 256 else view

        def wait_v_slot(eng, g):
            t = g - v_first
            if t >= 2:
                eng.wait_ge(v_stored[t % 2], 16 * (t // 2))

        with st.block() as block:

            @block.sync
            def _(sp):
                sp.dma_start(gain, k.w["norm_mix"][0:1, :].partition_broadcast(P)).then_inc(gain_in, 16)
                sp.dma_start(k.ident[:, :], k.w["ident"]).then_inc(const_in, 16)
                sp.dma_start(k.vec[:, :], k.w["vec"]).then_inc(const_in, 16)
                for t in range(TT):
                    if t >= 4:
                        sp.wait_ge(norm.scaled, t - 3)
                    sp.dma_start(xs[:, t % 4, :], k.w["x"][t * P:(t + 1) * P, :]).then_inc(x_in[t % 4], 16)
                    if t == 3:
                        load_chunk(k, sp, 0)
                        load_chunk(k, sp, 1)
                load_chunk(k, sp, 2)
                load_chunk(k, sp, 3)
                sp.wait_ge(product, 8)
                load_chunk(k, sp, 4)
                for t in range(TT):
                    g = v_first + t
                    sp.wait_ge((out_act, out_dve)[g % 2], g // 2 + 1)
                    sp.dma_start(k.v_dram[t * P:(t + 1) * P, :], v_out[:, t % 2, :]).then_inc(v_stored[t % 2], 16)
                for i in range(2):
                    sp.wait_ge(v_stored[i], 16 * (TT // 2))

            @block.gpsimd
            def _(pool):
                pool.memset(k.uP[:, :, 0:3], 0.0).then_inc(st.sem("u_padded"), 1)

            @block.scalar
            def _(act):
                norm.scalar(act)
                for g in range(0, len(groups), 2):
                    if g >= v_first:
                        wait_v_slot(act, g)
                    act.wait_ge(product, g + 1)
                    act.activation(groups[g][3], psum_of(g), ACT.Copy, scale=groups[g][4]).then_inc(out_act, 1)

            @block.vector
            def _(dve):
                dve.wait_ge(gain_in, 16)
                norm.vector(dve)
                for g in range(1, len(groups), 2):
                    if g >= v_first:
                        wait_v_slot(dve, g)
                    dve.wait_ge(product, g + 1)
                    if groups[g][4] == 1.0:
                        dve.tensor_copy(groups[g][3], psum_of(g)).then_inc(out_dve, 1)
                    else:
                        dve.tensor_scalar(groups[g][3], psum_of(g), groups[g][4], None, ALU.mult).then_inc(out_dve, 1)

            @block.tensor
            def _(pe):
                pe.wait_ge(const_in, 32)
                norm.tensor(pe)
                pe.wait_ge(norm.evac_act, TT)
                pe.wait_ge(norm.evac_dve, TT)
                for g, (lhs, rhs, (rows, cols), _, _, chunk) in enumerate(groups):
                    pe.wait_ge(k.chunk_in[chunk], 16)
                    if g >= 4:
                        pe.wait_ge((out_act, out_dve)[g % 2], (g - 4) // 2 + 1)
                    for c in range(KT):
                        last = pe.matmul(gb[g % 4][0:rows, 0:cols], lhs(c), rhs(c), start=(c == 0), stop=(c == KT - 1))
                    last.then_inc(product, 1)


def broadcast(ap, axis, n):
    shape = list(ap.shape)
    return ap.unsqueeze(axis).to_broadcast(shape[:axis] + [n] + shape[axis:])


def mlstm(k):
    HP = M_H // 2
    HC = M_H * NC
    Q4 = NC // 4
    with k.stage() as st:
        free = k.ring[:, 4 * SLOT:6 * SLOT].rearrange("p (n j t) -> p n j t", n=4, j=HP)
        cT, mqT, mkT, interB = (free[:, n, :, :] for n in range(4))
        free = k.ring[:, 0:SLOT].rearrange("p (n c l) -> p n c l", n=2, l=L)
        cmB, kw = free[:, 0, :, :], free[:, 1, :, :]
        state = k.yT[:, 2:6, :].rearrange("p a b -> p (a b)")[:, 0:HP * NC * (DH + 1)].rearrange(
            "p (c e) -> p c e", e=DH + 1)
        v1 = k.ring[:, 3 * SLOT:3 * SLOT + HP * NC * (DH + 1)].rearrange("p (c e) -> p c e", e=DH + 1)
        wts = st.sbuf("mlstm_weights", [P, HP, 3, P])
        gi = st.sbuf("gi", [HC, L])
        gf = st.sbuf("gf", [HC, L])
        tmp = st.sbuf("gate_tmp", [HC, 2, L])
        cum = st.sbuf("cum", [HC, L])
        rel = st.sbuf("rel", [HC, L])
        cmax = st.sbuf("cmax", [HC, L])
        zero = st.sbuf("zero", [HC, L])
        gm = st.sbuf("gm", [HC, 8])
        inter = st.sbuf("inter", [HC, L])
        dup = st.sbuf("dup", [HC, 4, 2, L])
        row = st.sbuf("row", [M_H, 4, NC + 1])
        col = st.sbuf("col", [P, 4, HP, NC])
        upd = st.sbuf("upd", [P, HP * NC, DH + 1])
        hn = upd
        sq = kw
        stat = st.sbuf("h_stat", [P, 4, HP * NC])
        bank = [st.psum(f"mb{i}", [P, HALF]) for i in range(8)]
        dram = {n: k.nc.dram_tensor(n, sh, F32, kind="Internal").ap() for n, sh in (
            ("gate_dram", [2 * M_H, S]), ("gm_dram", [2, HC]), ("m_dram", [2, HC]), ("cmax_dram", [M_H, S]),
            ("inter_dram", [M_H, S]))}
        sem = {n: st.sem("m_" + n) for n in (
            "weights_in gates_out gates_in gm_out gm_in m_out m_in cm_out inter_out cm_in inter_in pad bias "
            "act gate pool conv silu qk qk_act kv kv_act kv_dve cols cols_dve s_done ew qi u_done u_evac states "
            "o_done o_evac h_done hT_done y den").split()}
        vec = k.vec

        def V(name, j):
            a = VECS[name][0] + j
            return vec[:, a:a + 1]

        with st.block() as block:

            @block.sync
            def _(sp):
                for i in (5, 6):
                    load_chunk(k, sp, i)
                sp.dma_start(wts[:, :, :, :], k.w["mlstm_w"]).then_inc(sem["weights_in"], 16)
                sp.wait_ge(sem["bias"], 1)
                sp.dma_start(dram["gate_dram"], k.gateT[:, :]).then_inc(sem["gates_out"], 16)
                sp.wait_ge(sem["gates_out"], 16)
                gd = dram["gate_dram"]
                sp.dma_start(gi[:, :], gd[0:M_H, :].rearrange("h (c l) -> (h c) l", l=L)).then_inc(sem["gates_in"], 16)
                sp.dma_start(gf[:, :], gd[M_H:, :].rearrange("h (c l) -> (h c) l", l=L)).then_inc(sem["gates_in"], 16)
                sp.wait_ge(sem["gate"], 6)
                for i in range(2):
                    sp.dma_start(dram["gm_dram"][i:i + 1, :].rearrange("a n -> n a"), gm[:, i:i + 1]).then_inc(sem["gm_out"], 16)
                sp.wait_ge(sem["gm_out"], 32)
                for i in range(2):
                    sp.dma_start(row[:, i, 0:NC], dram["gm_dram"][i, :].rearrange("(h c) -> h c", c=NC)).then_inc(sem["gm_in"], 16)
                sp.wait_ge(sem["gate"], 7)
                for i in range(2):
                    sp.dma_start(dram["m_dram"][i, :].rearrange("(h c) -> h c", c=NC), row[:, 2, i:i + NC]).then_inc(sem["m_out"], 16)
                sp.wait_ge(sem["m_out"], 32)
                for i in range(2):
                    sp.dma_start(gm[:, 2 + i:3 + i], dram["m_dram"][i:i + 1, :].rearrange("a n -> n a")).then_inc(sem["m_in"], 16)
                sp.wait_ge(sem["gate"], 8)
                sp.dma_start(dram["cmax_dram"].rearrange("h (c l) -> (h c) l", l=L), cmax[:, :]).then_inc(sem["cm_out"], 16)
                sp.wait_ge(sem["cm_out"], 16)
                for q in range(2):
                    sp.dma_start(cmB[q * DH:(q + 1) * DH, :, :].rearrange("p (j c) l -> p j (c l)", j=HP),
                                 bcast_rows(dram["cmax_dram"], q, HP)).then_inc(sem["cm_in"], 16)
                sp.wait_ge(sem["act"], 4)
                sp.dma_start(dram["inter_dram"].rearrange("h (c l) -> (h c) l", l=L), inter[:, :]).then_inc(sem["inter_out"], 16)
                sp.wait_ge(sem["inter_out"], 16)
                for q in range(2):
                    sp.dma_start(interB[q * DH:(q + 1) * DH, :, :], bcast_rows(dram["inter_dram"], q, HP)).then_inc(sem["inter_in"], 16)

            @block.gpsimd
            def _(pool):
                pool.memset(zero[:, :], 0.0).then_inc(sem["pad"], 1)
                pool.memset(v1[:, :, DH:DH + 1], 1.0).then_inc(sem["pad"], 1)
                pool.memset(state[:, :, :], 0.0).then_inc(sem["pad"], 1)
                pool.memset(row[:, 2, 0:1], 0.0).then_inc(sem["pad"], 1)
                pool.wait_ge(sem["ew"], 1)
                for q in range(2):
                    part = cmB[q * DH:(q + 1) * DH, :, :]
                    pool.affine_select(out=part, in_=part, compare_op=ALU.is_ge, fill=NEG, base=0,
                                       pattern=[[0, HP * NC], [1, L]], channel_multiplier=-1).then_inc(sem["pool"], 1)

            @block.scalar
            def _(act):
                for j in range(HP):
                    act.wait_ge(sem["conv"], 4 * (j + 1))
                    act.activation(cT[:, j, :], cT[:, j, :], ACT.Silu, bias=V("conv_b", j)).then_inc(sem["silu"], 1)
                for g in range(8):
                    dst = (mqT, mkT)[g // 4]
                    act.wait_ge(sem["qk"], g + 1)
                    act.activation(dst[:, (g // 2) % 2, (g % 2) * HALF:(g % 2 + 1) * HALF], bank[g % 4][:, :], ACT.Copy,
                                   scale=(DH ** -0.5, 1.0)[g // 4]).then_inc(sem["qk_act"], 1)
                act.wait_ge(sem["gate"], 1)
                act.activation(tmp[:, 0, :], tmp[:, 0, :], ACT.Exp, scale=-1.0).then_inc(sem["act"], 1)
                act.wait_ge(sem["act"], 1)
                act.activation(tmp[:, 1, :], tmp[:, 0, :], ACT.Ln, bias=1.0).then_inc(sem["act"], 1)
                act.wait_ge(sem["gate"], 9)
                act.activation(dup[:, 1, 0, :], rel[:, :], ACT.Exp, bias=gm[:, 4:5]).then_inc(sem["act"], 1)
                act.activation(inter[:, :], cmax[:, :], ACT.Exp, scale=-1.0, bias=gm[:, 2:3]).then_inc(sem["act"], 1)
                act.activation(dup[:, 2, 0, :], tmp[:, 0, :], ACT.Exp, scale=-1.0).then_inc(sem["act"], 1)
                act.activation(dup[:, 3, 0, :], zero[:, :], ACT.Exp, bias=gm[:, 5:6]).then_inc(sem["act"], 1)
                act.wait_ge(sem["pool"], 2)
                act.activation(cmB[:, :, :], cmB[:, :, :], ACT.Exp).then_inc(sem["act"], 1)
                for g in range(4):
                    act.wait_ge(sem["kv"], 4 + g + 1)
                    act.activation(v1[:, 8 * g:8 * g + 8, 0:DH], bank[4 + g][:, :].rearrange("p (c e) -> p c e", e=DH),
                                   ACT.Copy).then_inc(sem["kv_act"], 1)
                for g in range(8):
                    act.wait_ge(sem["u_done"], g + 1)
                    act.activation(upd[:, 4 * g:4 * g + 4, :], bank[g % 4][:, 0:4 * (DH + 1)].rearrange(
                        "p (c e) -> p c e", e=DH + 1), ACT.Copy).then_inc(sem["u_evac"], 1)
                for g in range(8):
                    act.wait_ge(sem["o_done"], g + 1)
                    act.activation(hn[:, 4 * g:4 * g + 4, :], bank[4 + g % 4][:, 0:4 * (DH + 1)].rearrange(
                        "p (c e) -> p c e", e=DH + 1), ACT.Copy).then_inc(sem["o_evac"], 1)
                act.wait_ge(sem["h_done"], 4)
                act.activation(stat[:, 1, :], stat[:, 1, :], ACT.Sqrt).then_inc(sem["act"], 1)
                act.activation(k.oT[:, :, :], k.oT[:, :, :], ACT.Sigmoid).then_inc(sem["act"], 1)

            @block.vector
            def _(dve):
                dve.tensor_scalar(k.gateT[:, :], k.gateT[:, :], V("gate_b", 0)[0:2 * M_H, :], None, ALU.add).then_inc(sem["bias"], 1)
                for j in range(HP):
                    dve.tensor_scalar(cT[:, j, :], k.uP[:, j, 0:S], V("conv_w", 4 * j), None, ALU.mult).then_inc(sem["conv"], 1)
                    for tap in range(1, 4):
                        dve.wait_ge(sem["conv"], 4 * j + tap)
                        dve.scalar_tensor_tensor(out=cT[:, j, :], in0=k.uP[:, j, tap:tap + S], scalar=V("conv_w", 4 * j + tap),
                                                 in1=cT[:, j, :], op0=ALU.mult, op1=ALU.add).then_inc(sem["conv"], 1)
                dve.wait_ge(sem["gates_in"], 32)
                dve.scalar_tensor_tensor(out=tmp[:, 0, :], in0=gf[:, :], scalar=-1.0, in1=gf[:, :], op0=ALU.mult,
                                         op1=ALU.max).then_inc(sem["gate"], 1)
                dve.wait_ge(sem["act"], 2)
                dve.scalar_tensor_tensor(out=gf[:, :], in0=gf[:, :], scalar=0.0, in1=tmp[:, 1, :], op0=ALU.min,
                                         op1=ALU.subtract).then_inc(sem["gate"], 1)
                dve.wait_ge(sem["gate"], 2)
                dve.wait_ge(sem["pad"], 4)
                dve.tensor_tensor_scan(cum[:, :], gf[:, :], zero[:, :], 0.0, ALU.add, ALU.add).then_inc(sem["gate"], 1)
                dve.wait_ge(sem["gate"], 3)
                dve.tensor_tensor(rel[:, :], gi[:, :], cum[:, :], ALU.subtract).then_inc(sem["gate"], 1)
                dve.wait_ge(sem["gate"], 4)
                dve.tensor_scalar(gm[:, 0:1], cum[:, L - 1:L], 0.0, None, ALU.add).then_inc(sem["gate"], 1)
                dve.tensor_reduce(gm[:, 6:7], rel[:, :], AX_X, ALU.max).then_inc(sem["cols"], 1)
                dve.wait_ge(sem["cols"], 1)
                dve.tensor_tensor(gm[:, 1:2], gm[:, 6:7], cum[:, L - 1:L], ALU.add).then_inc(sem["gate"], 1)
                dve.wait_ge(sem["gm_in"], 32)
                dve.tensor_tensor_scan(row[:, 2, 1:NC + 1], row[:, 0, 0:NC], row[:, 1, 0:NC], 0.0, ALU.add,
                                       ALU.max).then_inc(sem["gate"], 1)
                dve.wait_ge(sem["m_in"], 32)
                dve.tensor_tensor_scan(cmax[:, :], rel[:, :], rel[:, :], gm[:, 2:3], ALU.max, ALU.max).then_inc(sem["gate"], 1)
                dve.tensor_tensor(gm[:, 4:5], gm[:, 0:1], gm[:, 3:4], ALU.subtract).then_inc(sem["cols"], 1)
                dve.wait_ge(sem["cols"], 2)
                dve.tensor_tensor(gm[:, 5:6], gm[:, 4:5], gm[:, 2:3], ALU.add).then_inc(sem["cols"], 1)
                dve.wait_ge(sem["gate"], 8)
                dve.tensor_tensor(tmp[:, 0, :], cum[:, :], cmax[:, :], ALU.add).then_inc(sem["cols"], 1)
                dve.wait_ge(sem["cols"], 4)
                dve.tensor_copy(dup[:, 0, 0, :], rel[:, :]).then_inc(sem["gate"], 1)
                dve.wait_ge(sem["act"], 6)
                dve.wait_ge(sem["gate"], 9)
                dve.tensor_copy(dup[:, :, 1, :], dup[:, :, 0, :]).then_inc(sem["gate"], 1)
                dve.wait_ge(sem["cols_dve"], 1)
                for q in range(2):
                    half = slice(q * DH, (q + 1) * DH)
                    view = bank[4][half, 0:4 * HC].rearrange("p (n j q c) -> p n j q c", n=4, j=HP, q=2)
                    dve.tensor_copy(col[half, :, :, :], view[:, :, :, q, :]).then_inc(sem["gate"], 1)
                dve.wait_ge(sem["gate"], 12)
                dve.wait_ge(sem["cm_in"], 32)
                rcol = col[:, 0, :, :].rearrange("p j c -> p (j c)")
                dve.tensor_tensor(cmB[:, :, :], broadcast(rcol, 2, L), cmB[:, :, :], ALU.subtract).then_inc(sem["ew"], 1)
                wcol = col[:, 1, :, :].rearrange("p j c -> p (j c)")
                for g in range(4):
                    dve.wait_ge(sem["kv"], g + 1)
                    dve.tensor_tensor(kw[:, 8 * g:8 * g + 8, :], bank[g][:, :].rearrange("p (c e) -> p c e", e=DH),
                                      broadcast(wcol[:, 8 * g:8 * g + 8], 2, DH), ALU.mult).then_inc(sem["kv_dve"], 1)
                dve.wait_ge(sem["inter_in"], 32)
                dve.wait_ge(sem["qk_act"], 8)
                dve.wait_ge(sem["s_done"], 4)
                dve.tensor_tensor(interB[:, :, :], mqT[:, :, :], interB[:, :, :], ALU.mult).then_inc(sem["qi"], 1)
                dve.wait_ge(sem["act"], 7)
                for g in range(4):
                    part = cmB[:, 8 * g:8 * g + 8, :]
                    dve.tensor_tensor(part, part, bank[4 + g][:, :].rearrange("p (c l) -> p c l", l=L), ALU.mult)\
                        .then_inc(sem["ew"], 1)
                dcol = col[:, 3, :, :].rearrange("p j c -> p (j c)")
                dve.wait_ge(sem["u_evac"], 8)
                n = 0
                for c in range(NC - 1):
                    for j in range(HP):
                        i = j * NC + c
                        if c:
                            dve.wait_ge(sem["states"], n - 1)
                        dve.scalar_tensor_tensor(out=state[:, i + 1, :], in0=state[:, i, :], scalar=dcol[:, i:i + 1],
                                                 in1=upd[:, i, :], op0=ALU.mult, op1=ALU.add).then_inc(sem["states"], 1)
                        n += 1
                dve.wait_ge(sem["o_evac"], 8)
                ecol = col[:, 2, :, :].rearrange("p j c -> p (j c)")
                dve.scalar_tensor_tensor(out=stat[:, 1, :], in0=hn[:, :, DH], scalar=-1.0, in1=hn[:, :, DH], op0=ALU.mult,
                                         op1=ALU.max).then_inc(sem["den"], 1)
                dve.wait_ge(sem["den"], 1)
                dve.tensor_tensor(stat[:, 0, :], stat[:, 1, :], ecol, ALU.max).then_inc(sem["h_done"], 1)
                dve.wait_ge(sem["h_done"], 1)
                dve.reciprocal(stat[:, 2, :], stat[:, 0, :]).then_inc(sem["cols"], 1)
                dve.wait_ge(sem["cols"], 5)
                dve.tensor_tensor(hn[:, :, 0:DH], hn[:, :, 0:DH], broadcast(stat[:, 2, :], 2, DH), ALU.mult).then_inc(sem["h_done"], 1)
                dve.wait_ge(sem["h_done"], 2)
                dve.tensor_tensor(sq[:, :, :], hn[:, :, 0:DH], hn[:, :, 0:DH], ALU.mult).then_inc(sem["h_done"], 1)
                dve.wait_ge(sem["h_done"], 3)
                dve.tensor_reduce(stat[:, 3, :], sq[:, :, :], AX_X, ALU.add).then_inc(sem["cols"], 1)
                dve.wait_ge(sem["cols"], 6)
                dve.tensor_scalar(stat[:, 1, :], stat[:, 3, :], 1.0 / DH, EPS, ALU.mult, ALU.add).then_inc(sem["h_done"], 1)
                dve.wait_ge(sem["act"], 8)
                dve.reciprocal(stat[:, 0, :], stat[:, 1, :]).then_inc(sem["cols"], 1)
                dve.wait_ge(sem["cols"], 7)
                dve.tensor_tensor(hn[:, :, 0:DH], hn[:, :, 0:DH], broadcast(stat[:, 0, :], 2, DH), ALU.mult).then_inc(sem["h_done"], 1)
                for j in range(HP):
                    dve.tensor_scalar(cT[:, j, :], cT[:, j, :], V("m_skip", j), None, ALU.mult).then_inc(sem["y"], 1)
                dve.wait_ge(sem["y"], 2)
                dve.wait_ge(sem["act"], 9)
                for g in range(4):
                    j, half = g // 2, slice((g % 2) * HALF, (g % 2 + 1) * HALF)
                    dve.wait_ge(sem["hT_done"], g + 1)
                    dve.scalar_tensor_tensor(out=cT[:, j, half], in0=bank[g][:, :], scalar=V("m_gain", j), in1=cT[:, j, half],
                                             op0=ALU.mult, op1=ALU.add).then_inc(sem["y"], 1)
                    dve.wait_ge(sem["y"], 3 + 2 * g)
                    dve.tensor_tensor(k.yT[:, j, half], cT[:, j, half], k.oT[:, j, half], ALU.mult).then_inc(sem["y"], 1)

            @block.tensor
            def _(pe):
                pe.wait_ge(sem["weights_in"], 16)
                pe.wait_ge(sem["silu"], HP)
                for g in range(8):
                    if g >= 4:
                        pe.wait_ge(sem["qk_act"], g - 3)
                    j = (g // 2) % 2
                    pe.matmul(bank[g % 4][:, :], wts[:, j, g // 4, :], cT[:, j, (g % 2) * HALF:(g % 2 + 1) * HALF],
                              start=True, stop=True).then_inc(sem["qk"], 1)
                pe.wait_ge(sem["gate"], 10)
                for n in range(4):
                    last = pe.transpose(bank[4][:, n * HC:(n + 1) * HC], dup[:, n, :, :].rearrange("p a l -> p (a l)"),
                                        k.ident[0:HC, 0:HC])
                last.then_inc(sem["cols_dve"], 1)

                def per_chunk(out, lhs, rhs, g, stop=True, start=True):
                    for i in range(8 * g, 8 * g + 8):
                        for q in range(2):
                            half = slice(q * DH, (q + 1) * DH)
                            last = pe.matmul(out[half, (i % 8) * DH:(i % 8 + 1) * DH], lhs(half, i), rhs(half, i),
                                             start=start, stop=stop)
                    return last

                pe.wait_ge(sem["qk_act"], 8)
                pe.wait_ge(sem["gate"], 12)
                for g in range(4):
                    per_chunk(bank[g], lambda half, i: cT[half, i // NC, (i % NC) * L:(i % NC + 1) * L],
                              lambda half, i: wts[half, i // NC, 1, half], g).then_inc(sem["kv"], 1)
                for g in range(4):
                    per_chunk(bank[4 + g], lambda half, i: k.uP[half, i // NC, 3 + (i % NC) * L:3 + (i % NC + 1) * L],
                              lambda half, i: wts[half, i // NC, 2, half], g).then_inc(sem["kv"], 1)
                for g in range(4):
                    pe.wait_ge(sem["kv_act"], g + 1)
                    per_chunk(bank[4 + g], lambda half, i: mkT[half, i // NC, (i % NC) * L:(i % NC + 1) * L],
                              lambda half, i: mqT[half, i // NC, (i % NC) * L:(i % NC + 1) * L], g).then_inc(sem["s_done"], 1)
                W = DH + 1

                def per_four(out, terms, g):
                    for i in range(4 * g, 4 * g + 4):
                        for q in range(2):
                            half = slice(q * DH, (q + 1) * DH)
                            for n, (lhs, rhs) in enumerate(terms):
                                last = pe.matmul(out[half, (i % 4) * W:(i % 4 + 1) * W], lhs(half, i), rhs(half, i),
                                                 start=(n == 0), stop=(n == len(terms) - 1))
                    return last

                pe.wait_ge(sem["kv_dve"], 4)
                for g in range(8):
                    if g >= 4:
                        pe.wait_ge(sem["u_evac"], g - 3)
                    per_four(bank[g % 4], [(lambda half, i: kw[half, i, :], lambda half, i: v1[half, i, :])], g)\
                        .then_inc(sem["u_done"], 1)
                pe.wait_ge(sem["ew"], 5)
                pe.wait_ge(sem["qi"], 1)
                pe.wait_ge(sem["states"], HP * (NC - 1))
                for g in range(8):
                    if g >= 4:
                        pe.wait_ge(sem["o_evac"], g - 3)
                    per_four(bank[4 + g % 4], [
                        (lambda half, i: cmB[half, i, :], lambda half, i: v1[half, i, :]),
                        (lambda half, i: interB[half, i // NC, (i % NC) * L:(i % NC + 1) * L], lambda half, i: state[half, i, :])],
                        g).then_inc(sem["o_done"], 1)
                pe.wait_ge(sem["h_done"], 5)
                for g in range(4):
                    per_chunk(bank[g], lambda half, i: hn[half, i, 0:DH], lambda half, i: k.ident[half, half], g)\
                        .then_inc(sem["hT_done"], 1)


def bcast_rows(rows, q, n):
    return rows.rearrange("(j q) t -> q j t", j=n)[q].partition_broadcast(DH)


def s5(k):
    GP = S5_G // 2
    C = S // S5_L
    SUB = 8
    RUNS = C // SUB
    with k.stage() as st:
        free = k.ring[:, 4 * SLOT:6 * SLOT].rearrange("p (n f) -> p n f", n=4)
        UT = free[:, 0, :].rearrange("p (g c) -> p g c", c=C)
        T = free[:, 1, :].rearrange("p (g c) -> p g c", c=P)
        z = free[:, 2, :].rearrange("p (t h) -> p t h", h=256)
        zT = free[:, 3, :].rearrange("p (n t c) -> p n t c", n=2, c=C)
        spare = k.yT[:, 4:8, :].rearrange("p a b -> p (a b)")
        WL = spare[:, 0:2 * GP * 9 * S5_C].rearrange("p (r g l h) -> p r g l h", r=2, g=GP, l=9)
        BT = k.oT[:, :, :].rearrange("p r (g s h) -> p r g s h", g=GP, s=S5_L)
        BG = k.uP[:, :, 3:].rearrange("p r (g s) -> p r g s", g=GP)
        X = st.sbuf("chunk_states", [P, 2, GP, C + 1])
        t1 = k.ring[:, 0:2048].rearrange("p (r x) -> p r x", r=2)
        t2 = k.ring[:, 2048:4096].rearrange("p (r x) -> p r x", r=2)
        Km = k.ring[0:S5_C, 3 * SLOT:3 * SLOT + S5_G * P]
        Km = Km.rearrange("p (g x) -> p g x", x=P)
        bc = st.sbuf("s5_bc", [P, 4, GP, S5_C])
        bb = st.sbuf("s5_b_bar", [P, 2, GP, S5_C])
        diag = st.sbuf("s5_diag", [S5_C, S5_G, S5_C])
        pw = st.sbuf("a_powers", [P, 2, 9, GP])
        pr = st.sbuf("a_powers_down", [P, 2, 8, GP])
        fp = st.sbuf("f_powers", [P, 2, 9, GP])
        ff = st.sbuf("recur_factors", [P, 2, 12, 2, GP])
        par = st.sbuf("s5_scalars", [P, 24, GP])
        wglu = k.ring[:, 3 * SLOT + 2048:3 * SLOT + 2560].rearrange("p (n h) -> p n h", n=2)
        bglu = st.sbuf("glu_bias", [P, 256])
        stat = st.sbuf("s5_stat", [P, 4, S5_L])
        bank = [st.psum(f"sb{i}", [P, HALF]) for i in range(8)]
        sem = {n: st.sem("s_" + n) for n in (
            "par_in b_in glu_in toep zero chain act pool bt bg_t bg ut_t ut km_done km xin_done xin "
            "rec y_done gelu zt_done zt glu_done gate_done norm yt_done yt").split()}
        a0 = VECS["a_re"][0]
        a_re, a_im, ldt = k.vec[:, a0:a0 + 8], k.vec[:, a0 + 8:a0 + 16], k.vec[:, a0 + 16:a0 + 24]
        N = {n: i for i, n in enumerate(
            "dt mag theta turns r s_half s_full cos re im xr den inv c_re c_im u v w x q f_re f_im".split())}

        def p_(n):
            return par[:, N[n], :]

        with st.block() as block:

            @block.sync
            def _(sp):
                sp.dma_start(bc[:, :, :, :], k.w["s5_bc"]).then_inc(sem["b_in"], 16)
                sp.dma_start(diag[:, :, :], k.w["s5_diag"]).then_inc(sem["b_in"], 16)
                sp.dma_start(wglu, k.w["s5_w_glu"].rearrange("(n p) h -> p n h", p=P)).then_inc(sem["glu_in"], 16)
                sp.dma_start(bglu[:, :], k.w["s5_b_glu"][0:1, :].partition_broadcast(P)).then_inc(sem["glu_in"], 16)
                sp.wait_ge(sem["km"], 4)
                sp.wait_ge(sem["zero"], 1)
                for s in range(S5_L):
                    rows = slice(s * S5_C, (s + 1) * S5_C)
                    sp.dma_start(T[rows, :, s * S5_C:], Km[:, :, 0:(S5_L - s) * S5_C]).then_inc(sem["toep"], 16)

            @block.gpsimd
            def _(pool):
                pool.memset(T, 0.0).then_inc(sem["zero"], 1)
                pool.memset(X[:, :, :, 0:1], 0.0).then_inc(sem["zero"], 1)

            @block.scalar
            def _(act):
                act.activation(p_("dt"), ldt, ACT.Exp).then_inc(sem["act"], 1)
                act.wait_ge(sem["chain"], 1)
                act.activation(p_("mag"), p_("mag"), ACT.Exp).then_inc(sem["act"], 1)
                act.wait_ge(sem["chain"], 10)
                act.activation(p_("s_half"), p_("r"), ACT.Sin, scale=0.5).then_inc(sem["act"], 1)
                act.activation(p_("s_full"), p_("r"), ACT.Sin).then_inc(sem["act"], 1)
                for b in range(4):
                    act.wait_ge(sem["ut_t"], b + 1)
                    act.activation(UT[:, 4 * b:4 * b + 4, :], bank[b][:, :].rearrange("p (g c) -> p g c", c=C), ACT.Copy)\
                        .then_inc(sem["ut"], 1)
                for b in range(4):
                    act.wait_ge(sem["bg_t"], b + 1)
                    act.activation(BG[:, b // 2, 4 * (b % 2):4 * (b % 2) + 4, :],
                                   bank[4 + b][:, :].rearrange("p (g c) -> p g c", c=P), ACT.Copy).then_inc(sem["bg"], 1)
                for b in range(4):
                    act.wait_ge(sem["xin_done"], b + 1)
                    act.activation(X[:, b // 2, 4 * (b % 2):4 * (b % 2) + 4, 1:],
                                   bank[b][:, :].rearrange("p (g c) -> p g c", c=C), ACT.Copy).then_inc(sem["xin"], 1)
                for b in range(4):
                    act.wait_ge(sem["y_done"], b + 1)
                    act.activation(z.rearrange("p t (g q h) -> p q g t h", q=2, h=S5_C)[:, b // 2, 4 * (b % 2):4 * (b % 2) + 4],
                                   bank[b][:, :].rearrange("p (g t h) -> p g t h", g=4, t=S5_L),
                                   ACT.Gelu_apprx_tanh).then_inc(sem["gelu"], 1)
                for b in range(4):
                    act.wait_ge(sem["zt_done"], b + 1)
                    act.activation(zT[:, b // 2, 4 * (b % 2):4 * (b % 2) + 4, :],
                                   bank[4 + b][:, :].rearrange("p (t c) -> p t c", c=C), ACT.Copy).then_inc(sem["zt"], 1)
                for b in range(4):
                    act.wait_ge(sem["glu_done"], b + 1)
                    part = t1.rearrange("p r x -> p (r x)")[:, HALF * b:HALF * (b + 1)]
                    act.activation(part, part, ACT.Sigmoid).then_inc(sem["gate_done"], 1)
                act.wait_ge(sem["norm"], 2)
                act.activation(stat[:, 2, :], stat[:, 1, :], ACT.Sqrt).then_inc(sem["norm"], 1)
                for b in range(4):
                    act.wait_ge(sem["yt_done"], b + 1)
                    j, g0 = b // 2, VECS["s_gain"][0] + b // 2
                    act.activation(k.yT[:, 2 + j, :].rearrange("p (c t) -> p t c", t=S5_L)[:, 4 * (b % 2):4 * (b % 2) + 4, :],
                                   bank[4 + b][:, :].rearrange("p (t c) -> p t c", c=C), ACT.Copy,
                                   scale=k.vec[:, g0:g0 + 1]).then_inc(sem["yt"], 1)

            @block.vector
            def _(dve):
                count = [0]

                def step(ins):
                    count[0] += 1
                    ins.then_inc(sem["chain"], 1)
                    dve.wait_ge(sem["chain"], count[0])

                def tt(out, x, y, op):
                    step(dve.tensor_tensor(out, x, y, op))

                def ts(out, x, a, op, b=None, op2=None):
                    step(dve.tensor_scalar(out, x, a, b, op, op2) if op2 else dve.tensor_scalar(out, x, a, None, op))

                sign = k.vec[:, VECS["sign"][0]:VECS["sign"][0] + 1]
                dve.wait_ge(sem["act"], 1)
                tt(p_("mag"), a_re, p_("dt"), ALU.mult)
                tt(p_("theta"), a_im, p_("dt"), ALU.mult)
                rounder = float(1.5 * 2.0 ** 23)
                ts(p_("turns"), p_("theta"), float(np.float32(0.5 / np.pi)), ALU.mult)
                ts(p_("turns"), p_("turns"), rounder, ALU.add)
                ts(p_("turns"), p_("turns"), rounder, ALU.subtract)
                at = p_("theta")
                for part in (6.28125, 0.0019350051879882812, 3.0199159819336793e-07):
                    step(dve.scalar_tensor_tensor(out=p_("r"), in0=p_("turns"), scalar=-part, in1=at, op0=ALU.mult, op1=ALU.add))
                    at = p_("r")
                ts(p_("r"), p_("r"), 3.1415925, ALU.min, -3.1415925, ALU.max)
                ts(p_("u"), p_("r"), 1.0, ALU.mult)
                dve.wait_ge(sem["act"], 4)
                tt(p_("cos"), p_("s_half"), p_("s_half"), ALU.mult)
                ts(p_("cos"), p_("cos"), -2.0, ALU.mult, 1.0, ALU.add)
                tt(p_("re"), p_("mag"), p_("cos"), ALU.mult)
                tt(p_("im"), p_("mag"), p_("s_full"), ALU.mult)
                ts(p_("xr"), p_("re"), -1.0, ALU.add)
                tt(p_("u"), a_re, a_re, ALU.mult)
                tt(p_("v"), a_im, a_im, ALU.mult)
                tt(p_("den"), p_("u"), p_("v"), ALU.add)
                step(dve.reciprocal(p_("inv"), p_("den")))
                tt(p_("u"), p_("xr"), a_re, ALU.mult)
                tt(p_("v"), p_("im"), a_im, ALU.mult)
                tt(p_("u"), p_("u"), p_("v"), ALU.add)
                tt(p_("c_re"), p_("u"), p_("inv"), ALU.mult)
                tt(p_("u"), p_("im"), a_re, ALU.mult)
                tt(p_("v"), p_("xr"), a_im, ALU.mult)
                tt(p_("u"), p_("u"), p_("v"), ALU.subtract)
                tt(p_("c_im"), p_("u"), p_("inv"), ALU.mult)

                def cmul(o_re, o_im, x_re, x_im, y_re, y_im, u, v):
                    tt(u, x_re, y_re, ALU.mult)
                    tt(v, x_im, y_im, ALU.mult)
                    tt(o_re, u, v, ALU.subtract)
                    tt(u, x_re, y_im, ALU.mult)
                    tt(v, x_im, y_re, ALU.mult)
                    tt(o_im, u, v, ALU.add)

                u_s = t1[:, 0, 0:8 * GP].rearrange("p (l g) -> p l g", g=GP)
                v_s = t1[:, 1, 0:8 * GP].rearrange("p (l g) -> p l g", g=GP)

                def powers(dst, re, im):
                    step(dve.memset(dst[:, 0, 0, :], 1.0))
                    step(dve.memset(dst[:, 1, 0, :], 0.0))
                    ts(dst[:, 0, 1, :], re, 1.0, ALU.mult)
                    ts(dst[:, 1, 1, :], im, 1.0, ALU.mult)
                    for n in (1, 2, 4):
                        cmul(dst[:, 0, n + 1:2 * n + 1, :], dst[:, 1, n + 1:2 * n + 1, :],
                             dst[:, 0, 1:n + 1, :], dst[:, 1, 1:n + 1, :], broadcast(dst[:, 0, n, :], 1, n),
                             broadcast(dst[:, 1, n, :], 1, n), u_s[:, 0:n, :], v_s[:, 0:n, :])

                powers(pw, p_("re"), p_("im"))
                for l in range(8):
                    ts(pr[:, :, l, :], pw[:, :, 7 - l, :], 1.0, ALU.mult)
                powers(fp, pw[:, 0, 8, :], pw[:, 1, 8, :])
                for n in range(11):
                    if n < 8:
                        re, im = fp[:, 0, n + 1, :], fp[:, 1, n + 1, :]
                    else:
                        a, b = ff[:, 0, n - 1, 0, :], ff[:, 1, n - 1, 1, :]
                        cmul(p_("f_re"), p_("f_im"), a, b, a, b, p_("u"), p_("v"))
                        re, im = p_("f_re"), p_("f_im")
                    ts(ff[:, 0, n, 0, :], re, 1.0, ALU.mult)
                    ts(ff[:, 0, n, 1, :], re, 1.0, ALU.mult)
                    ts(ff[:, 1, n, 0, :], im, -1.0, ALU.mult)
                    ts(ff[:, 1, n, 1, :], im, 1.0, ALU.mult)
                dve.wait_ge(sem["b_in"], 32)
                u_b = t1[:, 0, 0:GP * S5_C].rearrange("p (g h) -> p g h", g=GP)
                v_b = t1[:, 1, 0:GP * S5_C].rearrange("p (g h) -> p g h", g=GP)
                cmul(bb[:, 0, :, :], bb[:, 1, :, :], bc[:, 0, :, :], bc[:, 1, :, :],
                     broadcast(p_("c_re"), 2, S5_C), broadcast(p_("c_im"), 2, S5_C), u_b, v_b)
                u_w = t1[:, 0, 0:GP * 8 * S5_C].rearrange("p (g s h) -> p g s h", g=GP, s=8)
                v_w = t1[:, 1, 0:GP * 8 * S5_C].rearrange("p (g s h) -> p g s h", g=GP, s=8)
                down = [broadcast(pr[:, r, :, :].rearrange("p l g -> p g l"), 3, S5_C) for r in range(2)]
                cmul(BT[:, 0], BT[:, 1], broadcast(bb[:, 0], 2, 8), broadcast(bb[:, 1], 2, 8), down[0], down[1], u_w, v_w)
                dve.tensor_copy(p_("x"), p_("u")).then_inc(sem["bt"], 1)
                for l0 in (0, 8):
                    n = 8 if l0 == 0 else 1
                    up = [broadcast(pw[:, r, l0:l0 + n, :].rearrange("p l g -> p g l"), 3, S5_C) for r in range(2)]
                    c = [broadcast(bc[:, 2 + r], 2, n) for r in range(2)]
                    uu = t1[:, 0, 0:GP * n * S5_C].rearrange("p (g s h) -> p g s h", g=GP, s=n)
                    vv = t1[:, 1, 0:GP * n * S5_C].rearrange("p (g s h) -> p g s h", g=GP, s=n)
                    tt(uu, c[0], up[0], ALU.mult)
                    tt(vv, c[1], up[1], ALU.mult)
                    tt(WL[:, 0, :, l0:l0 + n, :], uu, vv, ALU.subtract)
                    tt(uu, c[0], up[1], ALU.mult)
                    tt(vv, c[1], up[0], ALU.mult)
                    step(dve.scalar_tensor_tensor(out=uu, in0=uu, scalar=-1.0, in1=vv, op0=ALU.mult, op1=ALU.subtract))
                    step(dve.tensor_copy(WL[:, 1, :, l0:l0 + n, :], uu))
                dve.tensor_copy(p_("x"), p_("u")).then_inc(sem["bt"], 1)
                for b in range(4):
                    dve.wait_ge(sem["km_done"], b + 1)
                    part = Km.rearrange("p (g q) x -> p q g x", q=2)[:, b // 2, 4 * (b % 2):4 * (b % 2) + 4, :]
                    step(dve.tensor_copy(part, bank[b][0:S5_C, :].rearrange("p (g x) -> p g x", x=P)))
                    dve.tensor_tensor(part[:, :, 0:S5_C], part[:, :, 0:S5_C], diag[:, :, :].rearrange(
                        "p (g q) x -> p q g x", q=2)[:, b // 2, 4 * (b % 2):4 * (b % 2) + 4, :], ALU.add)\
                        .then_inc(sem["km"], 1)
                dve.wait_ge(sem["xin"], 4)
                body = X[:, :, :, 1:].rearrange("p r g (n j) -> p r g n j", j=SUB)

                def advance(to, of, power, shape, last=False):
                    def factor(kind, r):
                        f = ff[:, kind, power, r, :]
                        for n in shape:
                            f = broadcast(f, len(f.shape), n)
                        return f

                    size = int(np.prod(shape)) * GP
                    names = ["g"] + [f"x{i}" for i in range(len(shape))]
                    dims = {f"x{i}": n for i, n in enumerate(shape)}
                    a, b = (t[:, :, 0:size].rearrange(f"p r ({' '.join(names)}) -> p r {' '.join(names)}", g=GP, **dims)
                            for t in (t1, t2))
                    for r in range(2):
                        dve.tensor_tensor(a[:, r], of[r], factor(0, r), ALU.mult).then_inc(sem["rec"], 1)
                        dve.tensor_tensor(b[:, r], of[1 - r], factor(1, r), ALU.mult).then_inc(sem["rec"], 1)
                    n_rec[0] += 4
                    dve.wait_ge(sem["rec"], n_rec[0])
                    for r in range(2):
                        step(dve.tensor_tensor(a[:, r], a[:, r], b[:, r], ALU.add))
                    for r in range(2):
                        step(dve.tensor_tensor(to[r], to[r], a[:, r], ALU.add))

                n_rec = [0]
                for j in range(1, SUB):
                    advance([body[:, r, :, :, j] for r in range(2)], [body[:, r, :, :, j - 1] for r in range(2)], 0, [RUNS])
                ends = [body[:, r, :, :, SUB - 1] for r in range(2)]
                for i in range(4):
                    d = 1 << i
                    advance([e[:, :, d:] for e in ends], [e[:, :, 0:RUNS - d] for e in ends], 7 + i, [RUNS - d])
                for j in range(SUB - 1):
                    advance([body[:, r, :, 1:, j] for r in range(2)], [e[:, :, 0:RUNS - 1] for e in ends], j, [RUNS - 1])
                dve.tensor_copy(p_("x"), p_("u")).then_inc(sem["bt"], 1)
                flat = t1.rearrange("p r x -> p (r x)")
                dve.wait_ge(sem["glu_in"], 32)
                for b in range(4):
                    dve.wait_ge(sem["y_done"], 4 + b + 1)
                    part = flat[:, HALF * b:HALF * (b + 1)].rearrange("p (t h) -> p t h", t=2)
                    dve.tensor_tensor(part, bank[b][:, :].rearrange("p (t h) -> p t h", t=2), broadcast(bglu[:, :], 1, 2),
                                      ALU.add).then_inc(sem["glu_done"], 1)
                zf = z.rearrange("p t h -> p (t h)")
                sq = t2.rearrange("p r x -> p (r x)")
                dve.wait_ge(sem["gate_done"], 4)
                tt(zf, zf, flat, ALU.mult)
                tt(sq, zf, zf, ALU.mult)
                dve.tensor_reduce(stat[:, 0, :], sq.rearrange("p (t h) -> p t h", h=256), AX_X, ALU.add).then_inc(sem["norm"], 1)
                dve.wait_ge(sem["norm"], 1)
                dve.tensor_scalar(stat[:, 1, :], stat[:, 0, :], 1.0 / 256, EPS, ALU.mult, ALU.add).then_inc(sem["norm"], 1)
                dve.wait_ge(sem["norm"], 3)
                step(dve.reciprocal(stat[:, 3, :], stat[:, 2, :]))
                dve.tensor_tensor(z, z, broadcast(stat[:, 3, :], 2, 256), ALU.mult).then_inc(sem["bt"], 1)

            @block.tensor
            def _(pe):
                for g in range(S5_G):
                    last = pe.transpose(bank[g // 4][:, (g % 4) * C:(g % 4 + 1) * C],
                                        k.s_in[:, g, :, :].rearrange("p s h -> p (s h)"), k.ident[:, :])
                    if g % 4 == 3:
                        last.then_inc(sem["ut_t"], 1)
                pe.wait_ge(sem["bt"], 1)
                for r in range(2):
                    for g in range(GP):
                        n = r * GP + g
                        last = pe.transpose(bank[4 + n // 4][:, (n % 4) * P:(n % 4 + 1) * P],
                                            BT[:, r, g].rearrange("p s h -> p (s h)"), k.ident[:, :])
                        if n % 4 == 3:
                            last.then_inc(sem["bg_t"], 1)
                pe.wait_ge(sem["bt"], 2)
                pe.wait_ge(sem["ut"], 4)
                for n in range(S5_G):
                    q, gp = n // GP, n % GP
                    half = slice(q * 64, (q + 1) * 64)
                    for r in range(2):
                        last = pe.matmul(bank[n // 4][0:S5_C, (n % 4) * P:(n % 4 + 1) * P], bb[half, r, gp, :],
                                         WL[half, r, gp, 0:8, :].rearrange("p l h -> p (l h)"), start=(r == 0), stop=(r == 1))
                    if n % 4 == 3:
                        last.then_inc(sem["km_done"], 1)
                pe.wait_ge(sem["bg"], 4)
                for r in range(2):
                    for gp in range(GP):
                        n = r * GP + gp
                        if n % 4 == 0:
                            pe.wait_ge(sem["km"], n // 4 + 1)
                        for q in range(2):
                            half = slice(q * 64, (q + 1) * 64)
                            last = pe.matmul(bank[n // 4][half, (n % 4) * C:(n % 4 + 1) * C], BG[:, r, gp, half],
                                             UT[:, 2 * gp + q, :], start=True, stop=True)
                        if n % 4 == 3:
                            last.then_inc(sem["xin_done"], 1)
                pe.wait_ge(sem["toep"], 16 * S5_L)
                pe.wait_ge(sem["zero"], 2)
                pe.wait_ge(sem["bt"], 3)
                for n in range(S5_G):
                    q, gp = n // GP, n % GP
                    half = slice(q * 64, (q + 1) * 64)
                    out = bank[n // 4][:, (n % 4) * P:(n % 4 + 1) * P]
                    pe.matmul(out, UT[:, 2 * gp + q, :], T[:, 2 * gp + q, :], start=True, stop=False)
                    for r in range(2):
                        last = pe.matmul(out, X[half, r, gp, 0:C],
                                         WL[half, r, gp, 1:9, :].rearrange("p l h -> p (l h)"), start=False, stop=(r == 1))
                    if n % 4 == 3:
                        last.then_inc(sem["y_done"], 1)
                pe.wait_ge(sem["gelu"], 4)
                for n in range(2):
                    for t in range(S5_L):
                        m = n * S5_L + t
                        last = pe.transpose(bank[4 + m // 4][:, (m % 4) * C:(m % 4 + 1) * C], z[:, t, n * P:(n + 1) * P],
                                            k.ident[:, :])
                        if m % 4 == 3:
                            last.then_inc(sem["zt_done"], 1)
                pe.wait_ge(sem["zt"], 4)
                pe.wait_ge(sem["glu_in"], 32)
                for t in range(S5_L):
                    for n in range(2):
                        last = pe.matmul(bank[t // 2][:, (t % 2) * 256:(t % 2 + 1) * 256], zT[:, n, t, :], wglu[:, n, :],
                                         start=(n == 0), stop=(n == 1))
                    if t % 2:
                        last.then_inc(sem["y_done"], 1)
                pe.wait_ge(sem["bt"], 4)
                for n in range(2):
                    for t in range(S5_L):
                        m = n * S5_L + t
                        last = pe.transpose(bank[4 + m // 4][:, (m % 4) * C:(m % 4 + 1) * C], z[:, t, n * P:(n + 1) * P],
                                            k.ident[:, :])
                        if m % 4 == 3:
                            last.then_inc(sem["yt_done"], 1)


PATTERNS = ((128, 1), (512, 4), (2048, 16))
BLK = 128
O_W = A_W + 2 * A_H


def attention(k):
    with k.stage() as st:
        v = [k.ring[:, 4 * SLOT:5 * SLOT].rearrange("p (t n) -> p t n", n=A_W),
             k.ring[:, 5 * SLOT:6 * SLOT].rearrange("p (t n) -> p t n", n=A_W),
             k.yT[:, 4:8, :].rearrange("p a (b n) -> p (a b) n", n=A_W)]
        bias = st.sbuf("attn_bias", [P, A_H, 5 * BLK])
        sx = st.sbuf("scores", [P, 3, 2 * BLK])
        pr = st.sbuf("probs", [P, 3, 2 * BLK])
        pT = st.sbuf("probsT", [P, 3, 2 * BLK])
        stage = st.sbuf("out_rows", [P, 2, O_W])
        sb = [st.psum(f"as{i}", [P, HALF]) for i in range(3)]
        tb = [st.psum(f"at{i}", [P, HALF]) for i in range(3)]
        ob = [st.psum(f"ob{i}", [P, HALF]) for i in range(2)]
        v_in = [st.sem(f"v_in{i}") for i in range(3)]
        bias_in = st.sem("bias_in")
        scored, biased, exped, turned, pt_act, pt_dve, summed, rows_out = (st.sem("a_" + n) for n in (
            "scored biased exped turned pt_act pt_dve summed rows_out").split())
        stored = [st.sem(f"rows_stored{i}") for i in range(2)]

        units = [(p, t, h) for p in range(3) for t in range(TT) for h in range(A_H)]

        def columns(src, p, t, h, keys):
            rows = src[(h % 2) * DH:(h % 2 + 1) * DH, h // 2, :]
            if p == 0:
                first = max(t - 1, 0) if keys else t
                return rows[:, first * BLK:(t + 1) * BLK]
            if p == 1:
                n, r = t // 4, t % 4
                first = 0 if keys else n
                return rows[:, first * 4 * BLK:(n + 1) * 4 * BLK].rearrange("p (i r) -> p r i", r=4)[:, r, :]
            return rows.rearrange("p (i u) -> p u i", u=TT)[:, t, :]

        def width(p, t):
            return 2 * BLK if (p == 0 and t) or (p == 1 and t >= 4) else BLK

        def bias_of(p, t, h):
            end = (2, 4, 5)[p] * BLK
            return bias[:, h, end - width(p, t):end]

        def values(p, t, h):
            tiles = {0: [t - 1, t], 1: [t - 4, t], 2: [t]}[p] if width(p, t) > BLK or p == 2 else [t]
            return [v[p][:, x, h * DH:(h + 1) * DH] for x in tiles]

        def wait_turned_out(eng, i):
            if i % 3 == 0:
                eng.wait_ge(pt_act, i // 3 + 1)
            else:
                eng.wait_ge(pt_dve, i - i // 3)

        def evacuate(eng, i, copy, sem):
            if i >= 3:
                eng.wait_ge(summed, i - 2)
            eng.wait_ge(turned, i + 1)
            w = width(*units[i][:2])
            copy(pT[:, i % 3, 0:w], tb[i % 3][:, 0:w]).then_inc(sem, 1)

        with st.block() as block:

            @block.sync
            def _(sp):
                sp.dma_start(bias[:, :, :], k.w["attn_bias"]).then_inc(bias_in, 16)
                sp.dma_start(v[0], k.v_dram.rearrange("(t i) n -> i t n", i=P)).then_inc(v_in[0], 16)
                sp.dma_start(v[1], k.v_dram.rearrange("(b i r) n -> i b r n", b=2, r=4)).then_inc(v_in[1], 16)
                sp.dma_start(v[2], k.v_dram.rearrange("(i u) n -> i u n", u=TT)).then_inc(v_in[2], 16)
                load_chunk(k, sp, 7)
                load_chunk(k, sp, 8)
                for n in range(3 * TT):
                    p, t = n // TT, n % TT
                    sp.wait_ge(rows_out, n + 1)
                    dst = k.attn_dram[p]
                    src = stage[:, n % 2, :]
                    if p == 0:
                        sp.dma_start(dst[t * BLK:(t + 1) * BLK, :], src).then_inc(stored[n % 2], 16)
                    elif p == 1:
                        sp.dma_start(dst.rearrange("(b i r) n -> b r i n", b=2, r=4)[t // 4, t % 4], src)\
                            .then_inc(stored[n % 2], 16)
                    else:
                        sp.dma_start(dst.rearrange("(i u) n -> u i n", u=TT)[t], src).then_inc(stored[n % 2], 16)
                for i in range(2):
                    sp.wait_ge(stored[i], 16 * (3 * TT // 2))

            def wait_stage(eng, n):
                if n >= 2:
                    eng.wait_ge(stored[n % 2], 16 * (n // 2))

            @block.scalar
            def _(act):
                for i in range(len(units) + 3):
                    if i < len(units):
                        p, t, h = units[i]
                        n = i // A_H
                        if h == 0:
                            wait_stage(act, n)
                        act.wait_ge(biased, i + 1)
                        if i >= 3:
                            act.wait_ge(turned, i - 2)
                        w = width(p, t)
                        act.activation(pr[:, i % 3, 0:w], sx[:, i % 3, 0:w], ACT.Exp, scale=-1.0,
                                       bias=stage[:, n % 2, A_W + h:A_W + h + 1],
                                       accum_out=stage[:, n % 2, A_W + A_H + h:A_W + A_H + h + 1]).then_inc(exped, 1)
                    if 1 <= i <= len(units) and (i - 1) % 3 == 0:
                        evacuate(act, i - 1, lambda o, x: act.activation(o, x, ACT.Copy), pt_act)
                    if i >= 3 and (i - 3) % A_H == A_H - 1:
                        n = (i - 3) // A_H
                        act.wait_ge(summed, A_H * (n + 1))
                        act.activation(stage[:, n % 2, 0:A_W], ob[n % 2][:, :], ACT.Copy).then_inc(rows_out, 1)

            @block.vector
            def _(dve):
                dve.wait_ge(bias_in, 16)
                for i in range(len(units) + 1):
                    if i < len(units):
                        p, t, h = units[i]
                        n = i // A_H
                        if h == 0:
                            wait_stage(dve, n)
                        dve.wait_ge(scored, i + 1)
                        if i >= 3:
                            dve.wait_ge(exped, i - 2)
                        w = width(p, t)
                        dve.tensor_tensor_reduce(sx[:, i % 3, 0:w], sb[i % 3][:, 0:w], bias_of(p, t, h), -1.0, -NEG,
                                                 ALU.add, ALU.min, stage[:, n % 2, A_W + h:A_W + h + 1]).then_inc(biased, 1)
                    if i >= 1 and (i - 1) % 3:
                        evacuate(dve, i - 1, lambda o, x: dve.tensor_copy(o, x), pt_dve)

            @block.tensor
            def _(pe):
                for i in range(len(units) + 2):
                    if i < len(units):
                        p, t, h = units[i]
                        if i >= 3:
                            pe.wait_ge(biased, i - 2)
                        pe.matmul(sb[i % 3][:, 0:width(p, t)], columns(k.qT, p, t, h, False), columns(k.kT, p, t, h, True),
                                  start=True, stop=True).then_inc(scored, 1)
                    if 1 <= i <= len(units):
                        j = i - 1
                        pe.wait_ge(exped, j + 1)
                        if j >= 3:
                            wait_turned_out(pe, j - 3)
                        for c in range(width(*units[j][:2]) // BLK):
                            last = pe.transpose(tb[j % 3][:, c * BLK:(c + 1) * BLK], pr[:, j % 3, c * BLK:(c + 1) * BLK],
                                                k.ident[:, :])
                        last.then_inc(turned, 1)
                    if i >= 2:
                        j = i - 2
                        p, t, h = units[j]
                        n = j // A_H
                        if t == 0 and h == 0:
                            pe.wait_ge(v_in[p], 16)
                        if h == 0 and n >= 2:
                            pe.wait_ge(rows_out, n - 1)
                        wait_turned_out(pe, j)
                        vs = values(p, t, h)
                        for c, x in enumerate(vs):
                            last = pe.matmul(ob[n % 2][:, h * DH:(h + 1) * DH], pT[:, j % 3, c * BLK:(c + 1) * BLK], x,
                                             start=(c == 0), stop=(c == len(vs) - 1))
                        last.then_inc(summed, 1)


def join_patterns(k):
    with k.stage() as st:
        rows = st.sbuf("pattern_rows", [P, 2, 3, O_W])
        e = st.sbuf("join_small", [P, 2, 10, A_H])
        y = st.sbuf("join_y", [P, 2, A_W])
        tmp = st.sbuf("join_tmp", [P, 2, 2, A_W])
        stat = st.sbuf("join_stat", [P, TT, 4])
        bank = [st.psum(f"jb{i}", [P, HALF]) for i in range(2)]
        rows_in = [[st.sem(f"rows_in{i}{p}") for p in range(3)] for i in range(2)]
        diff, exped, factor, mixed, pooled, added, squared, var, root, inv, scaled, turned, out, chain = (
            st.sem("j_" + n) for n in ("diff exped factor mixed pooled added squared var root inv scaled turned out "
                                       "chain").split())
        gain0 = VECS["a_gain"][0]

        def num(t, p):
            return rows[:, t % 2, p, 0:A_W].rearrange("p (h e) -> p h e", e=DH)

        with st.block() as block:

            @block.sync
            def _(sp):
                for t in range(TT):
                    if t >= 2:
                        sp.wait_ge(mixed, t - 1)
                        sp.wait_ge(pooled, 2 * (t - 1))
                    for p in range(3):
                        sp.dma_start(rows[:, t % 2, p, :], k.attn_dram[p, t * P:(t + 1) * P, :]).then_inc(rows_in[t % 2][p], 16)

            @block.gpsimd
            def _(pool):
                for t in range(TT):
                    pool.wait_ge(factor, t + 1)
                    if t >= 2:
                        pool.wait_ge(added, t - 1)
                    for p in (1, 2):
                        pool.tensor_tensor(tmp[:, t % 2, p - 1, :].rearrange("p (h e) -> p h e", e=DH), num(t, p),
                                           broadcast(e[:, t % 2, 6 + p, :], 2, DH), ALU.mult).then_inc(pooled, 1)

            @block.scalar
            def _(act):
                for t in range(TT):
                    act.wait_ge(diff, t + 1)
                    act.activation(e[:, t % 2, 1:4, :], e[:, t % 2, 1:4, :], ACT.Exp).then_inc(exped, 1)
                    act.wait_ge(added, t + 1)
                    act.activation(tmp[:, t % 2, 0, :], y[:, t % 2, :], ACT.Square, accum_out=stat[:, t, 0:1]).then_inc(squared, 1)
                    act.wait_ge(var, t + 1)
                    act.activation(stat[:, t, 2:3], stat[:, t, 1:2], ACT.Sqrt).then_inc(root, 1)

            @block.vector
            def _(dve):
                count = [0]

                def step(ins):
                    count[0] += 1
                    ins.then_inc(chain, 1)
                    dve.wait_ge(chain, count[0])

                def store(t):
                    dve.wait_ge(turned, t + 1)
                    dve.tensor_tensor(k.yT[:, 4:8, t * P:(t + 1) * P], bank[t % 2][:, :].rearrange("p (a b) -> p a b", a=4),
                                      broadcast(k.vec[:, gain0:gain0 + 4], 2, P), ALU.mult).then_inc(out, 1)

                for t in range(TT):
                    for p in range(3):
                        dve.wait_ge(rows_in[t % 2][p], 16 * (t // 2 + 1))
                    s = e[:, t % 2]
                    lo = [rows[:, t % 2, p, A_W:A_W + A_H] for p in range(3)]
                    total = rows[:, t % 2, :, A_W + A_H:]
                    step(dve.tensor_tensor(s[:, 0, :], lo[0], lo[1], ALU.min))
                    step(dve.tensor_tensor(s[:, 0, :], s[:, 0, :], lo[2], ALU.min))
                    dve.tensor_tensor(s[:, 1:4, :], broadcast(s[:, 0, :], 1, 3), rows[:, t % 2, :, A_W:A_W + A_H],
                                      ALU.subtract).then_inc(diff, 1)
                    dve.wait_ge(exped, t + 1)
                    step(dve.tensor_tensor(s[:, 4:7, :], s[:, 1:4, :], total, ALU.mult))
                    step(dve.tensor_tensor(s[:, 4, :], s[:, 4, :], s[:, 5, :], ALU.add))
                    step(dve.tensor_tensor(s[:, 4, :], s[:, 4, :], s[:, 6, :], ALU.add))
                    step(dve.reciprocal(s[:, 5, :], s[:, 4, :]))
                    if t >= 2:
                        dve.wait_ge(pooled, 2 * (t - 1))
                    dve.tensor_tensor(s[:, 6:9, :], s[:, 1:4, :], broadcast(s[:, 5, :], 1, 3), ALU.mult).then_inc(factor, 1)
                    dve.wait_ge(factor, t + 1)
                    yt = y[:, t % 2, :]
                    if t >= 2:
                        dve.wait_ge(turned, t - 1)
                    dve.tensor_tensor(yt.rearrange("p (h e) -> p h e", e=DH), num(t, 0), broadcast(s[:, 6, :], 2, DH),
                                      ALU.mult).then_inc(mixed, 1)
                    dve.wait_ge(mixed, t + 1)
                    dve.wait_ge(pooled, 2 * t + 2)
                    step(dve.tensor_tensor(yt, yt, tmp[:, t % 2, 0, :], ALU.add))
                    dve.tensor_tensor(yt, yt, tmp[:, t % 2, 1, :], ALU.add).then_inc(added, 1)
                    if t >= 1:
                        store(t - 1)
                    dve.wait_ge(squared, t + 1)
                    dve.tensor_scalar(stat[:, t, 1:2], stat[:, t, 0:1], 1.0 / A_W, EPS, ALU.mult, ALU.add).then_inc(var, 1)
                    dve.wait_ge(root, t + 1)
                    step(dve.reciprocal(stat[:, t, 3:4], stat[:, t, 2:3]))
                    dve.tensor_scalar(yt, yt, stat[:, t, 3:4], None, ALU.mult).then_inc(scaled, 1)
                store(TT - 1)

            @block.tensor
            def _(pe):
                for t in range(TT):
                    pe.wait_ge(scaled, t + 1)
                    if t >= 2:
                        pe.wait_ge(out, t - 1)
                    for a in range(4):
                        last = pe.transpose(bank[t % 2][:, a * P:(a + 1) * P], y[:, t % 2, a * P:(a + 1) * P], k.ident[:, :])
                    last.then_inc(turned, 1)


def output_projection(k, name, src, chunks, next_chunks, load_x):
    with k.stage() as st:
        bank = [st.psum(f"{name}_p{i}", [P, HALF]) for i in range(4)]
        product, added = st.sem(name + "_product"), st.sem(name + "_added")
        x_in = [st.sem(f"{name}_x_in{t}") for t in range(TT)] if load_x else []
        with st.block() as block:

            @block.sync
            def _(sp):
                for i in next_chunks:
                    load_chunk(k, sp, i)
                if load_x:
                    for t in range(TT):
                        sp.dma_start(k.x[:, t, :], k.w["x"][t * P:(t + 1) * P, :]).then_inc(x_in[t], 16)

            @block.vector
            def _(dve):
                for g in range(2 * TT):
                    t, h = g // 2, g % 2
                    if load_x and h == 0:
                        dve.wait_ge(x_in[t], 16)
                    dve.wait_ge(product, g + 1)
                    part = k.x[:, t, h * HALF:(h + 1) * HALF]
                    dve.tensor_tensor(part, part, bank[g % 4][:, :], ALU.add).then_inc(added, 1)

            @block.tensor
            def _(pe):
                for g in range(2 * TT):
                    t, h = g // 2, g % 2
                    if g < 2:
                        pe.wait_ge(k.chunk_in[chunks[h]], 16)
                    if g >= 4:
                        pe.wait_ge(added, g - 3)
                    for c in range(KT):
                        last = pe.matmul(bank[g % 4][:, :], src[:, c, t * P:(t + 1) * P], k.chunk(chunks[h], HALF)[:, c, :],
                                         start=(c == 0), stop=(c == KT - 1))
                    last.then_inc(product, 1)


def memory_projections(k):
    MT = MEM // P
    with k.stage() as st:
        ring, mem, gain = (k.xqT[:, 2 * n:2 * n + 2, :] for n in range(3))
        stat = st.sbuf("xa_stat", [P, TT, 4])
        mstat = st.sbuf("mem_stat", [P, MT, 4])
        memT = st.sbuf("memT", [P, KT, MEM])
        tb = [st.psum(f"xa_turn{i}", [P, HALF]) for i in range(4)]
        gb = [st.psum(f"xa_gemm{i}", [P, HALF]) for i in range(4)]
        gain_in, mem_in = st.sem("xa_gain_in"), st.sem("mem_in")
        product, out_act, out_dve = st.sem("xa_product"), st.sem("xa_out_act"), st.sem("xa_out_dve")
        mnorm = Norm(st, "mem", MT, lambda t: mem[:, t, :], gain[:, 1, :],
                     lambda t, h: memT[:, 4 * h:4 * h + 4, t * P:(t + 1) * P], tb, ring, mstat,
                     lambda eng, t: eng.wait_ge(mem_in, 16))
        xnorm = Norm(st, "xa", TT, lambda t: k.x[:, t, :], gain[:, 0, :],
                     lambda t, h: k.xnT[:, 4 * h:4 * h + 4, t * P:(t + 1) * P], tb, ring, stat, lambda eng, t: None)
        groups = []
        for m in range(KT):
            for h in range(2):
                i = 7 + m // 4
                groups.append((lambda c, m=m, i=i: k.chunk(i, HALF)[:, c, (m % 4) * P:(m % 4 + 1) * P],
                               lambda c, h=h: k.xnT[:, c, h * HALF:(h + 1) * HALF],
                               HALF, k.xqT[:, m, h * HALF:(h + 1) * HALF], X_DH ** -0.5, i))
        for m in range(KT):
            i = 9 + m // 4
            groups.append((lambda c, m=m, i=i: k.chunk(i, HALF)[:, c, (m % 4) * P:(m % 4 + 1) * P],
                           lambda c: memT[:, c, :], MEM, k.xkT[:, m, :], 1.0, i))
        for h in range(2):
            for t in range(MT):
                groups.append((lambda c, t=t: memT[:, c, t * P:(t + 1) * P], lambda c, h=h: k.chunk(11 + h, HALF)[:, c, :],
                               HALF, k.xv[:, t, h * HALF:(h + 1) * HALF], 1.0, 11 + h))

        with st.block() as block:

            @block.sync
            def _(sp):
                sp.dma_start(mem[:, :, :], k.w["mem"].rearrange("(t p) n -> p t n", p=P)).then_inc(mem_in, 16)
                sp.dma_start(gain[:, 0, :], k.w["norm_xattn"][0:1, :].partition_broadcast(P)).then_inc(gain_in, 16)
                sp.dma_start(gain[:, 1, :], k.w["norm_mem"][0:1, :].partition_broadcast(P)).then_inc(gain_in, 16)
                load_chunk(k, sp, 9)
                load_chunk(k, sp, 10)
                for i, g in ((11, 8), (12, 16), (13, 20), (14, 24)):
                    sp.wait_ge(product, g)
                    load_chunk(k, sp, i)

            @block.scalar
            def _(act):
                mnorm.scalar(act)
                act.wait_ge(mnorm.turned, 2 * MT)
                xnorm.scalar(act)
                for g in range(0, len(groups), 2):
                    act.wait_ge(product, g + 1)
                    act.activation(groups[g][3], gb[g % 4][:, 0:groups[g][2]], ACT.Copy, scale=groups[g][4]).then_inc(out_act, 1)

            @block.vector
            def _(dve):
                dve.wait_ge(gain_in, 32)
                mnorm.vector(dve)
                xnorm.vector(dve)
                for g in range(1, len(groups), 2):
                    dve.wait_ge(product, g + 1)
                    dve.tensor_scalar(groups[g][3], gb[g % 4][:, 0:groups[g][2]], groups[g][4], None, ALU.mult).then_inc(out_dve, 1)

            @block.tensor
            def _(pe):
                mnorm.tensor(pe)
                pe.wait_ge(mnorm.evac_act, MT)
                pe.wait_ge(mnorm.evac_dve, MT)
                xnorm.tensor(pe)
                pe.wait_ge(xnorm.evac_act, TT)
                pe.wait_ge(xnorm.evac_dve, TT)
                for g, (lhs, rhs, cols, _, _, chunk) in enumerate(groups):
                    pe.wait_ge(k.chunk_in[chunk], 16)
                    if g >= 4:
                        pe.wait_ge((out_act, out_dve)[g % 2], (g - 4) // 2 + 1)
                    for c in range(KT):
                        last = pe.matmul(gb[g % 4][:, 0:cols], lhs(c), rhs(c), start=(c == 0), stop=(c == KT - 1))
                    last.then_inc(product, 1)


def memory_attention(k):
    with k.stage() as st:
        pr = st.sbuf("xa_probs", [P, 3, MEM])
        pT = st.sbuf("xa_probsT", [P, 3, MEM])
        small = st.sbuf("xa_small", [P, X_H * TT, 4])
        sb = [st.psum(f"xs{i}", [P, HALF]) for i in range(3)]
        tb = [st.psum(f"xt{i}", [P, HALF]) for i in range(2)]
        ob = [st.psum(f"xo{i}", [P, HALF]) for i in range(2)]
        scored, maxed, exped, inverse, normed, turned, pt, mixed, out = (st.sem("x_" + n) for n in (
            "scored maxed exped inverse normed turned pt mixed out").split())
        units = [(t, h) for t in range(TT) for h in range(X_H)]
        n_units = len(units)
        oT = k.xnT

        with st.block() as block:

            @block.scalar
            def _(act):
                for i in range(n_units + 3):
                    if i < n_units:
                        act.wait_ge(maxed, i + 1)
                        if i >= 3:
                            act.wait_ge(turned, i - 2)
                        act.activation(pr[:, i % 3, :], sb[i % 3][:, 0:MEM], ACT.Exp, bias=small[:, i, 0:1],
                                       accum_out=small[:, i, 1:2]).then_inc(exped, 1)
                    if i >= 3:
                        j = i - 3
                        t, h = units[j]
                        act.wait_ge(mixed, j + 1)
                        act.activation(oT[:, 2 * h:2 * h + 2, t * P:(t + 1) * P],
                                       ob[j % 2][:, 0:2 * P].rearrange("p (a b) -> p a b", a=2), ACT.Copy).then_inc(out, 1)

            @block.vector
            def _(dve):
                for i in range(n_units + 2):
                    if i < n_units:
                        dve.wait_ge(scored, i + 1)
                        dve.tensor_reduce(small[:, i, 0:1], sb[i % 3][:, 0:MEM], AX_X, ALU.max, negate=True).then_inc(maxed, 1)
                    if 1 <= i <= n_units:
                        j = i - 1
                        dve.wait_ge(exped, j + 1)
                        dve.reciprocal(small[:, j, 2:3], small[:, j, 1:2]).then_inc(inverse, 1)
                        dve.wait_ge(inverse, j + 1)
                        dve.tensor_scalar(pr[:, j % 3, :], pr[:, j % 3, :], small[:, j, 2:3], None, ALU.mult).then_inc(normed, 1)
                    if i >= 2:
                        j = i - 2
                        dve.wait_ge(turned, j + 1)
                        if j >= 3:
                            dve.wait_ge(mixed, j - 2)
                        dve.tensor_copy(pT[:, j % 3, :], tb[j % 2][:, 0:MEM]).then_inc(pt, 1)

            @block.tensor
            def _(pe):
                for i in range(n_units + 2):
                    if i < n_units:
                        t, h = units[i]
                        if i >= 3:
                            pe.wait_ge(exped, i - 2)
                        for c in range(2):
                            last = pe.matmul(sb[i % 3][:, 0:MEM], k.xqT[:, 2 * h + c, t * P:(t + 1) * P], k.xkT[:, 2 * h + c, :],
                                             start=(c == 0), stop=(c == 1))
                        last.then_inc(scored, 1)
                    if 1 <= i <= n_units:
                        j = i - 1
                        pe.wait_ge(normed, j + 1)
                        if j >= 2:
                            pe.wait_ge(pt, j - 1)
                        for c in range(2):
                            last = pe.transpose(tb[j % 2][:, c * P:(c + 1) * P], pr[:, j % 3, c * P:(c + 1) * P], k.ident[:, :])
                        last.then_inc(turned, 1)
                    if i >= 2:
                        j = i - 2
                        t, h = units[j]
                        pe.wait_ge(pt, j + 1)
                        if j >= 2:
                            pe.wait_ge(out, j - 1)
                        for e in range(2):
                            for c in range(2):
                                last = pe.matmul(ob[j % 2][:, e * P:(e + 1) * P],
                                                 k.xv[:, c, h * X_DH + e * P:h * X_DH + (e + 1) * P],
                                                 pT[:, j % 3, c * P:(c + 1) * P], start=(c == 0), stop=(c == 1))
                        last.then_inc(mixed, 1)


GROUPS = 4
GROUP_E = 8
EXPERTS = GROUPS * GROUP_E
TOP_K = 2
ROUTES = GROUPS + EXPERTS
BLOCK = 128
DE = 512
GU_K, DN_K = D // P, DE // P
EXTRA = S * TOP_K // BLOCK
BLOCKS = EXPERTS + EXTRA


def load_expert(k, queue, e, par, gu_in, dn_in):
    queue.dma_start(k.w_gu(par), k.w["expert_w_gu"][e].rearrange("(k p) n -> p k n", p=P)).then_inc(gu_in, 16)
    queue.dma_start(k.w_dn(par), k.w["expert_w_down"][e].rearrange("(k p) n -> p k n", p=P)).then_inc(dn_in, 16)


class Count:

    def __init__(self):
        self.n = 0

    def up(self):
        self.n += 1
        return self.n


def router(k):
    with k.stage() as st:
        ring = st.sbuf("ffn_scaled", [P, 2, D])
        gain = st.sbuf("ffn_gain", [P, D])
        stat = st.sbuf("ffn_stat", [P, TT, 4])
        wr = st.sbuf("router_w", [P, KT, ROUTES])
        bias = st.sbuf("router_b", [P, ROUTES])
        const = st.sbuf("route_const", [P, P + EXPERTS])
        tri, numbers = const[:, 0:P], const[:, P:]
        ones = st.sbuf("ones", [P, P])
        zero = st.sbuf("idx_zero", [P, BLOCKS * BLOCK // P], U32)
        zero_row = st.sbuf("y_zero", [P, D])
        token = st.sbuf("token_ids", [P, TT], U32)
        logit = st.sbuf("logit", [P, TT, ROUTES])
        gp = st.sbuf("group_p", [P, TT, GROUPS])
        g1 = st.sbuf("group_tmp", [P, TT, GROUPS])
        pick = st.sbuf("pick", [P, TT, GROUP_E, GROUPS])
        ep = st.sbuf("expert_p", [P, TT, GROUP_E])
        e1 = st.sbuf("expert_tmp", [P, TT, GROUP_E])
        s = st.sbuf("route_small", [P, 12, TT])
        hot = st.sbuf("hot", [P, TOP_K, TT, EXPERTS])
        both = st.sbuf("both", [P, TT, EXPERTS])
        before = st.sbuf("before", [P, TT, EXPERTS])
        total = st.sbuf("total", [P, EXPERTS])
        place = st.sbuf("place", [P, TT, EXPERTS])
        spread = st.sbuf("spread", [P, TT, EXPERTS])
        dest = st.sbuf("dest_f", [P, TOP_K, TT])
        more = st.sbuf("more", [P, EXPERTS, TT])
        tables = st.sbuf("tables", [P, 3, EXPERTS])
        extra, upto, jump = (tables[:, i, :] for i in range(3))
        zrow = st.sbuf("zero_row", [P, EXPERTS])
        past = st.sbuf("past", [1, EXTRA, EXPERTS])
        owner = st.sbuf("owner", [1, EXTRA])
        tb = [st.psum(f"ffn_turn{i}", [P, HALF]) for i in range(4)]
        lb = st.psum("logits", [P, HALF])
        rb = st.psum("ranks", [P, HALF])
        cb = st.psum("counts", [P, HALF])
        gain_in, const_in, zeroed = st.sem("ffn_gain_in"), st.sem("route_const_in"), st.sem("zeroed")
        filled, product, ranked, exped, step, shifted, marked, placed = (st.sem(n) for n in
            "filled r_product ranked exped route_step shifted marked placed".split())
        keep = [st.sem(f"xn_stored{i}") for i in range(2)]
        norm = Norm(st, "ffn", TT, lambda t: k.x[:, t, :], gain[:, :],
                    lambda t, h: k.yT[:, 4 * h:4 * h + 4, t * P:(t + 1) * P], tb, ring, stat, lambda eng, t: None, keep)
        scattered, y_zeroed = st.sem("scattered"), st.sem("y_zeroed")
        gmax, gsum, gbest, gprob, emax, esum, pair_sum, unused = (s[:, i, :] for i in range(8))
        best = [s[:, 8, :], s[:, 9, :]]
        top = [s[:, 10, :], s[:, 11, :]]
        BIG = 64.0

        with st.block() as block:

            @block.sync
            def _(sp):
                sp.dma_start(gain[:, :], k.w["norm_ffn"][0:1, :].partition_broadcast(P)).then_inc(gain_in, 16)
                sp.dma_start(wr[:, :, :], k.w["router_w"].rearrange("(k p) n -> p k n", p=P)).then_inc(const_in, 16)
                sp.dma_start(bias[:, :], k.w["router_b"][0:1, :].partition_broadcast(P)).then_inc(const_in, 16)
                sp.dma_start(const[:, :], k.w["route_const"]).then_inc(const_in, 16)
                sp.wait_ge(filled, 2)
                sp.dma_start(k.idx_dram.rearrange("(p n) o -> p (n o)", p=P), zero[:, :]).then_inc(zeroed, 16)
                sp.wait_ge(filled, 5)
                sp.dma_start(k.y_dram[EXPERTS * BLOCK:, :].rearrange("(n p) d -> p n d", p=P),
                             broadcast(zero_row[:, :], 1, EXTRA)).then_inc(y_zeroed, 16)
                for t in range(TT):
                    sp.wait_ge(norm.scaled, t + 1)
                    sp.dma_start(k.xn_dram[t * P:(t + 1) * P, :], ring[:, t % 2, :]).then_inc(keep[t % 2], 16)
                for par in range(2):
                    load_expert(k, sp, par, par, k.gu_in[par], k.dn_in[par])
                for i in range(2):
                    sp.wait_ge(keep[i], 16 * (TT // 2))
                sp.wait_ge(y_zeroed, 16)

            @block.gpsimd
            def _(pool):
                pool.memset(ones[:, :], 1.0).then_inc(filled, 1)
                pool.memset(zero[:, :], 0).then_inc(filled, 1)
                pool.memset(zrow[:, :], 0.0).then_inc(filled, 1)
                pool.iota(token[:, :], [[P, TT]], base=0, channel_multiplier=1).then_inc(filled, 1)
                pool.memset(zero_row[:, :], 0.0).then_inc(filled, 1)
                pool.wait_ge(filled, 4)
                pool.wait_ge(zeroed, 16)
                pool.wait_ge(placed, 1)
                for j in range(TOP_K):
                    for t in range(TT):
                        i = j * TT + t
                        pool.indirect_dma_start(k.idx_dram, bass.IndirectOffsetOnAxis(k.dest[:, i:i + 1], 0),
                                                token[:, t:t + 1], None).then_inc(scattered, 16)
                        pool.wait_ge(scattered, 16 * (i + 1))

            @block.scalar
            def _(act):
                norm.scalar(act)
                act.wait_ge(shifted, 1)
                act.activation(gp[:, :, :], gp[:, :, :], ACT.Exp).then_inc(exped, 1)
                act.wait_ge(shifted, 2)
                act.activation(ep[:, :, :], ep[:, :, :], ACT.Exp).then_inc(exped, 1)

            @block.tensor
            def _(pe):
                norm.tensor(pe)
                pe.wait_ge(const_in, 48)
                for t in range(TT):
                    pe.wait_ge(norm.evac_act, t + 1)
                    pe.wait_ge(norm.evac_dve, t + 1)
                    for c in range(KT):
                        last = pe.matmul(lb[:, t * ROUTES:(t + 1) * ROUTES], k.yT[:, c, t * P:(t + 1) * P], wr[:, c, :],
                                         start=(c == 0), stop=(c == KT - 1))
                    last.then_inc(product, 1)
                pe.wait_ge(filled, 1)
                pe.wait_ge(marked, 1)
                cols = TT * EXPERTS
                flat = [v[:, :, :].rearrange("p t e -> p (t e)") for v in (both, before)]
                pe.matmul(rb[:, 0:cols], tri, flat[0], start=True, stop=False)
                pe.matmul(rb[:, 0:cols], ones[:, :], flat[1], start=False, stop=True).then_inc(ranked, 1)
                pe.matmul(cb[:, 0:EXPERTS], ones[:, :], total[:, :], start=True, stop=True).then_inc(ranked, 1)

            @block.vector
            def _(dve):
                n = Count()

                def first_index(p, top_p, width, tmp, out):
                    dve.tensor_tensor(tmp, p, broadcast(top_p, 2, width), ALU.is_equal).then_inc(step, 1)
                    dve.wait_ge(step, n.up())
                    dve.scalar_tensor_tensor(out=tmp, in0=tmp, scalar=-BIG, in1=broadcast(numbers[:, 0:width], 1, TT),
                                             op0=ALU.mult, op1=ALU.add).then_inc(step, 1)
                    dve.wait_ge(step, n.up())
                    dve.tensor_reduce(out, tmp, AX_X, ALU.min).then_inc(step, 1)
                    dve.wait_ge(step, n.up())
                    dve.tensor_scalar(out, out, BIG, None, ALU.add).then_inc(step, 1)
                    dve.wait_ge(step, n.up())

                dve.wait_ge(gain_in, 16)
                norm.vector(dve)
                dve.wait_ge(const_in, 48)
                dve.wait_ge(product, TT)
                dve.tensor_tensor(logit[:, :, :], lb[:, 0:TT * ROUTES].rearrange("p (t n) -> p t n", n=ROUTES),
                                  broadcast(bias[:, :], 1, TT), ALU.add).then_inc(step, 1)
                dve.wait_ge(step, n.up())
                dve.tensor_reduce(gmax, logit[:, :, 0:GROUPS], AX_X, ALU.max).then_inc(step, 1)
                dve.wait_ge(step, n.up())
                dve.tensor_tensor(gp[:, :, :], logit[:, :, 0:GROUPS], broadcast(gmax, 2, GROUPS), ALU.subtract)\
                    .then_inc(shifted, 1)
                dve.wait_ge(exped, 1)
                dve.tensor_reduce(gsum, gp[:, :, :], AX_X, ALU.add).then_inc(step, 1)
                dve.wait_ge(step, n.up())
                dve.reciprocal(gsum, gsum).then_inc(step, 1)
                dve.wait_ge(step, n.up())
                dve.tensor_tensor(gp[:, :, :], gp[:, :, :], broadcast(gsum, 2, GROUPS), ALU.mult).then_inc(step, 1)
                dve.wait_ge(step, n.up())
                dve.tensor_reduce(gprob, gp[:, :, :], AX_X, ALU.max).then_inc(step, 1)
                dve.wait_ge(step, n.up())
                first_index(gp[:, :, :], gprob, GROUPS, g1[:, :, :], gbest)
                dve.tensor_tensor(g1[:, :, :], broadcast(numbers[:, 0:GROUPS], 1, TT), broadcast(gbest, 2, GROUPS),
                                  ALU.is_equal).then_inc(step, 1)
                dve.wait_ge(step, n.up())
                dve.tensor_tensor(pick[:, :, :, :], logit[:, :, GROUPS:].rearrange("p t (g j) -> p t j g", g=GROUPS),
                                  broadcast(g1[:, :, :], 2, GROUP_E), ALU.mult).then_inc(step, 1)
                dve.wait_ge(step, n.up())
                dve.tensor_reduce(ep[:, :, :], pick[:, :, :, :], AX_X, ALU.add).then_inc(step, 1)
                dve.wait_ge(step, n.up())
                dve.tensor_reduce(emax, ep[:, :, :], AX_X, ALU.max).then_inc(step, 1)
                dve.wait_ge(step, n.up())
                dve.tensor_tensor(ep[:, :, :], ep[:, :, :], broadcast(emax, 2, GROUP_E), ALU.subtract).then_inc(shifted, 1)
                dve.wait_ge(exped, 2)
                dve.tensor_reduce(esum, ep[:, :, :], AX_X, ALU.add).then_inc(step, 1)
                dve.wait_ge(step, n.up())
                dve.reciprocal(esum, esum).then_inc(step, 1)
                dve.wait_ge(step, n.up())
                dve.tensor_tensor(ep[:, :, :], ep[:, :, :], broadcast(esum, 2, GROUP_E), ALU.mult).then_inc(step, 1)
                dve.wait_ge(step, n.up())
                for j in range(TOP_K):
                    dve.tensor_reduce(top[j], ep[:, :, :], AX_X, ALU.max).then_inc(step, 1)
                    dve.wait_ge(step, n.up())
                    first_index(ep[:, :, :], top[j], GROUP_E, e1[:, :, :], best[j])
                    if j == 0:
                        dve.tensor_tensor(e1[:, :, :], broadcast(numbers[:, 0:GROUP_E], 1, TT),
                                          broadcast(best[0], 2, GROUP_E), ALU.is_equal).then_inc(step, 1)
                        dve.wait_ge(step, n.up())
                        dve.scalar_tensor_tensor(out=ep[:, :, :], in0=e1[:, :, :], scalar=-2.0, in1=ep[:, :, :],
                                                 op0=ALU.mult, op1=ALU.add).then_inc(step, 1)
                        dve.wait_ge(step, n.up())
                for j in range(TOP_K):
                    dve.scalar_tensor_tensor(out=best[j], in0=gbest, scalar=float(GROUP_E), in1=best[j],
                                             op0=ALU.mult, op1=ALU.add).then_inc(step, 1)
                    dve.wait_ge(step, n.up())
                    dve.tensor_tensor(hot[:, j, :, :], broadcast(numbers, 1, TT), broadcast(best[j], 2, EXPERTS),
                                      ALU.is_equal).then_inc(step, 1)
                    dve.wait_ge(step, n.up())
                dve.tensor_tensor(both[:, :, :], hot[:, 0, :, :], hot[:, 1, :, :], ALU.add).then_inc(step, 1)
                dve.wait_ge(step, n.up())
                dve.tensor_scalar(before[:, 0, :], both[:, 0, :], 0.0, None, ALU.mult).then_inc(step, 1)
                dve.wait_ge(step, n.up())
                for t in range(1, TT):
                    dve.tensor_tensor(before[:, t, :], before[:, t - 1, :], both[:, t - 1, :], ALU.add).then_inc(step, 1)
                    dve.wait_ge(step, n.up())
                dve.tensor_tensor(total[:, :], before[:, TT - 1, :], both[:, TT - 1, :], ALU.add).then_inc(marked, 1)
                dve.tensor_tensor(pair_sum, top[0], top[1], ALU.add).then_inc(step, 1)
                dve.wait_ge(step, n.up())
                dve.reciprocal(pair_sum, pair_sum).then_inc(step, 1)
                dve.wait_ge(step, n.up())
                for j in range(TOP_K):
                    dve.tensor_tensor(top[j], top[j], gprob, ALU.mult).then_inc(step, 1)
                    dve.wait_ge(step, n.up())
                    dve.tensor_tensor(k.gate[:, j * TT:(j + 1) * TT], top[j], pair_sum, ALU.mult).then_inc(step, 1)
                    dve.wait_ge(step, n.up())
                dve.wait_ge(ranked, 2)
                dve.wait_ge(filled, 3)
                for j in range(1, TT):
                    dve.tensor_scalar(more[:, :, j - 1], cb[:, 0:EXPERTS], float(BLOCK * j), None, ALU.is_gt).then_inc(step, 1)
                    n.up()
                dve.wait_ge(step, n.n)
                dve.tensor_reduce(extra, more[:, :, 0:TT - 1], AX_X, ALU.add).then_inc(step, 1)
                dve.wait_ge(step, n.up())
                dve.tensor_tensor_scan(upto, extra, zrow[:, :], 0.0, ALU.add, ALU.add).then_inc(step, 1)
                dve.wait_ge(step, n.up())
                dve.tensor_tensor(jump, upto, extra, ALU.subtract).then_inc(step, 1)
                dve.wait_ge(step, n.up())
                dve.scalar_tensor_tensor(out=jump, in0=jump, scalar=float(EXPERTS - 1), in1=numbers, op0=ALU.add,
                                         op1=ALU.subtract).then_inc(step, 1)
                dve.wait_ge(step, n.up())
                ranks = rb[:, 0:TT * EXPERTS].rearrange("p (t e) -> p t e", e=EXPERTS)
                dve.tensor_scalar(place[:, :, :], ranks, float(BLOCK), None, ALU.is_ge).then_inc(step, 1)
                dve.wait_ge(step, n.up())
                dve.tensor_tensor(place[:, :, :], place[:, :, :], broadcast(jump, 1, TT), ALU.mult).then_inc(step, 1)
                dve.wait_ge(step, n.up())
                dve.tensor_tensor(place[:, :, :], place[:, :, :], broadcast(numbers, 1, TT), ALU.add).then_inc(step, 1)
                dve.wait_ge(step, n.up())
                dve.scalar_tensor_tensor(out=place[:, :, :], in0=place[:, :, :], scalar=float(BLOCK), in1=ranks,
                                         op0=ALU.mult, op1=ALU.add).then_inc(step, 1)
                dve.wait_ge(step, n.up())
                for j in range(TOP_K):
                    dve.tensor_tensor(spread[:, :, :], hot[:, j, :, :], place[:, :, :], ALU.mult).then_inc(step, 1)
                    dve.wait_ge(step, n.up())
                    dve.tensor_reduce(dest[:, j, :], spread[:, :, :], AX_X, ALU.add).then_inc(step, 1)
                    dve.wait_ge(step, n.up())
                dve.tensor_copy(k.dest[:, :], dest[:, :, :].rearrange("p j t -> p (j t)")).then_inc(placed, 1)
                dve.tensor_tensor(past[:, :, :], broadcast(upto[0:1, :], 1, EXTRA), broadcast(numbers[0:1, 0:EXTRA], 2, EXPERTS),
                                  ALU.is_le).then_inc(step, 1)
                dve.wait_ge(step, n.up())
                dve.tensor_reduce(owner[:, :], past[:, :, :], AX_X, ALU.add).then_inc(step, 1)
                dve.wait_ge(step, n.up())
                dve.tensor_copy(k.plan[:, 0:EXTRA], owner[:, :]).then_inc(step, 1)
                dve.tensor_copy(k.plan[:, EXTRA:EXTRA + 1], upto[0:1, EXPERTS - 1:EXPERTS]).then_inc(step, 1)


def expert_products(pe, k, gate_up, gate_bank, up_bank, half):
    for bank, first in ((gate_bank, 0), (up_bank, DE)):
        for m in range(2):
            col = first + (2 * half + m) * P
            for c in range(GU_K):
                last = pe.matmul(bank[:, m * BLOCK:(m + 1) * BLOCK], gate_up[:, c, col:col + P], k.xT[:, c, :],
                                 start=(c == 0), stop=(c == GU_K - 1))
    return last


def down_products(pe, k, down, bank, half):
    for c in range(DN_K):
        last = pe.matmul(bank[:, :], k.hT[:, c, :], down[:, c, half * HALF:(half + 1) * HALF],
                         start=(c == 0), stop=(c == DN_K - 1))
    return last


def turn_block(pe, k, rows, bank, half):
    for a in range(4):
        c = 4 * half + a
        last = pe.transpose(bank[:, a * P:(a + 1) * P], rows[:, c * P:(c + 1) * P], k.ident[:, :])
    return last


def experts(k):
    with k.stage() as st:
        flat = k.yT[:, :, :].rearrange("p a b -> p (a b)")
        rows = [flat[:, i * D:(i + 1) * D] for i in range(2)]
        y = [flat[:, (2 + i) * D:(3 + i) * D] for i in range(2)]
        k.xT = flat[:, 4 * D:5 * D].rearrange("p (c n) -> p c n", c=GU_K)
        k.hT = flat[:, 5 * D:5 * D + DN_K * BLOCK].rearrange("p (c n) -> p c n", c=DN_K)
        act_gate = flat[:, 6 * D:6 * D + DN_K * BLOCK].rearrange("p (c n) -> p c n", c=DN_K)
        index = st.sbuf("block_index", [P, 2], U32)
        indices = st.sbuf("indices", [P, EXPERTS], U32)
        ab = [st.psum(f"gate_bank{i}", [P, HALF]) for i in range(2)]
        bb = [st.psum(f"up_bank{i}", [P, HALF]) for i in range(2)]
        tb = [st.psum(f"turn_bank{i}", [P, HALF]) for i in range(2)]
        yb = [st.psum(f"down_bank{i}", [P, HALF]) for i in range(2)]
        gathered = [st.sem(f"gathered{i}") for i in range(2)]
        y_stored = [st.sem(f"y_stored{i}") for i in range(2)]
        issued = st.sem("e_issued")
        (index_in, index_set, turned, x_act, x_dve, hidden, silued, h_done, y_made, y_act, y_dve) = (
            st.sem("e_" + n) for n in "index_in index_set turned x_act x_dve hidden silued h_done y_made y_act y_dve".split())
        GROUP_COLS = 2 * BLOCK

        def half_view(tile, half):
            return tile[:, 2 * half:2 * half + 2, :].rearrange("p a b -> p (a b)")

        with st.block() as block:

            @block.sync
            def _(sp):
                sp.dma_start(indices[:, :], k.idx_dram[0:EXPERTS * BLOCK, :].rearrange("(e r) o -> r (e o)", r=BLOCK),
                             allow_slow_non_contiguous=True).then_inc(index_in, 16)

                def one(i, par, last):
                    e = 2 * i + par
                    if not last:
                        sp.wait_ge(hidden, 2 * e + 2)
                        sp.dma_start(k.w_gu(par), k.w["expert_w_gu"][bass.ds(e + 2, 1)].rearrange(
                            "a (k p) n -> p (a k) n", p=P)).then_inc(k.gu_in[par], 16)
                        sp.wait_ge(y_made, 2 * e + 2)
                        sp.dma_start(k.w_dn(par), k.w["expert_w_down"][bass.ds(e + 2, 1)].rearrange(
                            "a (k p) n -> p (a k) n", p=P)).then_inc(k.dn_in[par], 16)
                    sp.wait_ge(y_act, e + 1)
                    sp.wait_ge(y_dve, e + 1)
                    sp.dma_start(k.y_dram[bass.ds(e * BLOCK, BLOCK), :], y[par]).then_inc(y_stored[par], 16)

                with sp.Fori(0, EXPERTS // 2 - 1) as i:
                    for par in range(2):
                        one(i, par, False)
                for par in range(2):
                    one(EXPERTS // 2 - 1, par, True)
                for par in range(2):
                    sp.wait_ge(y_stored[par], 16 * (EXPERTS // 2))

            @block.gpsimd
            def _(pool):
                def one(i, par, first):
                    e = 2 * i + par
                    if not first:
                        pool.wait_ge(turned, 2 * e - 2)
                    pool.tensor_copy(index[:, par:par + 1], indices[:, bass.ds(e, 1)]).then_inc(index_set, 1)
                    pool.wait_ge(index_set, e + 1)
                    pool.sem_inc(issued, 1)
                    pool.indirect_dma_start(rows[par], None, k.xn_dram,
                                            bass.IndirectOffsetOnAxis(index[:, par:par + 1], 0)).then_inc(gathered[par], 16)

                pool.wait_ge(index_in, 16)
                for par in range(2):
                    one(0, par, True)
                with pool.Fori(1, EXPERTS // 2) as i:
                    for par in range(2):
                        one(i, par, False)

            @block.scalar
            def _(act):
                def x_out(e):
                    act.wait_ge(turned, 2 * e + 1)
                    act.activation(k.xT[:, 0:4, :].rearrange("p a b -> p (a b)"), tb[0][:, :], ACT.Copy).then_inc(x_act, 1)

                def one(i, par, first, last):
                    e = 2 * i + par
                    for half in range(2):
                        act.wait_ge(hidden, 2 * e + half + 1)
                        act.activation(half_view(act_gate, half), ab[half][:, 0:GROUP_COLS], ACT.Silu).then_inc(silued, 1)
                    if not last:
                        x_out(e + 1)
                    act.wait_ge(y_made, 2 * e + 1)
                    if not first:
                        act.wait_ge(y_stored[par], 16 * i)
                    act.activation(y[par][:, 0:HALF], yb[0][:, :], ACT.Copy).then_inc(y_act, 1)

                x_out(0)
                for par in range(2):
                    one(0, par, True, False)
                with act.Fori(1, EXPERTS // 2 - 1) as i:
                    for par in range(2):
                        one(i, par, False, False)
                for par in range(2):
                    one(EXPERTS // 2 - 1, par, False, par == 1)

            @block.vector
            def _(dve):
                def x_out(e):
                    dve.wait_ge(turned, 2 * e + 2)
                    dve.tensor_copy(k.xT[:, 4:8, :].rearrange("p a b -> p (a b)"), tb[1][:, :]).then_inc(x_dve, 1)

                def one(i, par, first, last):
                    e = 2 * i + par
                    for half in range(2):
                        dve.wait_ge(silued, 2 * e + half + 1)
                        dve.tensor_tensor(half_view(k.hT, half), half_view(act_gate, half), bb[half][:, 0:GROUP_COLS],
                                          ALU.mult).then_inc(h_done, 1)
                    if not last:
                        x_out(e + 1)
                    dve.wait_ge(y_made, 2 * e + 2)
                    if not first:
                        dve.wait_ge(y_stored[par], 16 * i)
                    dve.tensor_copy(y[par][:, HALF:], yb[1][:, :]).then_inc(y_dve, 1)

                x_out(0)
                for par in range(2):
                    one(0, par, True, False)
                with dve.Fori(1, EXPERTS // 2 - 1) as i:
                    for par in range(2):
                        one(i, par, False, False)
                for par in range(2):
                    one(EXPERTS // 2 - 1, par, False, par == 1)

            @block.tensor
            def _(pe):
                def turn(i, par):
                    pe.wait_ge(gathered[par], 16 * (i + 1))
                    for half in range(2):
                        turn_block(pe, k, rows[par], tb[half], half).then_inc(turned, 1)

                def one(i, par, first, last):
                    e = 2 * i + par
                    pe.wait_ge(k.gu_in[par], 16 * (i + 1))
                    pe.wait_ge(x_act, e + 1)
                    pe.wait_ge(x_dve, e + 1)
                    for half in range(2):
                        expert_products(pe, k, k.w_gu(par), ab[half], bb[half], half).then_inc(hidden, 1)
                    if not last:
                        turn(i + par, 1 - par)
                    pe.wait_ge(k.dn_in[par], 16 * (i + 1))
                    pe.wait_ge(h_done, 2 * e + 2)
                    for half in range(2):
                        if not first or par:
                            pe.wait_ge((y_act, y_dve)[half], e)
                        down_products(pe, k, k.w_dn(par), yb[half], half).then_inc(y_made, 1)

                turn(0, 0)
                for par in range(2):
                    one(0, par, True, False)
                with pe.Fori(1, EXPERTS // 2 - 1) as i:
                    for par in range(2):
                        one(i, par, False, False)
                for par in range(2):
                    one(EXPERTS // 2 - 1, par, False, par == 1)

    extra_blocks(k)


def extra_blocks(k):
    with k.stage() as st:
        flat = k.yT[:, :, :].rearrange("p a b -> p (a b)")
        rows, y = flat[:, 0:D], flat[:, 2 * D:3 * D]
        act_gate = flat[:, 6 * D:6 * D + DN_K * BLOCK].rearrange("p (c n) -> p c n", c=DN_K)
        index = st.sbuf("extra_index", [P, 1], U32)
        ab = [st.psum(f"extra_gate{i}", [P, HALF]) for i in range(2)]
        bb = [st.psum(f"extra_up{i}", [P, HALF]) for i in range(2)]
        tb = [st.psum(f"extra_turn{i}", [P, HALF]) for i in range(2)]
        yb = [st.psum(f"extra_down{i}", [P, HALF]) for i in range(2)]
        issued, finished = st.sem("extra_issued"), st.sem("extra_finished")
        (weights_in, index_in, gathered, turned, x_act, x_dve, hidden, silued, h_done, y_made, y_act, y_dve, stored) = (
            st.sem("extra_" + n) for n in ("weights_in index_in gathered turned x_act x_dve hidden silued h_done y_made y_act "
                                       "y_dve stored").split())

        def half_view(tile, half):
            return tile[:, 2 * half:2 * half + 2, :].rearrange("p a b -> p (a b)")

        def listed(eng, body):
            n = eng.value_load(k.plan[0:1, EXTRA:EXTRA + 1], min_val=0, max_val=EXTRA)
            with eng.If(n > 0):
                with eng.Fori(0, n) as b:
                    body(b)

        with st.block() as block:

            @block.sync
            def _(sp):
                def body(b):
                    e = sp.value_load(k.plan[0:1, bass.ds(b, 1)], min_val=0, max_val=EXPERTS - 1)
                    sp.dma_start(index[:, :], k.idx_dram[bass.ds(EXPERTS * BLOCK + b * BLOCK, BLOCK), :]).then_inc(index_in, 16)
                    sp.dma_start(k.w_gu(0), k.w["expert_w_gu"][bass.ds(e, 1)].rearrange(
                        "a (k p) n -> p (a k) n", p=P)).then_inc(weights_in, 16)
                    sp.dma_start(k.w_dn(0), k.w["expert_w_down"][bass.ds(e, 1)].rearrange(
                        "a (k p) n -> p (a k) n", p=P)).then_inc(weights_in, 16)
                    done, all_stored = sp.snap(b + 1), sp.snap(16 * b + 16)
                    sp.wait_ge(y_act, done)
                    sp.wait_ge(y_dve, done)
                    sp.dma_start(k.y_dram[bass.ds(EXPERTS * BLOCK + b * BLOCK, BLOCK), :], y).then_inc(stored, 16)
                    sp.wait_ge(stored, all_stored)
                    sp.sem_inc(finished, 1)

                listed(sp, body)

            @block.gpsimd
            def _(pool):
                def body(b):
                    pool.wait_ge(index_in, 16 * (b + 1))
                    pool.sem_inc(issued, 1)
                    pool.indirect_dma_start(rows, None, k.xn_dram,
                                            bass.IndirectOffsetOnAxis(index[:, :], 0)).then_inc(gathered, 16)

                listed(pool, body)

            @block.scalar
            def _(act):
                def body(b):
                    act.wait_ge(turned, 2 * b + 1)
                    act.activation(k.xT[:, 0:4, :].rearrange("p a b -> p (a b)"), tb[0][:, :], ACT.Copy).then_inc(x_act, 1)
                    for half in range(2):
                        act.wait_ge(hidden, 2 * b + half + 1)
                        act.activation(half_view(act_gate, half), ab[half][:, 0:2 * BLOCK], ACT.Silu).then_inc(silued, 1)
                    act.wait_ge(y_made, 2 * b + 1)
                    act.activation(y[:, 0:HALF], yb[0][:, :], ACT.Copy).then_inc(y_act, 1)

                listed(act, body)

            @block.vector
            def _(dve):
                def body(b):
                    dve.wait_ge(turned, 2 * b + 2)
                    dve.tensor_copy(k.xT[:, 4:8, :].rearrange("p a b -> p (a b)"), tb[1][:, :]).then_inc(x_dve, 1)
                    for half in range(2):
                        dve.wait_ge(silued, 2 * b + half + 1)
                        dve.tensor_tensor(half_view(k.hT, half), half_view(act_gate, half), bb[half][:, 0:2 * BLOCK],
                                          ALU.mult).then_inc(h_done, 1)
                    dve.wait_ge(y_made, 2 * b + 2)
                    dve.tensor_copy(y[:, HALF:], yb[1][:, :]).then_inc(y_dve, 1)

                listed(dve, body)

            @block.tensor
            def _(pe):
                def body(b):
                    pe.wait_ge(gathered, 16 * (b + 1))
                    for half in range(2):
                        turn_block(pe, k, rows, tb[half], half).then_inc(turned, 1)
                    pe.wait_ge(weights_in, 32 * (b + 1))
                    pe.wait_ge(x_act, b + 1)
                    pe.wait_ge(x_dve, b + 1)
                    for half in range(2):
                        expert_products(pe, k, k.w_gu(0), ab[half], bb[half], half).then_inc(hidden, 1)
                    pe.wait_ge(h_done, 2 * b + 2)
                    for half in range(2):
                        down_products(pe, k, k.w_dn(0), yb[half], half).then_inc(y_made, 1)

                listed(pe, body)


def combine(k):
    with k.stage() as st:
        flat = k.yT[:, :, :].rearrange("p a b -> p (a b)")
        SLOTS_Y = 4
        rows = [[k.ring[:, (2 * i + j) * D:(2 * i + j + 1) * D] for j in range(TOP_K)] for i in range(SLOTS_Y)]
        result = [flat[:, i * D:(i + 1) * D] for i in range(2)]
        gain = flat[:, 2 * D:3 * D]
        square = flat[:, 3 * D:4 * D]
        stat = st.sbuf("final_stat", [P, TT, 4])
        gain_in = st.sem("final_gain_in")
        gathered = [[st.sem(f"y_in{i}_{j}") for j in range(TOP_K)] for i in range(SLOTS_Y)]
        stored = [st.sem(f"out_stored{i}") for i in range(2)]
        added, squared, variance, root, inverse, ready = (
            st.sem("c_" + n) for n in "added squared variance root inverse ready".split())

        with st.block() as block:

            @block.gpsimd
            def _(pool):
                for t in range(TT):
                    if t >= SLOTS_Y:
                        pool.wait_ge(added, 2 * (t - SLOTS_Y) + 2)
                    for j in range(TOP_K):
                        i = j * TT + t
                        pool.indirect_dma_start(rows[t % SLOTS_Y][j], None, k.y_dram,
                                                bass.IndirectOffsetOnAxis(k.dest[:, i:i + 1], 0)).then_inc(
                            gathered[t % SLOTS_Y][j], 16)

            @block.vector
            def _(dve):
                dve.wait_ge(gain_in, 16)
                for t in range(TT + 2):
                    if t < TT:
                        for j in range(TOP_K):
                            dve.wait_ge(gathered[t % SLOTS_Y][j], 16 * (t // SLOTS_Y + 1))
                            if j:
                                dve.wait_ge(added, 2 * t + 1)
                            dve.scalar_tensor_tensor(out=k.x[:, t, :], in0=rows[t % SLOTS_Y][j],
                                                     scalar=k.gate[:, j * TT + t:j * TT + t + 1], in1=k.x[:, t, :],
                                                     op0=ALU.mult, op1=ALU.add).then_inc(added, 1)
                    if 1 <= t <= TT:
                        u = t - 1
                        dve.wait_ge(squared, u + 1)
                        dve.tensor_scalar(stat[:, u, 1:2], stat[:, u, 0:1], 1.0 / D, EPS, ALU.mult,
                                          ALU.add).then_inc(variance, 1)
                    if t >= 2:
                        u = t - 2
                        dve.wait_ge(root, u + 1)
                        dve.reciprocal(stat[:, u, 3:4], stat[:, u, 2:3]).then_inc(inverse, 1)
                        dve.wait_ge(inverse, u + 1)
                        if u >= 2:
                            dve.wait_ge(stored[u % 2], 16 * (u // 2))
                        dve.scalar_tensor_tensor(out=result[u % 2], in0=k.x[:, u, :], scalar=stat[:, u, 3:4], in1=gain,
                                                 op0=ALU.mult, op1=ALU.mult).then_inc(ready, 1)

            @block.scalar
            def _(act):
                for t in range(TT + 1):
                    if t < TT:
                        act.wait_ge(added, 2 * t + 2)
                        if t:
                            act.wait_ge(squared, t)
                        act.activation(square, k.x[:, t, :], ACT.Square, accum_out=stat[:, t, 0:1]).then_inc(squared, 1)
                    if t >= 1:
                        act.wait_ge(variance, t)
                        act.activation(stat[:, t - 1, 2:3], stat[:, t - 1, 1:2], ACT.Sqrt).then_inc(root, 1)

            @block.sync
            def _(sp):
                sp.dma_start(gain, k.w["final_norm"][0:1, :].partition_broadcast(P)).then_inc(gain_in, 16)
                for t in range(TT):
                    sp.wait_ge(ready, t + 1)
                    sp.dma_start(k.out[t * P:(t + 1) * P, :], result[t % 2]).then_inc(stored[t % 2], 16)
                for i in range(2):
                    sp.wait_ge(stored[i], 16 * (TT // 2))


class Core:
    pass


class Stage:

    def __init__(self, nc, ident):
        self.nc, self.ident, self.held, self.sems = nc, ident, ExitStack(), []

    def __enter__(self):
        return self

    def __exit__(self, *what):
        self.held.close()
        self.nc.clear_and_free_semaphores(self.sems)
        self.nc.all_engine_barrier()

    def sbuf(self, name, shape, dt=F32):
        return self.held.enter_context(self.nc.sbuf_tensor(name, shape, dt))

    def psum(self, name, shape, dt=F32):
        return self.held.enter_context(self.nc.psum_tensor(name, shape, dt))

    def sem(self, name):
        self.sems.append(self.nc.alloc_semaphore(name))
        return self.sems[-1]

    def block(self):
        return self.nc.Block()


def build(nc, w, out):
    k = Core()
    k.w, k.out, k.nc = w, out, nc
    with ExitStack() as ctx:
        def sbuf(name, shape, dt=F32):
            return ctx.enter_context(nc.sbuf_tensor(name, shape, dt))

        k.ident = sbuf("ident", [P, P])
        k.vec = sbuf("vec", [P, VEC_N])
        k.stage = lambda: Stage(nc, k.ident)
        k.ring = sbuf("weights", [P, SLOTS * SLOT])
        k.xnT = k.ring[:, 4 * SLOT:6 * SLOT].rearrange("p (k n) -> p k n", k=KT)
        w_in = w["w_in"]
        k.chunks = [(w_in[:, COL_UO:COL_GATE], HALF), (w_in[:, COL_GATE:COL_Q], 264), (w_in[:, COL_Q:COL_K], HALF),
                    (w_in[:, COL_K:COL_V], HALF), (w_in[:, COL_V:], HALF)]
        k.chunks += [(w["w_out"][:, h * HALF:(h + 1) * HALF], HALF) for h in range(2)]
        k.chunks += [(w["xattn_w_q"][:, h * HALF:(h + 1) * HALF], HALF) for h in range(2)]
        k.chunks += [(w["xattn_w_kv"][:, h * HALF:(h + 1) * HALF], HALF) for h in range(4)]
        k.chunks += [(w["xattn_w_o"][:, h * HALF:(h + 1) * HALF], HALF) for h in range(2)]
        k.chunk_in = [ctx.enter_context(nc.semaphore(f"chunk_in{i}")) for i in range(len(k.chunks))]
        k.chunk = lambda i, n: k.ring[:, (i % 4) * SLOT:(i % 4) * SLOT + KT * n].rearrange("p (k n) -> p k n", k=KT)
        k.v_dram = nc.dram_tensor("v_dram", [S, A_W], F32, kind="Internal").ap()
        k.attn_dram = nc.dram_tensor("attn_dram", [3, S, O_W], F32, kind="Internal").ap()
        k.yT = sbuf("yT", [P, KT, S])
        with ExitStack() as mixers:
            def mixer(name, shape):
                return mixers.enter_context(nc.sbuf_tensor(name, shape, F32))

            k.qT = mixer("qT", [P, 4, S])
            k.kT = mixer("kT", [P, 4, S])
            with ExitStack() as small:
                def small_mixer(name, shape):
                    return small.enter_context(nc.sbuf_tensor(name, shape, F32))

                k.uP = small_mixer("uP", [P, 2, 3 + S])
                k.oT = small_mixer("oT", [P, 2, S])
                k.s_in = small_mixer("s_in", [P, S5_G, S5_L, S5_C])
                k.gateT = small_mixer("gateT", [2 * M_H, S])
                in_projection(k)
                mlstm(k)
                s5(k)
            attention(k)
            join_patterns(k)
        k.x = sbuf("x_residual", [P, TT, D])
        output_projection(k, "mix_out", k.yT, (5, 6), (), True)
        with ExitStack() as cross:
            k.xqT = k.yT
            k.xkT = cross.enter_context(nc.sbuf_tensor("xkT", [P, KT, MEM], F32))
            k.xv = cross.enter_context(nc.sbuf_tensor("xv", [P, MEM // P, D], F32))
            memory_projections(k)
            memory_attention(k)
        output_projection(k, "xa_out", k.xnT, (13, 14), (), False)
        k.w_gu = lambda par: k.ring[:, 3 * par * SLOT:(3 * par + 2) * SLOT].rearrange("p (k n) -> p k n", k=GU_K)
        k.w_dn = lambda par: k.ring[:, (3 * par + 2) * SLOT:(3 * par + 3) * SLOT].rearrange("p (k n) -> p k n", k=DN_K)
        k.gu_in = [ctx.enter_context(nc.semaphore(f"gu_in{i}")) for i in range(2)]
        k.dn_in = [ctx.enter_context(nc.semaphore(f"dn_in{i}")) for i in range(2)]
        k.gate = sbuf("gate", [P, TOP_K * TT])
        k.dest = sbuf("dest", [P, TOP_K * TT], U32)
        k.plan = sbuf("plan", [1, EXTRA + 1], I32)
        k.idx_dram = nc.dram_tensor("idx_dram", [BLOCKS * BLOCK, 1], U32, kind="Internal").ap()
        k.xn_dram = nc.dram_tensor("xn_dram", [S, D], F32, kind="Internal").ap()
        k.y_dram = nc.dram_tensor("y_dram", [BLOCKS * BLOCK, D], F32, kind="Internal").ap()
        router(k)
        experts(k)
        combine(k)


def attention_bias(table):
    def bucket(dist):
        large = 16 + (np.log(np.maximum(dist, 1) / 16) / np.log(2048 / 16) * 16).astype(np.int32)
        return np.where(dist < 16, dist, np.minimum(large, 31))

    i, j = np.arange(BLK)[:, None], np.arange(2 * BLK)[None, :]
    off = BLK + i - j
    parts = []
    for window, dil in PATTERNS[:2]:
        band = (off >= 0) & (off <= window // dil)
        parts.append(np.where(band[:, None], table[bucket(np.maximum(off, 0) * dil)].transpose(0, 2, 1), np.float32(NEG)))
    i, j = np.arange(BLK)[:, None], np.arange(BLK)[None, :]
    off = i // 2 - j // 2
    band = (off >= 0) & (i % 2 == j % 2)
    parts.append(np.where(band[:, None], table[bucket(np.maximum(off, 0) * PATTERNS[2][1])].transpose(0, 2, 1), np.float32(NEG)))
    return np.concatenate(parts, axis=2).astype(np.float32)


def kernel(**inputs):
    import concourse.bacc as bacc
    from concourse.bass_utils import run_bass_kernel_spmd as run

    a = {n: np.ascontiguousarray(v) for n, v in inputs.items()}
    data = {"x": a["x"][0], "mem": a["mem"][0], "norm_mix": a["norm_mix"], "w_in": a["w_in"][0]}
    for n in ("w_out", "xattn_w_q", "xattn_w_kv", "xattn_w_o", "s5_w_glu", "expert_w_gu", "expert_w_down"):
        data[n] = a[n][0]
    for n in ("norm_xattn", "norm_mem", "norm_ffn", "s5_b_glu"):
        data[n] = a[n]
    data["final_norm"] = a["final_norm"][None]

    def channels(v, n):
        return v.reshape(n, P).T

    def pairs(v):
        return v.reshape(S5_G // 2, 2, 64).transpose(1, 2, 0).reshape(P, S5_G // 2)

    gate_b = np.zeros((P, 1), np.float32)
    gate_b[0:2 * M_H, 0] = a["mlstm_gate_bias"][0]
    data["vec"] = np.concatenate([
        a["mlstm_conv_w"][0].reshape(4, 2, P).transpose(2, 1, 0).reshape(P, 8), channels(a["mlstm_conv_b"][0], 2),
        channels(a["mlstm_norm"][0], 2), channels(a["mlstm_skip"][0], 2), channels(a["s5_out_norm"][0], 2),
        channels(a["attn_out_norm"][0], 4), gate_b, pairs(a["s5_a_re"][0]), pairs(a["s5_a_im"][0]),
        pairs(np.broadcast_to(a["s5_log_dt"][0][:, None], (S5_G, 64))),
        np.where(np.arange(P) < 64, 1.0, -1.0).astype(np.float32)[:, None]], axis=1)
    mw = np.zeros((2, DH, 2, 3, 2, DH), np.float32)
    for i, n in enumerate(("mlstm_wq", "mlstm_wk", "mlstm_wv")):
        for h in range(M_H):
            mw[h % 2, :, h // 2, i, h % 2, :] = a[n][0, h]
    data["mlstm_w"] = mw.reshape(P, 2, 3, P)

    def pair_rows(v):
        return v.reshape(S5_G // 2, 2, 64, S5_C).transpose(1, 2, 0, 3).reshape(P, S5_G // 2, S5_C)

    data["attn_bias"] = attention_bias(a["rel_bias"])
    data["s5_bc"] = np.stack([pair_rows(a["s5_b_re"][0]), pair_rows(a["s5_b_im"][0]),
                              pair_rows(a["s5_c_re"][0].transpose(0, 2, 1)),
                              pair_rows(a["s5_c_im"][0].transpose(0, 2, 1))], axis=1)
    diag = np.zeros((S5_C, S5_G, S5_C), np.float32)
    for c in range(S5_C):
        diag[c, :, c] = a["s5_d"][0, :, c]
    data["s5_diag"] = diag
    data["router_w"] = np.concatenate([a["router_w_group"][0], a["router_w_expert"][0]], axis=1)
    data["router_b"] = np.concatenate([a["router_b_group"], a["router_b_expert"]], axis=1)
    numbers = np.broadcast_to(np.arange(EXPERTS, dtype=np.float32), (P, EXPERTS))
    data["route_const"] = np.concatenate([np.triu(np.ones((P, P), np.float32), 1), numbers], axis=1)
    data["ident"] = np.eye(P, dtype=np.float32)
    data = {n: np.ascontiguousarray(v) for n, v in data.items()}
    nc = bacc.Bacc("TRN2", target_bir_lowering=False, num_devices=1)
    w = {n: nc.dram_tensor("in_" + n, v.shape, F32, kind="ExternalInput").ap()
                           for n, v in data.items()}
    out = nc.dram_tensor("out", (S, D), F32, kind="ExternalOutput").ap()
    build(nc, w, out)
    got = run(nc, [{"in_" + n: v for n, v in data.items()}], core_ids=[0])
    return got.results[0]["out"].reshape(1, S, D)
```

```python
from contextlib import ExitStack


import numpy as np

import concourse.bass as bass
from concourse import mybir

F32 = mybir.dt.float32
F32R = mybir.dt.float32r
U32 = mybir.dt.uint32
I32 = mybir.dt.int32
ALU = mybir.AluOpType
ACT = mybir.ActivationFunctionType
AX_X = mybir.AxisListType.X

P = 128
S = 1024
D = 1024
KT = D // P
TT = S // P
HALF = 512
EPS = 1e-6
DH = 64

M_W = 256
M_H = 4
L = 64
NC = S // L
S5_G = 16
S5_C = 16
S5_L = 8
A_W = 512
A_H = 8
MEM = 256
X_H = 4
X_DH = 256

COL_UO = 0
COL_GATE = 2 * M_W
COL_S = COL_GATE + 2 * M_H
COL_Q = COL_S + 256
COL_K = COL_Q + A_W
COL_V = COL_K + A_W

SLOT = KT * HALF
NEG = -1.0e30

VECS = {}
_at = 0
for _name, _n in (("conv_w", 8), ("conv_b", 2), ("m_gain", 2), ("m_skip", 2), ("s_gain", 2), ("a_gain", 4),
                  ("gate_b", 1), ("a_re", 8), ("a_im", 8), ("log_dt", 8), ("sign", 1)):
    VECS[_name] = (_at, _at + _n)
    _at += _n
VEC_N = _at




class Split:

    def __init__(self, st, name):
        self.rounded, self.done, self.n = st.sem(name + "_rounded"), st.sem(name + "_split"), 0

    def piece(self, dve, x, pair):
        high, low = pair
        dve.tensor_copy(high.bitcast(F32R), x).then_inc(self.rounded, 1)
        self.n += 1
        dve.wait_ge(self.rounded, self.n)
        dve.tensor_tensor(low.bitcast(F32R), x, high, ALU.subtract).then_inc(self.done, 1)


def split_product(pe, out, left, right, start, stop):
    (left_high, left_low), (right_high, right_low) = [[part.bitcast(F32R) for part in pair] for pair in (left, right)]
    pe.matmul(out, left_high, right_high, start=start, stop=False)
    pe.matmul(out, left_high, right_low, start=False, stop=False)
    return pe.matmul(out, left_low, right_high, start=False, stop=stop)


class Norm:

    def __init__(self, k, name, n, source, gain, dest, banks, ring, stat, wait_source, keep=None, low=None):
        self.k, self.n, self.source, self.gain, self.dest = k, n, source, gain, dest
        self.banks, self.ring, self.stat, self.wait_source, self.keep = banks, ring, stat, wait_source, keep
        self.low = low
        self.slots = ring.shape[1] - 1
        self.squared = k.sem(name + "_squared")
        self.variance = k.sem(name + "_variance")
        self.root = k.sem(name + "_root")
        self.inverse = k.sem(name + "_inverse")
        self.scaled = k.sem(name + "_scaled")
        self.turned = k.sem(name + "_turned")
        self.evac_act = k.sem(name + "_evac_act")
        self.evac_dve = k.sem(name + "_evac_dve")

    def bank_of(self, t, h):
        return self.banks[(2 * t + h) % 4][:, :].rearrange("p (a b) -> p a b", a=4)

    def wait_all(self, eng):
        if self.low is None:
            eng.wait_ge(self.evac_act, self.n)
        eng.wait_ge(self.evac_dve, self.n if self.low is None else 2 * self.n)

    def scalar(self, act):
        for i in range(self.n + 3):
            if i < self.n:
                self.wait_source(act, i)
                if i:
                    act.wait_ge(self.squared, i)
                act.activation(self.ring[:, self.slots, :], self.source(i), ACT.Square,
                               accum_out=self.stat[:, i, 0:1]).then_inc(self.squared, 1)
            if 1 <= i <= self.n:
                t = i - 1
                act.wait_ge(self.variance, t + 1)
                act.activation(self.stat[:, t, 2:3], self.stat[:, t, 1:2], ACT.Sqrt).then_inc(self.root, 1)
            if i >= 3 and self.low is not None:
                t = i - 3
                for h in range(2):
                    act.wait_ge(self.turned, 2 * t + h + 1)
                    act.activation(self.dest(t, h).bitcast(F32R), self.bank_of(t, h), ACT.Copy).then_inc(self.evac_act, 1)
            elif i >= 3:
                t = i - 3
                act.wait_ge(self.turned, 2 * t + 1)
                act.activation(self.dest(t, 0), self.banks[(2 * t) % 4][:, :].rearrange("p (a b) -> p a b", a=4),
                               ACT.Copy).then_inc(self.evac_act, 1)

    def vector(self, dve):
        for i in range(self.n + 3):
            if i < self.n:
                dve.wait_ge(self.squared, i + 1)
                dve.tensor_scalar(self.stat[:, i, 1:2], self.stat[:, i, 0:1], 1.0 / D, EPS, ALU.mult,
                                  ALU.add).then_inc(self.variance, 1)
            if 1 <= i <= self.n:
                t = i - 1
                dve.wait_ge(self.root, t + 1)
                dve.reciprocal(self.stat[:, t, 3:4], self.stat[:, t, 2:3]).then_inc(self.inverse, 1)
                dve.wait_ge(self.inverse, t + 1)
                if t >= self.slots:
                    dve.wait_ge(self.turned, 2 * (t - self.slots + 1))
                    if self.keep is not None:
                        dve.wait_ge(self.keep[t % 2], 16 * (t // 2))
                dve.scalar_tensor_tensor(out=self.ring[:, t % self.slots, :], in0=self.source(t),
                                         scalar=self.stat[:, t, 3:4], in1=self.gain,
                                         op0=ALU.mult, op1=ALU.mult).then_inc(self.scaled, 1)
            if i >= 3 and self.low is not None:
                t = i - 3
                for h in range(2):
                    dve.wait_ge(self.evac_act, 2 * t + h + 1)
                    dve.tensor_tensor(self.low(t, h).bitcast(F32R), self.bank_of(t, h), self.dest(t, h), ALU.subtract)\
                        .then_inc(self.evac_dve, 1)
            elif i >= 3:
                t = i - 3
                dve.wait_ge(self.turned, 2 * t + 2)
                dve.tensor_copy(self.dest(t, 1), self.banks[(2 * t + 1) % 4][:, :].rearrange(
                    "p (a b) -> p a b", a=4)).then_inc(self.evac_dve, 1)

    def tensor(self, pe):
        for t in range(self.n):
            pe.wait_ge(self.scaled, t + 1)
            for h in range(2):
                if t >= 2 and self.low is None:
                    pe.wait_ge((self.evac_act, self.evac_dve)[h], t - 1)
                elif t >= 2:
                    pe.wait_ge(self.evac_dve, 2 * (t - 2) + h + 1)
                bank = self.banks[(2 * t + h) % 4]
                for a in range(4):
                    c = 4 * h + a
                    last = pe.transpose(bank[:, a * P:(a + 1) * P], self.ring[:, t % self.slots, c * P:(c + 1) * P],
                                        self.k.ident[:, :])
                last.then_inc(self.turned, 1)


def load_chunk(k, queue, i):
    source, n = k.chunks[i]
    queue.dma_start(k.chunk(i, n), source.rearrange("(k p) n -> p k n", p=P)).then_inc(k.chunk_in[i], 16)


class Pieces:

    def __init__(self, k, st, name):
        self.k, self.split = k, Split(st, name)
        self.ring = [st.sbuf(f"{name}_{part}", [P, 2, KT * P]) for part in ("high", "low")]
        self.pieces, self.groups, self.last_use, self.side = [], [], [0, 0], 0

    def add(self, chunk, n, a, b):
        width = b - a
        if width > P:
            sides = (0, 1)
            pair = [r[:, :, :].rearrange("p s n -> p (s n)")[:, 0:KT * width].rearrange("p (k n) -> p k n", k=KT)
                    for r in self.ring]
        else:
            sides = (self.side,)
            pair = [r[:, self.side, 0:KT * width].rearrange("p (k n) -> p k n", k=KT) for r in self.ring]
            self.side = 1 - self.side
        free = max(self.last_use[side] for side in sides)
        self.pieces.append((chunk, self.k.chunk(chunk, n)[:, :, a:b], pair, free, len(self.groups)))
        self.sides = sides
        return pair

    def group(self, *what):
        self.groups.append(what)
        for side in self.sides:
            self.last_use[side] = len(self.groups)

    def firsts(self):
        return [p[4] for p in self.pieces] + [len(self.groups)]

    def chunk_end(self, chunk):
        return max(n + 1 for n, p in enumerate(self.pieces) if p[0] == chunk)

    def vector(self, dve, n, product):
        chunk, source, pair, free, _ = self.pieces[n]
        dve.wait_ge(self.k.chunk_in[chunk], 16)
        if free:
            dve.wait_ge(product, free)
        self.split.piece(dve, source, pair)


def columns(pair, a, b, step=1):
    return lambda c: [part[:, c, a:b:step] for part in pair]


def in_projection(k):
    with k.stage() as st:
        xs, ring, gain = k.yT[:, 0:3, :], k.yT[:, 3:6, :], k.yT[:, 6, :]
        v_out = k.yT[:, 7, :].rearrange("p (a b) -> p a b", a=4)
        stat = st.sbuf("mix_stat", [P, TT, 4])
        tb = [st.psum(f"turn{i}", [P, HALF]) for i in range(4)]
        gb = [st.psum(f"gemm{i}", [P, HALF]) for i in range(4)]
        const_in = st.sem("const_in")
        gain_in = st.sem("mix_gain_in")
        x_in = [st.sem(f"x_in{i}") for i in range(3)]
        product = st.sem("product")
        out_act = st.sem("out_act")
        out_dve = st.sem("out_dve")
        v_stored = [st.sem(f"v_stored{i}") for i in range(4)]

        def wait_x(eng, t):
            eng.wait_ge(x_in[t % 3], 16 * (t // 3 + 1))

        def transposes(n):
            return lambda t, h: k.xn[n][:, 4 * h:4 * h + 4, t * P:(t + 1) * P]

        norm = Norm(st, "mix", TT, lambda t: xs[:, t % 3, :], gain, transposes(0), tb, ring, stat, wait_x,
                    low=transposes(1))

        w = Pieces(k, st, "mix_w")
        for m in range(4):
            dest = k.uP[:, m, 3:] if m < 2 else k.oT[:, m - 2, :]
            part = w.add(0, HALF, m * P, (m + 1) * P)
            for h in range(2):
                half = slice(h * HALF, (h + 1) * HALF)
                w.group(columns(part, 0, P), columns(k.xn, half.start, half.stop), (P, HALF), dest[:, half], 1.0)
        part = w.add(1, 264, 0, 8)
        for h in range(2):
            half = slice(h * HALF, (h + 1) * HALF)
            w.group(columns(part, 0, 8), columns(k.xn, half.start, half.stop), (8, HALF), k.gateT[:, half], 1.0)
        part = w.add(1, 264, 8, 264)
        for s in range(S5_L):
            w.group(columns(k.xn, s, S, S5_L), columns(part, 0, 256), (P, 256), k.s_in[:, :, s, :], 1.0)
        for i, dst, scale in ((2, k.qT, DH ** -0.5), (3, k.kT, 1.0)):
            for m in range(4):
                part = w.add(i, HALF, m * P, (m + 1) * P)
                for h in range(2):
                    half = slice(h * HALF, (h + 1) * HALF)
                    w.group(columns(part, 0, P), columns(k.xn, half.start, half.stop), (P, HALF), dst[:, m, half], scale)
        v_first = len(w.groups)
        for h in range(2):
            part = w.add(4, HALF, 256 * h, 256 * (h + 1))
            for t in range(TT):
                n = h * TT + t
                w.group(columns(k.xn, t * P, (t + 1) * P), columns(part, 0, 256), (P, 256), v_out[:, n % 4, :], 1.0)
        groups, firsts = w.groups, w.firsts()

        def psum_of(g):
            rows, cols = groups[g][2]
            view = gb[g % 4][0:rows, 0:cols]
            return view.rearrange("p (a b) -> p a b", b=S5_C) if cols == 256 and g < v_first else view

        def wait_v_slot(eng, g):
            n = g - v_first
            if n >= 4:
                eng.wait_ge(v_stored[n % 4], 16 * (n // 4))

        with st.block() as block:

            @block.sync
            def _(sp):
                sp.dma_start(gain, k.w["norm_mix"][0:1, :].partition_broadcast(P)).then_inc(gain_in, 16)
                sp.dma_start(k.ident[:, :], k.w["ident"]).then_inc(const_in, 16)
                sp.dma_start(k.vec[:, :], k.w["vec"]).then_inc(const_in, 16)
                for t in range(TT):
                    if t >= 3:
                        sp.wait_ge(norm.scaled, t - 2)
                    sp.dma_start(xs[:, t % 3, :], k.w["x"][t * P:(t + 1) * P, :]).then_inc(x_in[t % 3], 16)
                    if t == 3:
                        load_chunk(k, sp, 0)
                        load_chunk(k, sp, 1)
                for i in range(2, 5):
                    sp.wait_ge(w.split.done, w.chunk_end(i - 2))
                    load_chunk(k, sp, i)
                for n in range(2 * TT):
                    g = v_first + n
                    h, t = n // TT, n % TT
                    sp.wait_ge((out_act, out_dve)[g % 2], g // 2 + 1)
                    sp.dma_start(k.v_dram[t * P:(t + 1) * P, 256 * h:256 * (h + 1)], v_out[:, n % 4, :])\
                        .then_inc(v_stored[n % 4], 16)
                for i in range(4):
                    sp.wait_ge(v_stored[i], 16 * (2 * TT // 4))

            @block.gpsimd
            def _(pool):
                pool.memset(k.uP[:, :, 0:3], 0.0).then_inc(st.sem("u_padded"), 1)

            @block.scalar
            def _(act):
                norm.scalar(act)
                for g in range(0, len(groups), 2):
                    if g >= v_first:
                        wait_v_slot(act, g)
                    act.wait_ge(product, g + 1)
                    act.activation(groups[g][3], psum_of(g), ACT.Copy, scale=groups[g][4]).then_inc(out_act, 1)

            @block.vector
            def _(dve):
                dve.wait_ge(gain_in, 16)
                norm.vector(dve)
                w.vector(dve, 0, product)
                for n in range(len(w.pieces)):
                    for g in range(firsts[n], firsts[n + 1]):
                        if n + 1 < len(w.pieces) and g == max(firsts[n], w.pieces[n + 1][3] - 1):
                            w.vector(dve, n + 1, product)
                        if g % 2:
                            if g >= v_first:
                                wait_v_slot(dve, g)
                            dve.wait_ge(product, g + 1)
                            dve.tensor_scalar(groups[g][3], psum_of(g), groups[g][4], None, ALU.mult).then_inc(out_dve, 1)

            @block.tensor
            def _(pe):
                pe.wait_ge(const_in, 32)
                norm.tensor(pe)
                norm.wait_all(pe)
                for g, (lhs, rhs, (rows, cols), _, _) in enumerate(groups):
                    if g in firsts:
                        pe.wait_ge(w.split.done, firsts.index(g) + 1)
                    if g >= 4:
                        pe.wait_ge((out_act, out_dve)[g % 2], (g - 4) // 2 + 1)
                    for c in range(KT):
                        last = split_product(pe, gb[g % 4][0:rows, 0:cols], lhs(c), rhs(c), c == 0, c == KT - 1)
                    last.then_inc(product, 1)


def broadcast(ap, axis, n):
    shape = list(ap.shape)
    return ap.unsqueeze(axis).to_broadcast(shape[:axis] + [n] + shape[axis:])


def mlstm(k):
    HP = M_H // 2
    HC = M_H * NC
    Q4 = NC // 4
    with k.stage() as st:
        free = k.ring[:, 2 * SLOT:4 * SLOT].rearrange("p (n j t) -> p n j t", n=4, j=HP)
        cT, mqT, mkT, interB = (free[:, n, :, :] for n in range(4))
        free = k.ring[:, 0:SLOT].rearrange("p (n c l) -> p n c l", n=2, l=L)
        cmB, kw = free[:, 0, :, :], free[:, 1, :, :]
        state = k.yT[:, 2:6, :].rearrange("p a b -> p (a b)")[:, 0:HP * NC * (DH + 1)].rearrange(
            "p (c e) -> p c e", e=DH + 1)
        v1 = k.ring[:, SLOT:SLOT + HP * NC * (DH + 1)].rearrange("p (c e) -> p c e", e=DH + 1)
        wts = st.sbuf("mlstm_weights", [P, HP, 3, P])
        gi = st.sbuf("gi", [HC, L])
        gf = st.sbuf("gf", [HC, L])
        tmp = st.sbuf("gate_tmp", [HC, 2, L])
        cum = st.sbuf("cum", [HC, L])
        rel = st.sbuf("rel", [HC, L])
        cmax = st.sbuf("cmax", [HC, L])
        zero = st.sbuf("zero", [HC, L])
        gm = st.sbuf("gm", [HC, 8])
        inter = st.sbuf("inter", [HC, L])
        dup = st.sbuf("dup", [HC, 4, 2, L])
        row = st.sbuf("row", [M_H, 4, NC + 1])
        col = st.sbuf("col", [P, 4, HP, NC])
        upd = st.sbuf("upd", [P, HP * NC, DH + 1])
        hn = upd
        sq = kw
        stat = st.sbuf("h_stat", [P, 4, HP * NC])
        bank = [st.psum(f"mb{i}", [P, HALF]) for i in range(8)]
        dram = {n: k.nc.dram_tensor(n, sh, F32, kind="Internal").ap() for n, sh in (
            ("gate_dram", [2 * M_H, S]), ("gm_dram", [2, HC]), ("m_dram", [2, HC]), ("cmax_dram", [M_H, S]),
            ("inter_dram", [M_H, S]))}
        sem = {n: st.sem("m_" + n) for n in (
            "weights_in gates_out gates_in gm_out gm_in m_out m_in cm_out inter_out cm_in inter_in pad bias "
            "act gate pool conv silu qk qk_act kv kv_act kv_dve cols cols_dve s_done ew qi u_done u_evac states "
            "o_done o_evac h_done hT_done y den").split()}
        vec = k.vec

        def V(name, j):
            a = VECS[name][0] + j
            return vec[:, a:a + 1]

        with st.block() as block:

            @block.sync
            def _(sp):
                for i in (5, 6):
                    load_chunk(k, sp, i)
                sp.dma_start(wts[:, :, :, :], k.w["mlstm_w"]).then_inc(sem["weights_in"], 16)
                sp.wait_ge(sem["bias"], 1)
                sp.dma_start(dram["gate_dram"], k.gateT[:, :]).then_inc(sem["gates_out"], 16)
                sp.wait_ge(sem["gates_out"], 16)
                gd = dram["gate_dram"]
                sp.dma_start(gi[:, :], gd[0:M_H, :].rearrange("h (c l) -> (h c) l", l=L)).then_inc(sem["gates_in"], 16)
                sp.dma_start(gf[:, :], gd[M_H:, :].rearrange("h (c l) -> (h c) l", l=L)).then_inc(sem["gates_in"], 16)
                sp.wait_ge(sem["gate"], 6)
                for i in range(2):
                    sp.dma_start(dram["gm_dram"][i:i + 1, :].rearrange("a n -> n a"), gm[:, i:i + 1]).then_inc(sem["gm_out"], 16)
                sp.wait_ge(sem["gm_out"], 32)
                for i in range(2):
                    sp.dma_start(row[:, i, 0:NC], dram["gm_dram"][i, :].rearrange("(h c) -> h c", c=NC)).then_inc(sem["gm_in"], 16)
                sp.wait_ge(sem["gate"], 7)
                for i in range(2):
                    sp.dma_start(dram["m_dram"][i, :].rearrange("(h c) -> h c", c=NC), row[:, 2, i:i + NC]).then_inc(sem["m_out"], 16)
                sp.wait_ge(sem["m_out"], 32)
                for i in range(2):
                    sp.dma_start(gm[:, 2 + i:3 + i], dram["m_dram"][i:i + 1, :].rearrange("a n -> n a")).then_inc(sem["m_in"], 16)
                sp.wait_ge(sem["gate"], 8)
                sp.dma_start(dram["cmax_dram"].rearrange("h (c l) -> (h c) l", l=L), cmax[:, :]).then_inc(sem["cm_out"], 16)
                sp.wait_ge(sem["cm_out"], 16)
                for q in range(2):
                    sp.dma_start(cmB[q * DH:(q + 1) * DH, :, :].rearrange("p (j c) l -> p j (c l)", j=HP),
                                 bcast_rows(dram["cmax_dram"], q, HP)).then_inc(sem["cm_in"], 16)
                sp.wait_ge(sem["act"], 4)
                sp.dma_start(dram["inter_dram"].rearrange("h (c l) -> (h c) l", l=L), inter[:, :]).then_inc(sem["inter_out"], 16)
                sp.wait_ge(sem["inter_out"], 16)
                for q in range(2):
                    sp.dma_start(interB[q * DH:(q + 1) * DH, :, :], bcast_rows(dram["inter_dram"], q, HP)).then_inc(sem["inter_in"], 16)

            @block.gpsimd
            def _(pool):
                pool.memset(zero[:, :], 0.0).then_inc(sem["pad"], 1)
                pool.memset(v1[:, :, DH:DH + 1], 1.0).then_inc(sem["pad"], 1)
                pool.memset(state[:, :, :], 0.0).then_inc(sem["pad"], 1)
                pool.memset(row[:, 2, 0:1], 0.0).then_inc(sem["pad"], 1)
                pool.wait_ge(sem["ew"], 1)
                for q in range(2):
                    part = cmB[q * DH:(q + 1) * DH, :, :]
                    pool.affine_select(out=part, in_=part, compare_op=ALU.is_ge, fill=NEG, base=0,
                                       pattern=[[0, HP * NC], [1, L]], channel_multiplier=-1).then_inc(sem["pool"], 1)

            @block.scalar
            def _(act):
                for j in range(HP):
                    act.wait_ge(sem["conv"], 4 * (j + 1))
                    act.activation(cT[:, j, :], cT[:, j, :], ACT.Silu, bias=V("conv_b", j)).then_inc(sem["silu"], 1)
                for g in range(8):
                    dst = (mqT, mkT)[g // 4]
                    act.wait_ge(sem["qk"], g + 1)
                    act.activation(dst[:, (g // 2) % 2, (g % 2) * HALF:(g % 2 + 1) * HALF], bank[g % 4][:, :], ACT.Copy,
                                   scale=(DH ** -0.5, 1.0)[g // 4]).then_inc(sem["qk_act"], 1)
                act.wait_ge(sem["gate"], 1)
                act.activation(tmp[:, 0, :], tmp[:, 0, :], ACT.Exp, scale=-1.0).then_inc(sem["act"], 1)
                act.wait_ge(sem["act"], 1)
                act.activation(tmp[:, 1, :], tmp[:, 0, :], ACT.Ln, bias=1.0).then_inc(sem["act"], 1)
                act.wait_ge(sem["gate"], 9)
                act.activation(dup[:, 1, 0, :], rel[:, :], ACT.Exp, bias=gm[:, 4:5]).then_inc(sem["act"], 1)
                act.activation(inter[:, :], cmax[:, :], ACT.Exp, scale=-1.0, bias=gm[:, 2:3]).then_inc(sem["act"], 1)
                act.activation(dup[:, 2, 0, :], tmp[:, 0, :], ACT.Exp, scale=-1.0).then_inc(sem["act"], 1)
                act.activation(dup[:, 3, 0, :], zero[:, :], ACT.Exp, bias=gm[:, 5:6]).then_inc(sem["act"], 1)
                act.wait_ge(sem["pool"], 2)
                act.activation(cmB[:, :, :], cmB[:, :, :], ACT.Exp).then_inc(sem["act"], 1)
                for g in range(4):
                    act.wait_ge(sem["kv"], 4 + g + 1)
                    act.activation(v1[:, 8 * g:8 * g + 8, 0:DH], bank[4 + g][:, :].rearrange("p (c e) -> p c e", e=DH),
                                   ACT.Copy).then_inc(sem["kv_act"], 1)
                for g in range(8):
                    act.wait_ge(sem["u_done"], g + 1)
                    act.activation(upd[:, 4 * g:4 * g + 4, :], bank[g % 4][:, 0:4 * (DH + 1)].rearrange(
                        "p (c e) -> p c e", e=DH + 1), ACT.Copy).then_inc(sem["u_evac"], 1)
                for g in range(8):
                    act.wait_ge(sem["o_done"], g + 1)
                    act.activation(hn[:, 4 * g:4 * g + 4, :], bank[4 + g % 4][:, 0:4 * (DH + 1)].rearrange(
                        "p (c e) -> p c e", e=DH + 1), ACT.Copy).then_inc(sem["o_evac"], 1)
                act.wait_ge(sem["h_done"], 4)
                act.activation(stat[:, 1, :], stat[:, 1, :], ACT.Sqrt).then_inc(sem["act"], 1)
                act.activation(k.oT[:, :, :], k.oT[:, :, :], ACT.Sigmoid).then_inc(sem["act"], 1)

            @block.vector
            def _(dve):
                dve.tensor_scalar(k.gateT[:, :], k.gateT[:, :], V("gate_b", 0)[0:2 * M_H, :], None, ALU.add).then_inc(sem["bias"], 1)
                for j in range(HP):
                    dve.tensor_scalar(cT[:, j, :], k.uP[:, j, 0:S], V("conv_w", 4 * j), None, ALU.mult).then_inc(sem["conv"], 1)
                    for tap in range(1, 4):
                        dve.wait_ge(sem["conv"], 4 * j + tap)
                        dve.scalar_tensor_tensor(out=cT[:, j, :], in0=k.uP[:, j, tap:tap + S], scalar=V("conv_w", 4 * j + tap),
                                                 in1=cT[:, j, :], op0=ALU.mult, op1=ALU.add).then_inc(sem["conv"], 1)
                dve.wait_ge(sem["gates_in"], 32)
                dve.scalar_tensor_tensor(out=tmp[:, 0, :], in0=gf[:, :], scalar=-1.0, in1=gf[:, :], op0=ALU.mult,
                                         op1=ALU.max).then_inc(sem["gate"], 1)
                dve.wait_ge(sem["act"], 2)
                dve.scalar_tensor_tensor(out=gf[:, :], in0=gf[:, :], scalar=0.0, in1=tmp[:, 1, :], op0=ALU.min,
                                         op1=ALU.subtract).then_inc(sem["gate"], 1)
                dve.wait_ge(sem["gate"], 2)
                dve.wait_ge(sem["pad"], 4)
                dve.tensor_tensor_scan(cum[:, :], gf[:, :], zero[:, :], 0.0, ALU.add, ALU.add).then_inc(sem["gate"], 1)
                dve.wait_ge(sem["gate"], 3)
                dve.tensor_tensor(rel[:, :], gi[:, :], cum[:, :], ALU.subtract).then_inc(sem["gate"], 1)
                dve.wait_ge(sem["gate"], 4)
                dve.tensor_scalar(gm[:, 0:1], cum[:, L - 1:L], 0.0, None, ALU.add).then_inc(sem["gate"], 1)
                dve.tensor_reduce(gm[:, 6:7], rel[:, :], AX_X, ALU.max).then_inc(sem["cols"], 1)
                dve.wait_ge(sem["cols"], 1)
                dve.tensor_tensor(gm[:, 1:2], gm[:, 6:7], cum[:, L - 1:L], ALU.add).then_inc(sem["gate"], 1)
                dve.wait_ge(sem["gm_in"], 32)
                dve.tensor_tensor_scan(row[:, 2, 1:NC + 1], row[:, 0, 0:NC], row[:, 1, 0:NC], 0.0, ALU.add,
                                       ALU.max).then_inc(sem["gate"], 1)
                dve.wait_ge(sem["m_in"], 32)
                dve.tensor_tensor_scan(cmax[:, :], rel[:, :], rel[:, :], gm[:, 2:3], ALU.max, ALU.max).then_inc(sem["gate"], 1)
                dve.tensor_tensor(gm[:, 4:5], gm[:, 0:1], gm[:, 3:4], ALU.subtract).then_inc(sem["cols"], 1)
                dve.wait_ge(sem["cols"], 2)
                dve.tensor_tensor(gm[:, 5:6], gm[:, 4:5], gm[:, 2:3], ALU.add).then_inc(sem["cols"], 1)
                dve.wait_ge(sem["gate"], 8)
                dve.tensor_tensor(tmp[:, 0, :], cum[:, :], cmax[:, :], ALU.add).then_inc(sem["cols"], 1)
                dve.wait_ge(sem["cols"], 4)
                dve.tensor_copy(dup[:, 0, 0, :], rel[:, :]).then_inc(sem["gate"], 1)
                dve.wait_ge(sem["act"], 6)
                dve.wait_ge(sem["gate"], 9)
                dve.tensor_copy(dup[:, :, 1, :], dup[:, :, 0, :]).then_inc(sem["gate"], 1)
                dve.wait_ge(sem["cols_dve"], 1)
                for q in range(2):
                    half = slice(q * DH, (q + 1) * DH)
                    view = bank[4][half, 0:4 * HC].rearrange("p (n j q c) -> p n j q c", n=4, j=HP, q=2)
                    dve.tensor_copy(col[half, :, :, :], view[:, :, :, q, :]).then_inc(sem["gate"], 1)
                dve.wait_ge(sem["gate"], 12)
                dve.wait_ge(sem["cm_in"], 32)
                rcol = col[:, 0, :, :].rearrange("p j c -> p (j c)")
                dve.tensor_tensor(cmB[:, :, :], broadcast(rcol, 2, L), cmB[:, :, :], ALU.subtract).then_inc(sem["ew"], 1)
                wcol = col[:, 1, :, :].rearrange("p j c -> p (j c)")
                for g in range(4):
                    dve.wait_ge(sem["kv"], g + 1)
                    dve.tensor_tensor(kw[:, 8 * g:8 * g + 8, :], bank[g][:, :].rearrange("p (c e) -> p c e", e=DH),
                                      broadcast(wcol[:, 8 * g:8 * g + 8], 2, DH), ALU.mult).then_inc(sem["kv_dve"], 1)
                dve.wait_ge(sem["inter_in"], 32)
                dve.wait_ge(sem["qk_act"], 8)
                dve.wait_ge(sem["s_done"], 4)
                dve.tensor_tensor(interB[:, :, :], mqT[:, :, :], interB[:, :, :], ALU.mult).then_inc(sem["qi"], 1)
                dve.wait_ge(sem["act"], 7)
                for g in range(4):
                    part = cmB[:, 8 * g:8 * g + 8, :]
                    dve.tensor_tensor(part, part, bank[4 + g][:, :].rearrange("p (c l) -> p c l", l=L), ALU.mult)\
                        .then_inc(sem["ew"], 1)
                dcol = col[:, 3, :, :].rearrange("p j c -> p (j c)")
                dve.wait_ge(sem["u_evac"], 8)
                n = 0
                for c in range(NC - 1):
                    for j in range(HP):
                        i = j * NC + c
                        if c:
                            dve.wait_ge(sem["states"], n - 1)
                        dve.scalar_tensor_tensor(out=state[:, i + 1, :], in0=state[:, i, :], scalar=dcol[:, i:i + 1],
                                                 in1=upd[:, i, :], op0=ALU.mult, op1=ALU.add).then_inc(sem["states"], 1)
                        n += 1
                dve.wait_ge(sem["o_evac"], 8)
                ecol = col[:, 2, :, :].rearrange("p j c -> p (j c)")
                dve.scalar_tensor_tensor(out=stat[:, 1, :], in0=hn[:, :, DH], scalar=-1.0, in1=hn[:, :, DH], op0=ALU.mult,
                                         op1=ALU.max).then_inc(sem["den"], 1)
                dve.wait_ge(sem["den"], 1)
                dve.tensor_tensor(stat[:, 0, :], stat[:, 1, :], ecol, ALU.max).then_inc(sem["h_done"], 1)
                dve.wait_ge(sem["h_done"], 1)
                dve.reciprocal(stat[:, 2, :], stat[:, 0, :]).then_inc(sem["cols"], 1)
                dve.wait_ge(sem["cols"], 5)
                dve.tensor_tensor(hn[:, :, 0:DH], hn[:, :, 0:DH], broadcast(stat[:, 2, :], 2, DH), ALU.mult).then_inc(sem["h_done"], 1)
                dve.wait_ge(sem["h_done"], 2)
                dve.tensor_tensor(sq[:, :, :], hn[:, :, 0:DH], hn[:, :, 0:DH], ALU.mult).then_inc(sem["h_done"], 1)
                dve.wait_ge(sem["h_done"], 3)
                dve.tensor_reduce(stat[:, 3, :], sq[:, :, :], AX_X, ALU.add).then_inc(sem["cols"], 1)
                dve.wait_ge(sem["cols"], 6)
                dve.tensor_scalar(stat[:, 1, :], stat[:, 3, :], 1.0 / DH, EPS, ALU.mult, ALU.add).then_inc(sem["h_done"], 1)
                dve.wait_ge(sem["act"], 8)
                dve.reciprocal(stat[:, 0, :], stat[:, 1, :]).then_inc(sem["cols"], 1)
                dve.wait_ge(sem["cols"], 7)
                dve.tensor_tensor(hn[:, :, 0:DH], hn[:, :, 0:DH], broadcast(stat[:, 0, :], 2, DH), ALU.mult).then_inc(sem["h_done"], 1)
                for j in range(HP):
                    dve.tensor_scalar(cT[:, j, :], cT[:, j, :], V("m_skip", j), None, ALU.mult).then_inc(sem["y"], 1)
                dve.wait_ge(sem["y"], 2)
                dve.wait_ge(sem["act"], 9)
                for g in range(4):
                    j, half = g // 2, slice((g % 2) * HALF, (g % 2 + 1) * HALF)
                    dve.wait_ge(sem["hT_done"], g + 1)
                    dve.scalar_tensor_tensor(out=cT[:, j, half], in0=bank[g][:, :], scalar=V("m_gain", j), in1=cT[:, j, half],
                                             op0=ALU.mult, op1=ALU.add).then_inc(sem["y"], 1)
                    dve.wait_ge(sem["y"], 3 + 2 * g)
                    dve.tensor_tensor(k.yT[:, j, half], cT[:, j, half], k.oT[:, j, half], ALU.mult).then_inc(sem["y"], 1)

            @block.tensor
            def _(pe):
                pe.wait_ge(sem["weights_in"], 16)
                pe.wait_ge(sem["silu"], HP)
                for g in range(8):
                    if g >= 4:
                        pe.wait_ge(sem["qk_act"], g - 3)
                    j = (g // 2) % 2
                    pe.matmul(bank[g % 4][:, :], wts[:, j, g // 4, :], cT[:, j, (g % 2) * HALF:(g % 2 + 1) * HALF],
                              start=True, stop=True).then_inc(sem["qk"], 1)
                pe.wait_ge(sem["gate"], 10)
                for n in range(4):
                    last = pe.transpose(bank[4][:, n * HC:(n + 1) * HC], dup[:, n, :, :].rearrange("p a l -> p (a l)"),
                                        k.ident[0:HC, 0:HC])
                last.then_inc(sem["cols_dve"], 1)

                def per_chunk(out, lhs, rhs, g, stop=True, start=True):
                    for i in range(8 * g, 8 * g + 8):
                        for q in range(2):
                            half = slice(q * DH, (q + 1) * DH)
                            last = pe.matmul(out[half, (i % 8) * DH:(i % 8 + 1) * DH], lhs(half, i), rhs(half, i),
                                             start=start, stop=stop)
                    return last

                pe.wait_ge(sem["qk_act"], 8)
                pe.wait_ge(sem["gate"], 12)
                for g in range(4):
                    per_chunk(bank[g], lambda half, i: cT[half, i // NC, (i % NC) * L:(i % NC + 1) * L],
                              lambda half, i: wts[half, i // NC, 1, half], g).then_inc(sem["kv"], 1)
                for g in range(4):
                    per_chunk(bank[4 + g], lambda half, i: k.uP[half, i // NC, 3 + (i % NC) * L:3 + (i % NC + 1) * L],
                              lambda half, i: wts[half, i // NC, 2, half], g).then_inc(sem["kv"], 1)
                for g in range(4):
                    pe.wait_ge(sem["kv_act"], g + 1)
                    per_chunk(bank[4 + g], lambda half, i: mkT[half, i // NC, (i % NC) * L:(i % NC + 1) * L],
                              lambda half, i: mqT[half, i // NC, (i % NC) * L:(i % NC + 1) * L], g).then_inc(sem["s_done"], 1)
                W = DH + 1

                def per_four(out, terms, g):
                    for i in range(4 * g, 4 * g + 4):
                        for q in range(2):
                            half = slice(q * DH, (q + 1) * DH)
                            for n, (lhs, rhs) in enumerate(terms):
                                last = pe.matmul(out[half, (i % 4) * W:(i % 4 + 1) * W], lhs(half, i), rhs(half, i),
                                                 start=(n == 0), stop=(n == len(terms) - 1))
                    return last

                pe.wait_ge(sem["kv_dve"], 4)
                for g in range(8):
                    if g >= 4:
                        pe.wait_ge(sem["u_evac"], g - 3)
                    per_four(bank[g % 4], [(lambda half, i: kw[half, i, :], lambda half, i: v1[half, i, :])], g)\
                        .then_inc(sem["u_done"], 1)
                pe.wait_ge(sem["ew"], 5)
                pe.wait_ge(sem["qi"], 1)
                pe.wait_ge(sem["states"], HP * (NC - 1))
                for g in range(8):
                    if g >= 4:
                        pe.wait_ge(sem["o_evac"], g - 3)
                    per_four(bank[4 + g % 4], [
                        (lambda half, i: cmB[half, i, :], lambda half, i: v1[half, i, :]),
                        (lambda half, i: interB[half, i // NC, (i % NC) * L:(i % NC + 1) * L], lambda half, i: state[half, i, :])],
                        g).then_inc(sem["o_done"], 1)
                pe.wait_ge(sem["h_done"], 5)
                for g in range(4):
                    per_chunk(bank[g], lambda half, i: hn[half, i, 0:DH], lambda half, i: k.ident[half, half], g)\
                        .then_inc(sem["hT_done"], 1)


def bcast_rows(rows, q, n):
    return rows.rearrange("(j q) t -> q j t", j=n)[q].partition_broadcast(DH)


def s5(k):
    GP = S5_G // 2
    C = S // S5_L
    SUB = 8
    RUNS = C // SUB
    with k.stage() as st:
        free = k.ring[:, 2 * SLOT:4 * SLOT].rearrange("p (n f) -> p n f", n=4)
        UT = free[:, 0, :].rearrange("p (g c) -> p g c", c=C)
        T = free[:, 1, :].rearrange("p (g c) -> p g c", c=P)
        z = free[:, 2, :].rearrange("p (t h) -> p t h", h=256)
        zT = free[:, 3, :].rearrange("p (n t c) -> p n t c", n=2, c=C)
        spare = k.yT[:, 4:8, :].rearrange("p a b -> p (a b)")
        WL = spare[:, 0:2 * GP * 9 * S5_C].rearrange("p (r g l h) -> p r g l h", r=2, g=GP, l=9)
        BT = k.oT[:, :, :].rearrange("p r (g s h) -> p r g s h", g=GP, s=S5_L)
        BG = k.uP[:, :, 3:].rearrange("p r (g s) -> p r g s", g=GP)
        X = st.sbuf("chunk_states", [P, 2, GP, C + 1])
        t1 = k.ring[:, 0:2048].rearrange("p (r x) -> p r x", r=2)
        t2 = k.ring[:, 2048:4096].rearrange("p (r x) -> p r x", r=2)
        Km = k.ring[0:S5_C, SLOT:SLOT + S5_G * P]
        Km = Km.rearrange("p (g x) -> p g x", x=P)
        bc = st.sbuf("s5_bc", [P, 4, GP, S5_C])
        bb = st.sbuf("s5_b_bar", [P, 2, GP, S5_C])
        diag = st.sbuf("s5_diag", [S5_C, S5_G, S5_C])
        pw = st.sbuf("a_powers", [P, 2, 9, GP])
        pr = st.sbuf("a_powers_down", [P, 2, 8, GP])
        fp = st.sbuf("f_powers", [P, 2, 9, GP])
        ff = st.sbuf("recur_factors", [P, 2, 12, 2, GP])
        par = st.sbuf("s5_scalars", [P, 24, GP])
        wglu = k.ring[:, SLOT + 2048:SLOT + 2560].rearrange("p (n h) -> p n h", n=2)
        bglu = st.sbuf("glu_bias", [P, 256])
        stat = st.sbuf("s5_stat", [P, 4, S5_L])
        bank = [st.psum(f"sb{i}", [P, HALF]) for i in range(8)]
        sem = {n: st.sem("s_" + n) for n in (
            "par_in b_in glu_in toep zero chain act pool bt bg_t bg ut_t ut km_done km xin_done xin "
            "rec y_done gelu zt_done zt glu_done gate_done norm yt_done yt").split()}
        a0 = VECS["a_re"][0]
        a_re, a_im, ldt = k.vec[:, a0:a0 + 8], k.vec[:, a0 + 8:a0 + 16], k.vec[:, a0 + 16:a0 + 24]
        N = {n: i for i, n in enumerate(
            "dt mag theta turns r s_half s_full cos re im xr den inv c_re c_im u v w x q f_re f_im".split())}

        def p_(n):
            return par[:, N[n], :]

        with st.block() as block:

            @block.sync
            def _(sp):
                sp.dma_start(bc[:, :, :, :], k.w["s5_bc"]).then_inc(sem["b_in"], 16)
                sp.dma_start(diag[:, :, :], k.w["s5_diag"]).then_inc(sem["b_in"], 16)
                sp.dma_start(wglu, k.w["s5_w_glu"].rearrange("(n p) h -> p n h", p=P)).then_inc(sem["glu_in"], 16)
                sp.dma_start(bglu[:, :], k.w["s5_b_glu"][0:1, :].partition_broadcast(P)).then_inc(sem["glu_in"], 16)
                sp.wait_ge(sem["km"], 4)
                sp.wait_ge(sem["zero"], 1)
                for s in range(S5_L):
                    rows = slice(s * S5_C, (s + 1) * S5_C)
                    sp.dma_start(T[rows, :, s * S5_C:], Km[:, :, 0:(S5_L - s) * S5_C]).then_inc(sem["toep"], 16)

            @block.gpsimd
            def _(pool):
                pool.memset(T, 0.0).then_inc(sem["zero"], 1)
                pool.memset(X[:, :, :, 0:1], 0.0).then_inc(sem["zero"], 1)

            @block.scalar
            def _(act):
                act.activation(p_("dt"), ldt, ACT.Exp).then_inc(sem["act"], 1)
                act.wait_ge(sem["chain"], 1)
                act.activation(p_("mag"), p_("mag"), ACT.Exp).then_inc(sem["act"], 1)
                act.wait_ge(sem["chain"], 10)
                act.activation(p_("s_half"), p_("r"), ACT.Sin, scale=0.5).then_inc(sem["act"], 1)
                act.activation(p_("s_full"), p_("r"), ACT.Sin).then_inc(sem["act"], 1)
                for b in range(4):
                    act.wait_ge(sem["ut_t"], b + 1)
                    act.activation(UT[:, 4 * b:4 * b + 4, :], bank[b][:, :].rearrange("p (g c) -> p g c", c=C), ACT.Copy)\
                        .then_inc(sem["ut"], 1)
                for b in range(4):
                    act.wait_ge(sem["bg_t"], b + 1)
                    act.activation(BG[:, b // 2, 4 * (b % 2):4 * (b % 2) + 4, :],
                                   bank[4 + b][:, :].rearrange("p (g c) -> p g c", c=P), ACT.Copy).then_inc(sem["bg"], 1)
                for b in range(4):
                    act.wait_ge(sem["xin_done"], b + 1)
                    act.activation(X[:, b // 2, 4 * (b % 2):4 * (b % 2) + 4, 1:],
                                   bank[b][:, :].rearrange("p (g c) -> p g c", c=C), ACT.Copy).then_inc(sem["xin"], 1)
                for b in range(4):
                    act.wait_ge(sem["y_done"], b + 1)
                    act.activation(z.rearrange("p t (g q h) -> p q g t h", q=2, h=S5_C)[:, b // 2, 4 * (b % 2):4 * (b % 2) + 4],
                                   bank[b][:, :].rearrange("p (g t h) -> p g t h", g=4, t=S5_L),
                                   ACT.Gelu_apprx_tanh).then_inc(sem["gelu"], 1)
                for b in range(4):
                    act.wait_ge(sem["zt_done"], b + 1)
                    act.activation(zT[:, b // 2, 4 * (b % 2):4 * (b % 2) + 4, :],
                                   bank[4 + b][:, :].rearrange("p (t c) -> p t c", c=C), ACT.Copy).then_inc(sem["zt"], 1)
                for b in range(4):
                    act.wait_ge(sem["glu_done"], b + 1)
                    part = t1.rearrange("p r x -> p (r x)")[:, HALF * b:HALF * (b + 1)]
                    act.activation(part, part, ACT.Sigmoid).then_inc(sem["gate_done"], 1)
                act.wait_ge(sem["norm"], 2)
                act.activation(stat[:, 2, :], stat[:, 1, :], ACT.Sqrt).then_inc(sem["norm"], 1)
                for b in range(4):
                    act.wait_ge(sem["yt_done"], b + 1)
                    j, g0 = b // 2, VECS["s_gain"][0] + b // 2
                    act.activation(k.yT[:, 2 + j, :].rearrange("p (c t) -> p t c", t=S5_L)[:, 4 * (b % 2):4 * (b % 2) + 4, :],
                                   bank[4 + b][:, :].rearrange("p (t c) -> p t c", c=C), ACT.Copy,
                                   scale=k.vec[:, g0:g0 + 1]).then_inc(sem["yt"], 1)

            @block.vector
            def _(dve):
                count = [0]

                def step(ins):
                    count[0] += 1
                    ins.then_inc(sem["chain"], 1)
                    dve.wait_ge(sem["chain"], count[0])

                def tt(out, x, y, op):
                    step(dve.tensor_tensor(out, x, y, op))

                def ts(out, x, a, op, b=None, op2=None):
                    step(dve.tensor_scalar(out, x, a, b, op, op2) if op2 else dve.tensor_scalar(out, x, a, None, op))

                sign = k.vec[:, VECS["sign"][0]:VECS["sign"][0] + 1]
                dve.wait_ge(sem["act"], 1)
                tt(p_("mag"), a_re, p_("dt"), ALU.mult)
                tt(p_("theta"), a_im, p_("dt"), ALU.mult)
                rounder = float(1.5 * 2.0 ** 23)
                ts(p_("turns"), p_("theta"), float(np.float32(0.5 / np.pi)), ALU.mult)
                ts(p_("turns"), p_("turns"), rounder, ALU.add)
                ts(p_("turns"), p_("turns"), rounder, ALU.subtract)
                at = p_("theta")
                for part in (6.28125, 0.0019350051879882812, 3.0199159819336793e-07):
                    step(dve.scalar_tensor_tensor(out=p_("r"), in0=p_("turns"), scalar=-part, in1=at, op0=ALU.mult, op1=ALU.add))
                    at = p_("r")
                ts(p_("r"), p_("r"), 3.1415925, ALU.min, -3.1415925, ALU.max)
                ts(p_("u"), p_("r"), 1.0, ALU.mult)
                dve.wait_ge(sem["act"], 4)
                tt(p_("cos"), p_("s_half"), p_("s_half"), ALU.mult)
                ts(p_("cos"), p_("cos"), -2.0, ALU.mult, 1.0, ALU.add)
                tt(p_("re"), p_("mag"), p_("cos"), ALU.mult)
                tt(p_("im"), p_("mag"), p_("s_full"), ALU.mult)
                ts(p_("xr"), p_("re"), -1.0, ALU.add)
                tt(p_("u"), a_re, a_re, ALU.mult)
                tt(p_("v"), a_im, a_im, ALU.mult)
                tt(p_("den"), p_("u"), p_("v"), ALU.add)
                step(dve.reciprocal(p_("inv"), p_("den")))
                tt(p_("u"), p_("xr"), a_re, ALU.mult)
                tt(p_("v"), p_("im"), a_im, ALU.mult)
                tt(p_("u"), p_("u"), p_("v"), ALU.add)
                tt(p_("c_re"), p_("u"), p_("inv"), ALU.mult)
                tt(p_("u"), p_("im"), a_re, ALU.mult)
                tt(p_("v"), p_("xr"), a_im, ALU.mult)
                tt(p_("u"), p_("u"), p_("v"), ALU.subtract)
                tt(p_("c_im"), p_("u"), p_("inv"), ALU.mult)

                def cmul(o_re, o_im, x_re, x_im, y_re, y_im, u, v):
                    tt(u, x_re, y_re, ALU.mult)
                    tt(v, x_im, y_im, ALU.mult)
                    tt(o_re, u, v, ALU.subtract)
                    tt(u, x_re, y_im, ALU.mult)
                    tt(v, x_im, y_re, ALU.mult)
                    tt(o_im, u, v, ALU.add)

                u_s = t1[:, 0, 0:8 * GP].rearrange("p (l g) -> p l g", g=GP)
                v_s = t1[:, 1, 0:8 * GP].rearrange("p (l g) -> p l g", g=GP)

                def powers(dst, re, im):
                    step(dve.memset(dst[:, 0, 0, :], 1.0))
                    step(dve.memset(dst[:, 1, 0, :], 0.0))
                    ts(dst[:, 0, 1, :], re, 1.0, ALU.mult)
                    ts(dst[:, 1, 1, :], im, 1.0, ALU.mult)
                    for n in (1, 2, 4):
                        cmul(dst[:, 0, n + 1:2 * n + 1, :], dst[:, 1, n + 1:2 * n + 1, :],
                             dst[:, 0, 1:n + 1, :], dst[:, 1, 1:n + 1, :], broadcast(dst[:, 0, n, :], 1, n),
                             broadcast(dst[:, 1, n, :], 1, n), u_s[:, 0:n, :], v_s[:, 0:n, :])

                powers(pw, p_("re"), p_("im"))
                for l in range(8):
                    ts(pr[:, :, l, :], pw[:, :, 7 - l, :], 1.0, ALU.mult)
                powers(fp, pw[:, 0, 8, :], pw[:, 1, 8, :])
                for n in range(11):
                    if n < 8:
                        re, im = fp[:, 0, n + 1, :], fp[:, 1, n + 1, :]
                    else:
                        a, b = ff[:, 0, n - 1, 0, :], ff[:, 1, n - 1, 1, :]
                        cmul(p_("f_re"), p_("f_im"), a, b, a, b, p_("u"), p_("v"))
                        re, im = p_("f_re"), p_("f_im")
                    ts(ff[:, 0, n, 0, :], re, 1.0, ALU.mult)
                    ts(ff[:, 0, n, 1, :], re, 1.0, ALU.mult)
                    ts(ff[:, 1, n, 0, :], im, -1.0, ALU.mult)
                    ts(ff[:, 1, n, 1, :], im, 1.0, ALU.mult)
                dve.wait_ge(sem["b_in"], 32)
                u_b = t1[:, 0, 0:GP * S5_C].rearrange("p (g h) -> p g h", g=GP)
                v_b = t1[:, 1, 0:GP * S5_C].rearrange("p (g h) -> p g h", g=GP)
                cmul(bb[:, 0, :, :], bb[:, 1, :, :], bc[:, 0, :, :], bc[:, 1, :, :],
                     broadcast(p_("c_re"), 2, S5_C), broadcast(p_("c_im"), 2, S5_C), u_b, v_b)
                u_w = t1[:, 0, 0:GP * 8 * S5_C].rearrange("p (g s h) -> p g s h", g=GP, s=8)
                v_w = t1[:, 1, 0:GP * 8 * S5_C].rearrange("p (g s h) -> p g s h", g=GP, s=8)
                down = [broadcast(pr[:, r, :, :].rearrange("p l g -> p g l"), 3, S5_C) for r in range(2)]
                cmul(BT[:, 0], BT[:, 1], broadcast(bb[:, 0], 2, 8), broadcast(bb[:, 1], 2, 8), down[0], down[1], u_w, v_w)
                dve.tensor_copy(p_("x"), p_("u")).then_inc(sem["bt"], 1)
                for l0 in (0, 8):
                    n = 8 if l0 == 0 else 1
                    up = [broadcast(pw[:, r, l0:l0 + n, :].rearrange("p l g -> p g l"), 3, S5_C) for r in range(2)]
                    c = [broadcast(bc[:, 2 + r], 2, n) for r in range(2)]
                    uu = t1[:, 0, 0:GP * n * S5_C].rearrange("p (g s h) -> p g s h", g=GP, s=n)
                    vv = t1[:, 1, 0:GP * n * S5_C].rearrange("p (g s h) -> p g s h", g=GP, s=n)
                    tt(uu, c[0], up[0], ALU.mult)
                    tt(vv, c[1], up[1], ALU.mult)
                    tt(WL[:, 0, :, l0:l0 + n, :], uu, vv, ALU.subtract)
                    tt(uu, c[0], up[1], ALU.mult)
                    tt(vv, c[1], up[0], ALU.mult)
                    step(dve.scalar_tensor_tensor(out=uu, in0=uu, scalar=-1.0, in1=vv, op0=ALU.mult, op1=ALU.subtract))
                    step(dve.tensor_copy(WL[:, 1, :, l0:l0 + n, :], uu))
                dve.tensor_copy(p_("x"), p_("u")).then_inc(sem["bt"], 1)
                for b in range(4):
                    dve.wait_ge(sem["km_done"], b + 1)
                    part = Km.rearrange("p (g q) x -> p q g x", q=2)[:, b // 2, 4 * (b % 2):4 * (b % 2) + 4, :]
                    step(dve.tensor_copy(part, bank[b][0:S5_C, :].rearrange("p (g x) -> p g x", x=P)))
                    dve.tensor_tensor(part[:, :, 0:S5_C], part[:, :, 0:S5_C], diag[:, :, :].rearrange(
                        "p (g q) x -> p q g x", q=2)[:, b // 2, 4 * (b % 2):4 * (b % 2) + 4, :], ALU.add)\
                        .then_inc(sem["km"], 1)
                dve.wait_ge(sem["xin"], 4)
                body = X[:, :, :, 1:].rearrange("p r g (n j) -> p r g n j", j=SUB)

                def advance(to, of, power, shape, last=False):
                    def factor(kind, r):
                        f = ff[:, kind, power, r, :]
                        for n in shape:
                            f = broadcast(f, len(f.shape), n)
                        return f

                    size = int(np.prod(shape)) * GP
                    names = ["g"] + [f"x{i}" for i in range(len(shape))]
                    dims = {f"x{i}": n for i, n in enumerate(shape)}
                    a, b = (t[:, :, 0:size].rearrange(f"p r ({' '.join(names)}) -> p r {' '.join(names)}", g=GP, **dims)
                            for t in (t1, t2))
                    for r in range(2):
                        dve.tensor_tensor(a[:, r], of[r], factor(0, r), ALU.mult).then_inc(sem["rec"], 1)
                        dve.tensor_tensor(b[:, r], of[1 - r], factor(1, r), ALU.mult).then_inc(sem["rec"], 1)
                    n_rec[0] += 4
                    dve.wait_ge(sem["rec"], n_rec[0])
                    for r in range(2):
                        step(dve.tensor_tensor(a[:, r], a[:, r], b[:, r], ALU.add))
                    for r in range(2):
                        step(dve.tensor_tensor(to[r], to[r], a[:, r], ALU.add))

                n_rec = [0]
                for j in range(1, SUB):
                    advance([body[:, r, :, :, j] for r in range(2)], [body[:, r, :, :, j - 1] for r in range(2)], 0, [RUNS])
                ends = [body[:, r, :, :, SUB - 1] for r in range(2)]
                for i in range(4):
                    d = 1 << i
                    advance([e[:, :, d:] for e in ends], [e[:, :, 0:RUNS - d] for e in ends], 7 + i, [RUNS - d])
                for j in range(SUB - 1):
                    advance([body[:, r, :, 1:, j] for r in range(2)], [e[:, :, 0:RUNS - 1] for e in ends], j, [RUNS - 1])
                dve.tensor_copy(p_("x"), p_("u")).then_inc(sem["bt"], 1)
                flat = t1.rearrange("p r x -> p (r x)")
                dve.wait_ge(sem["glu_in"], 32)
                for b in range(4):
                    dve.wait_ge(sem["y_done"], 4 + b + 1)
                    part = flat[:, HALF * b:HALF * (b + 1)].rearrange("p (t h) -> p t h", t=2)
                    dve.tensor_tensor(part, bank[b][:, :].rearrange("p (t h) -> p t h", t=2), broadcast(bglu[:, :], 1, 2),
                                      ALU.add).then_inc(sem["glu_done"], 1)
                zf = z.rearrange("p t h -> p (t h)")
                sq = t2.rearrange("p r x -> p (r x)")
                dve.wait_ge(sem["gate_done"], 4)
                tt(zf, zf, flat, ALU.mult)
                tt(sq, zf, zf, ALU.mult)
                dve.tensor_reduce(stat[:, 0, :], sq.rearrange("p (t h) -> p t h", h=256), AX_X, ALU.add).then_inc(sem["norm"], 1)
                dve.wait_ge(sem["norm"], 1)
                dve.tensor_scalar(stat[:, 1, :], stat[:, 0, :], 1.0 / 256, EPS, ALU.mult, ALU.add).then_inc(sem["norm"], 1)
                dve.wait_ge(sem["norm"], 3)
                step(dve.reciprocal(stat[:, 3, :], stat[:, 2, :]))
                dve.tensor_tensor(z, z, broadcast(stat[:, 3, :], 2, 256), ALU.mult).then_inc(sem["bt"], 1)

            @block.tensor
            def _(pe):
                for g in range(S5_G):
                    last = pe.transpose(bank[g // 4][:, (g % 4) * C:(g % 4 + 1) * C],
                                        k.s_in[:, g, :, :].rearrange("p s h -> p (s h)"), k.ident[:, :])
                    if g % 4 == 3:
                        last.then_inc(sem["ut_t"], 1)
                pe.wait_ge(sem["bt"], 1)
                for r in range(2):
                    for g in range(GP):
                        n = r * GP + g
                        last = pe.transpose(bank[4 + n // 4][:, (n % 4) * P:(n % 4 + 1) * P],
                                            BT[:, r, g].rearrange("p s h -> p (s h)"), k.ident[:, :])
                        if n % 4 == 3:
                            last.then_inc(sem["bg_t"], 1)
                pe.wait_ge(sem["bt"], 2)
                pe.wait_ge(sem["ut"], 4)
                for n in range(S5_G):
                    q, gp = n // GP, n % GP
                    half = slice(q * 64, (q + 1) * 64)
                    for r in range(2):
                        last = pe.matmul(bank[n // 4][0:S5_C, (n % 4) * P:(n % 4 + 1) * P], bb[half, r, gp, :],
                                         WL[half, r, gp, 0:8, :].rearrange("p l h -> p (l h)"), start=(r == 0), stop=(r == 1))
                    if n % 4 == 3:
                        last.then_inc(sem["km_done"], 1)
                pe.wait_ge(sem["bg"], 4)
                for r in range(2):
                    for gp in range(GP):
                        n = r * GP + gp
                        if n % 4 == 0:
                            pe.wait_ge(sem["km"], n // 4 + 1)
                        for q in range(2):
                            half = slice(q * 64, (q + 1) * 64)
                            last = pe.matmul(bank[n // 4][half, (n % 4) * C:(n % 4 + 1) * C], BG[:, r, gp, half],
                                             UT[:, 2 * gp + q, :], start=True, stop=True)
                        if n % 4 == 3:
                            last.then_inc(sem["xin_done"], 1)
                pe.wait_ge(sem["toep"], 16 * S5_L)
                pe.wait_ge(sem["zero"], 2)
                pe.wait_ge(sem["bt"], 3)
                for n in range(S5_G):
                    q, gp = n // GP, n % GP
                    half = slice(q * 64, (q + 1) * 64)
                    out = bank[n // 4][:, (n % 4) * P:(n % 4 + 1) * P]
                    pe.matmul(out, UT[:, 2 * gp + q, :], T[:, 2 * gp + q, :], start=True, stop=False)
                    for r in range(2):
                        last = pe.matmul(out, X[half, r, gp, 0:C],
                                         WL[half, r, gp, 1:9, :].rearrange("p l h -> p (l h)"), start=False, stop=(r == 1))
                    if n % 4 == 3:
                        last.then_inc(sem["y_done"], 1)
                pe.wait_ge(sem["gelu"], 4)
                for n in range(2):
                    for t in range(S5_L):
                        m = n * S5_L + t
                        last = pe.transpose(bank[4 + m // 4][:, (m % 4) * C:(m % 4 + 1) * C], z[:, t, n * P:(n + 1) * P],
                                            k.ident[:, :])
                        if m % 4 == 3:
                            last.then_inc(sem["zt_done"], 1)
                pe.wait_ge(sem["zt"], 4)
                pe.wait_ge(sem["glu_in"], 32)
                for t in range(S5_L):
                    for n in range(2):
                        last = pe.matmul(bank[t // 2][:, (t % 2) * 256:(t % 2 + 1) * 256], zT[:, n, t, :], wglu[:, n, :],
                                         start=(n == 0), stop=(n == 1))
                    if t % 2:
                        last.then_inc(sem["y_done"], 1)
                pe.wait_ge(sem["bt"], 4)
                for n in range(2):
                    for t in range(S5_L):
                        m = n * S5_L + t
                        last = pe.transpose(bank[4 + m // 4][:, (m % 4) * C:(m % 4 + 1) * C], z[:, t, n * P:(n + 1) * P],
                                            k.ident[:, :])
                        if m % 4 == 3:
                            last.then_inc(sem["yt_done"], 1)


PATTERNS = ((128, 1), (512, 4), (2048, 16))
BLK = 128
O_W = A_W + 2 * A_H


TURN_LAG, SUM_LAG = 2, 3
RING = 4


def attention(k):
    with k.stage() as st:
        v = [k.ring[:, 2 * SLOT:3 * SLOT].rearrange("p (t n) -> p t n", n=A_W),
             k.ring[:, 3 * SLOT:4 * SLOT].rearrange("p (t n) -> p t n", n=A_W),
             k.yT[:, 4:8, :].rearrange("p a (b n) -> p (a b) n", n=A_W)]
        bias = st.sbuf("attn_bias", [P, A_H, 5 * BLK])
        sx = st.sbuf("scores", [P, RING, 2 * BLK])
        pr = st.sbuf("probs", [P, RING, 2 * BLK])
        pT = st.sbuf("probsT", [P, RING, 2 * BLK])
        stage = st.sbuf("out_rows", [P, 2, O_W])
        sb = [st.psum(f"as{i}", [P, HALF]) for i in range(3)]
        tb = [st.psum(f"at{i}", [P, HALF]) for i in range(3)]
        ob = [st.psum(f"ob{i}", [P, HALF]) for i in range(2)]
        v_in = [st.sem(f"v_in{i}") for i in range(3)]
        bias_in = st.sem("bias_in")
        scored, biased, exped, turned, pt_act, pt_dve, summed, rows_out = (st.sem("a_" + n) for n in (
            "scored biased exped turned pt_act pt_dve summed rows_out").split())
        stored = [st.sem(f"rows_stored{i}") for i in range(2)]

        units = [(p, t, h) for p in range(3) for t in range(TT) for h in range(A_H)]

        def columns(src, p, t, h, keys):
            rows = src[(h % 2) * DH:(h % 2 + 1) * DH, h // 2, :]
            if p == 0:
                first = max(t - 1, 0) if keys else t
                return rows[:, first * BLK:(t + 1) * BLK]
            if p == 1:
                n, r = t // 4, t % 4
                first = 0 if keys else n
                return rows[:, first * 4 * BLK:(n + 1) * 4 * BLK].rearrange("p (i r) -> p r i", r=4)[:, r, :]
            return rows.rearrange("p (i u) -> p u i", u=TT)[:, t, :]

        def width(p, t):
            return 2 * BLK if (p == 0 and t) or (p == 1 and t >= 4) else BLK

        def bias_of(p, t, h):
            end = (2, 4, 5)[p] * BLK
            return bias[:, h, end - width(p, t):end]

        def values(p, t, h):
            tiles = {0: [t - 1, t], 1: [t - 4, t], 2: [t]}[p] if width(p, t) > BLK or p == 2 else [t]
            return [v[p][:, x, h * DH:(h + 1) * DH] for x in tiles]

        def wait_turned_out(eng, i):
            if i % 3 == 0:
                eng.wait_ge(pt_act, i // 3 + 1)
            else:
                eng.wait_ge(pt_dve, i - i // 3)

        def evacuate(eng, i, copy, sem):
            if i >= RING:
                eng.wait_ge(summed, i - RING + 1)
            eng.wait_ge(turned, i + 1)
            w = width(*units[i][:2])
            copy(pT[:, i % RING, 0:w], tb[i % 3][:, 0:w]).then_inc(sem, 1)

        with st.block() as block:

            @block.sync
            def _(sp):
                sp.dma_start(bias[:, :, :], k.w["attn_bias"]).then_inc(bias_in, 16)
                sp.dma_start(v[0], k.v_dram.rearrange("(t i) n -> i t n", i=P)).then_inc(v_in[0], 16)
                sp.dma_start(v[1], k.v_dram.rearrange("(b i r) n -> i b r n", b=2, r=4)).then_inc(v_in[1], 16)
                sp.dma_start(v[2], k.v_dram.rearrange("(i u) n -> i u n", u=TT)).then_inc(v_in[2], 16)
                for n in range(3 * TT):
                    p, t = n // TT, n % TT
                    sp.wait_ge(rows_out, n + 1)
                    dst = k.attn_dram[p]
                    src = stage[:, n % 2, :]
                    if p == 0:
                        sp.dma_start(dst[t * BLK:(t + 1) * BLK, :], src).then_inc(stored[n % 2], 16)
                    elif p == 1:
                        sp.dma_start(dst.rearrange("(b i r) n -> b r i n", b=2, r=4)[t // 4, t % 4], src)\
                            .then_inc(stored[n % 2], 16)
                    else:
                        sp.dma_start(dst.rearrange("(i u) n -> u i n", u=TT)[t], src).then_inc(stored[n % 2], 16)
                for i in range(2):
                    sp.wait_ge(stored[i], 16 * (3 * TT // 2))

            def wait_stage(eng, n):
                if n >= 2:
                    eng.wait_ge(stored[n % 2], 16 * (n // 2))

            @block.scalar
            def _(act):
                for i in range(len(units) + SUM_LAG + 1):
                    if i < len(units):
                        p, t, h = units[i]
                        n = i // A_H
                        if h == 0:
                            wait_stage(act, n)
                        act.wait_ge(biased, i + 1)
                        if i >= RING:
                            act.wait_ge(turned, i - RING + 1)
                        w = width(p, t)
                        act.activation(pr[:, i % RING, 0:w], sx[:, i % RING, 0:w], ACT.Exp, scale=-1.0,
                                       bias=stage[:, n % 2, A_W + h:A_W + h + 1],
                                       accum_out=stage[:, n % 2, A_W + A_H + h:A_W + A_H + h + 1]).then_inc(exped, 1)
                    if TURN_LAG <= i < len(units) + TURN_LAG and (i - TURN_LAG) % 3 == 0:
                        evacuate(act, i - TURN_LAG, lambda o, x: act.activation(o, x, ACT.Copy), pt_act)
                    j = i - SUM_LAG - 1
                    if j >= 0 and j % A_H == A_H - 1:
                        n = j // A_H
                        act.wait_ge(summed, A_H * (n + 1))
                        act.activation(stage[:, n % 2, 0:A_W], ob[n % 2][:, :], ACT.Copy).then_inc(rows_out, 1)

            @block.vector
            def _(dve):
                dve.wait_ge(bias_in, 16)
                for i in range(len(units) + TURN_LAG):
                    if i < len(units):
                        p, t, h = units[i]
                        n = i // A_H
                        if h == 0:
                            wait_stage(dve, n)
                        dve.wait_ge(scored, i + 1)
                        if i >= RING:
                            dve.wait_ge(exped, i - RING + 1)
                        w = width(p, t)
                        dve.tensor_tensor_reduce(sx[:, i % RING, 0:w], sb[i % 3][:, 0:w], bias_of(p, t, h), -1.0, -NEG,
                                                 ALU.add, ALU.min, stage[:, n % 2, A_W + h:A_W + h + 1]).then_inc(biased, 1)
                    if i >= TURN_LAG and (i - TURN_LAG) % 3:
                        evacuate(dve, i - TURN_LAG, lambda o, x: dve.tensor_copy(o, x), pt_dve)

            @block.tensor
            def _(pe):
                for i in range(len(units) + SUM_LAG):
                    if i < len(units):
                        p, t, h = units[i]
                        if i >= 3:
                            pe.wait_ge(biased, i - 2)
                        pe.matmul(sb[i % 3][:, 0:width(p, t)], columns(k.qT, p, t, h, False), columns(k.kT, p, t, h, True),
                                  start=True, stop=True).then_inc(scored, 1)
                    if TURN_LAG <= i < len(units) + TURN_LAG:
                        j = i - TURN_LAG
                        pe.wait_ge(exped, j + 1)
                        if j >= 3:
                            wait_turned_out(pe, j - 3)
                        for c in range(width(*units[j][:2]) // BLK):
                            last = pe.transpose(tb[j % 3][:, c * BLK:(c + 1) * BLK], pr[:, j % RING, c * BLK:(c + 1) * BLK],
                                                k.ident[:, :])
                        last.then_inc(turned, 1)
                    if i >= SUM_LAG:
                        j = i - SUM_LAG
                        p, t, h = units[j]
                        n = j // A_H
                        if t == 0 and h == 0:
                            pe.wait_ge(v_in[p], 16)
                        if h == 0 and n >= 2:
                            pe.wait_ge(rows_out, n - 1)
                        wait_turned_out(pe, j)
                        vs = values(p, t, h)
                        for c, x in enumerate(vs):
                            last = pe.matmul(ob[n % 2][:, h * DH:(h + 1) * DH], pT[:, j % RING, c * BLK:(c + 1) * BLK], x,
                                             start=(c == 0), stop=(c == len(vs) - 1))
                        last.then_inc(summed, 1)


def join_patterns(k):
    with k.stage() as st:
        rows = st.sbuf("pattern_rows", [P, 2, 3, O_W])
        e = st.sbuf("join_small", [P, 2, 10, A_H])
        y = st.sbuf("join_y", [P, 2, A_W])
        tmp = st.sbuf("join_tmp", [P, 2, 2, A_W])
        stat = st.sbuf("join_stat", [P, TT, 4])
        bank = [st.psum(f"jb{i}", [P, HALF]) for i in range(2)]
        rows_in = [[st.sem(f"rows_in{i}{p}") for p in range(3)] for i in range(2)]
        diff, exped, factor, mixed, pooled, added, squared, var, root, inv, scaled, turned, out, chain = (
            st.sem("j_" + n) for n in ("diff exped factor mixed pooled added squared var root inv scaled turned out "
                                       "chain").split())
        gain0 = VECS["a_gain"][0]

        def num(t, p):
            return rows[:, t % 2, p, 0:A_W].rearrange("p (h e) -> p h e", e=DH)

        with st.block() as block:

            @block.sync
            def _(sp):
                for t in range(TT):
                    if t >= 2:
                        sp.wait_ge(mixed, t - 1)
                        sp.wait_ge(pooled, 2 * (t - 1))
                    for p in range(3):
                        sp.dma_start(rows[:, t % 2, p, :], k.attn_dram[p, t * P:(t + 1) * P, :]).then_inc(rows_in[t % 2][p], 16)

            @block.gpsimd
            def _(pool):
                for t in range(TT):
                    pool.wait_ge(factor, t + 1)
                    if t >= 2:
                        pool.wait_ge(added, t - 1)
                    for p in (1, 2):
                        pool.tensor_tensor(tmp[:, t % 2, p - 1, :].rearrange("p (h e) -> p h e", e=DH), num(t, p),
                                           broadcast(e[:, t % 2, 6 + p, :], 2, DH), ALU.mult).then_inc(pooled, 1)

            @block.scalar
            def _(act):
                for t in range(TT):
                    act.wait_ge(diff, t + 1)
                    act.activation(e[:, t % 2, 1:4, :], e[:, t % 2, 1:4, :], ACT.Exp).then_inc(exped, 1)
                    act.wait_ge(added, t + 1)
                    act.activation(tmp[:, t % 2, 0, :], y[:, t % 2, :], ACT.Square, accum_out=stat[:, t, 0:1]).then_inc(squared, 1)
                    act.wait_ge(var, t + 1)
                    act.activation(stat[:, t, 2:3], stat[:, t, 1:2], ACT.Sqrt).then_inc(root, 1)

            @block.vector
            def _(dve):
                count = [0]

                def step(ins):
                    count[0] += 1
                    ins.then_inc(chain, 1)
                    dve.wait_ge(chain, count[0])

                def store(t):
                    dve.wait_ge(turned, t + 1)
                    dve.tensor_tensor(k.yT[:, 4:8, t * P:(t + 1) * P], bank[t % 2][:, :].rearrange("p (a b) -> p a b", a=4),
                                      broadcast(k.vec[:, gain0:gain0 + 4], 2, P), ALU.mult).then_inc(out, 1)

                for t in range(TT):
                    for p in range(3):
                        dve.wait_ge(rows_in[t % 2][p], 16 * (t // 2 + 1))
                    s = e[:, t % 2]
                    lo = [rows[:, t % 2, p, A_W:A_W + A_H] for p in range(3)]
                    total = rows[:, t % 2, :, A_W + A_H:]
                    step(dve.tensor_tensor(s[:, 0, :], lo[0], lo[1], ALU.min))
                    step(dve.tensor_tensor(s[:, 0, :], s[:, 0, :], lo[2], ALU.min))
                    dve.tensor_tensor(s[:, 1:4, :], broadcast(s[:, 0, :], 1, 3), rows[:, t % 2, :, A_W:A_W + A_H],
                                      ALU.subtract).then_inc(diff, 1)
                    dve.wait_ge(exped, t + 1)
                    step(dve.tensor_tensor(s[:, 4:7, :], s[:, 1:4, :], total, ALU.mult))
                    step(dve.tensor_tensor(s[:, 4, :], s[:, 4, :], s[:, 5, :], ALU.add))
                    step(dve.tensor_tensor(s[:, 4, :], s[:, 4, :], s[:, 6, :], ALU.add))
                    step(dve.reciprocal(s[:, 5, :], s[:, 4, :]))
                    if t >= 2:
                        dve.wait_ge(pooled, 2 * (t - 1))
                    dve.tensor_tensor(s[:, 6:9, :], s[:, 1:4, :], broadcast(s[:, 5, :], 1, 3), ALU.mult).then_inc(factor, 1)
                    dve.wait_ge(factor, t + 1)
                    yt = y[:, t % 2, :]
                    if t >= 2:
                        dve.wait_ge(turned, t - 1)
                    dve.tensor_tensor(yt.rearrange("p (h e) -> p h e", e=DH), num(t, 0), broadcast(s[:, 6, :], 2, DH),
                                      ALU.mult).then_inc(mixed, 1)
                    dve.wait_ge(mixed, t + 1)
                    dve.wait_ge(pooled, 2 * t + 2)
                    step(dve.tensor_tensor(yt, yt, tmp[:, t % 2, 0, :], ALU.add))
                    dve.tensor_tensor(yt, yt, tmp[:, t % 2, 1, :], ALU.add).then_inc(added, 1)
                    if t >= 1:
                        store(t - 1)
                    dve.wait_ge(squared, t + 1)
                    dve.tensor_scalar(stat[:, t, 1:2], stat[:, t, 0:1], 1.0 / A_W, EPS, ALU.mult, ALU.add).then_inc(var, 1)
                    dve.wait_ge(root, t + 1)
                    step(dve.reciprocal(stat[:, t, 3:4], stat[:, t, 2:3]))
                    dve.tensor_scalar(yt, yt, stat[:, t, 3:4], None, ALU.mult).then_inc(scaled, 1)
                store(TT - 1)

            @block.tensor
            def _(pe):
                for t in range(TT):
                    pe.wait_ge(scaled, t + 1)
                    if t >= 2:
                        pe.wait_ge(out, t - 1)
                    for a in range(4):
                        last = pe.transpose(bank[t % 2][:, a * P:(a + 1) * P], y[:, t % 2, a * P:(a + 1) * P], k.ident[:, :])
                    last.then_inc(turned, 1)


def output_projection(k, name, src, chunks, load_x):
    with k.stage() as st:
        bank = [st.psum(f"{name}_p{i}", [P, HALF]) for i in range(4)]
        product, added = st.sem(name + "_product"), st.sem(name + "_added")
        x_in = [st.sem(f"{name}_x_in{t}") for t in range(TT)] if load_x else []
        tiles, weights = Split(st, name + "_tiles"), Split(st, name + "_weights")
        w = [st.sbuf(f"{name}_w{part}", [P, KT, HALF]) for part in ("high", "low")]
        tile = [st.sbuf(f"{name}_t{part}", [P, 2, KT, P]) for part in ("high", "low")]
        n_groups = 2 * TT
        with st.block() as block:

            @block.sync
            def _(sp):
                if load_x:
                    for t in range(TT):
                        sp.dma_start(k.x[:, t, :], k.w["x"][t * P:(t + 1) * P, :]).then_inc(x_in[t], 16)

            @block.vector
            def _(dve):
                def split_tile(g):
                    t = g % TT
                    if g >= 2:
                        dve.wait_ge(product, g - 1)
                    tiles.piece(dve, src[:, :, t * P:(t + 1) * P], [part[:, g % 2] for part in tile])

                def add(g):
                    h, t = g // TT, g % TT
                    if load_x:
                        dve.wait_ge(x_in[t], 16)
                    dve.wait_ge(product, g + 1)
                    part = k.x[:, t, h * HALF:(h + 1) * HALF]
                    dve.tensor_tensor(part, part, bank[g % 4][:, :], ALU.add).then_inc(added, 1)

                for g in range(n_groups):
                    h = g // TT
                    if g == 0:
                        split_tile(0)
                    if g % TT == 0:
                        dve.wait_ge(k.chunk_in[chunks[h]], 16)
                        if g:
                            dve.wait_ge(product, g)
                        for c in range(KT):
                            weights.piece(dve, k.chunk(chunks[h], HALF)[:, c, :], [part[:, c, :] for part in w])
                    if g + 1 < n_groups:
                        split_tile(g + 1)
                    if g:
                        add(g - 1)
                add(n_groups - 1)

            @block.tensor
            def _(pe):
                for g in range(n_groups):
                    h, t = g // TT, g % TT
                    if g >= 4:
                        pe.wait_ge(added, g - 3)
                    pe.wait_ge(tiles.done, g + 1)
                    for c in range(KT):
                        if t == 0:
                            pe.wait_ge(weights.done, KT * h + c + 1)
                        last = split_product(pe, bank[g % 4][:, :], [part[:, g % 2, c, :] for part in tile],
                                             [part[:, c, :] for part in w], c == 0, c == KT - 1)
                    last.then_inc(product, 1)


def memory_projections(k):
    MT = MEM // P
    with k.stage() as st:
        mem, gain, ring = k.xqT[:, 0:2, :], k.xqT[:, 2:4, :], k.xqT[:, 4:8, :]
        stat = st.sbuf("xa_stat", [P, TT, 4])
        mstat = st.sbuf("mem_stat", [P, MT, 4])
        memory = [st.sbuf(f"memory_{part}", [P, KT, MEM]) for part in ("high", "low")]
        tb = [st.psum(f"xa_turn{i}", [P, HALF]) for i in range(4)]
        gb = [st.psum(f"xa_gemm{i}", [P, HALF]) for i in range(4)]
        gain_in, mem_in = st.sem("xa_gain_in"), st.sem("mem_in")
        product, out_act, out_dve = st.sem("xa_product"), st.sem("xa_out_act"), st.sem("xa_out_dve")

        def transposes(part):
            return lambda t, h: part[:, 4 * h:4 * h + 4, t * P:(t + 1) * P]

        mnorm = Norm(st, "mem", MT, lambda t: mem[:, t, :], gain[:, 1, :], transposes(memory[0]), tb, ring, mstat,
                     lambda eng, t: eng.wait_ge(mem_in, 16), low=transposes(memory[1]))
        xnorm = Norm(st, "xa", TT, lambda t: k.x[:, t, :], gain[:, 0, :], transposes(k.xn[0]), tb, ring, stat,
                     lambda eng, t: None, low=transposes(k.xn[1]))
        w = Pieces(k, st, "xa_w")
        for m in range(KT):
            part = w.add(7 + m // 2, 256, (m % 2) * P, (m % 2 + 1) * P)
            for h in range(2):
                half = slice(h * HALF, (h + 1) * HALF)
                w.group(columns(part, 0, P), columns(k.xn, half.start, half.stop), HALF, k.xqT[:, m, half], X_DH ** -0.5)
        for m in range(KT):
            part = w.add(11 + m // 2, 256, (m % 2) * P, (m % 2 + 1) * P)
            w.group(columns(part, 0, P), columns(memory, 0, MEM), MEM, k.xkT[:, m, :], 1.0)
        for h in range(4):
            part = w.add(15 + h, 256, 0, 256)
            for t in range(MT):
                w.group(columns(memory, t * P, (t + 1) * P), columns(part, 0, 256), 256,
                        k.xv[:, t, h * 256:(h + 1) * 256], 1.0)
        groups, firsts = w.groups, w.firsts()

        with st.block() as block:

            @block.sync
            def _(sp):
                sp.dma_start(mem, k.w["mem"].rearrange("(t p) n -> p t n", p=P)).then_inc(mem_in, 16)
                sp.dma_start(gain[:, 1, :], k.w["norm_mem"][0:1, :].partition_broadcast(P)).then_inc(gain_in, 16)
                sp.dma_start(gain[:, 0, :], k.w["norm_xattn"][0:1, :].partition_broadcast(P)).then_inc(gain_in, 16)
                for i in range(7, 19):
                    if i >= 10:
                        sp.wait_ge(w.split.done, w.chunk_end(i - 3))
                    load_chunk(k, sp, i)

            @block.scalar
            def _(act):
                mnorm.scalar(act)
                act.wait_ge(mnorm.turned, 2 * MT)
                xnorm.scalar(act)
                for g in range(0, len(groups), 2):
                    act.wait_ge(product, g + 1)
                    act.activation(groups[g][3], gb[g % 4][:, 0:groups[g][2]], ACT.Copy, scale=groups[g][4]).then_inc(out_act, 1)

            @block.vector
            def _(dve):
                dve.wait_ge(gain_in, 32)
                mnorm.vector(dve)
                xnorm.vector(dve)
                w.vector(dve, 0, product)
                for n in range(len(w.pieces)):
                    for g in range(firsts[n], firsts[n + 1]):
                        if n + 1 < len(w.pieces) and g == max(firsts[n], w.pieces[n + 1][3] - 1):
                            w.vector(dve, n + 1, product)
                        if g % 2:
                            dve.wait_ge(product, g + 1)
                            dve.tensor_scalar(groups[g][3], gb[g % 4][:, 0:groups[g][2]], groups[g][4], None, ALU.mult)\
                                .then_inc(out_dve, 1)

            @block.tensor
            def _(pe):
                mnorm.tensor(pe)
                mnorm.wait_all(pe)
                xnorm.tensor(pe)
                xnorm.wait_all(pe)
                for g, (lhs, rhs, cols, _, _) in enumerate(groups):
                    if g in firsts:
                        pe.wait_ge(w.split.done, firsts.index(g) + 1)
                    if g >= 4:
                        pe.wait_ge((out_act, out_dve)[g % 2], (g - 4) // 2 + 1)
                    for c in range(KT):
                        last = split_product(pe, gb[g % 4][:, 0:cols], lhs(c), rhs(c), c == 0, c == KT - 1)
                    last.then_inc(product, 1)


def memory_attention(k):
    with k.stage() as st:
        pr = st.sbuf("xa_probs", [P, RING, MEM])
        pT = st.sbuf("xa_probsT", [P, RING, MEM])
        small = st.sbuf("xa_small", [P, X_H * TT, 4])
        sb = [st.psum(f"xs{i}", [P, HALF]) for i in range(3)]
        tb = [st.psum(f"xt{i}", [P, HALF]) for i in range(2)]
        ob = [st.psum(f"xo{i}", [P, HALF]) for i in range(2)]
        scored, maxed, exped, inverse, normed, turned, pt, mixed, out = (st.sem("x_" + n) for n in (
            "scored maxed exped inverse normed turned pt mixed out").split())
        units = [(t, h) for t in range(TT) for h in range(X_H)]
        n_units = len(units)
        oT = k.mixedT
        zero_row = st.sbuf("y_zero", [P, D])
        cleared, y_zeroed = st.sem("zero_row_set"), st.sem("y_zeroed")

        with st.block() as block:

            @block.gpsimd
            def _(pool):
                pool.memset(zero_row[:, :], 0.0).then_inc(cleared, 1)

            @block.sync
            def _(sp):
                load_chunk(k, sp, 19)
                load_chunk(k, sp, 20)
                sp.wait_ge(cleared, 1)
                sp.dma_start(k.y_dram[EXPERTS * BLOCK:, :].rearrange("(n p) d -> p n d", p=P),
                             broadcast(zero_row[:, :], 1, EXTRA)).then_inc(y_zeroed, 16)
                sp.wait_ge(y_zeroed, 16)

            @block.scalar
            def _(act):
                for i in range(n_units + SUM_LAG + 1):
                    if i < n_units:
                        act.wait_ge(maxed, i + 1)
                        if i >= RING:
                            act.wait_ge(turned, i - RING + 1)
                        act.activation(pr[:, i % RING, :], sb[i % 3][:, 0:MEM], ACT.Exp, bias=small[:, i, 0:1],
                                       accum_out=small[:, i, 1:2]).then_inc(exped, 1)
                    if i >= SUM_LAG + 1:
                        j = i - SUM_LAG - 1
                        t, h = units[j]
                        act.wait_ge(mixed, j + 1)
                        act.activation(oT[:, 2 * h:2 * h + 2, t * P:(t + 1) * P],
                                       ob[j % 2][:, 0:2 * P].rearrange("p (a b) -> p a b", a=2), ACT.Copy).then_inc(out, 1)

            @block.vector
            def _(dve):
                for i in range(n_units + TURN_LAG):
                    if i < n_units:
                        dve.wait_ge(scored, i + 1)
                        dve.tensor_reduce(small[:, i, 0:1], sb[i % 3][:, 0:MEM], AX_X, ALU.max, negate=True).then_inc(maxed, 1)
                    if 1 <= i <= n_units:
                        j = i - 1
                        dve.wait_ge(exped, j + 1)
                        dve.reciprocal(small[:, j, 2:3], small[:, j, 1:2]).then_inc(inverse, 1)
                        dve.wait_ge(inverse, j + 1)
                        dve.tensor_scalar(pr[:, j % RING, :], pr[:, j % RING, :], small[:, j, 2:3], None, ALU.mult).then_inc(normed, 1)
                    if i >= TURN_LAG:
                        j = i - TURN_LAG
                        dve.wait_ge(turned, j + 1)
                        if j >= RING:
                            dve.wait_ge(mixed, j - RING + 1)
                        dve.tensor_copy(pT[:, j % RING, :], tb[j % 2][:, 0:MEM]).then_inc(pt, 1)

            @block.tensor
            def _(pe):
                for i in range(n_units + SUM_LAG):
                    if i < n_units:
                        t, h = units[i]
                        if i >= 3:
                            pe.wait_ge(exped, i - 2)
                        for c in range(2):
                            last = pe.matmul(sb[i % 3][:, 0:MEM], k.xqT[:, 2 * h + c, t * P:(t + 1) * P], k.xkT[:, 2 * h + c, :],
                                             start=(c == 0), stop=(c == 1))
                        last.then_inc(scored, 1)
                    if TURN_LAG <= i < n_units + TURN_LAG:
                        j = i - TURN_LAG
                        pe.wait_ge(normed, j + 1)
                        if j >= 2:
                            pe.wait_ge(pt, j - 1)
                        for c in range(2):
                            last = pe.transpose(tb[j % 2][:, c * P:(c + 1) * P], pr[:, j % RING, c * P:(c + 1) * P], k.ident[:, :])
                        last.then_inc(turned, 1)
                    if i >= SUM_LAG:
                        j = i - SUM_LAG
                        t, h = units[j]
                        pe.wait_ge(pt, j + 1)
                        if j >= 2:
                            pe.wait_ge(out, j - 1)
                        for e in range(2):
                            for c in range(2):
                                last = pe.matmul(ob[j % 2][:, e * P:(e + 1) * P],
                                                 k.xv[:, c, h * X_DH + e * P:h * X_DH + (e + 1) * P],
                                                 pT[:, j % RING, c * P:(c + 1) * P], start=(c == 0), stop=(c == 1))
                        last.then_inc(mixed, 1)


GROUPS = 4
GROUP_E = 8
EXPERTS = GROUPS * GROUP_E
TOP_K = 2
ROUTES = GROUPS + EXPERTS
BLOCK = 128
DE = 512
GU_K, DN_K = D // P, DE // P
EXTRA = S * TOP_K // BLOCK
BLOCKS = EXPERTS + EXTRA


def load_expert(k, queue, e, par, gu_in, dn_in):
    queue.dma_start(k.w_gu(par), k.w["expert_w_gu"][e].rearrange("(k p) n -> p k n", p=P)).then_inc(gu_in, 16)
    queue.dma_start(k.w_dn(par), k.w["expert_w_down"][e].rearrange("(k p) n -> p k n", p=P)).then_inc(dn_in, 16)


class Count:

    def __init__(self):
        self.n = 0

    def up(self):
        self.n += 1
        return self.n


def router(k):
    with k.stage() as st:
        ring = st.sbuf("ffn_scaled", [P, 3, D])
        gain = st.sbuf("ffn_gain", [P, D])
        stat = st.sbuf("ffn_stat", [P, TT, 4])
        wr = st.sbuf("router_w", [P, KT, ROUTES])
        bias = st.sbuf("router_b", [P, ROUTES])
        const = st.sbuf("route_const", [P, P + EXPERTS])
        tri, numbers = const[:, 0:P], const[:, P:]
        ones = st.sbuf("ones", [P, P])
        zero = st.sbuf("idx_zero", [P, BLOCKS * BLOCK // P], U32)
        token = st.sbuf("token_ids", [P, TT], U32)
        logit = st.sbuf("logit", [P, TT, ROUTES])
        gp = st.sbuf("group_p", [P, TT, GROUPS])
        g1 = st.sbuf("group_tmp", [P, TT, GROUPS])
        pick = st.sbuf("pick", [P, TT, GROUP_E, GROUPS])
        ep = st.sbuf("expert_p", [P, TT, GROUP_E])
        e1 = st.sbuf("expert_tmp", [P, TT, GROUP_E])
        s = st.sbuf("route_small", [P, 12, TT])
        hot = st.sbuf("hot", [P, TOP_K, TT, EXPERTS])
        both = st.sbuf("both", [P, TT, EXPERTS])
        before = st.sbuf("before", [P, TT, EXPERTS])
        total = st.sbuf("total", [P, EXPERTS])
        place = st.sbuf("place", [P, TT, EXPERTS])
        spread = st.sbuf("spread", [P, TT, EXPERTS])
        dest = st.sbuf("dest_f", [P, TOP_K, TT])
        more = st.sbuf("more", [P, EXPERTS, TT])
        tables = st.sbuf("tables", [P, 3, EXPERTS])
        extra, upto, jump = (tables[:, i, :] for i in range(3))
        zrow = st.sbuf("zero_row", [P, EXPERTS])
        past = st.sbuf("past", [1, EXTRA, EXPERTS])
        owner = st.sbuf("owner", [1, EXTRA])
        tb = [st.psum(f"ffn_turn{i}", [P, HALF]) for i in range(4)]
        lb = st.psum("logits", [P, HALF])
        rb = st.psum("ranks", [P, HALF])
        cb = st.psum("counts", [P, HALF])
        gain_in, const_in, zeroed = st.sem("ffn_gain_in"), st.sem("route_const_in"), st.sem("zeroed")
        filled, product, ranked, exped, step, shifted, marked, placed = (st.sem(n) for n in
            "filled r_product ranked exped route_step shifted marked placed".split())
        keep = [st.sem(f"xn_stored{i}") for i in range(2)]
        norm = Norm(st, "ffn", TT, lambda t: k.x[:, t, :], gain[:, :],
                    lambda t, h: k.yT[:, 4 * h:4 * h + 4, t * P:(t + 1) * P], tb, ring, stat, lambda eng, t: None, keep)
        scattered = st.sem("scattered")
        gmax, gsum, gbest, gprob, emax, esum, pair_sum, unused = (s[:, i, :] for i in range(8))
        best = [s[:, 8, :], s[:, 9, :]]
        top = [s[:, 10, :], s[:, 11, :]]
        BIG = 64.0

        with st.block() as block:

            @block.sync
            def _(sp):
                sp.dma_start(gain[:, :], k.w["norm_ffn"][0:1, :].partition_broadcast(P)).then_inc(gain_in, 16)
                sp.dma_start(wr[:, :, :], k.w["router_w"].rearrange("(k p) n -> p k n", p=P)).then_inc(const_in, 16)
                sp.dma_start(bias[:, :], k.w["router_b"][0:1, :].partition_broadcast(P)).then_inc(const_in, 16)
                sp.dma_start(const[:, :], k.w["route_const"]).then_inc(const_in, 16)
                sp.wait_ge(filled, 2)
                sp.dma_start(k.idx_dram.rearrange("(p n) o -> p (n o)", p=P), zero[:, :]).then_inc(zeroed, 16)
                for t in range(TT):
                    sp.wait_ge(norm.scaled, t + 1)
                    sp.dma_start(k.xn_dram[t * P:(t + 1) * P, :], ring[:, t % 2, :]).then_inc(keep[t % 2], 16)
                for par in range(2):
                    load_expert(k, sp, par, par, k.gu_in[par], k.dn_in[par])
                for i in range(2):
                    sp.wait_ge(keep[i], 16 * (TT // 2))

            @block.gpsimd
            def _(pool):
                pool.memset(ones[:, :], 1.0).then_inc(filled, 1)
                pool.memset(zero[:, :], 0).then_inc(filled, 1)
                pool.memset(zrow[:, :], 0.0).then_inc(filled, 1)
                pool.iota(token[:, :], [[P, TT]], base=0, channel_multiplier=1).then_inc(filled, 1)
                pool.wait_ge(filled, 4)
                pool.wait_ge(zeroed, 16)
                pool.wait_ge(placed, 1)
                for j in range(TOP_K):
                    for t in range(TT):
                        i = j * TT + t
                        pool.indirect_dma_start(k.idx_dram, bass.IndirectOffsetOnAxis(k.dest[:, i:i + 1], 0),
                                                token[:, t:t + 1], None).then_inc(scattered, 16)
                pool.wait_ge(scattered, 16 * TOP_K * TT)

            @block.scalar
            def _(act):
                norm.scalar(act)
                act.wait_ge(shifted, 1)
                act.activation(gp[:, :, :], gp[:, :, :], ACT.Exp).then_inc(exped, 1)
                act.wait_ge(shifted, 2)
                act.activation(ep[:, :, :], ep[:, :, :], ACT.Exp).then_inc(exped, 1)

            @block.tensor
            def _(pe):
                norm.tensor(pe)
                pe.wait_ge(const_in, 48)
                for t in range(TT):
                    pe.wait_ge(norm.evac_act, t + 1)
                    pe.wait_ge(norm.evac_dve, t + 1)
                    for c in range(KT):
                        last = pe.matmul(lb[:, t * ROUTES:(t + 1) * ROUTES], k.yT[:, c, t * P:(t + 1) * P], wr[:, c, :],
                                         start=(c == 0), stop=(c == KT - 1))
                    last.then_inc(product, 1)
                pe.wait_ge(filled, 1)
                pe.wait_ge(marked, 1)
                cols = TT * EXPERTS
                flat = [v[:, :, :].rearrange("p t e -> p (t e)") for v in (both, before)]
                pe.matmul(rb[:, 0:cols], tri, flat[0], start=True, stop=False)
                pe.matmul(rb[:, 0:cols], ones[:, :], flat[1], start=False, stop=True).then_inc(ranked, 1)
                pe.matmul(cb[:, 0:EXPERTS], ones[:, :], total[:, :], start=True, stop=True).then_inc(ranked, 1)

            @block.vector
            def _(dve):
                n = Count()

                def first_index(p, top_p, width, tmp, out):
                    dve.tensor_tensor(tmp, p, broadcast(top_p, 2, width), ALU.is_equal).then_inc(step, 1)
                    dve.wait_ge(step, n.up())
                    dve.scalar_tensor_tensor(out=tmp, in0=tmp, scalar=-BIG, in1=broadcast(numbers[:, 0:width], 1, TT),
                                             op0=ALU.mult, op1=ALU.add).then_inc(step, 1)
                    dve.wait_ge(step, n.up())
                    dve.tensor_reduce(out, tmp, AX_X, ALU.min).then_inc(step, 1)
                    dve.wait_ge(step, n.up())
                    dve.tensor_scalar(out, out, BIG, None, ALU.add).then_inc(step, 1)
                    dve.wait_ge(step, n.up())

                dve.wait_ge(gain_in, 16)
                norm.vector(dve)
                dve.wait_ge(const_in, 48)
                dve.wait_ge(product, TT)
                dve.tensor_tensor(logit[:, :, :], lb[:, 0:TT * ROUTES].rearrange("p (t n) -> p t n", n=ROUTES),
                                  broadcast(bias[:, :], 1, TT), ALU.add).then_inc(step, 1)
                dve.wait_ge(step, n.up())
                dve.tensor_reduce(gmax, logit[:, :, 0:GROUPS], AX_X, ALU.max).then_inc(step, 1)
                dve.wait_ge(step, n.up())
                dve.tensor_tensor(gp[:, :, :], logit[:, :, 0:GROUPS], broadcast(gmax, 2, GROUPS), ALU.subtract)\
                    .then_inc(shifted, 1)
                dve.wait_ge(exped, 1)
                dve.tensor_reduce(gsum, gp[:, :, :], AX_X, ALU.add).then_inc(step, 1)
                dve.wait_ge(step, n.up())
                dve.reciprocal(gsum, gsum).then_inc(step, 1)
                dve.wait_ge(step, n.up())
                dve.tensor_tensor(gp[:, :, :], gp[:, :, :], broadcast(gsum, 2, GROUPS), ALU.mult).then_inc(step, 1)
                dve.wait_ge(step, n.up())
                dve.tensor_reduce(gprob, gp[:, :, :], AX_X, ALU.max).then_inc(step, 1)
                dve.wait_ge(step, n.up())
                first_index(gp[:, :, :], gprob, GROUPS, g1[:, :, :], gbest)
                dve.tensor_tensor(g1[:, :, :], broadcast(numbers[:, 0:GROUPS], 1, TT), broadcast(gbest, 2, GROUPS),
                                  ALU.is_equal).then_inc(step, 1)
                dve.wait_ge(step, n.up())
                dve.tensor_tensor(pick[:, :, :, :], logit[:, :, GROUPS:].rearrange("p t (g j) -> p t j g", g=GROUPS),
                                  broadcast(g1[:, :, :], 2, GROUP_E), ALU.mult).then_inc(step, 1)
                dve.wait_ge(step, n.up())
                dve.tensor_reduce(ep[:, :, :], pick[:, :, :, :], AX_X, ALU.add).then_inc(step, 1)
                dve.wait_ge(step, n.up())
                dve.tensor_reduce(emax, ep[:, :, :], AX_X, ALU.max).then_inc(step, 1)
                dve.wait_ge(step, n.up())
                dve.tensor_tensor(ep[:, :, :], ep[:, :, :], broadcast(emax, 2, GROUP_E), ALU.subtract).then_inc(shifted, 1)
                dve.wait_ge(exped, 2)
                dve.tensor_reduce(esum, ep[:, :, :], AX_X, ALU.add).then_inc(step, 1)
                dve.wait_ge(step, n.up())
                dve.reciprocal(esum, esum).then_inc(step, 1)
                dve.wait_ge(step, n.up())
                dve.tensor_tensor(ep[:, :, :], ep[:, :, :], broadcast(esum, 2, GROUP_E), ALU.mult).then_inc(step, 1)
                dve.wait_ge(step, n.up())
                for j in range(TOP_K):
                    dve.tensor_reduce(top[j], ep[:, :, :], AX_X, ALU.max).then_inc(step, 1)
                    dve.wait_ge(step, n.up())
                    first_index(ep[:, :, :], top[j], GROUP_E, e1[:, :, :], best[j])
                    if j == 0:
                        dve.tensor_tensor(e1[:, :, :], broadcast(numbers[:, 0:GROUP_E], 1, TT),
                                          broadcast(best[0], 2, GROUP_E), ALU.is_equal).then_inc(step, 1)
                        dve.wait_ge(step, n.up())
                        dve.scalar_tensor_tensor(out=ep[:, :, :], in0=e1[:, :, :], scalar=-2.0, in1=ep[:, :, :],
                                                 op0=ALU.mult, op1=ALU.add).then_inc(step, 1)
                        dve.wait_ge(step, n.up())
                for j in range(TOP_K):
                    dve.scalar_tensor_tensor(out=best[j], in0=gbest, scalar=float(GROUP_E), in1=best[j],
                                             op0=ALU.mult, op1=ALU.add).then_inc(step, 1)
                    dve.wait_ge(step, n.up())
                    dve.tensor_tensor(hot[:, j, :, :], broadcast(numbers, 1, TT), broadcast(best[j], 2, EXPERTS),
                                      ALU.is_equal).then_inc(step, 1)
                    dve.wait_ge(step, n.up())
                dve.tensor_tensor(both[:, :, :], hot[:, 0, :, :], hot[:, 1, :, :], ALU.add).then_inc(step, 1)
                dve.wait_ge(step, n.up())
                dve.tensor_scalar(before[:, 0, :], both[:, 0, :], 0.0, None, ALU.mult).then_inc(step, 1)
                dve.wait_ge(step, n.up())
                for t in range(1, TT):
                    dve.tensor_tensor(before[:, t, :], before[:, t - 1, :], both[:, t - 1, :], ALU.add).then_inc(step, 1)
                    dve.wait_ge(step, n.up())
                dve.tensor_tensor(total[:, :], before[:, TT - 1, :], both[:, TT - 1, :], ALU.add).then_inc(marked, 1)
                dve.tensor_tensor(pair_sum, top[0], top[1], ALU.add).then_inc(step, 1)
                dve.wait_ge(step, n.up())
                dve.reciprocal(pair_sum, pair_sum).then_inc(step, 1)
                dve.wait_ge(step, n.up())
                for j in range(TOP_K):
                    dve.tensor_tensor(top[j], top[j], gprob, ALU.mult).then_inc(step, 1)
                    dve.wait_ge(step, n.up())
                    dve.tensor_tensor(k.gate[:, j * TT:(j + 1) * TT], top[j], pair_sum, ALU.mult).then_inc(step, 1)
                    dve.wait_ge(step, n.up())
                dve.wait_ge(ranked, 2)
                dve.wait_ge(filled, 3)
                for j in range(1, TT):
                    dve.tensor_scalar(more[:, :, j - 1], cb[:, 0:EXPERTS], float(BLOCK * j), None, ALU.is_gt).then_inc(step, 1)
                    n.up()
                dve.wait_ge(step, n.n)
                dve.tensor_reduce(extra, more[:, :, 0:TT - 1], AX_X, ALU.add).then_inc(step, 1)
                dve.wait_ge(step, n.up())
                dve.tensor_tensor_scan(upto, extra, zrow[:, :], 0.0, ALU.add, ALU.add).then_inc(step, 1)
                dve.wait_ge(step, n.up())
                dve.tensor_tensor(jump, upto, extra, ALU.subtract).then_inc(step, 1)
                dve.wait_ge(step, n.up())
                dve.scalar_tensor_tensor(out=jump, in0=jump, scalar=float(EXPERTS - 1), in1=numbers, op0=ALU.add,
                                         op1=ALU.subtract).then_inc(step, 1)
                dve.wait_ge(step, n.up())
                ranks = rb[:, 0:TT * EXPERTS].rearrange("p (t e) -> p t e", e=EXPERTS)
                dve.tensor_scalar(place[:, :, :], ranks, float(BLOCK), None, ALU.is_ge).then_inc(step, 1)
                dve.wait_ge(step, n.up())
                dve.tensor_tensor(place[:, :, :], place[:, :, :], broadcast(jump, 1, TT), ALU.mult).then_inc(step, 1)
                dve.wait_ge(step, n.up())
                dve.tensor_tensor(place[:, :, :], place[:, :, :], broadcast(numbers, 1, TT), ALU.add).then_inc(step, 1)
                dve.wait_ge(step, n.up())
                dve.scalar_tensor_tensor(out=place[:, :, :], in0=place[:, :, :], scalar=float(BLOCK), in1=ranks,
                                         op0=ALU.mult, op1=ALU.add).then_inc(step, 1)
                dve.wait_ge(step, n.up())
                for j in range(TOP_K):
                    dve.tensor_tensor(spread[:, :, :], hot[:, j, :, :], place[:, :, :], ALU.mult).then_inc(step, 1)
                    dve.wait_ge(step, n.up())
                    dve.tensor_reduce(dest[:, j, :], spread[:, :, :], AX_X, ALU.add).then_inc(step, 1)
                    dve.wait_ge(step, n.up())
                dve.tensor_copy(k.dest[:, :], dest[:, :, :].rearrange("p j t -> p (j t)")).then_inc(placed, 1)
                dve.tensor_tensor(past[:, :, :], broadcast(upto[0:1, :], 1, EXTRA), broadcast(numbers[0:1, 0:EXTRA], 2, EXPERTS),
                                  ALU.is_le).then_inc(step, 1)
                dve.wait_ge(step, n.up())
                dve.tensor_reduce(owner[:, :], past[:, :, :], AX_X, ALU.add).then_inc(step, 1)
                dve.wait_ge(step, n.up())
                dve.tensor_copy(k.plan[:, 0:EXTRA], owner[:, :]).then_inc(step, 1)
                dve.tensor_copy(k.plan[:, EXTRA:EXTRA + 1], upto[0:1, EXPERTS - 1:EXPERTS]).then_inc(step, 1)


def expert_products(pe, k, gate_up, gate_bank, up_bank, half):
    for bank, first in ((gate_bank, 0), (up_bank, DE)):
        for m in range(2):
            col = first + (2 * half + m) * P
            for c in range(GU_K):
                last = pe.matmul(bank[:, m * BLOCK:(m + 1) * BLOCK], gate_up[:, c, col:col + P], k.xT[:, c, :],
                                 start=(c == 0), stop=(c == GU_K - 1))
    return last


def down_products(pe, k, down, bank, half):
    for c in range(DN_K):
        last = pe.matmul(bank[:, :], k.hT[:, c, :], down[:, c, half * HALF:(half + 1) * HALF],
                         start=(c == 0), stop=(c == DN_K - 1))
    return last


def turn_block(pe, k, rows, bank, half):
    for a in range(4):
        c = 4 * half + a
        last = pe.transpose(bank[:, a * P:(a + 1) * P], rows[:, c * P:(c + 1) * P], k.ident[:, :])
    return last


def experts(k):
    with k.stage() as st:
        flat = k.yT[:, :, :].rearrange("p a b -> p (a b)")
        rows = [flat[:, i * D:(i + 1) * D] for i in range(2)]
        y = [flat[:, (2 + i) * D:(3 + i) * D] for i in range(2)]
        k.xT = flat[:, 4 * D:5 * D].rearrange("p (c n) -> p c n", c=GU_K)
        k.hT = flat[:, 5 * D:5 * D + DN_K * BLOCK].rearrange("p (c n) -> p c n", c=DN_K)
        act_gate = flat[:, 6 * D:6 * D + DN_K * BLOCK].rearrange("p (c n) -> p c n", c=DN_K)
        index = st.sbuf("block_index", [P, 2], U32)
        indices = st.sbuf("indices", [P, EXPERTS], U32)
        ab = [st.psum(f"gate_bank{i}", [P, HALF]) for i in range(2)]
        bb = [st.psum(f"up_bank{i}", [P, HALF]) for i in range(2)]
        tb = [st.psum(f"turn_bank{i}", [P, HALF]) for i in range(2)]
        yb = [st.psum(f"down_bank{i}", [P, HALF]) for i in range(2)]
        gathered = [st.sem(f"gathered{i}") for i in range(2)]
        y_stored = [st.sem(f"y_stored{i}") for i in range(2)]
        issued = st.sem("e_issued")
        (index_in, index_set, turned, x_act, x_dve, hidden, silued, h_done, y_made, y_act, y_dve) = (
            st.sem("e_" + n) for n in "index_in index_set turned x_act x_dve hidden silued h_done y_made y_act y_dve".split())
        GROUP_COLS = 2 * BLOCK

        def half_view(tile, half):
            return tile[:, 2 * half:2 * half + 2, :].rearrange("p a b -> p (a b)")

        with st.block() as block:

            @block.sync
            def _(sp):
                sp.dma_start(indices[:, :], k.idx_dram[0:EXPERTS * BLOCK, :].rearrange("(e r) o -> r (e o)", r=BLOCK),
                             allow_slow_non_contiguous=True).then_inc(index_in, 16)

                def one(i, par, last):
                    e = 2 * i + par
                    if not last:
                        sp.wait_ge(hidden, 2 * e + 2)
                        sp.dma_start(k.w_gu(par), k.w["expert_w_gu"][bass.ds(e + 2, 1)].rearrange(
                            "a (k p) n -> p (a k) n", p=P)).then_inc(k.gu_in[par], 16)
                        sp.wait_ge(y_made, 2 * e + 2)
                        sp.dma_start(k.w_dn(par), k.w["expert_w_down"][bass.ds(e + 2, 1)].rearrange(
                            "a (k p) n -> p (a k) n", p=P)).then_inc(k.dn_in[par], 16)
                    sp.wait_ge(y_act, e + 1)
                    sp.wait_ge(y_dve, e + 1)
                    sp.dma_start(k.y_dram[bass.ds(e * BLOCK, BLOCK), :], y[par]).then_inc(y_stored[par], 16)

                with sp.Fori(0, EXPERTS // 2 - 1) as i:
                    for par in range(2):
                        one(i, par, False)
                for par in range(2):
                    one(EXPERTS // 2 - 1, par, True)
                for par in range(2):
                    sp.wait_ge(y_stored[par], 16 * (EXPERTS // 2))

            @block.gpsimd
            def _(pool):
                def one(i, par, first):
                    e = 2 * i + par
                    if not first:
                        pool.wait_ge(turned, 2 * e - 2)
                    pool.tensor_copy(index[:, par:par + 1], indices[:, bass.ds(e, 1)]).then_inc(index_set, 1)
                    pool.wait_ge(index_set, e + 1)
                    pool.sem_inc(issued, 1)
                    pool.indirect_dma_start(rows[par], None, k.xn_dram,
                                            bass.IndirectOffsetOnAxis(index[:, par:par + 1], 0)).then_inc(gathered[par], 16)

                pool.wait_ge(index_in, 16)
                for par in range(2):
                    one(0, par, True)
                with pool.Fori(1, EXPERTS // 2) as i:
                    for par in range(2):
                        one(i, par, False)

            @block.scalar
            def _(act):
                def x_out(e):
                    act.wait_ge(turned, 2 * e + 1)
                    act.activation(k.xT[:, 0:4, :].rearrange("p a b -> p (a b)"), tb[0][:, :], ACT.Copy).then_inc(x_act, 1)

                def one(i, par, first, last):
                    e = 2 * i + par
                    for half in range(2):
                        act.wait_ge(hidden, 2 * e + half + 1)
                        act.activation(half_view(act_gate, half), ab[half][:, 0:GROUP_COLS], ACT.Silu).then_inc(silued, 1)
                    if not last:
                        x_out(e + 1)
                    act.wait_ge(y_made, 2 * e + 1)
                    if not first:
                        act.wait_ge(y_stored[par], 16 * i)
                    act.activation(y[par][:, 0:HALF], yb[0][:, :], ACT.Copy).then_inc(y_act, 1)

                x_out(0)
                for par in range(2):
                    one(0, par, True, False)
                with act.Fori(1, EXPERTS // 2 - 1) as i:
                    for par in range(2):
                        one(i, par, False, False)
                for par in range(2):
                    one(EXPERTS // 2 - 1, par, False, par == 1)

            @block.vector
            def _(dve):
                def x_out(e):
                    dve.wait_ge(turned, 2 * e + 2)
                    dve.tensor_copy(k.xT[:, 4:8, :].rearrange("p a b -> p (a b)"), tb[1][:, :]).then_inc(x_dve, 1)

                def one(i, par, first, last):
                    e = 2 * i + par
                    for half in range(2):
                        dve.wait_ge(silued, 2 * e + half + 1)
                        dve.tensor_tensor(half_view(k.hT, half), half_view(act_gate, half), bb[half][:, 0:GROUP_COLS],
                                          ALU.mult).then_inc(h_done, 1)
                    if not last:
                        x_out(e + 1)
                    dve.wait_ge(y_made, 2 * e + 2)
                    if not first:
                        dve.wait_ge(y_stored[par], 16 * i)
                    dve.tensor_copy(y[par][:, HALF:], yb[1][:, :]).then_inc(y_dve, 1)

                x_out(0)
                for par in range(2):
                    one(0, par, True, False)
                with dve.Fori(1, EXPERTS // 2 - 1) as i:
                    for par in range(2):
                        one(i, par, False, False)
                for par in range(2):
                    one(EXPERTS // 2 - 1, par, False, par == 1)

            @block.tensor
            def _(pe):
                def turn(i, par):
                    pe.wait_ge(gathered[par], 16 * (i + 1))
                    for half in range(2):
                        turn_block(pe, k, rows[par], tb[half], half).then_inc(turned, 1)

                def one(i, par, first, last):
                    e = 2 * i + par
                    pe.wait_ge(k.gu_in[par], 16 * (i + 1))
                    pe.wait_ge(x_act, e + 1)
                    pe.wait_ge(x_dve, e + 1)
                    for half in range(2):
                        expert_products(pe, k, k.w_gu(par), ab[half], bb[half], half).then_inc(hidden, 1)
                    if not last:
                        turn(i + par, 1 - par)
                    pe.wait_ge(k.dn_in[par], 16 * (i + 1))
                    pe.wait_ge(h_done, 2 * e + 2)
                    for half in range(2):
                        if not first or par:
                            pe.wait_ge((y_act, y_dve)[half], e)
                        down_products(pe, k, k.w_dn(par), yb[half], half).then_inc(y_made, 1)

                turn(0, 0)
                for par in range(2):
                    one(0, par, True, False)
                with pe.Fori(1, EXPERTS // 2 - 1) as i:
                    for par in range(2):
                        one(i, par, False, False)
                for par in range(2):
                    one(EXPERTS // 2 - 1, par, False, par == 1)

    extra_blocks(k)


def extra_blocks(k):
    with k.stage() as st:
        flat = k.yT[:, :, :].rearrange("p a b -> p (a b)")
        rows, y = flat[:, 0:D], flat[:, 2 * D:3 * D]
        act_gate = flat[:, 6 * D:6 * D + DN_K * BLOCK].rearrange("p (c n) -> p c n", c=DN_K)
        index = st.sbuf("extra_index", [P, 1], U32)
        ab = [st.psum(f"extra_gate{i}", [P, HALF]) for i in range(2)]
        bb = [st.psum(f"extra_up{i}", [P, HALF]) for i in range(2)]
        tb = [st.psum(f"extra_turn{i}", [P, HALF]) for i in range(2)]
        yb = [st.psum(f"extra_down{i}", [P, HALF]) for i in range(2)]
        issued, finished = st.sem("extra_issued"), st.sem("extra_finished")
        (weights_in, index_in, gathered, turned, x_act, x_dve, hidden, silued, h_done, y_made, y_act, y_dve, stored) = (
            st.sem("extra_" + n) for n in ("weights_in index_in gathered turned x_act x_dve hidden silued h_done y_made y_act "
                                       "y_dve stored").split())

        def half_view(tile, half):
            return tile[:, 2 * half:2 * half + 2, :].rearrange("p a b -> p (a b)")

        def listed(eng, body):
            n = eng.value_load(k.plan[0:1, EXTRA:EXTRA + 1], min_val=0, max_val=EXTRA)
            with eng.If(n > 0):
                with eng.Fori(0, n) as b:
                    body(b)

        with st.block() as block:

            @block.sync
            def _(sp):
                def body(b):
                    e = sp.value_load(k.plan[0:1, bass.ds(b, 1)], min_val=0, max_val=EXPERTS - 1)
                    sp.dma_start(index[:, :], k.idx_dram[bass.ds(EXPERTS * BLOCK + b * BLOCK, BLOCK), :]).then_inc(index_in, 16)
                    sp.dma_start(k.w_gu(0), k.w["expert_w_gu"][bass.ds(e, 1)].rearrange(
                        "a (k p) n -> p (a k) n", p=P)).then_inc(weights_in, 16)
                    sp.dma_start(k.w_dn(0), k.w["expert_w_down"][bass.ds(e, 1)].rearrange(
                        "a (k p) n -> p (a k) n", p=P)).then_inc(weights_in, 16)
                    done, all_stored = sp.snap(b + 1), sp.snap(16 * b + 16)
                    sp.wait_ge(y_act, done)
                    sp.wait_ge(y_dve, done)
                    sp.dma_start(k.y_dram[bass.ds(EXPERTS * BLOCK + b * BLOCK, BLOCK), :], y).then_inc(stored, 16)
                    sp.wait_ge(stored, all_stored)
                    sp.sem_inc(finished, 1)

                listed(sp, body)

            @block.gpsimd
            def _(pool):
                def body(b):
                    pool.wait_ge(index_in, 16 * (b + 1))
                    pool.sem_inc(issued, 1)
                    pool.indirect_dma_start(rows, None, k.xn_dram,
                                            bass.IndirectOffsetOnAxis(index[:, :], 0)).then_inc(gathered, 16)

                listed(pool, body)

            @block.scalar
            def _(act):
                def body(b):
                    act.wait_ge(turned, 2 * b + 1)
                    act.activation(k.xT[:, 0:4, :].rearrange("p a b -> p (a b)"), tb[0][:, :], ACT.Copy).then_inc(x_act, 1)
                    for half in range(2):
                        act.wait_ge(hidden, 2 * b + half + 1)
                        act.activation(half_view(act_gate, half), ab[half][:, 0:2 * BLOCK], ACT.Silu).then_inc(silued, 1)
                    act.wait_ge(y_made, 2 * b + 1)
                    act.activation(y[:, 0:HALF], yb[0][:, :], ACT.Copy).then_inc(y_act, 1)

                listed(act, body)

            @block.vector
            def _(dve):
                def body(b):
                    dve.wait_ge(turned, 2 * b + 2)
                    dve.tensor_copy(k.xT[:, 4:8, :].rearrange("p a b -> p (a b)"), tb[1][:, :]).then_inc(x_dve, 1)
                    for half in range(2):
                        dve.wait_ge(silued, 2 * b + half + 1)
                        dve.tensor_tensor(half_view(k.hT, half), half_view(act_gate, half), bb[half][:, 0:2 * BLOCK],
                                          ALU.mult).then_inc(h_done, 1)
                    dve.wait_ge(y_made, 2 * b + 2)
                    dve.tensor_copy(y[:, HALF:], yb[1][:, :]).then_inc(y_dve, 1)

                listed(dve, body)

            @block.tensor
            def _(pe):
                def body(b):
                    pe.wait_ge(gathered, 16 * (b + 1))
                    for half in range(2):
                        turn_block(pe, k, rows, tb[half], half).then_inc(turned, 1)
                    pe.wait_ge(weights_in, 32 * (b + 1))
                    pe.wait_ge(x_act, b + 1)
                    pe.wait_ge(x_dve, b + 1)
                    for half in range(2):
                        expert_products(pe, k, k.w_gu(0), ab[half], bb[half], half).then_inc(hidden, 1)
                    pe.wait_ge(h_done, 2 * b + 2)
                    for half in range(2):
                        down_products(pe, k, k.w_dn(0), yb[half], half).then_inc(y_made, 1)

                listed(pe, body)


def combine(k):
    with k.stage() as st:
        flat = k.yT[:, :, :].rearrange("p a b -> p (a b)")
        SLOTS_Y = 4
        rows = [[k.ring[:, (2 * i + j) * D:(2 * i + j + 1) * D] for j in range(TOP_K)] for i in range(SLOTS_Y)]
        result = [flat[:, i * D:(i + 1) * D] for i in range(2)]
        gain = flat[:, 2 * D:3 * D]
        square = flat[:, 3 * D:4 * D]
        stat = st.sbuf("final_stat", [P, TT, 4])
        gain_in = st.sem("final_gain_in")
        gathered = [[st.sem(f"y_in{i}_{j}") for j in range(TOP_K)] for i in range(SLOTS_Y)]
        stored = [st.sem(f"out_stored{i}") for i in range(2)]
        added, squared, variance, root, inverse, ready = (
            st.sem("c_" + n) for n in "added squared variance root inverse ready".split())

        with st.block() as block:

            @block.gpsimd
            def _(pool):
                for t in range(TT):
                    if t >= SLOTS_Y:
                        pool.wait_ge(added, 2 * (t - SLOTS_Y) + 2)
                    for j in range(TOP_K):
                        i = j * TT + t
                        pool.indirect_dma_start(rows[t % SLOTS_Y][j], None, k.y_dram,
                                                bass.IndirectOffsetOnAxis(k.dest[:, i:i + 1], 0)).then_inc(
                            gathered[t % SLOTS_Y][j], 16)

            @block.vector
            def _(dve):
                dve.wait_ge(gain_in, 16)
                for t in range(TT + 2):
                    if t < TT:
                        for j in range(TOP_K):
                            dve.wait_ge(gathered[t % SLOTS_Y][j], 16 * (t // SLOTS_Y + 1))
                            if j:
                                dve.wait_ge(added, 2 * t + 1)
                            dve.scalar_tensor_tensor(out=k.x[:, t, :], in0=rows[t % SLOTS_Y][j],
                                                     scalar=k.gate[:, j * TT + t:j * TT + t + 1], in1=k.x[:, t, :],
                                                     op0=ALU.mult, op1=ALU.add).then_inc(added, 1)
                    if 1 <= t <= TT:
                        u = t - 1
                        dve.wait_ge(squared, u + 1)
                        dve.tensor_scalar(stat[:, u, 1:2], stat[:, u, 0:1], 1.0 / D, EPS, ALU.mult,
                                          ALU.add).then_inc(variance, 1)
                    if t >= 2:
                        u = t - 2
                        dve.wait_ge(root, u + 1)
                        dve.reciprocal(stat[:, u, 3:4], stat[:, u, 2:3]).then_inc(inverse, 1)
                        dve.wait_ge(inverse, u + 1)
                        if u >= 2:
                            dve.wait_ge(stored[u % 2], 16 * (u // 2))
                        dve.scalar_tensor_tensor(out=result[u % 2], in0=k.x[:, u, :], scalar=stat[:, u, 3:4], in1=gain,
                                                 op0=ALU.mult, op1=ALU.mult).then_inc(ready, 1)

            @block.scalar
            def _(act):
                for t in range(TT + 1):
                    if t < TT:
                        act.wait_ge(added, 2 * t + 2)
                        if t:
                            act.wait_ge(squared, t)
                        act.activation(square, k.x[:, t, :], ACT.Square, accum_out=stat[:, t, 0:1]).then_inc(squared, 1)
                    if t >= 1:
                        act.wait_ge(variance, t)
                        act.activation(stat[:, t - 1, 2:3], stat[:, t - 1, 1:2], ACT.Sqrt).then_inc(root, 1)

            @block.sync
            def _(sp):
                sp.dma_start(gain, k.w["final_norm"][0:1, :].partition_broadcast(P)).then_inc(gain_in, 16)
                for t in range(TT):
                    sp.wait_ge(ready, t + 1)
                    sp.dma_start(k.out[t * P:(t + 1) * P, :], result[t % 2]).then_inc(stored[t % 2], 16)
                for i in range(2):
                    sp.wait_ge(stored[i], 16 * (TT // 2))


class Core:
    pass


class Stage:

    def __init__(self, nc, ident):
        self.nc, self.ident, self.held, self.sems = nc, ident, ExitStack(), []

    def __enter__(self):
        return self

    def __exit__(self, *what):
        self.held.close()
        self.nc.clear_and_free_semaphores(self.sems)
        self.nc.all_engine_barrier()

    def sbuf(self, name, shape, dt=F32):
        return self.held.enter_context(self.nc.sbuf_tensor(name, shape, dt))

    def psum(self, name, shape, dt=F32):
        return self.held.enter_context(self.nc.psum_tensor(name, shape, dt))

    def sem(self, name):
        self.sems.append(self.nc.alloc_semaphore(name))
        return self.sems[-1]

    def block(self):
        return self.nc.Block()


def build(nc, w, out):
    k = Core()
    k.w, k.out, k.nc = w, out, nc
    with ExitStack() as ctx:
        def sbuf(name, shape, dt=F32):
            return ctx.enter_context(nc.sbuf_tensor(name, shape, dt))

        k.ident = sbuf("ident", [P, P])
        k.vec = sbuf("vec", [P, VEC_N])
        k.stage = lambda: Stage(nc, k.ident)
        w_in = w["w_in"]
        k.chunks = [(w_in[:, COL_UO:COL_GATE], HALF), (w_in[:, COL_GATE:COL_Q], 264), (w_in[:, COL_Q:COL_K], HALF),
                    (w_in[:, COL_K:COL_V], HALF), (w_in[:, COL_V:], HALF)]
        k.chunks += [(w["w_out"][:, h * HALF:(h + 1) * HALF], HALF) for h in range(2)]
        k.chunks += [(w["xattn_w_q"][:, h * 256:(h + 1) * 256], 256) for h in range(4)]
        k.chunks += [(w["xattn_w_kv"][:, h * 256:(h + 1) * 256], 256) for h in range(8)]
        k.chunks += [(w["xattn_w_o"][:, h * HALF:(h + 1) * HALF], HALF) for h in range(2)]
        k.chunk_in = [ctx.enter_context(nc.semaphore(f"chunk_in{i}")) for i in range(len(k.chunks))]

        def large_buffers(held, name, parts):
            return [held.enter_context(nc.sbuf_tensor(f"{name}_{part}", [P, n], F32, side="right")) for part, n in parts]

        def weights_at(i, buffer, at):
            k.place[i] = (buffer, at)

        k.place = {}
        k.chunk = lambda i, n: k.place[i][0][:, k.place[i][1]:k.place[i][1] + KT * n].rearrange("p (k n) -> p k n", k=KT)

        def split_input(held, name, slots, slot, chunks):
            chunk_space, high, low = large_buffers(held, name, (("chunks", slots * slot), ("xn_high", KT * S),
                                                                ("xn_low", KT * S)))
            k.xn = [part[:, :].rearrange("p (k n) -> p k n", k=KT) for part in (high, low)]
            for n, i in enumerate(chunks):
                weights_at(i, chunk_space, (n % slots) * slot)

        k.v_dram = nc.dram_tensor("v_dram", [S, A_W], F32, kind="Internal").ap()
        k.attn_dram = nc.dram_tensor("attn_dram", [3, S, O_W], F32, kind="Internal").ap()
        k.y_dram = nc.dram_tensor("y_dram", [BLOCKS * BLOCK, D], F32, kind="Internal").ap()
        k.yT = sbuf("yT", [P, KT, S])
        mixing = ExitStack()
        with ExitStack() as mixers:
            def mixer(name, shape):
                return mixers.enter_context(nc.sbuf_tensor(name, shape, F32))

            k.qT = mixer("qT", [P, 4, S])
            k.kT = mixer("kT", [P, 4, S])
            with ExitStack() as small:
                def small_mixer(name, shape):
                    return small.enter_context(nc.sbuf_tensor(name, shape, F32))

                k.uP = small_mixer("uP", [P, 2, 3 + S])
                k.oT = small_mixer("oT", [P, 2, S])
                k.s_in = small_mixer("s_in", [P, S5_G, S5_L, S5_C])
                k.gateT = small_mixer("gateT", [2 * M_H, S])
                with ExitStack() as held:
                    split_input(held, "mix", 2, SLOT, range(5))
                    in_projection(k)
                out_weights, = large_buffers(mixing, "mix", (("out_weights", 2 * SLOT),))
                weights_at(5, out_weights, 0)
                weights_at(6, out_weights, SLOT)
                mixer_space = ExitStack()
                k.ring, = large_buffers(mixer_space, "mixers", (("ring", 4 * SLOT),))
                mlstm(k)
                s5(k)
            attention(k)
            join_patterns(k)
            mixer_space.close()
        k.x = sbuf("x_residual", [P, TT, D])
        output_projection(k, "mix_out", k.yT, (5, 6), True)
        mixing.close()
        with ExitStack() as cross:
            k.xqT = k.yT
            k.xkT = cross.enter_context(nc.sbuf_tensor("xkT", [P, KT, MEM], F32))
            k.xv = cross.enter_context(nc.sbuf_tensor("xv", [P, MEM // P, D], F32))
            with ExitStack() as held:
                split_input(held, "xa", 3, KT * 256, range(7, 19))
                memory_projections(k)
            crossing = ExitStack()
            out_weights, mixed = large_buffers(crossing, "xa", (("out_weights", 2 * SLOT), ("mixed", KT * S)))
            weights_at(19, out_weights, 0)
            weights_at(20, out_weights, SLOT)
            k.mixedT = mixed[:, :].rearrange("p (k n) -> p k n", k=KT)
            memory_attention(k)
        output_projection(k, "xa_out", k.mixedT, (19, 20), False)
        crossing.close()
        k.ring, = large_buffers(ctx, "experts", (("ring", 6 * SLOT),))
        k.w_gu = lambda par: k.ring[:, 3 * par * SLOT:(3 * par + 2) * SLOT].rearrange("p (k n) -> p k n", k=GU_K)
        k.w_dn = lambda par: k.ring[:, (3 * par + 2) * SLOT:(3 * par + 3) * SLOT].rearrange("p (k n) -> p k n", k=DN_K)
        k.gu_in = [ctx.enter_context(nc.semaphore(f"gu_in{i}")) for i in range(2)]
        k.dn_in = [ctx.enter_context(nc.semaphore(f"dn_in{i}")) for i in range(2)]
        k.gate = sbuf("gate", [P, TOP_K * TT])
        k.dest = sbuf("dest", [P, TOP_K * TT], U32)
        k.plan = sbuf("plan", [1, EXTRA + 1], I32)
        k.idx_dram = nc.dram_tensor("idx_dram", [BLOCKS * BLOCK, 1], U32, kind="Internal").ap()
        k.xn_dram = nc.dram_tensor("xn_dram", [S, D], F32, kind="Internal").ap()
        router(k)
        experts(k)
        combine(k)


def attention_bias(table):
    def bucket(dist):
        large = 16 + (np.log(np.maximum(dist, 1) / 16) / np.log(2048 / 16) * 16).astype(np.int32)
        return np.where(dist < 16, dist, np.minimum(large, 31))

    i, j = np.arange(BLK)[:, None], np.arange(2 * BLK)[None, :]
    off = BLK + i - j
    parts = []
    for window, dil in PATTERNS[:2]:
        band = (off >= 0) & (off <= window // dil)
        parts.append(np.where(band[:, None], table[bucket(np.maximum(off, 0) * dil)].transpose(0, 2, 1), np.float32(NEG)))
    i, j = np.arange(BLK)[:, None], np.arange(BLK)[None, :]
    off = i // 2 - j // 2
    band = (off >= 0) & (i % 2 == j % 2)
    parts.append(np.where(band[:, None], table[bucket(np.maximum(off, 0) * PATTERNS[2][1])].transpose(0, 2, 1), np.float32(NEG)))
    return np.concatenate(parts, axis=2).astype(np.float32)


def kernel(**inputs):
    import concourse.bacc as bacc
    from concourse.bass_utils import run_bass_kernel_spmd as run

    a = {n: np.ascontiguousarray(v) for n, v in inputs.items()}
    data = {"x": a["x"][0], "mem": a["mem"][0], "norm_mix": a["norm_mix"], "w_in": a["w_in"][0]}
    for n in ("w_out", "xattn_w_q", "xattn_w_kv", "xattn_w_o", "s5_w_glu", "expert_w_gu", "expert_w_down"):
        data[n] = a[n][0]
    for n in ("norm_xattn", "norm_mem", "norm_ffn", "s5_b_glu"):
        data[n] = a[n]
    data["final_norm"] = a["final_norm"][None]

    def channels(v, n):
        return v.reshape(n, P).T

    def pairs(v):
        return v.reshape(S5_G // 2, 2, 64).transpose(1, 2, 0).reshape(P, S5_G // 2)

    gate_b = np.zeros((P, 1), np.float32)
    gate_b[0:2 * M_H, 0] = a["mlstm_gate_bias"][0]
    data["vec"] = np.concatenate([
        a["mlstm_conv_w"][0].reshape(4, 2, P).transpose(2, 1, 0).reshape(P, 8), channels(a["mlstm_conv_b"][0], 2),
        channels(a["mlstm_norm"][0], 2), channels(a["mlstm_skip"][0], 2), channels(a["s5_out_norm"][0], 2),
        channels(a["attn_out_norm"][0], 4), gate_b, pairs(a["s5_a_re"][0]), pairs(a["s5_a_im"][0]),
        pairs(np.broadcast_to(a["s5_log_dt"][0][:, None], (S5_G, 64))),
        np.where(np.arange(P) < 64, 1.0, -1.0).astype(np.float32)[:, None]], axis=1)
    mw = np.zeros((2, DH, 2, 3, 2, DH), np.float32)
    for i, n in enumerate(("mlstm_wq", "mlstm_wk", "mlstm_wv")):
        for h in range(M_H):
            mw[h % 2, :, h // 2, i, h % 2, :] = a[n][0, h]
    data["mlstm_w"] = mw.reshape(P, 2, 3, P)

    def pair_rows(v):
        return v.reshape(S5_G // 2, 2, 64, S5_C).transpose(1, 2, 0, 3).reshape(P, S5_G // 2, S5_C)

    data["attn_bias"] = attention_bias(a["rel_bias"])
    data["s5_bc"] = np.stack([pair_rows(a["s5_b_re"][0]), pair_rows(a["s5_b_im"][0]),
                              pair_rows(a["s5_c_re"][0].transpose(0, 2, 1)),
                              pair_rows(a["s5_c_im"][0].transpose(0, 2, 1))], axis=1)
    diag = np.zeros((S5_C, S5_G, S5_C), np.float32)
    for c in range(S5_C):
        diag[c, :, c] = a["s5_d"][0, :, c]
    data["s5_diag"] = diag
    data["router_w"] = np.concatenate([a["router_w_group"][0], a["router_w_expert"][0]], axis=1)
    data["router_b"] = np.concatenate([a["router_b_group"], a["router_b_expert"]], axis=1)
    numbers = np.broadcast_to(np.arange(EXPERTS, dtype=np.float32), (P, EXPERTS))
    data["route_const"] = np.concatenate([np.triu(np.ones((P, P), np.float32), 1), numbers], axis=1)
    data["ident"] = np.eye(P, dtype=np.float32)
    data = {n: np.ascontiguousarray(v) for n, v in data.items()}
    nc = bacc.Bacc("TRN2", target_bir_lowering=False, num_devices=1)
    w = {n: nc.dram_tensor("in_" + n, v.shape, F32, kind="ExternalInput").ap()
                           for n, v in data.items()}
    out = nc.dram_tensor("out", (S, D), F32, kind="ExternalOutput").ap()
    build(nc, w, out)
    got = run(nc, [{"in_" + n: v for n, v in data.items()}], core_ids=[0])
    return got.results[0]["out"].reshape(1, S, D)
```

```python
from contextlib import ExitStack


import numpy as np

import concourse.bass as bass
from concourse import mybir

F32 = mybir.dt.float32
F32R = mybir.dt.float32r
U32 = mybir.dt.uint32
I32 = mybir.dt.int32
ALU = mybir.AluOpType
ACT = mybir.ActivationFunctionType
AX_X = mybir.AxisListType.X

P = 128
S = 1024
D = 1024
KT = D // P
TT = S // P
HALF = 512
EPS = 1e-6
DH = 64

M_W = 256
M_H = 4
L = 64
NC = S // L
S5_G = 16
S5_C = 16
S5_L = 8
A_W = 512
A_H = 8
MEM = 256
X_H = 4
X_DH = 256

COL_UO = 0
COL_GATE = 2 * M_W
COL_S = COL_GATE + 2 * M_H
COL_Q = COL_S + 256
COL_K = COL_Q + A_W
COL_V = COL_K + A_W

SLOT = KT * HALF
NEG = -1.0e30

VECS = {}
_at = 0
for _name, _n in (("conv_w", 8), ("conv_b", 2), ("m_gain", 2), ("m_skip", 2), ("s_gain", 2), ("a_gain", 4),
                  ("gate_b", 1), ("a_re", 8), ("a_im", 8), ("log_dt", 8), ("sign", 1)):
    VECS[_name] = (_at, _at + _n)
    _at += _n
VEC_N = _at




class Split:

    def __init__(self, st, name):
        self.rounded, self.done, self.n = st.sem(name + "_rounded"), st.sem(name + "_split"), 0

    def piece(self, dve, x, pair):
        high, low = pair
        dve.tensor_copy(high.bitcast(F32R), x).then_inc(self.rounded, 1)
        self.n += 1
        dve.wait_ge(self.rounded, self.n)
        dve.tensor_tensor(low.bitcast(F32R), x, high, ALU.subtract).then_inc(self.done, 1)


def split_product(pe, out, left, right, start, stop):
    (left_high, left_low), (right_high, right_low) = [[part.bitcast(F32R) for part in pair] for pair in (left, right)]
    pe.matmul(out, left_high, right_high, start=start, stop=False)
    pe.matmul(out, left_high, right_low, start=False, stop=False)
    return pe.matmul(out, left_low, right_high, start=False, stop=stop)


class Norm:

    def __init__(self, k, name, n, source, gain, dest, banks, ring, stat, wait_source, keep=None, low=None):
        self.k, self.n, self.source, self.gain, self.dest = k, n, source, gain, dest
        self.banks, self.ring, self.stat, self.wait_source, self.keep = banks, ring, stat, wait_source, keep
        self.low = low
        self.slots = ring.shape[1] - 1
        self.squared = k.sem(name + "_squared")
        self.variance = k.sem(name + "_variance")
        self.root = k.sem(name + "_root")
        self.inverse = k.sem(name + "_inverse")
        self.scaled = k.sem(name + "_scaled")
        self.turned = k.sem(name + "_turned")
        self.evac_act = k.sem(name + "_evac_act")
        self.evac_dve = k.sem(name + "_evac_dve")

    def bank_of(self, t, h):
        return self.banks[(2 * t + h) % 4][:, :].rearrange("p (a b) -> p a b", a=4)

    def wait_all(self, eng):
        if self.low is None:
            eng.wait_ge(self.evac_act, self.n)
        eng.wait_ge(self.evac_dve, self.n if self.low is None else 2 * self.n)

    def scalar(self, act):
        for i in range(self.n + 3):
            if i < self.n:
                self.wait_source(act, i)
                if i:
                    act.wait_ge(self.squared, i)
                act.activation(self.ring[:, self.slots, :], self.source(i), ACT.Square,
                               accum_out=self.stat[:, i, 0:1]).then_inc(self.squared, 1)
            if 1 <= i <= self.n:
                t = i - 1
                act.wait_ge(self.variance, t + 1)
                act.activation(self.stat[:, t, 2:3], self.stat[:, t, 1:2], ACT.Sqrt).then_inc(self.root, 1)
            if i >= 3 and self.low is not None:
                t = i - 3
                for h in range(2):
                    act.wait_ge(self.turned, 2 * t + h + 1)
                    act.activation(self.dest(t, h).bitcast(F32R), self.bank_of(t, h), ACT.Copy).then_inc(self.evac_act, 1)
            elif i >= 3:
                t = i - 3
                act.wait_ge(self.turned, 2 * t + 1)
                act.activation(self.dest(t, 0), self.banks[(2 * t) % 4][:, :].rearrange("p (a b) -> p a b", a=4),
                               ACT.Copy).then_inc(self.evac_act, 1)

    def vector(self, dve):
        for i in range(self.n + 3):
            if i < self.n:
                dve.wait_ge(self.squared, i + 1)
                dve.tensor_scalar(self.stat[:, i, 1:2], self.stat[:, i, 0:1], 1.0 / D, EPS, ALU.mult,
                                  ALU.add).then_inc(self.variance, 1)
            if 1 <= i <= self.n:
                t = i - 1
                dve.wait_ge(self.root, t + 1)
                dve.reciprocal(self.stat[:, t, 3:4], self.stat[:, t, 2:3]).then_inc(self.inverse, 1)
                dve.wait_ge(self.inverse, t + 1)
                if t >= self.slots:
                    dve.wait_ge(self.turned, 2 * (t - self.slots + 1))
                    if self.keep is not None:
                        dve.wait_ge(self.keep[t % 2], 16 * (t // 2))
                dve.scalar_tensor_tensor(out=self.ring[:, t % self.slots, :], in0=self.source(t),
                                         scalar=self.stat[:, t, 3:4], in1=self.gain,
                                         op0=ALU.mult, op1=ALU.mult).then_inc(self.scaled, 1)
            if i >= 3 and self.low is not None:
                t = i - 3
                for h in range(2):
                    dve.wait_ge(self.evac_act, 2 * t + h + 1)
                    dve.tensor_tensor(self.low(t, h).bitcast(F32R), self.bank_of(t, h), self.dest(t, h), ALU.subtract)\
                        .then_inc(self.evac_dve, 1)
            elif i >= 3:
                t = i - 3
                dve.wait_ge(self.turned, 2 * t + 2)
                dve.tensor_copy(self.dest(t, 1), self.banks[(2 * t + 1) % 4][:, :].rearrange(
                    "p (a b) -> p a b", a=4)).then_inc(self.evac_dve, 1)

    def tensor(self, pe, behind=None):
        for t in range(self.n + (2 if behind else 0)):
            if t >= 2 and behind:
                behind(t - 2)
            if t >= self.n:
                continue
            pe.wait_ge(self.scaled, t + 1)
            for h in range(2):
                if t >= 2 and self.low is None:
                    pe.wait_ge((self.evac_act, self.evac_dve)[h], t - 1)
                elif t >= 2:
                    pe.wait_ge(self.evac_dve, 2 * (t - 2) + h + 1)
                bank = self.banks[(2 * t + h) % 4]
                for a in range(4):
                    c = 4 * h + a
                    last = pe.transpose(bank[:, a * P:(a + 1) * P], self.ring[:, t % self.slots, c * P:(c + 1) * P],
                                        self.k.ident[:, :])
                last.then_inc(self.turned, 1)


def load_chunk(k, queue, i):
    source, n = k.chunks[i]
    queue.dma_start(k.chunk(i, n), source.rearrange("(k p) n -> p k n", p=P)).then_inc(k.chunk_in[i], 16)


class Pieces:

    def __init__(self, k, st, name):
        self.k, self.split = k, Split(st, name)
        self.ring = [st.sbuf(f"{name}_{part}", [P, 2, KT * P]) for part in ("high", "low")]
        self.pieces, self.groups, self.last_use, self.side = [], [], [0, 0], 0

    def add(self, chunk, n, a, b):
        width = b - a
        if width > P:
            sides = (0, 1)
            pair = [r[:, :, :].rearrange("p s n -> p (s n)")[:, 0:KT * width].rearrange("p (k n) -> p k n", k=KT)
                    for r in self.ring]
        else:
            sides = (self.side,)
            pair = [r[:, self.side, 0:KT * width].rearrange("p (k n) -> p k n", k=KT) for r in self.ring]
            self.side = 1 - self.side
        free = max(self.last_use[side] for side in sides)
        self.pieces.append((chunk, self.k.chunk(chunk, n)[:, :, a:b], pair, free, len(self.groups)))
        self.sides = sides
        return pair

    def group(self, *what):
        self.groups.append(what)
        for side in self.sides:
            self.last_use[side] = len(self.groups)

    def firsts(self):
        return [p[4] for p in self.pieces] + [len(self.groups)]

    def chunk_end(self, chunk):
        return max(n + 1 for n, p in enumerate(self.pieces) if p[0] == chunk)

    def vector(self, dve, n, product):
        chunk, source, pair, free, _ = self.pieces[n]
        dve.wait_ge(self.k.chunk_in[chunk], 16)
        if free:
            dve.wait_ge(product, free)
        self.split.piece(dve, source, pair)


def columns(pair, a, b, step=1):
    return lambda c: [part[:, c, a:b:step] for part in pair]


def in_projection(k):
    with k.stage() as st:
        xs, ring, gain = k.yT[:, 0:3, :], k.yT[:, 3:6, :], k.yT[:, 6, :]
        v_out = k.yT[:, 7, :].rearrange("p (a b) -> p a b", a=4)
        stat = st.sbuf("mix_stat", [P, TT, 4])
        tb = [st.psum(f"turn{i}", [P, HALF]) for i in range(4)]
        gb = [st.psum(f"gemm{i}", [P, HALF]) for i in range(4)]
        const_in = st.sem("const_in")
        gain_in = st.sem("mix_gain_in")
        x_in = [st.sem(f"x_in{i}") for i in range(3)]
        product = st.sem("product")
        out_act = st.sem("out_act")
        out_dve = st.sem("out_dve")
        v_stored = [st.sem(f"v_stored{i}") for i in range(4)]

        def wait_x(eng, t):
            eng.wait_ge(x_in[t % 3], 16 * (t // 3 + 1))

        def transposes(n):
            return lambda t, h: k.xn[n][:, 4 * h:4 * h + 4, t * P:(t + 1) * P]

        norm = Norm(st, "mix", TT, lambda t: xs[:, t % 3, :], gain, transposes(0), tb, ring, stat, wait_x,
                    low=transposes(1))

        w = Pieces(k, st, "mix_w")
        for m in range(4):
            dest = k.uP[:, m, 3:] if m < 2 else k.oT[:, m - 2, :]
            part = w.add(0, HALF, m * P, (m + 1) * P)
            for h in range(2):
                half = slice(h * HALF, (h + 1) * HALF)
                w.group(columns(part, 0, P), columns(k.xn, half.start, half.stop), (P, HALF), dest[:, half], 1.0)
        part = w.add(1, 264, 0, 8)
        for h in range(2):
            half = slice(h * HALF, (h + 1) * HALF)
            w.group(columns(part, 0, 8), columns(k.xn, half.start, half.stop), (8, HALF), k.gateT[:, half], 1.0)
        part = w.add(1, 264, 8, 264)
        for s in range(S5_L):
            w.group(columns(k.xn, s, S, S5_L), columns(part, 0, 256), (P, 256), k.s_in[:, :, s, :], 1.0)
        for i, dst, scale in ((2, k.qT, DH ** -0.5), (3, k.kT, 1.0)):
            for m in range(4):
                part = w.add(i, HALF, m * P, (m + 1) * P)
                for h in range(2):
                    half = slice(h * HALF, (h + 1) * HALF)
                    w.group(columns(part, 0, P), columns(k.xn, half.start, half.stop), (P, HALF), dst[:, m, half], scale)
        v_first = len(w.groups)
        for h in range(2):
            part = w.add(4, HALF, 256 * h, 256 * (h + 1))
            for t in range(TT):
                n = h * TT + t
                w.group(columns(k.xn, t * P, (t + 1) * P), columns(part, 0, 256), (P, 256), v_out[:, n % 4, :], 1.0)
        groups, firsts = w.groups, w.firsts()

        def psum_of(g):
            rows, cols = groups[g][2]
            view = gb[g % 4][0:rows, 0:cols]
            return view.rearrange("p (a b) -> p a b", b=S5_C) if cols == 256 and g < v_first else view

        def wait_v_slot(eng, g):
            n = g - v_first
            if n >= 4:
                eng.wait_ge(v_stored[n % 4], 16 * (n // 4))

        with st.block() as block:

            @block.sync
            def _(sp):
                sp.dma_start(gain, k.w["norm_mix"][0:1, :].partition_broadcast(P)).then_inc(gain_in, 16)
                sp.dma_start(k.ident[:, :], k.w["ident"]).then_inc(const_in, 16)
                sp.dma_start(k.vec[:, :], k.w["vec"]).then_inc(const_in, 16)
                for t in range(TT):
                    if t >= 3:
                        sp.wait_ge(norm.scaled, t - 2)
                    sp.dma_start(xs[:, t % 3, :], k.w["x"][t * P:(t + 1) * P, :]).then_inc(x_in[t % 3], 16)
                for i in range(5):
                    if i >= 2:
                        sp.wait_ge(w.split.done, w.chunk_end(i - 2))
                    load_chunk(k, sp, i)
                for n in range(2 * TT):
                    g = v_first + n
                    h, t = n // TT, n % TT
                    sp.wait_ge((out_act, out_dve)[g % 2], g // 2 + 1)
                    sp.dma_start(k.v_dram[t * P:(t + 1) * P, 256 * h:256 * (h + 1)], v_out[:, n % 4, :])\
                        .then_inc(v_stored[n % 4], 16)
                for i in range(4):
                    sp.wait_ge(v_stored[i], 16 * (2 * TT // 4))

            @block.gpsimd
            def _(pool):
                pool.memset(k.uP[:, :, 0:3], 0.0).then_inc(st.sem("u_padded"), 1)

            @block.scalar
            def _(act):
                norm.scalar(act)
                for g in range(0, len(groups), 2):
                    if g >= v_first:
                        wait_v_slot(act, g)
                    act.wait_ge(product, g + 1)
                    act.activation(groups[g][3], psum_of(g), ACT.Copy, scale=groups[g][4]).then_inc(out_act, 1)

            @block.vector
            def _(dve):
                dve.wait_ge(gain_in, 16)
                norm.vector(dve)
                w.vector(dve, 0, product)
                for n in range(len(w.pieces)):
                    for g in range(firsts[n], firsts[n + 1]):
                        if n + 1 < len(w.pieces) and g == max(firsts[n], w.pieces[n + 1][3] - 1):
                            w.vector(dve, n + 1, product)
                        if g % 2:
                            if g >= v_first:
                                wait_v_slot(dve, g)
                            dve.wait_ge(product, g + 1)
                            dve.tensor_scalar(groups[g][3], psum_of(g), groups[g][4], None, ALU.mult).then_inc(out_dve, 1)

            @block.tensor
            def _(pe):
                pe.wait_ge(const_in, 32)
                norm.tensor(pe)
                norm.wait_all(pe)
                for g, (lhs, rhs, (rows, cols), _, _) in enumerate(groups):
                    if g in firsts:
                        pe.wait_ge(w.split.done, firsts.index(g) + 1)
                    if g >= 4:
                        pe.wait_ge((out_act, out_dve)[g % 2], (g - 4) // 2 + 1)
                    for c in range(KT):
                        last = split_product(pe, gb[g % 4][0:rows, 0:cols], lhs(c), rhs(c), c == 0, c == KT - 1)
                    last.then_inc(product, 1)


def broadcast(ap, axis, n):
    shape = list(ap.shape)
    return ap.unsqueeze(axis).to_broadcast(shape[:axis] + [n] + shape[axis:])


def mlstm(k):
    HP = M_H // 2
    HC = M_H * NC
    with k.stage() as st:
        free = k.ring[:, 2 * SLOT:4 * SLOT].rearrange("p (n j t) -> p n j t", n=4, j=HP)
        cT, mqT, mkT, interB = (free[:, n, :, :] for n in range(4))
        free = k.ring[:, 0:SLOT].rearrange("p (n c l) -> p n c l", n=2, l=L)
        cmB, kw = free[:, 0, :, :], free[:, 1, :, :]
        state = k.yT[:, 2:6, :].rearrange("p a b -> p (a b)")[:, 0:HP * NC * (DH + 1)].rearrange(
            "p (c e) -> p c e", e=DH + 1)
        v1 = k.ring[:, SLOT:SLOT + HP * NC * (DH + 1)].rearrange("p (c e) -> p c e", e=DH + 1)
        wts = st.sbuf("mlstm_weights", [P, HP, 3, P])
        gi = st.sbuf("gi", [HC, L])
        gf = st.sbuf("gf", [HC, L])
        tmp = st.sbuf("gate_tmp", [HC, 2, L])
        cum = st.sbuf("cum", [HC, L])
        rel = st.sbuf("rel", [HC, L])
        cmax = st.sbuf("cmax", [HC, L])
        zero = st.sbuf("zero", [HC, L])
        gm = st.sbuf("gm", [HC, 8])
        inter = st.sbuf("inter", [HC, L])
        dup = st.sbuf("dup", [HC, 4, 2, L])
        row = st.sbuf("row", [M_H, 4, NC + 1])
        col = st.sbuf("col", [P, 4, HP, NC])
        upd = st.sbuf("upd", [P, HP * NC, DH + 1])
        hn = upd
        sq = kw
        stat = st.sbuf("h_stat", [P, 4, HP * NC])
        bank = [st.psum(f"mb{i}", [P, HALF]) for i in range(8)]
        dram = {n: k.nc.dram_tensor(n, sh, F32, kind="Internal").ap() for n, sh in (
            ("gate_dram", [2 * M_H, S]), ("gm_dram", [2, HC]), ("m_dram", [2, HC]), ("cmax_dram", [M_H, S]),
            ("inter_dram", [M_H, S]))}
        sem = {n: st.sem("m_" + n) for n in (
            "weights_in gates_out gates_in gm_out gm_in m_out m_in cm_out inter_out cm_in inter_in pad bias "
            "act gate pool conv silu qk qk_act kv kv_act kv_dve cols cols_dve s_done ew qi u_done u_evac states "
            "o_done o_evac h_done hT_done y den").split()}
        vec = k.vec

        def V(name, j):
            a = VECS[name][0] + j
            return vec[:, a:a + 1]

        with st.block() as block:

            @block.sync
            def _(sp):
                sp.dma_start(wts[:, :, :, :], k.w["mlstm_w"]).then_inc(sem["weights_in"], 16)
                sp.wait_ge(sem["bias"], 1)
                sp.dma_start(dram["gate_dram"], k.gateT[:, :]).then_inc(sem["gates_out"], 16)
                sp.wait_ge(sem["gates_out"], 16)
                gd = dram["gate_dram"]
                sp.dma_start(gi[:, :], gd[0:M_H, :].rearrange("h (c l) -> (h c) l", l=L)).then_inc(sem["gates_in"], 16)
                sp.dma_start(gf[:, :], gd[M_H:, :].rearrange("h (c l) -> (h c) l", l=L)).then_inc(sem["gates_in"], 16)
                sp.wait_ge(sem["gate"], 6)
                for i in range(2):
                    sp.dma_start(dram["gm_dram"][i:i + 1, :].rearrange("a n -> n a"), gm[:, i:i + 1]).then_inc(sem["gm_out"], 16)
                sp.wait_ge(sem["gm_out"], 32)
                for i in range(2):
                    sp.dma_start(row[:, i, 0:NC], dram["gm_dram"][i, :].rearrange("(h c) -> h c", c=NC)).then_inc(sem["gm_in"], 16)
                sp.wait_ge(sem["gate"], 7)
                for i in range(2):
                    sp.dma_start(dram["m_dram"][i, :].rearrange("(h c) -> h c", c=NC), row[:, 2, i:i + NC]).then_inc(sem["m_out"], 16)
                sp.wait_ge(sem["m_out"], 32)
                for i in range(2):
                    sp.dma_start(gm[:, 2 + i:3 + i], dram["m_dram"][i:i + 1, :].rearrange("a n -> n a")).then_inc(sem["m_in"], 16)
                sp.wait_ge(sem["gate"], 8)
                sp.dma_start(dram["cmax_dram"].rearrange("h (c l) -> (h c) l", l=L), cmax[:, :]).then_inc(sem["cm_out"], 16)
                sp.wait_ge(sem["cm_out"], 16)
                for q in range(2):
                    sp.dma_start(cmB[q * DH:(q + 1) * DH, :, :].rearrange("p (j c) l -> p j (c l)", j=HP),
                                 bcast_rows(dram["cmax_dram"], q, HP)).then_inc(sem["cm_in"], 16)
                sp.wait_ge(sem["act"], 4)
                sp.dma_start(dram["inter_dram"].rearrange("h (c l) -> (h c) l", l=L), inter[:, :]).then_inc(sem["inter_out"], 16)
                sp.wait_ge(sem["inter_out"], 16)
                for q in range(2):
                    sp.dma_start(interB[q * DH:(q + 1) * DH, :, :], bcast_rows(dram["inter_dram"], q, HP)).then_inc(sem["inter_in"], 16)
                for i in (5, 6):
                    load_chunk(k, sp, i)

            @block.gpsimd
            def _(pool):
                pool.memset(zero[:, :], 0.0).then_inc(sem["pad"], 1)
                pool.memset(v1[:, :, DH:DH + 1], 1.0).then_inc(sem["pad"], 1)
                pool.memset(state[:, :, :], 0.0).then_inc(sem["pad"], 1)
                pool.memset(row[:, 2, 0:1], 0.0).then_inc(sem["pad"], 1)
                pool.wait_ge(sem["ew"], 1)
                for q in range(2):
                    part = cmB[q * DH:(q + 1) * DH, :, :]
                    pool.affine_select(out=part, in_=part, compare_op=ALU.is_ge, fill=NEG, base=0,
                                       pattern=[[0, HP * NC], [1, L]], channel_multiplier=-1).then_inc(sem["pool"], 1)

            @block.scalar
            def _(act):
                for g in range(4):
                    act.wait_ge(sem["kv"], g + 1)
                    act.activation(v1[:, 8 * g:8 * g + 8, 0:DH], bank[4 + g][:, :].rearrange("p (c e) -> p c e", e=DH),
                                   ACT.Copy).then_inc(sem["kv_act"], 1)
                for j in range(HP):
                    act.wait_ge(sem["conv"], 4 * (j + 1))
                    act.activation(cT[:, j, :], cT[:, j, :], ACT.Silu, bias=V("conv_b", j)).then_inc(sem["silu"], 1)
                for g in range(8):
                    dst = (mqT, mkT)[g // 4]
                    act.wait_ge(sem["qk"], g + 1)
                    act.activation(dst[:, (g // 2) % 2, (g % 2) * HALF:(g % 2 + 1) * HALF], bank[g % 4][:, :], ACT.Copy,
                                   scale=(DH ** -0.5, 1.0)[g // 4]).then_inc(sem["qk_act"], 1)
                act.wait_ge(sem["gate"], 1)
                act.activation(tmp[:, 0, :], tmp[:, 0, :], ACT.Exp, scale=-1.0).then_inc(sem["act"], 1)
                act.wait_ge(sem["act"], 1)
                act.activation(tmp[:, 1, :], tmp[:, 0, :], ACT.Ln, bias=1.0).then_inc(sem["act"], 1)
                act.wait_ge(sem["gate"], 9)
                act.activation(dup[:, 1, 0, :], rel[:, :], ACT.Exp, bias=gm[:, 4:5]).then_inc(sem["act"], 1)
                act.activation(inter[:, :], cmax[:, :], ACT.Exp, scale=-1.0, bias=gm[:, 2:3]).then_inc(sem["act"], 1)
                act.activation(dup[:, 2, 0, :], tmp[:, 0, :], ACT.Exp, scale=-1.0).then_inc(sem["act"], 1)
                act.activation(dup[:, 3, 0, :], zero[:, :], ACT.Exp, bias=gm[:, 5:6]).then_inc(sem["act"], 1)
                act.wait_ge(sem["pool"], 2)
                act.activation(cmB[:, :, :], cmB[:, :, :], ACT.Exp).then_inc(sem["act"], 1)
                for g in range(8):
                    act.wait_ge(sem["u_done"], g + 1)
                    act.activation(upd[:, 4 * g:4 * g + 4, :], bank[g % 4][:, 0:4 * (DH + 1)].rearrange(
                        "p (c e) -> p c e", e=DH + 1), ACT.Copy).then_inc(sem["u_evac"], 1)
                for g in range(8):
                    act.wait_ge(sem["o_done"], g + 1)
                    act.activation(hn[:, 4 * g:4 * g + 4, :], bank[4 + g % 4][:, 0:4 * (DH + 1)].rearrange(
                        "p (c e) -> p c e", e=DH + 1), ACT.Copy).then_inc(sem["o_evac"], 1)
                act.wait_ge(sem["h_done"], 4)
                act.activation(stat[:, 1, :], stat[:, 1, :], ACT.Sqrt).then_inc(sem["act"], 1)
                act.activation(k.oT[:, :, :], k.oT[:, :, :], ACT.Sigmoid).then_inc(sem["act"], 1)

            @block.vector
            def _(dve):
                dve.tensor_scalar(k.gateT[:, :], k.gateT[:, :], V("gate_b", 0)[0:2 * M_H, :], None, ALU.add).then_inc(sem["bias"], 1)
                for j in range(HP):
                    dve.tensor_scalar(cT[:, j, :], k.uP[:, j, 0:S], V("conv_w", 4 * j), None, ALU.mult).then_inc(sem["conv"], 1)
                    for tap in range(1, 4):
                        dve.wait_ge(sem["conv"], 4 * j + tap)
                        dve.scalar_tensor_tensor(out=cT[:, j, :], in0=k.uP[:, j, tap:tap + S], scalar=V("conv_w", 4 * j + tap),
                                                 in1=cT[:, j, :], op0=ALU.mult, op1=ALU.add).then_inc(sem["conv"], 1)
                dve.wait_ge(sem["gates_in"], 32)
                dve.scalar_tensor_tensor(out=tmp[:, 0, :], in0=gf[:, :], scalar=-1.0, in1=gf[:, :], op0=ALU.mult,
                                         op1=ALU.max).then_inc(sem["gate"], 1)
                dve.wait_ge(sem["act"], 2)
                dve.scalar_tensor_tensor(out=gf[:, :], in0=gf[:, :], scalar=0.0, in1=tmp[:, 1, :], op0=ALU.min,
                                         op1=ALU.subtract).then_inc(sem["gate"], 1)
                dve.wait_ge(sem["gate"], 2)
                dve.wait_ge(sem["pad"], 4)
                dve.tensor_tensor_scan(cum[:, :], gf[:, :], zero[:, :], 0.0, ALU.add, ALU.add).then_inc(sem["gate"], 1)
                dve.wait_ge(sem["gate"], 3)
                dve.tensor_tensor(rel[:, :], gi[:, :], cum[:, :], ALU.subtract).then_inc(sem["gate"], 1)
                dve.wait_ge(sem["gate"], 4)
                dve.tensor_scalar(gm[:, 0:1], cum[:, L - 1:L], 0.0, None, ALU.add).then_inc(sem["gate"], 1)
                dve.tensor_reduce(gm[:, 6:7], rel[:, :], AX_X, ALU.max).then_inc(sem["cols"], 1)
                dve.wait_ge(sem["cols"], 1)
                dve.tensor_tensor(gm[:, 1:2], gm[:, 6:7], cum[:, L - 1:L], ALU.add).then_inc(sem["gate"], 1)
                dve.wait_ge(sem["gm_in"], 32)
                dve.tensor_tensor_scan(row[:, 2, 1:NC + 1], row[:, 0, 0:NC], row[:, 1, 0:NC], 0.0, ALU.add,
                                       ALU.max).then_inc(sem["gate"], 1)
                dve.wait_ge(sem["m_in"], 32)
                dve.tensor_tensor_scan(cmax[:, :], rel[:, :], rel[:, :], gm[:, 2:3], ALU.max, ALU.max).then_inc(sem["gate"], 1)
                dve.tensor_tensor(gm[:, 4:5], gm[:, 0:1], gm[:, 3:4], ALU.subtract).then_inc(sem["cols"], 1)
                dve.wait_ge(sem["cols"], 2)
                dve.tensor_tensor(gm[:, 5:6], gm[:, 4:5], gm[:, 2:3], ALU.add).then_inc(sem["cols"], 1)
                dve.wait_ge(sem["gate"], 8)
                dve.tensor_tensor(tmp[:, 0, :], cum[:, :], cmax[:, :], ALU.add).then_inc(sem["cols"], 1)
                dve.wait_ge(sem["cols"], 4)
                dve.tensor_copy(dup[:, 0, 0, :], rel[:, :]).then_inc(sem["gate"], 1)
                dve.wait_ge(sem["act"], 6)
                dve.wait_ge(sem["gate"], 9)
                dve.tensor_copy(dup[:, :, 1, :], dup[:, :, 0, :]).then_inc(sem["gate"], 1)
                dve.wait_ge(sem["cols_dve"], 1)
                for q in range(2):
                    half = slice(q * DH, (q + 1) * DH)
                    view = bank[4][half, 0:4 * HC].rearrange("p (n j q c) -> p n j q c", n=4, j=HP, q=2)
                    dve.tensor_copy(col[half, :, :, :], view[:, :, :, q, :]).then_inc(sem["gate"], 1)
                dve.wait_ge(sem["gate"], 12)
                dve.wait_ge(sem["cm_in"], 32)
                rcol = col[:, 0, :, :].rearrange("p j c -> p (j c)")
                dve.tensor_tensor(cmB[:, :, :], broadcast(rcol, 2, L), cmB[:, :, :], ALU.subtract).then_inc(sem["ew"], 1)
                wcol = col[:, 1, :, :].rearrange("p j c -> p (j c)")
                for g in range(4):
                    dve.wait_ge(sem["kv"], 4 + g + 1)
                    dve.tensor_tensor(kw[:, 8 * g:8 * g + 8, :], bank[g][:, :].rearrange("p (c e) -> p c e", e=DH),
                                      broadcast(wcol[:, 8 * g:8 * g + 8], 2, DH), ALU.mult).then_inc(sem["kv_dve"], 1)
                dve.wait_ge(sem["inter_in"], 32)
                dve.wait_ge(sem["qk_act"], 8)
                dve.wait_ge(sem["s_done"], 4)
                dve.tensor_tensor(interB[:, :, :], mqT[:, :, :], interB[:, :, :], ALU.mult).then_inc(sem["qi"], 1)
                dve.wait_ge(sem["act"], 7)
                for g in range(4):
                    part = cmB[:, 8 * g:8 * g + 8, :]
                    dve.tensor_tensor(part, part, bank[4 + g][:, :].rearrange("p (c l) -> p c l", l=L), ALU.mult)\
                        .then_inc(sem["ew"], 1)
                dcol = col[:, 3, :, :].rearrange("p j c -> p (j c)")
                dve.wait_ge(sem["u_evac"], 8)
                n = 0
                for c in range(NC - 1):
                    for j in range(HP):
                        i = j * NC + c
                        if c:
                            dve.wait_ge(sem["states"], n - 1)
                        dve.scalar_tensor_tensor(out=state[:, i + 1, :], in0=state[:, i, :], scalar=dcol[:, i:i + 1],
                                                 in1=upd[:, i, :], op0=ALU.mult, op1=ALU.add).then_inc(sem["states"], 1)
                        n += 1
                dve.wait_ge(sem["o_evac"], 8)
                ecol = col[:, 2, :, :].rearrange("p j c -> p (j c)")
                dve.scalar_tensor_tensor(out=stat[:, 1, :], in0=hn[:, :, DH], scalar=-1.0, in1=hn[:, :, DH], op0=ALU.mult,
                                         op1=ALU.max).then_inc(sem["den"], 1)
                dve.wait_ge(sem["den"], 1)
                dve.tensor_tensor(stat[:, 0, :], stat[:, 1, :], ecol, ALU.max).then_inc(sem["h_done"], 1)
                dve.wait_ge(sem["h_done"], 1)
                dve.reciprocal(stat[:, 2, :], stat[:, 0, :]).then_inc(sem["cols"], 1)
                dve.wait_ge(sem["cols"], 5)
                dve.tensor_tensor(hn[:, :, 0:DH], hn[:, :, 0:DH], broadcast(stat[:, 2, :], 2, DH), ALU.mult).then_inc(sem["h_done"], 1)
                dve.wait_ge(sem["h_done"], 2)
                dve.tensor_tensor(sq[:, :, :], hn[:, :, 0:DH], hn[:, :, 0:DH], ALU.mult).then_inc(sem["h_done"], 1)
                dve.wait_ge(sem["h_done"], 3)
                dve.tensor_reduce(stat[:, 3, :], sq[:, :, :], AX_X, ALU.add).then_inc(sem["cols"], 1)
                dve.wait_ge(sem["cols"], 6)
                dve.tensor_scalar(stat[:, 1, :], stat[:, 3, :], 1.0 / DH, EPS, ALU.mult, ALU.add).then_inc(sem["h_done"], 1)
                dve.wait_ge(sem["act"], 8)
                dve.reciprocal(stat[:, 0, :], stat[:, 1, :]).then_inc(sem["cols"], 1)
                dve.wait_ge(sem["cols"], 7)
                dve.tensor_tensor(hn[:, :, 0:DH], hn[:, :, 0:DH], broadcast(stat[:, 0, :], 2, DH), ALU.mult).then_inc(sem["h_done"], 1)
                for j in range(HP):
                    dve.tensor_scalar(cT[:, j, :], cT[:, j, :], V("m_skip", j), None, ALU.mult).then_inc(sem["y"], 1)
                dve.wait_ge(sem["y"], 2)
                dve.wait_ge(sem["act"], 9)
                for g in range(4):
                    j, half = g // 2, slice((g % 2) * HALF, (g % 2 + 1) * HALF)
                    dve.wait_ge(sem["hT_done"], g + 1)
                    dve.scalar_tensor_tensor(out=cT[:, j, half], in0=bank[g][:, :], scalar=V("m_gain", j), in1=cT[:, j, half],
                                             op0=ALU.mult, op1=ALU.add).then_inc(sem["y"], 1)
                    dve.wait_ge(sem["y"], 3 + 2 * g)
                    dve.tensor_tensor(k.yT[:, j, half], cT[:, j, half], k.oT[:, j, half], ALU.mult).then_inc(sem["y"], 1)

            @block.tensor
            def _(pe):
                def per_chunk(out, lhs, rhs, g, stop=True, start=True):
                    for i in range(8 * g, 8 * g + 8):
                        for q in range(2):
                            half = slice(q * DH, (q + 1) * DH)
                            last = pe.matmul(out[half, (i % 8) * DH:(i % 8 + 1) * DH], lhs(half, i), rhs(half, i),
                                             start=start, stop=stop)
                    return last

                pe.wait_ge(sem["weights_in"], 16)
                for g in range(4):
                    per_chunk(bank[4 + g], lambda half, i: k.uP[half, i // NC, 3 + (i % NC) * L:3 + (i % NC + 1) * L],
                              lambda half, i: wts[half, i // NC, 2, half], g).then_inc(sem["kv"], 1)
                pe.wait_ge(sem["silu"], HP)
                for g in range(8):
                    if g >= 4:
                        pe.wait_ge(sem["qk_act"], g - 3)
                    j = (g // 2) % 2
                    pe.matmul(bank[g % 4][:, :], wts[:, j, g // 4, :], cT[:, j, (g % 2) * HALF:(g % 2 + 1) * HALF],
                              start=True, stop=True).then_inc(sem["qk"], 1)
                pe.wait_ge(sem["gate"], 10)
                pe.wait_ge(sem["kv_act"], 1)
                for n in range(4):
                    last = pe.transpose(bank[4][:, n * HC:(n + 1) * HC], dup[:, n, :, :].rearrange("p a l -> p (a l)"),
                                        k.ident[0:HC, 0:HC])
                last.then_inc(sem["cols_dve"], 1)

                pe.wait_ge(sem["qk_act"], 8)
                pe.wait_ge(sem["gate"], 12)
                for g in range(4):
                    per_chunk(bank[g], lambda half, i: cT[half, i // NC, (i % NC) * L:(i % NC + 1) * L],
                              lambda half, i: wts[half, i // NC, 1, half], g).then_inc(sem["kv"], 1)
                for g in range(4):
                    pe.wait_ge(sem["kv_act"], g + 1)
                    per_chunk(bank[4 + g], lambda half, i: mkT[half, i // NC, (i % NC) * L:(i % NC + 1) * L],
                              lambda half, i: mqT[half, i // NC, (i % NC) * L:(i % NC + 1) * L], g).then_inc(sem["s_done"], 1)
                W = DH + 1

                def per_four(out, terms, g):
                    for i in range(4 * g, 4 * g + 4):
                        for q in range(2):
                            half = slice(q * DH, (q + 1) * DH)
                            for n, (lhs, rhs) in enumerate(terms):
                                last = pe.matmul(out[half, (i % 4) * W:(i % 4 + 1) * W], lhs(half, i), rhs(half, i),
                                                 start=(n == 0), stop=(n == len(terms) - 1))
                    return last

                pe.wait_ge(sem["kv_dve"], 4)
                for g in range(8):
                    if g >= 4:
                        pe.wait_ge(sem["u_evac"], g - 3)
                    per_four(bank[g % 4], [(lambda half, i: kw[half, i, :], lambda half, i: v1[half, i, :])], g)\
                        .then_inc(sem["u_done"], 1)
                pe.wait_ge(sem["ew"], 5)
                pe.wait_ge(sem["qi"], 1)
                pe.wait_ge(sem["states"], HP * (NC - 1))
                for g in range(8):
                    if g >= 4:
                        pe.wait_ge(sem["o_evac"], g - 3)
                    per_four(bank[4 + g % 4], [
                        (lambda half, i: cmB[half, i, :], lambda half, i: v1[half, i, :]),
                        (lambda half, i: interB[half, i // NC, (i % NC) * L:(i % NC + 1) * L], lambda half, i: state[half, i, :])],
                        g).then_inc(sem["o_done"], 1)
                pe.wait_ge(sem["h_done"], 5)
                for g in range(4):
                    per_chunk(bank[g], lambda half, i: hn[half, i, 0:DH], lambda half, i: k.ident[half, half], g)\
                        .then_inc(sem["hT_done"], 1)


def bcast_rows(rows, q, n):
    return rows.rearrange("(j q) t -> q j t", j=n)[q].partition_broadcast(DH)


def s5(k):
    GP = S5_G // 2
    C = S // S5_L
    SUB = 8
    RUNS = C // SUB
    with k.stage() as st:
        free = k.ring[:, 2 * SLOT:4 * SLOT].rearrange("p (n f) -> p n f", n=4)
        UT = free[:, 0, :].rearrange("p (g c) -> p g c", c=C)
        T = free[:, 1, :].rearrange("p (g c) -> p g c", c=P)
        z = free[:, 2, :].rearrange("p (t h) -> p t h", h=256)
        zT = free[:, 3, :].rearrange("p (n t c) -> p n t c", n=2, c=C)
        spare = k.yT[:, 4:8, :].rearrange("p a b -> p (a b)")
        WL = spare[:, 0:2 * GP * 9 * S5_C].rearrange("p (r g l h) -> p r g l h", r=2, g=GP, l=9)
        BT = k.oT[:, :, :].rearrange("p r (g s h) -> p r g s h", g=GP, s=S5_L)
        BG = k.uP[:, :, 3:].rearrange("p r (g s) -> p r g s", g=GP)
        X = st.sbuf("chunk_states", [P, 2, GP, C + 1])
        t1 = k.ring[:, 0:2048].rearrange("p (r x) -> p r x", r=2)
        t2 = k.ring[:, 2048:4096].rearrange("p (r x) -> p r x", r=2)
        Km = k.ring[0:S5_C, SLOT:SLOT + S5_G * P]
        Km = Km.rearrange("p (g x) -> p g x", x=P)
        bc = st.sbuf("s5_bc", [P, 4, GP, S5_C])
        bb = st.sbuf("s5_b_bar", [P, 2, GP, S5_C])
        diag = st.sbuf("s5_diag", [S5_C, S5_G, S5_C])
        pw = st.sbuf("a_powers", [P, 2, 9, GP])
        pr = st.sbuf("a_powers_down", [P, 2, 8, GP])
        fp = st.sbuf("f_powers", [P, 2, 9, GP])
        ff = st.sbuf("recur_factors", [P, 2, 12, 2, GP])
        par = st.sbuf("s5_scalars", [P, 24, GP])
        wglu = k.ring[:, SLOT + 2048:SLOT + 2560].rearrange("p (n h) -> p n h", n=2)
        bglu = st.sbuf("glu_bias", [P, 256])
        stat = st.sbuf("s5_stat", [P, 4, S5_L])
        bank = [st.psum(f"sb{i}", [P, HALF]) for i in range(8)]
        sem = {n: st.sem("s_" + n) for n in (
            "par_in b_in glu_in toep zero chain act bt bg_t bg ut_t ut km_done km xin_done xin "
            "y_done gelu zt_done zt glu_done gate_done norm yt_done yt").split()}
        a0 = VECS["a_re"][0]
        a_re, a_im, ldt = k.vec[:, a0:a0 + 8], k.vec[:, a0 + 8:a0 + 16], k.vec[:, a0 + 16:a0 + 24]
        N = {n: i for i, n in enumerate(
            "dt mag theta turns r s_half s_full cos re im xr den inv c_re c_im u v x f_re f_im".split())}

        def p_(n):
            return par[:, N[n], :]

        with st.block() as block:

            @block.sync
            def _(sp):
                sp.dma_start(bc[:, :, :, :], k.w["s5_bc"]).then_inc(sem["b_in"], 16)
                sp.dma_start(diag[:, :, :], k.w["s5_diag"]).then_inc(sem["b_in"], 16)
                sp.dma_start(wglu, k.w["s5_w_glu"].rearrange("(n p) h -> p n h", p=P)).then_inc(sem["glu_in"], 16)
                sp.dma_start(bglu[:, :], k.w["s5_b_glu"][0:1, :].partition_broadcast(P)).then_inc(sem["glu_in"], 16)
                sp.wait_ge(sem["km"], 4)
                sp.wait_ge(sem["zero"], 1)
                for s in range(S5_L):
                    rows = slice(s * S5_C, (s + 1) * S5_C)
                    sp.dma_start(T[rows, :, s * S5_C:], Km[:, :, 0:(S5_L - s) * S5_C]).then_inc(sem["toep"], 16)

            @block.gpsimd
            def _(pool):
                pool.memset(T, 0.0).then_inc(sem["zero"], 1)
                pool.memset(X[:, :, :, 0:1], 0.0).then_inc(sem["zero"], 1)

            @block.scalar
            def _(act):
                act.activation(p_("dt"), ldt, ACT.Exp).then_inc(sem["act"], 1)
                act.wait_ge(sem["chain"], 1)
                act.activation(p_("mag"), p_("mag"), ACT.Exp).then_inc(sem["act"], 1)
                act.wait_ge(sem["chain"], 10)
                act.activation(p_("s_half"), p_("r"), ACT.Sin, scale=0.5).then_inc(sem["act"], 1)
                act.activation(p_("s_full"), p_("r"), ACT.Sin).then_inc(sem["act"], 1)
                for b in range(4):
                    act.wait_ge(sem["ut_t"], b + 1)
                    act.activation(UT[:, 4 * b:4 * b + 4, :], bank[b][:, :].rearrange("p (g c) -> p g c", c=C), ACT.Copy)\
                        .then_inc(sem["ut"], 1)
                for b in range(4):
                    act.wait_ge(sem["bg_t"], b + 1)
                    act.activation(BG[:, b // 2, 4 * (b % 2):4 * (b % 2) + 4, :],
                                   bank[4 + b][:, :].rearrange("p (g c) -> p g c", c=P), ACT.Copy).then_inc(sem["bg"], 1)
                for b in range(4):
                    act.wait_ge(sem["xin_done"], b + 1)
                    act.activation(X[:, b // 2, 4 * (b % 2):4 * (b % 2) + 4, 1:],
                                   bank[b][:, :].rearrange("p (g c) -> p g c", c=C), ACT.Copy).then_inc(sem["xin"], 1)
                for b in range(4):
                    act.wait_ge(sem["y_done"], b + 1)
                    act.activation(z.rearrange("p t (g q h) -> p q g t h", q=2, h=S5_C)[:, b // 2, 4 * (b % 2):4 * (b % 2) + 4],
                                   bank[b][:, :].rearrange("p (g t h) -> p g t h", g=4, t=S5_L),
                                   ACT.Gelu_apprx_tanh).then_inc(sem["gelu"], 1)
                for b in range(4):
                    act.wait_ge(sem["zt_done"], b + 1)
                    act.activation(zT[:, b // 2, 4 * (b % 2):4 * (b % 2) + 4, :],
                                   bank[4 + b][:, :].rearrange("p (t c) -> p t c", c=C), ACT.Copy).then_inc(sem["zt"], 1)
                for b in range(4):
                    act.wait_ge(sem["glu_done"], b + 1)
                    part = t1.rearrange("p r x -> p (r x)")[:, HALF * b:HALF * (b + 1)]
                    act.activation(part, part, ACT.Sigmoid).then_inc(sem["gate_done"], 1)
                act.wait_ge(sem["norm"], 2)
                act.activation(stat[:, 2, :], stat[:, 1, :], ACT.Sqrt).then_inc(sem["norm"], 1)
                for b in range(4):
                    act.wait_ge(sem["yt_done"], b + 1)
                    j, g0 = b // 2, VECS["s_gain"][0] + b // 2
                    act.activation(k.yT[:, 2 + j, :].rearrange("p (c t) -> p t c", t=S5_L)[:, 4 * (b % 2):4 * (b % 2) + 4, :],
                                   bank[4 + b][:, :].rearrange("p (t c) -> p t c", c=C), ACT.Copy,
                                   scale=k.vec[:, g0:g0 + 1]).then_inc(sem["yt"], 1)

            @block.vector
            def _(dve):
                count = [0]

                def step(ins, ready=True):
                    count[0] += 1
                    ins.then_inc(sem["chain"], 1)
                    if ready:
                        dve.wait_ge(sem["chain"], count[0])

                def tt(out, x, y, op, ready=True):
                    step(dve.tensor_tensor(out, x, y, op), ready)

                def ts(out, x, a, op, b=None, op2=None, ready=True):
                    step(dve.tensor_scalar(out, x, a, b, op, op2) if op2 else dve.tensor_scalar(out, x, a, None, op), ready)

                dve.wait_ge(sem["act"], 1)
                tt(p_("mag"), a_re, p_("dt"), ALU.mult)
                tt(p_("theta"), a_im, p_("dt"), ALU.mult)
                rounder = float(1.5 * 2.0 ** 23)
                ts(p_("turns"), p_("theta"), float(np.float32(0.5 / np.pi)), ALU.mult)
                ts(p_("turns"), p_("turns"), rounder, ALU.add)
                ts(p_("turns"), p_("turns"), rounder, ALU.subtract)
                at = p_("theta")
                for part in (6.28125, 0.0019350051879882812, 3.0199159819336793e-07):
                    step(dve.scalar_tensor_tensor(out=p_("r"), in0=p_("turns"), scalar=-part, in1=at, op0=ALU.mult, op1=ALU.add))
                    at = p_("r")
                ts(p_("r"), p_("r"), 3.1415925, ALU.min, -3.1415925, ALU.max)
                ts(p_("u"), p_("r"), 1.0, ALU.mult)
                dve.wait_ge(sem["act"], 4)
                tt(p_("cos"), p_("s_half"), p_("s_half"), ALU.mult)
                ts(p_("cos"), p_("cos"), -2.0, ALU.mult, 1.0, ALU.add)
                tt(p_("re"), p_("mag"), p_("cos"), ALU.mult, ready=False)
                tt(p_("im"), p_("mag"), p_("s_full"), ALU.mult)
                ts(p_("xr"), p_("re"), -1.0, ALU.add, ready=False)
                tt(p_("u"), a_re, a_re, ALU.mult, ready=False)
                tt(p_("v"), a_im, a_im, ALU.mult)
                tt(p_("den"), p_("u"), p_("v"), ALU.add)
                step(dve.reciprocal(p_("inv"), p_("den")), ready=False)
                tt(p_("u"), p_("xr"), a_re, ALU.mult, ready=False)
                tt(p_("v"), p_("im"), a_im, ALU.mult)
                tt(p_("u"), p_("u"), p_("v"), ALU.add)
                tt(p_("c_re"), p_("u"), p_("inv"), ALU.mult)
                tt(p_("u"), p_("im"), a_re, ALU.mult, ready=False)
                tt(p_("v"), p_("xr"), a_im, ALU.mult)
                tt(p_("u"), p_("u"), p_("v"), ALU.subtract)
                tt(p_("c_im"), p_("u"), p_("inv"), ALU.mult)

                def cmul(o_re, o_im, x_re, x_im, y_re, y_im, u, v):
                    tt(u, x_re, y_re, ALU.mult, ready=False)
                    tt(v, x_im, y_im, ALU.mult)
                    tt(o_re, u, v, ALU.subtract)
                    tt(u, x_re, y_im, ALU.mult, ready=False)
                    tt(v, x_im, y_re, ALU.mult)
                    tt(o_im, u, v, ALU.add)

                u_s = t1[:, 0, 0:8 * GP].rearrange("p (l g) -> p l g", g=GP)
                v_s = t1[:, 1, 0:8 * GP].rearrange("p (l g) -> p l g", g=GP)

                def powers(dst, re, im):
                    step(dve.memset(dst[:, 0, 0, :], 1.0), ready=False)
                    step(dve.memset(dst[:, 1, 0, :], 0.0), ready=False)
                    ts(dst[:, 0, 1, :], re, 1.0, ALU.mult, ready=False)
                    ts(dst[:, 1, 1, :], im, 1.0, ALU.mult)
                    for n in (1, 2, 4):
                        cmul(dst[:, 0, n + 1:2 * n + 1, :], dst[:, 1, n + 1:2 * n + 1, :],
                             dst[:, 0, 1:n + 1, :], dst[:, 1, 1:n + 1, :], broadcast(dst[:, 0, n, :], 1, n),
                             broadcast(dst[:, 1, n, :], 1, n), u_s[:, 0:n, :], v_s[:, 0:n, :])

                powers(pw, p_("re"), p_("im"))
                for l in range(8):
                    ts(pr[:, :, l, :], pw[:, :, 7 - l, :], 1.0, ALU.mult, ready=False)
                powers(fp, pw[:, 0, 8, :], pw[:, 1, 8, :])
                for n in range(11):
                    if n < 8:
                        re, im = fp[:, 0, n + 1, :], fp[:, 1, n + 1, :]
                    else:
                        a, b = ff[:, 0, n - 1, 0, :], ff[:, 1, n - 1, 1, :]
                        cmul(p_("f_re"), p_("f_im"), a, b, a, b, p_("u"), p_("v"))
                        re, im = p_("f_re"), p_("f_im")
                    ts(ff[:, 0, n, 0, :], re, 1.0, ALU.mult, ready=False)
                    ts(ff[:, 0, n, 1, :], re, 1.0, ALU.mult, ready=False)
                    ts(ff[:, 1, n, 0, :], im, -1.0, ALU.mult, ready=False)
                    ts(ff[:, 1, n, 1, :], im, 1.0, ALU.mult)
                dve.wait_ge(sem["b_in"], 32)
                u_b = t1[:, 0, 0:GP * S5_C].rearrange("p (g h) -> p g h", g=GP)
                v_b = t1[:, 1, 0:GP * S5_C].rearrange("p (g h) -> p g h", g=GP)
                cmul(bb[:, 0, :, :], bb[:, 1, :, :], bc[:, 0, :, :], bc[:, 1, :, :],
                     broadcast(p_("c_re"), 2, S5_C), broadcast(p_("c_im"), 2, S5_C), u_b, v_b)
                u_w = t1[:, 0, 0:GP * 8 * S5_C].rearrange("p (g s h) -> p g s h", g=GP, s=8)
                v_w = t1[:, 1, 0:GP * 8 * S5_C].rearrange("p (g s h) -> p g s h", g=GP, s=8)
                down = [broadcast(pr[:, r, :, :].rearrange("p l g -> p g l"), 3, S5_C) for r in range(2)]
                cmul(BT[:, 0], BT[:, 1], broadcast(bb[:, 0], 2, 8), broadcast(bb[:, 1], 2, 8), down[0], down[1], u_w, v_w)
                dve.tensor_copy(p_("x"), p_("u")).then_inc(sem["bt"], 1)
                for l0 in (0, 8):
                    n = 8 if l0 == 0 else 1
                    up = [broadcast(pw[:, r, l0:l0 + n, :].rearrange("p l g -> p g l"), 3, S5_C) for r in range(2)]
                    c = [broadcast(bc[:, 2 + r], 2, n) for r in range(2)]
                    uu = t1[:, 0, 0:GP * n * S5_C].rearrange("p (g s h) -> p g s h", g=GP, s=n)
                    vv = t1[:, 1, 0:GP * n * S5_C].rearrange("p (g s h) -> p g s h", g=GP, s=n)
                    tt(uu, c[0], up[0], ALU.mult, ready=False)
                    tt(vv, c[1], up[1], ALU.mult)
                    tt(WL[:, 0, :, l0:l0 + n, :], uu, vv, ALU.subtract)
                    tt(uu, c[0], up[1], ALU.mult, ready=False)
                    tt(vv, c[1], up[0], ALU.mult)
                    step(dve.scalar_tensor_tensor(out=uu, in0=uu, scalar=-1.0, in1=vv, op0=ALU.mult, op1=ALU.subtract))
                    step(dve.tensor_copy(WL[:, 1, :, l0:l0 + n, :], uu))
                dve.tensor_copy(p_("x"), p_("u")).then_inc(sem["bt"], 1)
                for b in range(4):
                    dve.wait_ge(sem["km_done"], b + 1)
                    part = Km.rearrange("p (g q) x -> p q g x", q=2)[:, b // 2, 4 * (b % 2):4 * (b % 2) + 4, :]
                    step(dve.tensor_copy(part, bank[b][0:S5_C, :].rearrange("p (g x) -> p g x", x=P)))
                    dve.tensor_tensor(part[:, :, 0:S5_C], part[:, :, 0:S5_C], diag[:, :, :].rearrange(
                        "p (g q) x -> p q g x", q=2)[:, b // 2, 4 * (b % 2):4 * (b % 2) + 4, :], ALU.add)\
                        .then_inc(sem["km"], 1)
                dve.wait_ge(sem["xin"], 4)
                body = X[:, :, :, 1:].rearrange("p r g (n j) -> p r g n j", j=SUB)

                def advance(to, of, power, n):
                    def factor(kind):
                        return broadcast(ff[:, kind, power, :, :], 3, n)

                    a, b = (t[:, :, 0:n * GP].rearrange("p r (g n) -> p r g n", g=GP) for t in (t1, t2))
                    cross = factor(1)
                    tt(a, of, factor(0), ALU.mult, ready=False)
                    tt(b[:, 0], of[:, 1], cross[:, 0], ALU.mult, ready=False)
                    tt(b[:, 1], of[:, 0], cross[:, 1], ALU.mult)
                    tt(a, a, b, ALU.add)
                    tt(to, to, a, ALU.add)

                for j in range(1, SUB):
                    advance(body[:, :, :, :, j], body[:, :, :, :, j - 1], 0, RUNS)
                ends = body[:, :, :, :, SUB - 1]
                for i in range(4):
                    d = 1 << i
                    advance(ends[:, :, :, d:], ends[:, :, :, 0:RUNS - d], 7 + i, RUNS - d)
                for j in range(SUB - 1):
                    advance(body[:, :, :, 1:, j], ends[:, :, :, 0:RUNS - 1], j, RUNS - 1)
                dve.tensor_copy(p_("x"), p_("u")).then_inc(sem["bt"], 1)
                flat = t1.rearrange("p r x -> p (r x)")
                dve.wait_ge(sem["glu_in"], 32)
                for b in range(4):
                    dve.wait_ge(sem["y_done"], 4 + b + 1)
                    part = flat[:, HALF * b:HALF * (b + 1)].rearrange("p (t h) -> p t h", t=2)
                    dve.tensor_tensor(part, bank[b][:, :].rearrange("p (t h) -> p t h", t=2), broadcast(bglu[:, :], 1, 2),
                                      ALU.add).then_inc(sem["glu_done"], 1)
                zf = z.rearrange("p t h -> p (t h)")
                sq = t2.rearrange("p r x -> p (r x)")
                dve.wait_ge(sem["gate_done"], 4)
                tt(zf, zf, flat, ALU.mult)
                tt(sq, zf, zf, ALU.mult)
                dve.tensor_reduce(stat[:, 0, :], sq.rearrange("p (t h) -> p t h", h=256), AX_X, ALU.add).then_inc(sem["norm"], 1)
                dve.wait_ge(sem["norm"], 1)
                dve.tensor_scalar(stat[:, 1, :], stat[:, 0, :], 1.0 / 256, EPS, ALU.mult, ALU.add).then_inc(sem["norm"], 1)
                dve.wait_ge(sem["norm"], 3)
                step(dve.reciprocal(stat[:, 3, :], stat[:, 2, :]))
                dve.tensor_tensor(z, z, broadcast(stat[:, 3, :], 2, 256), ALU.mult).then_inc(sem["bt"], 1)

            @block.tensor
            def _(pe):
                for g in range(S5_G):
                    last = pe.transpose(bank[g // 4][:, (g % 4) * C:(g % 4 + 1) * C],
                                        k.s_in[:, g, :, :].rearrange("p s h -> p (s h)"), k.ident[:, :])
                    if g % 4 == 3:
                        last.then_inc(sem["ut_t"], 1)
                pe.wait_ge(sem["bt"], 1)
                for r in range(2):
                    for g in range(GP):
                        n = r * GP + g
                        last = pe.transpose(bank[4 + n // 4][:, (n % 4) * P:(n % 4 + 1) * P],
                                            BT[:, r, g].rearrange("p s h -> p (s h)"), k.ident[:, :])
                        if n % 4 == 3:
                            last.then_inc(sem["bg_t"], 1)
                pe.wait_ge(sem["bt"], 2)
                pe.wait_ge(sem["ut"], 4)
                for n in range(S5_G):
                    q, gp = n // GP, n % GP
                    half = slice(q * 64, (q + 1) * 64)
                    for r in range(2):
                        last = pe.matmul(bank[n // 4][0:S5_C, (n % 4) * P:(n % 4 + 1) * P], bb[half, r, gp, :],
                                         WL[half, r, gp, 0:8, :].rearrange("p l h -> p (l h)"), start=(r == 0), stop=(r == 1))
                    if n % 4 == 3:
                        last.then_inc(sem["km_done"], 1)
                pe.wait_ge(sem["bg"], 4)
                for r in range(2):
                    for gp in range(GP):
                        n = r * GP + gp
                        if n % 4 == 0:
                            pe.wait_ge(sem["km"], n // 4 + 1)
                        for q in range(2):
                            half = slice(q * 64, (q + 1) * 64)
                            last = pe.matmul(bank[n // 4][half, (n % 4) * C:(n % 4 + 1) * C], BG[:, r, gp, half],
                                             UT[:, 2 * gp + q, :], start=True, stop=True)
                        if n % 4 == 3:
                            last.then_inc(sem["xin_done"], 1)
                pe.wait_ge(sem["toep"], 16 * S5_L)
                pe.wait_ge(sem["zero"], 2)
                pe.wait_ge(sem["xin"], 4)
                for n in range(S5_G):
                    q, gp = n // GP, n % GP
                    pe.matmul(bank[n // 4][:, (n % 4) * P:(n % 4 + 1) * P], UT[:, 2 * gp + q, :], T[:, 2 * gp + q, :],
                              start=(n % 4 == 0), stop=False)
                pe.wait_ge(sem["bt"], 3)
                for n in range(S5_G):
                    q, gp = n // GP, n % GP
                    half = slice(q * 64, (q + 1) * 64)
                    out = bank[n // 4][:, (n % 4) * P:(n % 4 + 1) * P]
                    for r in range(2):
                        last = pe.matmul(out, X[half, r, gp, 0:C],
                                         WL[half, r, gp, 1:9, :].rearrange("p l h -> p (l h)"), start=False, stop=(n % 4 == 3 and r == 1))
                    if n % 4 == 3:
                        last.then_inc(sem["y_done"], 1)
                pe.wait_ge(sem["gelu"], 4)
                for n in range(2):
                    for t in range(S5_L):
                        m = n * S5_L + t
                        last = pe.transpose(bank[4 + m // 4][:, (m % 4) * C:(m % 4 + 1) * C], z[:, t, n * P:(n + 1) * P],
                                            k.ident[:, :])
                        if m % 4 == 3:
                            last.then_inc(sem["zt_done"], 1)
                pe.wait_ge(sem["zt"], 4)
                pe.wait_ge(sem["glu_in"], 32)
                for t in range(S5_L):
                    for n in range(2):
                        last = pe.matmul(bank[t // 2][:, (t % 2) * 256:(t % 2 + 1) * 256], zT[:, n, t, :], wglu[:, n, :],
                                         start=(n == 0), stop=(n == 1))
                    if t % 2:
                        last.then_inc(sem["y_done"], 1)
                pe.wait_ge(sem["bt"], 4)
                for n in range(2):
                    for t in range(S5_L):
                        m = n * S5_L + t
                        last = pe.transpose(bank[4 + m // 4][:, (m % 4) * C:(m % 4 + 1) * C], z[:, t, n * P:(n + 1) * P],
                                            k.ident[:, :])
                        if m % 4 == 3:
                            last.then_inc(sem["yt_done"], 1)


PATTERNS = ((128, 1), (512, 4), (2048, 16))
BLK = 128
O_W = A_W + 2 * A_H


TURN_LAG, SUM_LAG = 2, 3
RING = 4


def attention(k):
    with k.stage() as st:
        v = [k.ring[:, 2 * SLOT:3 * SLOT].rearrange("p (t n) -> p t n", n=A_W),
             k.ring[:, 3 * SLOT:4 * SLOT].rearrange("p (t n) -> p t n", n=A_W),
             k.yT[:, 4:8, :].rearrange("p a (b n) -> p (a b) n", n=A_W)]
        bias = st.sbuf("attn_bias", [P, A_H, 5 * BLK])
        sx = st.sbuf("scores", [P, RING, 2 * BLK])
        pr = st.sbuf("probs", [P, RING, 2 * BLK])
        pT = st.sbuf("probsT", [P, RING, 2 * BLK])
        stage = st.sbuf("out_rows", [P, 2, O_W])
        sb = [st.psum(f"as{i}", [P, HALF]) for i in range(3)]
        tb = [st.psum(f"at{i}", [P, HALF]) for i in range(3)]
        ob = [st.psum(f"ob{i}", [P, HALF]) for i in range(2)]
        v_in = [st.sem(f"v_in{i}") for i in range(3)]
        bias_in = [st.sem(f"bias_in{i}") for i in range(2)]
        scored, biased, exped, turned, pt_act, pt_dve, summed, rows_out = (st.sem("a_" + n) for n in (
            "scored biased exped turned pt_act pt_dve summed rows_out").split())
        stored = [st.sem(f"rows_stored{i}") for i in range(2)]

        units = [(p, t, h) for p in range(3) for t in range(TT) for h in range(A_H)]

        def columns(src, p, t, h, keys):
            rows = src[(h % 2) * DH:(h % 2 + 1) * DH, h // 2, :]
            if p == 0:
                first = max(t - 1, 0) if keys else t
                return rows[:, first * BLK:(t + 1) * BLK]
            if p == 1:
                n, r = t // 4, t % 4
                first = 0 if keys else n
                return rows[:, first * 4 * BLK:(n + 1) * 4 * BLK].rearrange("p (i r) -> p r i", r=4)[:, r, :]
            return rows.rearrange("p (i u) -> p u i", u=TT)[:, t, :]

        def width(p, t):
            return 2 * BLK if (p == 0 and t) or (p == 1 and t >= 4) else BLK

        def bias_of(p, t, h):
            end = (2, 4, 5)[p] * BLK
            return bias[:, h, end - width(p, t):end]

        def values(p, t, h):
            tiles = {0: [t - 1, t], 1: [t - 4, t], 2: [t]}[p] if width(p, t) > BLK or p == 2 else [t]
            return [v[p][:, x, h * DH:(h + 1) * DH] for x in tiles]

        def wait_turned_out(eng, i):
            if i % 3 == 0:
                eng.wait_ge(pt_act, i // 3 + 1)
            else:
                eng.wait_ge(pt_dve, i - i // 3)

        def evacuate(eng, i, copy, sem):
            if i >= RING:
                eng.wait_ge(summed, i - RING + 1)
            eng.wait_ge(turned, i + 1)
            w = width(*units[i][:2])
            copy(pT[:, i % RING, 0:w], tb[i % 3][:, 0:w]).then_inc(sem, 1)

        with st.block() as block:

            @block.sync
            def _(sp):
                first = slice(0, 2 * BLK)
                sp.dma_start(bias[:, :, first], k.w["attn_bias"][:, :, first]).then_inc(bias_in[0], 16)
                sp.dma_start(v[0], k.v_dram.rearrange("(t i) n -> i t n", i=P)).then_inc(v_in[0], 16)
                rest = slice(2 * BLK, 5 * BLK)
                sp.dma_start(bias[:, :, rest], k.w["attn_bias"][:, :, rest]).then_inc(bias_in[1], 16)
                sp.dma_start(v[1], k.v_dram.rearrange("(b i r) n -> i b r n", b=2, r=4)).then_inc(v_in[1], 16)
                sp.dma_start(v[2], k.v_dram.rearrange("(i u) n -> i u n", u=TT)).then_inc(v_in[2], 16)
                for n in range(3 * TT):
                    p, t = n // TT, n % TT
                    sp.wait_ge(rows_out, n + 1)
                    dst = k.attn_dram[p]
                    src = stage[:, n % 2, :]
                    if p == 0:
                        sp.dma_start(dst[t * BLK:(t + 1) * BLK, :], src).then_inc(stored[n % 2], 16)
                    elif p == 1:
                        sp.dma_start(dst.rearrange("(b i r) n -> b r i n", b=2, r=4)[t // 4, t % 4], src)\
                            .then_inc(stored[n % 2], 16)
                    else:
                        sp.dma_start(dst.rearrange("(i u) n -> u i n", u=TT)[t], src).then_inc(stored[n % 2], 16)
                for i in range(2):
                    sp.wait_ge(stored[i], 16 * (3 * TT // 2))

            def wait_stage(eng, n):
                if n >= 2:
                    eng.wait_ge(stored[n % 2], 16 * (n // 2))

            @block.scalar
            def _(act):
                for i in range(len(units) + SUM_LAG + 1):
                    if i < len(units):
                        p, t, h = units[i]
                        n = i // A_H
                        if h == 0:
                            wait_stage(act, n)
                        act.wait_ge(biased, i + 1)
                        if i >= RING:
                            act.wait_ge(turned, i - RING + 1)
                        w = width(p, t)
                        act.activation(pr[:, i % RING, 0:w], sx[:, i % RING, 0:w], ACT.Exp, scale=-1.0,
                                       bias=stage[:, n % 2, A_W + h:A_W + h + 1],
                                       accum_out=stage[:, n % 2, A_W + A_H + h:A_W + A_H + h + 1]).then_inc(exped, 1)
                    if TURN_LAG <= i < len(units) + TURN_LAG and (i - TURN_LAG) % 3 == 0:
                        evacuate(act, i - TURN_LAG, lambda o, x: act.activation(o, x, ACT.Copy), pt_act)
                    j = i - SUM_LAG - 1
                    if j >= 0 and j % A_H == A_H - 1:
                        n = j // A_H
                        act.wait_ge(summed, A_H * (n + 1))
                        act.activation(stage[:, n % 2, 0:A_W], ob[n % 2][:, :], ACT.Copy).then_inc(rows_out, 1)

            @block.vector
            def _(dve):
                dve.wait_ge(bias_in[0], 16)
                for i in range(len(units) + TURN_LAG):
                    if i < len(units):
                        p, t, h = units[i]
                        n = i // A_H
                        if h == 0:
                            wait_stage(dve, n)
                            if n == TT:
                                dve.wait_ge(bias_in[1], 16)
                        dve.wait_ge(scored, i + 1)
                        if i >= RING:
                            dve.wait_ge(exped, i - RING + 1)
                        w = width(p, t)
                        dve.tensor_tensor_reduce(sx[:, i % RING, 0:w], sb[i % 3][:, 0:w], bias_of(p, t, h), -1.0, -NEG,
                                                 ALU.add, ALU.min, stage[:, n % 2, A_W + h:A_W + h + 1]).then_inc(biased, 1)
                    if i >= TURN_LAG and (i - TURN_LAG) % 3:
                        evacuate(dve, i - TURN_LAG, lambda o, x: dve.tensor_copy(o, x), pt_dve)

            @block.tensor
            def _(pe):
                for i in range(len(units) + SUM_LAG):
                    if i < len(units):
                        p, t, h = units[i]
                        if i >= 3:
                            pe.wait_ge(biased, i - 2)
                        pe.matmul(sb[i % 3][:, 0:width(p, t)], columns(k.qT, p, t, h, False), columns(k.kT, p, t, h, True),
                                  start=True, stop=True).then_inc(scored, 1)
                    if TURN_LAG <= i < len(units) + TURN_LAG:
                        j = i - TURN_LAG
                        pe.wait_ge(exped, j + 1)
                        if j >= 3:
                            wait_turned_out(pe, j - 3)
                        for c in range(width(*units[j][:2]) // BLK):
                            last = pe.transpose(tb[j % 3][:, c * BLK:(c + 1) * BLK], pr[:, j % RING, c * BLK:(c + 1) * BLK],
                                                k.ident[:, :])
                        last.then_inc(turned, 1)
                    if i >= SUM_LAG:
                        j = i - SUM_LAG
                        p, t, h = units[j]
                        n = j // A_H
                        if t == 0 and h == 0:
                            pe.wait_ge(v_in[p], 16)
                        if h == 0 and n >= 2:
                            pe.wait_ge(rows_out, n - 1)
                        wait_turned_out(pe, j)
                        vs = values(p, t, h)
                        for c, x in enumerate(vs):
                            last = pe.matmul(ob[n % 2][:, h * DH:(h + 1) * DH], pT[:, j % RING, c * BLK:(c + 1) * BLK], x,
                                             start=(c == 0), stop=(c == len(vs) - 1))
                        last.then_inc(summed, 1)


def join_patterns(k):
    with k.stage() as st:
        R = 3
        rows = st.sbuf("pattern_rows", [P, R, 3, A_W])
        ends = st.sbuf("join_ends", [P, 3, TT, 2 * A_H])
        low = st.sbuf("join_low", [P, TT, A_H])
        e = st.sbuf("join_factors", [P, 3, TT, A_H])
        part = st.sbuf("join_parts", [P, 3, TT, A_H])
        y = st.sbuf("join_y", [P, R, A_W])
        tmp = st.sbuf("join_tmp", [P, R, 2, A_W])
        stat = st.sbuf("join_stat", [P, TT, 4])
        bank = [st.psum(f"jb{i}", [P, HALF]) for i in range(2)]
        rows_in = [[st.sem(f"rows_in{i}{p}") for p in range(3)] for i in range(R)]
        ends_in, diff, exped, factor, mixed, pooled, added, squared, var, root, scaled, turned, out, chain = (
            st.sem("j_" + n) for n in ("ends_in diff exped factor mixed pooled added squared var root scaled turned out "
                                       "chain").split())
        gain0 = VECS["a_gain"][0]

        def num(t, p):
            return rows[:, t % R, p, :].rearrange("p (h e) -> p h e", e=DH)

        with st.block() as block:

            @block.sync
            def _(sp):
                for p in range(3):
                    sp.dma_start(ends[:, p, :, :], k.attn_dram[p].rearrange("(t r) w -> r t w", r=P)[:, :, A_W:])\
                        .then_inc(ends_in, 16)
                for t in range(TT):
                    if t >= R:
                        sp.wait_ge(mixed, t - R + 1)
                        sp.wait_ge(pooled, 2 * (t - R + 1))
                    for p in range(3):
                        sp.dma_start(rows[:, t % R, p, :], k.attn_dram[p, t * P:(t + 1) * P, 0:A_W]).then_inc(rows_in[t % R][p], 16)

            @block.gpsimd
            def _(pool):
                pool.wait_ge(factor, 1)
                for t in range(TT):
                    if t >= R:
                        pool.wait_ge(squared, t - R + 1)
                    for p in (1, 2):
                        pool.wait_ge(rows_in[t % R][p], 16 * (t // R + 1))
                        pool.tensor_tensor(tmp[:, t % R, p - 1, :].rearrange("p (h e) -> p h e", e=DH), num(t, p),
                                           broadcast(e[:, p, t, :], 2, DH), ALU.mult).then_inc(pooled, 1)

            @block.scalar
            def _(act):
                act.wait_ge(diff, 1)
                act.activation(e[:, :, :, :], e[:, :, :, :], ACT.Exp).then_inc(exped, 1)
                for i in range(TT + 1):
                    if i < TT:
                        act.wait_ge(added, i + 1)
                        act.activation(tmp[:, i % R, 0, :], y[:, i % R, :], ACT.Square, accum_out=stat[:, i, 0:1])\
                            .then_inc(squared, 1)
                        act.wait_ge(var, i + 1)
                        act.activation(stat[:, i, 2:3], stat[:, i, 1:2], ACT.Sqrt).then_inc(root, 1)
                    if i >= 1:
                        t = i - 1
                        act.wait_ge(turned, t + 1)
                        for a in range(4):
                            last = act.activation(k.yT[:, 4 + a, t * P:(t + 1) * P], bank[t % 2][:, a * P:(a + 1) * P],
                                                  ACT.Copy, scale=k.vec[:, gain0 + a:gain0 + a + 1])
                        last.then_inc(out, 1)

            @block.vector
            def _(dve):
                count = [0]

                def step(ins):
                    count[0] += 1
                    ins.then_inc(chain, 1)
                    dve.wait_ge(chain, count[0])

                dve.wait_ge(ends_in, 48)
                step(dve.tensor_tensor(low[:, :, :], ends[:, 0, :, 0:A_H], ends[:, 1, :, 0:A_H], ALU.min))
                step(dve.tensor_tensor(low[:, :, :], low[:, :, :], ends[:, 2, :, 0:A_H], ALU.min))
                dve.tensor_tensor(e[:, :, :, :], broadcast(low[:, :, :], 1, 3), ends[:, :, :, 0:A_H], ALU.subtract)\
                    .then_inc(diff, 1)
                dve.wait_ge(exped, 1)
                step(dve.tensor_tensor(part[:, :, :, :], e[:, :, :, :], ends[:, :, :, A_H:], ALU.mult))
                step(dve.tensor_tensor(low[:, :, :], part[:, 0], part[:, 1], ALU.add))
                step(dve.tensor_tensor(low[:, :, :], low[:, :, :], part[:, 2], ALU.add))
                step(dve.reciprocal(low[:, :, :], low[:, :, :]))
                dve.tensor_tensor(e[:, :, :, :], e[:, :, :, :], broadcast(low[:, :, :], 1, 3), ALU.mult).then_inc(factor, 1)
                dve.wait_ge(factor, 1)

                def share(t):
                    dve.wait_ge(rows_in[t % R][0], 16 * (t // R + 1))
                    if t >= R:
                        dve.wait_ge(turned, t - R + 1)
                    dve.tensor_tensor(y[:, t % R, :].rearrange("p (h e) -> p h e", e=DH), num(t, 0),
                                      broadcast(e[:, 0, t, :], 2, DH), ALU.mult).then_inc(mixed, 1)

                def add(t):
                    yt = y[:, t % R, :]
                    dve.wait_ge(mixed, t + 1)
                    dve.wait_ge(pooled, 2 * t + 2)
                    step(dve.tensor_tensor(yt, yt, tmp[:, t % R, 0, :], ALU.add))
                    dve.tensor_tensor(yt, yt, tmp[:, t % R, 1, :], ALU.add).then_inc(added, 1)

                def scale(t):
                    dve.wait_ge(squared, t + 1)
                    dve.tensor_scalar(stat[:, t, 1:2], stat[:, t, 0:1], 1.0 / A_W, EPS, ALU.mult, ALU.add).then_inc(var, 1)
                    dve.wait_ge(root, t + 1)
                    step(dve.reciprocal(stat[:, t, 3:4], stat[:, t, 2:3]))
                    dve.tensor_scalar(y[:, t % R, :], y[:, t % R, :], stat[:, t, 3:4], None, ALU.mult).then_inc(scaled, 1)

                for t in range(TT + 1):
                    if t < TT:
                        share(t)
                        add(t)
                    if t >= 1:
                        scale(t - 1)

            @block.tensor
            def _(pe):
                for t in range(TT):
                    pe.wait_ge(scaled, t + 1)
                    if t >= 2:
                        pe.wait_ge(out, t - 1)
                    for a in range(4):
                        last = pe.transpose(bank[t % 2][:, a * P:(a + 1) * P], y[:, t % R, a * P:(a + 1) * P], k.ident[:, :])
                    last.then_inc(turned, 1)


def output_projection(k, name, src, chunks, load_x):
    with k.stage() as st:
        bank = [st.psum(f"{name}_p{i}", [P, HALF]) for i in range(4)]
        product, added = st.sem(name + "_product"), st.sem(name + "_added")
        x_in = [st.sem(f"{name}_x_in{t}") for t in range(TT)] if load_x else []
        tiles, weights = Split(st, name + "_tiles"), Split(st, name + "_weights")
        w = [st.sbuf(f"{name}_w{part}", [P, KT, HALF]) for part in ("high", "low")]
        tile = [st.sbuf(f"{name}_t{part}", [P, 2, KT, P]) for part in ("high", "low")]
        n_groups = 2 * TT
        with st.block() as block:

            @block.sync
            def _(sp):
                if load_x:
                    for t in range(TT):
                        sp.dma_start(k.x[:, t, :], k.w["x"][t * P:(t + 1) * P, :]).then_inc(x_in[t], 16)

            @block.vector
            def _(dve):
                def split_tile(g):
                    t = g % TT
                    if g >= 2:
                        dve.wait_ge(product, g - 1)
                    tiles.piece(dve, src[:, :, t * P:(t + 1) * P], [part[:, g % 2] for part in tile])

                def add(g):
                    h, t = g // TT, g % TT
                    if load_x:
                        dve.wait_ge(x_in[t], 16)
                    dve.wait_ge(product, g + 1)
                    part = k.x[:, t, h * HALF:(h + 1) * HALF]
                    dve.tensor_tensor(part, part, bank[g % 4][:, :], ALU.add).then_inc(added, 1)

                for g in range(n_groups):
                    h = g // TT
                    if g == 0:
                        split_tile(0)
                    if g % TT == 0:
                        dve.wait_ge(k.chunk_in[chunks[h]], 16)
                        if g:
                            dve.wait_ge(product, g)
                        for c in range(KT):
                            weights.piece(dve, k.chunk(chunks[h], HALF)[:, c, :], [part[:, c, :] for part in w])
                    if g + 1 < n_groups:
                        split_tile(g + 1)
                    if g:
                        add(g - 1)
                add(n_groups - 1)

            @block.tensor
            def _(pe):
                for g in range(n_groups):
                    h, t = g // TT, g % TT
                    if g >= 4:
                        pe.wait_ge(added, g - 3)
                    pe.wait_ge(tiles.done, g + 1)
                    for c in range(KT):
                        if t == 0:
                            pe.wait_ge(weights.done, KT * h + c + 1)
                        last = split_product(pe, bank[g % 4][:, :], [part[:, g % 2, c, :] for part in tile],
                                             [part[:, c, :] for part in w], c == 0, c == KT - 1)
                    last.then_inc(product, 1)


def memory_projections(k):
    MT = MEM // P
    with k.stage() as st:
        mem, gain, ring = k.xqT[:, 0:2, :], k.xqT[:, 2:4, :], k.xqT[:, 4:8, :]
        stat = st.sbuf("xa_stat", [P, TT, 4])
        mstat = st.sbuf("mem_stat", [P, MT, 4])
        memory = [st.sbuf(f"memory_{part}", [P, KT, MEM]) for part in ("high", "low")]
        tb = [st.psum(f"xa_turn{i}", [P, HALF]) for i in range(4)]
        gb = [st.psum(f"xa_gemm{i}", [P, HALF]) for i in range(4)]
        gain_in, mem_in = [st.sem(f"xa_gain_in{i}") for i in range(2)], st.sem("mem_in")
        product, out_act, out_dve = st.sem("xa_product"), st.sem("xa_out_act"), st.sem("xa_out_dve")

        def transposes(part):
            return lambda t, h: part[:, 4 * h:4 * h + 4, t * P:(t + 1) * P]

        mnorm = Norm(st, "mem", MT, lambda t: mem[:, t, :], gain[:, 1, :], transposes(memory[0]), tb, ring, mstat,
                     lambda eng, t: eng.wait_ge(mem_in, 16), low=transposes(memory[1]))
        xnorm = Norm(st, "xa", TT, lambda t: k.x[:, t, :], gain[:, 0, :], transposes(k.xn[0]), tb, ring, stat,
                     lambda eng, t: None, low=transposes(k.xn[1]))
        w = Pieces(k, st, "xa_w")
        for m in range(KT):
            part = w.add(7 + m // 2, 256, (m % 2) * P, (m % 2 + 1) * P)
            for h in range(2):
                half = slice(h * HALF, (h + 1) * HALF)
                w.group(columns(part, 0, P), columns(k.xn, half.start, half.stop), HALF, k.xqT[:, m, half], X_DH ** -0.5)
        for m in range(KT):
            part = w.add(11 + m // 2, 256, (m % 2) * P, (m % 2 + 1) * P)
            w.group(columns(part, 0, P), columns(memory, 0, MEM), MEM, k.xkT[:, m, :], 1.0)
        for h in range(4):
            part = w.add(15 + h, 256, 0, 256)
            for t in range(MT):
                w.group(columns(memory, t * P, (t + 1) * P), columns(part, 0, 256), 256,
                        k.xv[:, t, h * 256:(h + 1) * 256], 1.0)
        groups, firsts = w.groups, w.firsts()

        with st.block() as block:

            @block.sync
            def _(sp):
                sp.dma_start(gain[:, 0, :], k.w["norm_xattn"][0:1, :].partition_broadcast(P)).then_inc(gain_in[0], 16)
                sp.dma_start(gain[:, 1, :], k.w["norm_mem"][0:1, :].partition_broadcast(P)).then_inc(gain_in[1], 16)
                sp.dma_start(mem, k.w["mem"].rearrange("(t p) n -> p t n", p=P)).then_inc(mem_in, 16)
                for i in range(7, 19):
                    if i >= 10:
                        sp.wait_ge(w.split.done, w.chunk_end(i - 3))
                    load_chunk(k, sp, i)

            @block.scalar
            def _(act):
                xnorm.scalar(act)
                mnorm.scalar(act)
                for g in range(0, len(groups), 2):
                    act.wait_ge(product, g + 1)
                    act.activation(groups[g][3], gb[g % 4][:, 0:groups[g][2]], ACT.Copy, scale=groups[g][4]).then_inc(out_act, 1)

            @block.vector
            def _(dve):
                dve.wait_ge(gain_in[0], 16)
                xnorm.vector(dve)
                dve.wait_ge(gain_in[1], 16)
                mnorm.vector(dve)
                w.vector(dve, 0, product)
                for n in range(len(w.pieces)):
                    for g in range(firsts[n], firsts[n + 1]):
                        if n + 1 < len(w.pieces) and g == max(firsts[n], w.pieces[n + 1][3] - 1):
                            w.vector(dve, n + 1, product)
                        if g % 2:
                            dve.wait_ge(product, g + 1)
                            dve.tensor_scalar(groups[g][3], gb[g % 4][:, 0:groups[g][2]], groups[g][4], None, ALU.mult)\
                                .then_inc(out_dve, 1)

            @block.tensor
            def _(pe):
                xnorm.tensor(pe)
                xnorm.wait_all(pe)
                mnorm.tensor(pe)
                mnorm.wait_all(pe)
                for g, (lhs, rhs, cols, _, _) in enumerate(groups):
                    if g in firsts:
                        pe.wait_ge(w.split.done, firsts.index(g) + 1)
                    if g >= 4:
                        pe.wait_ge((out_act, out_dve)[g % 2], (g - 4) // 2 + 1)
                    for c in range(KT):
                        last = split_product(pe, gb[g % 4][:, 0:cols], lhs(c), rhs(c), c == 0, c == KT - 1)
                    last.then_inc(product, 1)


def memory_attention(k):
    with k.stage() as st:
        pr = st.sbuf("xa_probs", [P, RING, MEM])
        pT = st.sbuf("xa_probsT", [P, RING, MEM])
        small = st.sbuf("xa_small", [P, X_H * TT, 4])
        sb = [st.psum(f"xs{i}", [P, HALF]) for i in range(3)]
        tb = [st.psum(f"xt{i}", [P, HALF]) for i in range(2)]
        ob = [st.psum(f"xo{i}", [P, HALF]) for i in range(2)]
        scored, maxed, exped, inverse, normed, turned, pt, mixed, out = (st.sem("x_" + n) for n in (
            "scored maxed exped inverse normed turned pt mixed out").split())
        units = [(t, h) for t in range(TT) for h in range(X_H)]
        n_units = len(units)
        oT = k.mixedT
        zero_row = st.sbuf("y_zero", [P, D])
        cleared, y_zeroed = st.sem("zero_row_set"), st.sem("y_zeroed")

        with st.block() as block:

            @block.gpsimd
            def _(pool):
                pool.memset(zero_row[:, :], 0.0).then_inc(cleared, 1)

            @block.sync
            def _(sp):
                load_chunk(k, sp, 19)
                load_chunk(k, sp, 20)
                sp.wait_ge(cleared, 1)
                sp.dma_start(k.y_dram[EXPERTS * BLOCK:, :].rearrange("(n p) d -> p n d", p=P),
                             broadcast(zero_row[:, :], 1, EXTRA)).then_inc(y_zeroed, 16)
                sp.wait_ge(y_zeroed, 16)

            @block.scalar
            def _(act):
                for i in range(n_units + SUM_LAG + 1):
                    if i < n_units:
                        act.wait_ge(maxed, i + 1)
                        if i >= RING:
                            act.wait_ge(turned, i - RING + 1)
                        act.activation(pr[:, i % RING, :], sb[i % 3][:, 0:MEM], ACT.Exp, bias=small[:, i, 0:1],
                                       accum_out=small[:, i, 1:2]).then_inc(exped, 1)
                    if i >= SUM_LAG + 1:
                        j = i - SUM_LAG - 1
                        t, h = units[j]
                        act.wait_ge(mixed, j + 1)
                        act.activation(oT[:, 2 * h:2 * h + 2, t * P:(t + 1) * P],
                                       ob[j % 2][:, 0:2 * P].rearrange("p (a b) -> p a b", a=2), ACT.Copy).then_inc(out, 1)

            @block.vector
            def _(dve):
                for i in range(n_units + TURN_LAG):
                    if i < n_units:
                        dve.wait_ge(scored, i + 1)
                        dve.tensor_reduce(small[:, i, 0:1], sb[i % 3][:, 0:MEM], AX_X, ALU.max, negate=True).then_inc(maxed, 1)
                    if 1 <= i <= n_units:
                        j = i - 1
                        dve.wait_ge(exped, j + 1)
                        dve.reciprocal(small[:, j, 2:3], small[:, j, 1:2]).then_inc(inverse, 1)
                        dve.wait_ge(inverse, j + 1)
                        dve.tensor_scalar(pr[:, j % RING, :], pr[:, j % RING, :], small[:, j, 2:3], None, ALU.mult).then_inc(normed, 1)
                    if i >= TURN_LAG:
                        j = i - TURN_LAG
                        dve.wait_ge(turned, j + 1)
                        if j >= RING:
                            dve.wait_ge(mixed, j - RING + 1)
                        dve.tensor_copy(pT[:, j % RING, :], tb[j % 2][:, 0:MEM]).then_inc(pt, 1)

            @block.tensor
            def _(pe):
                for i in range(n_units + SUM_LAG):
                    if i < n_units:
                        t, h = units[i]
                        if i >= 3:
                            pe.wait_ge(exped, i - 2)
                        for c in range(2):
                            last = pe.matmul(sb[i % 3][:, 0:MEM], k.xqT[:, 2 * h + c, t * P:(t + 1) * P], k.xkT[:, 2 * h + c, :],
                                             start=(c == 0), stop=(c == 1))
                        last.then_inc(scored, 1)
                    if TURN_LAG <= i < n_units + TURN_LAG:
                        j = i - TURN_LAG
                        pe.wait_ge(normed, j + 1)
                        if j >= 2:
                            pe.wait_ge(pt, j - 1)
                        for c in range(2):
                            last = pe.transpose(tb[j % 2][:, c * P:(c + 1) * P], pr[:, j % RING, c * P:(c + 1) * P], k.ident[:, :])
                        last.then_inc(turned, 1)
                    if i >= SUM_LAG:
                        j = i - SUM_LAG
                        t, h = units[j]
                        pe.wait_ge(pt, j + 1)
                        if j >= 2:
                            pe.wait_ge(out, j - 1)
                        for e in range(2):
                            for c in range(2):
                                last = pe.matmul(ob[j % 2][:, e * P:(e + 1) * P],
                                                 k.xv[:, c, h * X_DH + e * P:h * X_DH + (e + 1) * P],
                                                 pT[:, j % RING, c * P:(c + 1) * P], start=(c == 0), stop=(c == 1))
                        last.then_inc(mixed, 1)


GROUPS = 4
GROUP_E = 8
EXPERTS = GROUPS * GROUP_E
TOP_K = 2
ROUTES = GROUPS + EXPERTS
BLOCK = 128
DE = 512
GU_K, DN_K = D // P, DE // P
EXTRA = S * TOP_K // BLOCK
BLOCKS = EXPERTS + EXTRA


def load_expert(k, queue, e, part):
    if part < 2:
        source = k.w["expert_w_gu"][bass.ds(e, 1), :, part * DE:(part + 1) * DE]
    else:
        source = k.w["expert_w_down"][bass.ds(e, 1)]
    queue.dma_start(k.raw[part], source.rearrange("a (k p) n -> p (a k) n", p=P)).then_inc(k.raw_in[part], 16)


class Count:

    def __init__(self):
        self.n = 0

    def up(self):
        self.n += 1
        return self.n


def router(k):
    with k.stage() as st:
        ring = st.sbuf("ffn_scaled", [P, 3, D])
        gain = st.sbuf("ffn_gain", [P, D])
        stat = st.sbuf("ffn_stat", [P, TT, 4])
        wr = st.sbuf("router_w", [P, KT, ROUTES])
        bias = st.sbuf("router_b", [P, ROUTES])
        const = st.sbuf("route_const", [P, 2 * P + TT])
        tri, counting, token = const[:, 0:P], const[:, P:2 * P], const[:, 2 * P:]
        numbers = counting[:, 0:EXPERTS]
        ones = st.sbuf("ones", [P, P])
        logit = st.sbuf("logit", [P, TT, ROUTES])
        gp = st.sbuf("group_p", [P, TT, GROUPS])
        g1 = st.sbuf("group_tmp", [P, TT, GROUPS])
        pick = st.sbuf("pick", [P, TT, GROUP_E, GROUPS])
        ep = st.sbuf("expert_p", [P, TT, GROUP_E])
        e1 = st.sbuf("expert_tmp", [P, TT, GROUP_E])
        s = st.sbuf("route_small", [P, 12, TT])
        hot = st.sbuf("hot", [P, TOP_K, TT, EXPERTS])
        both = st.sbuf("both", [P, TT, EXPERTS])
        before = st.sbuf("before", [P, TT, EXPERTS])
        total = st.sbuf("total", [P, EXPERTS])
        place = st.sbuf("place", [P, TT, EXPERTS])
        spread = st.sbuf("spread", [P, TT, EXPERTS])
        dest = st.sbuf("dest_f", [P, TOP_K, TT])
        more = st.sbuf("more", [P, EXPERTS, TT])
        tables = st.sbuf("tables", [P, 3, EXPERTS])
        extra, upto, jump = (tables[:, i, :] for i in range(3))
        zrow = st.sbuf("zero_row", [P, EXPERTS])
        past = st.sbuf("past", [1, EXTRA, EXPERTS])
        owner = st.sbuf("owner", [1, EXTRA])
        at = st.sbuf("block_and_row", [P, 2, TOP_K * TT])
        row_hot = st.sbuf("row_hot", [P, TOP_K * TT, BLOCK])
        block_hot = st.sbuf("block_hot", [P, TOP_K * TT, BLOCKS])
        tb = [st.psum(f"ffn_turn{i}", [P, HALF]) for i in range(4)]
        lb = st.psum("logits", [P, HALF])
        rb = st.psum("ranks", [P, HALF])
        cb = st.psum("counts", [P, HALF])
        ib = st.psum("index_bank", [P, HALF])
        gain_in, const_in = st.sem("ffn_gain_in"), st.sem("route_const_in")
        filled, product, ranked, exped, step, shifted, marked, placed, listed = (st.sem(n) for n in
            "filled r_product ranked exped route_step shifted marked placed listed".split())
        keep = [st.sem(f"xn_stored{i}") for i in range(2)]
        norm = Norm(st, "ffn", TT, lambda t: k.x[:, t, :], gain[:, :],
                    lambda t, h: k.yT[:, 4 * h:4 * h + 4, t * P:(t + 1) * P], tb, ring, stat, lambda eng, t: None, keep)
        gmax, gsum, gbest, gprob, emax, esum, pair_sum, unused = (s[:, i, :] for i in range(8))
        best = [s[:, 8, :], s[:, 9, :]]
        top = [s[:, 10, :], s[:, 11, :]]
        BIG = 64.0

        with st.block() as block:

            @block.sync
            def _(sp):
                sp.dma_start(gain[:, :], k.w["norm_ffn"][0:1, :].partition_broadcast(P)).then_inc(gain_in, 16)
                sp.dma_start(wr[:, :, :], k.w["router_w"].rearrange("(k p) n -> p k n", p=P)).then_inc(const_in, 16)
                sp.dma_start(bias[:, :], k.w["router_b"][0:1, :].partition_broadcast(P)).then_inc(const_in, 16)
                sp.dma_start(const[:, :], k.w["route_const"]).then_inc(const_in, 16)
                for t in range(TT):
                    sp.wait_ge(norm.scaled, t + 1)
                    sp.dma_start(k.xn_dram[t * P:(t + 1) * P, :], ring[:, t % 2, :]).then_inc(keep[t % 2], 16)
                for part in range(2):
                    load_expert(k, sp, 0, part)
                for i in range(2):
                    sp.wait_ge(keep[i], 16 * (TT // 2))

            @block.gpsimd
            def _(pool):
                pool.memset(ones[:, :], 1.0).then_inc(filled, 1)
                pool.memset(zrow[:, :], 0.0).then_inc(filled, 1)

            @block.scalar
            def _(act):
                norm.scalar(act)
                act.wait_ge(shifted, 1)
                act.activation(gp[:, :, :], gp[:, :, :], ACT.Exp).then_inc(exped, 1)
                act.wait_ge(shifted, 2)
                act.activation(ep[:, :, :], ep[:, :, :], ACT.Exp).then_inc(exped, 1)

            @block.tensor
            def _(pe):
                def logits(t):
                    if t == 0:
                        pe.wait_ge(const_in, 48)
                    pe.wait_ge(norm.evac_act, t + 1)
                    pe.wait_ge(norm.evac_dve, t + 1)
                    for c in range(KT):
                        last = pe.matmul(lb[:, t * ROUTES:(t + 1) * ROUTES], k.yT[:, c, t * P:(t + 1) * P], wr[:, c, :],
                                         start=(c == 0), stop=(c == KT - 1))
                    last.then_inc(product, 1)

                norm.tensor(pe, behind=logits)
                pe.wait_ge(filled, 1)
                pe.wait_ge(marked, 1)
                cols = TT * EXPERTS
                flat = [v[:, :, :].rearrange("p t e -> p (t e)") for v in (both, before)]
                pe.matmul(rb[:, 0:cols], tri, flat[0], start=True, stop=False)
                pe.matmul(rb[:, 0:cols], ones[:, :], flat[1], start=False, stop=True).then_inc(ranked, 1)
                pe.matmul(cb[:, 0:EXPERTS], ones[:, :], total[:, :], start=True, stop=True).then_inc(ranked, 1)
                pe.wait_ge(placed, 1)
                for i in range(TOP_K * TT):
                    last = pe.matmul(ib[:, 0:BLOCKS], row_hot[:, i, :], block_hot[:, i, :],
                                     start=(i == 0), stop=(i == TOP_K * TT - 1))
                last.then_inc(listed, 1)

            @block.vector
            def _(dve):
                n = Count()

                def first_index(p, top_p, width, tmp, out):
                    dve.tensor_tensor(tmp, p, broadcast(top_p, 2, width), ALU.is_equal).then_inc(step, 1)
                    dve.wait_ge(step, n.up())
                    dve.scalar_tensor_tensor(out=tmp, in0=tmp, scalar=-BIG, in1=broadcast(numbers[:, 0:width], 1, TT),
                                             op0=ALU.mult, op1=ALU.add).then_inc(step, 1)
                    dve.wait_ge(step, n.up())
                    dve.tensor_reduce(out, tmp, AX_X, ALU.min).then_inc(step, 1)
                    dve.wait_ge(step, n.up())
                    dve.tensor_scalar(out, out, BIG, None, ALU.add).then_inc(step, 1)
                    dve.wait_ge(step, n.up())

                dve.wait_ge(gain_in, 16)
                norm.vector(dve)
                dve.wait_ge(const_in, 48)
                dve.wait_ge(product, TT)
                dve.tensor_tensor(logit[:, :, :], lb[:, 0:TT * ROUTES].rearrange("p (t n) -> p t n", n=ROUTES),
                                  broadcast(bias[:, :], 1, TT), ALU.add).then_inc(step, 1)
                dve.wait_ge(step, n.up())
                dve.tensor_reduce(gmax, logit[:, :, 0:GROUPS], AX_X, ALU.max).then_inc(step, 1)
                dve.wait_ge(step, n.up())
                dve.tensor_tensor(gp[:, :, :], logit[:, :, 0:GROUPS], broadcast(gmax, 2, GROUPS), ALU.subtract)\
                    .then_inc(shifted, 1)
                dve.wait_ge(exped, 1)
                dve.tensor_reduce(gsum, gp[:, :, :], AX_X, ALU.add).then_inc(step, 1)
                dve.wait_ge(step, n.up())
                dve.reciprocal(gsum, gsum).then_inc(step, 1)
                dve.wait_ge(step, n.up())
                dve.tensor_tensor(gp[:, :, :], gp[:, :, :], broadcast(gsum, 2, GROUPS), ALU.mult).then_inc(step, 1)
                dve.wait_ge(step, n.up())
                dve.tensor_reduce(gprob, gp[:, :, :], AX_X, ALU.max).then_inc(step, 1)
                dve.wait_ge(step, n.up())
                first_index(gp[:, :, :], gprob, GROUPS, g1[:, :, :], gbest)
                dve.tensor_tensor(g1[:, :, :], broadcast(numbers[:, 0:GROUPS], 1, TT), broadcast(gbest, 2, GROUPS),
                                  ALU.is_equal).then_inc(step, 1)
                dve.wait_ge(step, n.up())
                dve.tensor_tensor(pick[:, :, :, :], logit[:, :, GROUPS:].rearrange("p t (g j) -> p t j g", g=GROUPS),
                                  broadcast(g1[:, :, :], 2, GROUP_E), ALU.mult).then_inc(step, 1)
                dve.wait_ge(step, n.up())
                dve.tensor_reduce(ep[:, :, :], pick[:, :, :, :], AX_X, ALU.add).then_inc(step, 1)
                dve.wait_ge(step, n.up())
                dve.tensor_reduce(emax, ep[:, :, :], AX_X, ALU.max).then_inc(step, 1)
                dve.wait_ge(step, n.up())
                dve.tensor_tensor(ep[:, :, :], ep[:, :, :], broadcast(emax, 2, GROUP_E), ALU.subtract).then_inc(shifted, 1)
                dve.wait_ge(exped, 2)
                dve.tensor_reduce(esum, ep[:, :, :], AX_X, ALU.add).then_inc(step, 1)
                dve.wait_ge(step, n.up())
                dve.reciprocal(esum, esum).then_inc(step, 1)
                dve.wait_ge(step, n.up())
                dve.tensor_tensor(ep[:, :, :], ep[:, :, :], broadcast(esum, 2, GROUP_E), ALU.mult).then_inc(step, 1)
                dve.wait_ge(step, n.up())
                for j in range(TOP_K):
                    dve.tensor_reduce(top[j], ep[:, :, :], AX_X, ALU.max).then_inc(step, 1)
                    dve.wait_ge(step, n.up())
                    first_index(ep[:, :, :], top[j], GROUP_E, e1[:, :, :], best[j])
                    if j == 0:
                        dve.tensor_tensor(e1[:, :, :], broadcast(numbers[:, 0:GROUP_E], 1, TT),
                                          broadcast(best[0], 2, GROUP_E), ALU.is_equal).then_inc(step, 1)
                        dve.wait_ge(step, n.up())
                        dve.scalar_tensor_tensor(out=ep[:, :, :], in0=e1[:, :, :], scalar=-2.0, in1=ep[:, :, :],
                                                 op0=ALU.mult, op1=ALU.add).then_inc(step, 1)
                        dve.wait_ge(step, n.up())
                for j in range(TOP_K):
                    dve.scalar_tensor_tensor(out=best[j], in0=gbest, scalar=float(GROUP_E), in1=best[j],
                                             op0=ALU.mult, op1=ALU.add).then_inc(step, 1)
                    dve.wait_ge(step, n.up())
                    dve.tensor_tensor(hot[:, j, :, :], broadcast(numbers, 1, TT), broadcast(best[j], 2, EXPERTS),
                                      ALU.is_equal).then_inc(step, 1)
                    dve.wait_ge(step, n.up())
                dve.tensor_tensor(both[:, :, :], hot[:, 0, :, :], hot[:, 1, :, :], ALU.add).then_inc(step, 1)
                dve.wait_ge(step, n.up())
                dve.tensor_scalar(before[:, 0, :], both[:, 0, :], 0.0, None, ALU.mult).then_inc(step, 1)
                dve.wait_ge(step, n.up())
                for t in range(1, TT):
                    dve.tensor_tensor(before[:, t, :], before[:, t - 1, :], both[:, t - 1, :], ALU.add).then_inc(step, 1)
                    dve.wait_ge(step, n.up())
                dve.tensor_tensor(total[:, :], before[:, TT - 1, :], both[:, TT - 1, :], ALU.add).then_inc(marked, 1)
                dve.tensor_tensor(pair_sum, top[0], top[1], ALU.add).then_inc(step, 1)
                dve.wait_ge(step, n.up())
                dve.reciprocal(pair_sum, pair_sum).then_inc(step, 1)
                dve.wait_ge(step, n.up())
                for j in range(TOP_K):
                    dve.tensor_tensor(top[j], top[j], gprob, ALU.mult).then_inc(step, 1)
                    dve.wait_ge(step, n.up())
                    dve.tensor_tensor(k.gate[:, j * TT:(j + 1) * TT], top[j], pair_sum, ALU.mult).then_inc(step, 1)
                    dve.wait_ge(step, n.up())
                dve.wait_ge(ranked, 2)
                dve.wait_ge(filled, 2)
                for j in range(1, TT):
                    dve.tensor_scalar(more[:, :, j - 1], cb[:, 0:EXPERTS], float(BLOCK * j), None, ALU.is_gt).then_inc(step, 1)
                    n.up()
                dve.wait_ge(step, n.n)
                dve.tensor_reduce(extra, more[:, :, 0:TT - 1], AX_X, ALU.add).then_inc(step, 1)
                dve.wait_ge(step, n.up())
                dve.tensor_tensor_scan(upto, extra, zrow[:, :], 0.0, ALU.add, ALU.add).then_inc(step, 1)
                dve.wait_ge(step, n.up())
                dve.tensor_tensor(jump, upto, extra, ALU.subtract).then_inc(step, 1)
                dve.wait_ge(step, n.up())
                dve.scalar_tensor_tensor(out=jump, in0=jump, scalar=float(EXPERTS - 1), in1=numbers, op0=ALU.add,
                                         op1=ALU.subtract).then_inc(step, 1)
                dve.wait_ge(step, n.up())
                ranks = rb[:, 0:TT * EXPERTS].rearrange("p (t e) -> p t e", e=EXPERTS)
                dve.tensor_scalar(place[:, :, :], ranks, float(BLOCK), None, ALU.is_ge).then_inc(step, 1)
                dve.wait_ge(step, n.up())
                dve.tensor_tensor(place[:, :, :], place[:, :, :], broadcast(jump, 1, TT), ALU.mult).then_inc(step, 1)
                dve.wait_ge(step, n.up())
                dve.tensor_tensor(place[:, :, :], place[:, :, :], broadcast(numbers, 1, TT), ALU.add).then_inc(step, 1)
                dve.wait_ge(step, n.up())
                dve.scalar_tensor_tensor(out=place[:, :, :], in0=place[:, :, :], scalar=float(BLOCK), in1=ranks,
                                         op0=ALU.mult, op1=ALU.add).then_inc(step, 1)
                dve.wait_ge(step, n.up())
                for j in range(TOP_K):
                    dve.tensor_tensor(spread[:, :, :], hot[:, j, :, :], place[:, :, :], ALU.mult).then_inc(step, 1)
                    dve.wait_ge(step, n.up())
                    dve.tensor_reduce(dest[:, j, :], spread[:, :, :], AX_X, ALU.add).then_inc(step, 1)
                    dve.wait_ge(step, n.up())
                places = dest[:, :, :].rearrange("p j t -> p (j t)")
                block_of, row_of = at[:, 0, :], at[:, 1, :]
                dve.tensor_copy(k.dest[:, :], places).then_inc(step, 1)
                n.up()
                dve.tensor_scalar(row_of, places, 1.0 / BLOCK, None, ALU.mult).then_inc(step, 1)
                dve.wait_ge(step, n.up())
                dve.tensor_tensor(block_hot[:, :, 1:], broadcast(row_of, 2, BLOCKS - 1),
                                  broadcast(counting[:, 1:BLOCKS], 1, TOP_K * TT), ALU.is_ge).then_inc(step, 1)
                dve.wait_ge(step, n.up())
                dve.tensor_reduce(block_of, block_hot[:, :, 1:], AX_X, ALU.add).then_inc(step, 1)
                dve.wait_ge(step, n.up())
                dve.scalar_tensor_tensor(out=row_of, in0=block_of, scalar=-float(BLOCK), in1=places,
                                         op0=ALU.mult, op1=ALU.add).then_inc(step, 1)
                dve.tensor_tensor(block_hot[:, :, :], broadcast(block_of, 2, BLOCKS),
                                  broadcast(counting[:, 0:BLOCKS], 1, TOP_K * TT), ALU.is_equal).then_inc(step, 1)
                n.up()
                dve.wait_ge(step, n.up())
                for j in range(TOP_K):
                    part = block_hot[:, j * TT:(j + 1) * TT, :]
                    dve.tensor_tensor(part, part, broadcast(token, 2, BLOCKS), ALU.mult).then_inc(step, 1)
                    n.up()
                dve.wait_ge(step, n.n)
                dve.tensor_tensor(row_hot[:, :, :], broadcast(row_of, 2, BLOCK), broadcast(counting, 1, TOP_K * TT),
                                  ALU.is_equal).then_inc(placed, 1)
                dve.tensor_tensor(past[:, :, :], broadcast(upto[0:1, :], 1, EXTRA), broadcast(numbers[0:1, 0:EXTRA], 2, EXPERTS),
                                  ALU.is_le).then_inc(step, 1)
                dve.wait_ge(step, n.up())
                dve.tensor_reduce(owner[:, :], past[:, :, :], AX_X, ALU.add).then_inc(step, 1)
                dve.wait_ge(step, n.up())
                dve.wait_ge(listed, 1)
                dve.tensor_copy(k.indices[:, :], ib[:, 0:BLOCKS]).then_inc(step, 1)
                dve.tensor_copy(k.plan[:, 0:EXTRA], owner[:, :]).then_inc(step, 1)
                dve.tensor_copy(k.plan[:, EXTRA:EXTRA + 1], upto[0:1, EXPERTS - 1:EXPERTS]).then_inc(step, 1)


def since(e, n):
    return not isinstance(e, int) or e >= n


def until(e, n):
    return not isinstance(e, int) or e < n


def experts(k):
    with k.stage() as st:
        flat = k.yT[:, :, :].rearrange("p a b -> p (a b)")
        rows, y, gated = flat[:, 0:D], flat[:, D:2 * D], flat[:, 2 * D:2 * D + DE]
        x = [st.sbuf(f"block_{part}", [P, GU_K, BLOCK]) for part in ("high", "low")]
        hT = [st.sbuf(f"hidden_{part}", [P, DN_K, BLOCK]) for part in ("high", "low")]
        index = st.sbuf("block_index", [P, 1], U32)
        gate_bank, up_bank, hidden_bank = (st.psum(n, [P, HALF]) for n in ("gate_bank", "up_bank", "hidden_bank"))
        xb = [st.psum(f"turn_bank{i}", [P, HALF]) for i in range(2)]
        yb = [st.psum(f"down_bank{i}", [P, HALF]) for i in range(2)]
        high = [st.sem(f"w_high{part}") for part in range(3)]
        low = [st.sem(f"w_low{part}") for part in range(3)]
        (index_set, issued, gathered, turned, x_high, x_low, gate_done, up_done, silued, h_done, h_turned,
         h_high, h_low, y_made, y_act, y_dve, y_stored) = (st.sem("e_" + n) for n in (
             "index_set issued gathered turned x_high x_low gate_done up_done silued h_done h_turned "
             "h_high h_low y_made y_act y_dve y_stored").split())
        LOOP = (3, EXPERTS - 2)

        def half_of(tile, half):
            n = tile.shape[1] // 2
            return tile[:, half * n:(half + 1) * n, :]

        def all_cycles(eng, cycle, end):
            for e in range(LOOP[0]):
                cycle(e)
            with eng.Fori(*LOOP) as e:
                cycle(e)
            for e in range(LOOP[1], end):
                cycle(e)

        with st.block() as block:

            @block.sync
            def _(sp):
                for part in range(2):
                    sp.wait_ge(low[part], 2)
                    load_expert(k, sp, 1, part)

                def cycle(e):
                    if since(e, 2):
                        sp.wait_ge(y_act, e - 1)
                        sp.wait_ge(y_dve, e - 1)
                        sp.dma_start(k.y_dram[bass.ds((e - 2) * BLOCK, BLOCK), :], y).then_inc(y_stored, 16)
                    if until(e, EXPERTS):
                        if since(e, 1):
                            sp.wait_ge(low[2], 2 * e)
                        load_expert(k, sp, e, 2)
                    if until(e, EXPERTS - 2):
                        for part in range(2):
                            sp.wait_ge(low[part], 2 * e + 4)
                            load_expert(k, sp, e + 2, part)

                all_cycles(sp, cycle, EXPERTS + 2)
                sp.wait_ge(y_stored, 16 * EXPERTS)

            @block.gpsimd
            def _(pool):
                def cycle(e):
                    if since(e, 1):
                        pool.wait_ge(turned, 2 * e)
                    pool.tensor_copy(index[:, :], k.indices[:, bass.ds(e, 1)]).then_inc(index_set, 1)
                    pool.wait_ge(index_set, e + 1)
                    pool.sem_inc(issued, 1)
                    pool.indirect_dma_start(rows, None, k.xn_dram, bass.IndirectOffsetOnAxis(index[:, :], 0))\
                        .then_inc(gathered, 16)

                all_cycles(pool, cycle, EXPERTS)

            @block.scalar
            def _(act):
                def weights_high(e, part):
                    act.wait_ge(k.raw_in[part], 16 * e + 16)
                    for half in range(2):
                        act.activation(half_of(k.parts[part][0], half).bitcast(F32R), half_of(k.raw[part], half), ACT.Copy)\
                            .then_inc(high[part], 1)

                def tokens_high(e):
                    for half in range(2):
                        act.wait_ge(turned, 2 * e + half + 1)
                        act.activation(half_of(x[0], half).bitcast(F32R),
                                       xb[half][:, :].rearrange("p (c n) -> p c n", c=4), ACT.Copy).then_inc(x_high, 1)

                def cycle(e):
                    if since(e, 2):
                        act.wait_ge(y_made, 2 * e - 3)
                        if since(e, 3):
                            act.wait_ge(y_stored, 16 * e - 32)
                        act.activation(y[:, 0:HALF], yb[0][:, :], ACT.Copy).then_inc(y_act, 1)
                    if since(e, 1) and until(e, EXPERTS + 1):
                        if since(e, 2):
                            act.wait_ge(y_made, 2 * e - 2)
                        weights_high(e - 1, 2)
                        act.wait_ge(h_turned, e)
                        act.activation(hT[0][:, :, :].bitcast(F32R), hidden_bank[:, :].rearrange("p (c n) -> p c n", c=DN_K),
                                       ACT.Copy).then_inc(h_high, 1)
                    if until(e, EXPERTS):
                        act.wait_ge(gate_done, e + 1)
                        act.activation(gated, gate_bank[:, :], ACT.Silu).then_inc(silued, 1)
                    if until(e, EXPERTS - 1):
                        weights_high(e + 1, 0)
                        tokens_high(e + 1)
                        act.wait_ge(up_done, e + 1)
                        weights_high(e + 1, 1)

                weights_high(0, 0)
                tokens_high(0)
                weights_high(0, 1)
                all_cycles(act, cycle, EXPERTS + 2)

            @block.vector
            def _(dve):
                def weights_low(e, part):
                    for half in range(2):
                        dve.wait_ge(high[part], 2 * e + half + 1)
                        dve.tensor_tensor(half_of(k.parts[part][1], half).bitcast(F32R), half_of(k.raw[part], half),
                                          half_of(k.parts[part][0], half), ALU.subtract).then_inc(low[part], 1)

                def tokens_low(e):
                    for half in range(2):
                        dve.wait_ge(x_high, 2 * e + half + 1)
                        dve.tensor_tensor(half_of(x[1], half).bitcast(F32R),
                                          xb[half][:, :].rearrange("p (c n) -> p c n", c=4),
                                          half_of(x[0], half), ALU.subtract).then_inc(x_low, 1)

                def cycle(e):
                    if since(e, 2):
                        dve.wait_ge(y_made, 2 * e - 2)
                        if since(e, 3):
                            dve.wait_ge(y_stored, 16 * e - 32)
                        dve.tensor_copy(y[:, HALF:], yb[1][:, :]).then_inc(y_dve, 1)
                    if since(e, 1) and until(e, EXPERTS + 1):
                        weights_low(e - 1, 2)
                        dve.wait_ge(h_high, e)
                        dve.tensor_tensor(hT[1][:, :, :].bitcast(F32R), hidden_bank[:, :].rearrange("p (c n) -> p c n", c=DN_K),
                                          hT[0][:, :, :], ALU.subtract).then_inc(h_low, 1)
                    if until(e, EXPERTS - 1):
                        weights_low(e + 1, 0)
                    if until(e, EXPERTS):
                        dve.wait_ge(silued, e + 1)
                        dve.wait_ge(up_done, e + 1)
                        dve.tensor_tensor(gated, gated, up_bank[:, :], ALU.mult).then_inc(h_done, 1)
                    if until(e, EXPERTS - 1):
                        tokens_low(e + 1)
                        weights_low(e + 1, 1)

                weights_low(0, 0)
                tokens_low(0)
                weights_low(0, 1)
                all_cycles(dve, cycle, EXPERTS + 2)

            @block.tensor
            def _(pe):
                def products(bank, e, part):
                    for c in range(GU_K):
                        if c % (GU_K // 2) == 0:
                            pe.wait_ge(low[part], 2 * e + 1 + c // (GU_K // 2))
                        last = split_product(pe, bank[:, :], [t[:, c, :] for t in x], [t[:, c, :] for t in k.parts[part]],
                                             c == 0, c == GU_K - 1)
                    return last

                def turn_tokens(e):
                    pe.wait_ge(gathered, 16 * e + 16)
                    for half in range(2):
                        turn_block(pe, k, rows, xb[half], half).then_inc(turned, 1)

                def cycle(e):
                    if until(e, EXPERTS):
                        pe.wait_ge(x_low, 2 * e + 2)
                        if since(e, 1):
                            pe.wait_ge(silued, e)
                        products(gate_bank, e, 0).then_inc(gate_done, 1)
                    if since(e, 1):
                        pe.wait_ge(h_done, e)
                        for c in range(DN_K):
                            last = pe.transpose(hidden_bank[:, c * P:(c + 1) * P], gated[:, c * P:(c + 1) * P], k.ident[:, :])
                        last.then_inc(h_turned, 1)
                    if until(e, EXPERTS):
                        products(up_bank, e, 1).then_inc(up_done, 1)
                    if until(e, EXPERTS - 1):
                        turn_tokens(e + 1)
                    if since(e, 1):
                        pe.wait_ge(low[2], 2 * e)
                        pe.wait_ge(h_low, e)
                        for half in range(2):
                            if since(e, 2):
                                pe.wait_ge((y_act, y_dve)[half], e - 1)
                            for c in range(DN_K):
                                last = split_product(pe, yb[half][:, :], [t[:, c, :] for t in hT],
                                                     [t[:, c, half * HALF:(half + 1) * HALF] for t in k.parts[2]],
                                                     c == 0, c == DN_K - 1)
                            last.then_inc(y_made, 1)

                turn_tokens(0)
                all_cycles(pe, cycle, EXPERTS + 1)

    extra_blocks(k)


def expert_products(pe, k, gate_bank, up_bank, half):
    for bank, weights in ((gate_bank, k.raw[0]), (up_bank, k.raw[1])):
        for m in range(2):
            col = (2 * half + m) * P
            for c in range(GU_K):
                last = pe.matmul(bank[:, m * BLOCK:(m + 1) * BLOCK], weights[:, c, col:col + P], k.xT[:, c, :],
                                 start=(c == 0), stop=(c == GU_K - 1))
    return last


def down_products(pe, k, bank, half):
    for c in range(DN_K):
        last = pe.matmul(bank[:, :], k.hT[:, c, :], k.raw[2][:, c, half * HALF:(half + 1) * HALF],
                         start=(c == 0), stop=(c == DN_K - 1))
    return last


def turn_block(pe, k, rows, bank, half):
    for a in range(4):
        c = 4 * half + a
        last = pe.transpose(bank[:, a * P:(a + 1) * P], rows[:, c * P:(c + 1) * P], k.ident[:, :])
    return last


def extra_blocks(k):
    with k.stage() as st:
        flat = k.yT[:, :, :].rearrange("p a b -> p (a b)")
        rows, y = flat[:, 0:D], flat[:, D:2 * D]
        k.xT = flat[:, 2 * D:3 * D].rearrange("p (c n) -> p c n", c=GU_K)
        k.hT = flat[:, 3 * D:3 * D + DE].rearrange("p (c n) -> p c n", c=DN_K)
        act_gate = flat[:, 3 * D + DE:4 * D].rearrange("p (c n) -> p c n", c=DN_K)
        index = st.sbuf("extra_index", [P, 1], U32)
        ab = [st.psum(f"extra_gate{i}", [P, HALF]) for i in range(2)]
        bb = [st.psum(f"extra_up{i}", [P, HALF]) for i in range(2)]
        tb = [st.psum(f"extra_turn{i}", [P, HALF]) for i in range(2)]
        yb = [st.psum(f"extra_down{i}", [P, HALF]) for i in range(2)]
        issued, finished = st.sem("extra_issued"), st.sem("extra_finished")
        (index_set, gathered, turned, x_act, x_dve, hidden, silued, h_done, y_made, y_act, y_dve, stored) = (
            st.sem("extra_" + n) for n in ("index_set gathered turned x_act x_dve hidden silued h_done y_made y_act "
                                       "y_dve stored").split())

        def half_view(tile, half):
            return tile[:, 2 * half:2 * half + 2, :].rearrange("p a b -> p (a b)")

        def listed(eng, body):
            n = eng.value_load(k.plan[0:1, EXTRA:EXTRA + 1], min_val=0, max_val=EXTRA)
            with eng.If(n > 0):
                with eng.Fori(0, n) as b:
                    body(b)

        with st.block() as block:

            @block.sync
            def _(sp):
                def body(b):
                    e = sp.value_load(k.plan[0:1, bass.ds(b, 1)], min_val=0, max_val=EXPERTS - 1)
                    for part in range(3):
                        load_expert(k, sp, e, part)
                    done, all_stored = sp.snap(b + 1), sp.snap(16 * b + 16)
                    sp.wait_ge(y_act, done)
                    sp.wait_ge(y_dve, done)
                    sp.dma_start(k.y_dram[bass.ds(EXPERTS * BLOCK + b * BLOCK, BLOCK), :], y).then_inc(stored, 16)
                    sp.wait_ge(stored, all_stored)
                    sp.sem_inc(finished, 1)

                listed(sp, body)

            @block.gpsimd
            def _(pool):
                def body(b):
                    pool.tensor_copy(index[:, :], k.indices[:, bass.ds(b + EXPERTS, 1)]).then_inc(index_set, 1)
                    pool.wait_ge(index_set, b + 1)
                    pool.sem_inc(issued, 1)
                    pool.indirect_dma_start(rows, None, k.xn_dram,
                                            bass.IndirectOffsetOnAxis(index[:, :], 0)).then_inc(gathered, 16)
                    pool.wait_ge(turned, 2 * b + 2)
                    pool.sem_inc(issued, 1)

                listed(pool, body)

            @block.scalar
            def _(act):
                def body(b):
                    act.wait_ge(turned, 2 * b + 1)
                    act.activation(k.xT[:, 0:4, :].rearrange("p a b -> p (a b)"), tb[0][:, :], ACT.Copy).then_inc(x_act, 1)
                    for half in range(2):
                        act.wait_ge(hidden, 2 * b + half + 1)
                        act.activation(half_view(act_gate, half), ab[half][:, 0:2 * BLOCK], ACT.Silu).then_inc(silued, 1)
                    act.wait_ge(y_made, 2 * b + 1)
                    act.activation(y[:, 0:HALF], yb[0][:, :], ACT.Copy).then_inc(y_act, 1)

                listed(act, body)

            @block.vector
            def _(dve):
                def body(b):
                    dve.wait_ge(turned, 2 * b + 2)
                    dve.tensor_copy(k.xT[:, 4:8, :].rearrange("p a b -> p (a b)"), tb[1][:, :]).then_inc(x_dve, 1)
                    for half in range(2):
                        dve.wait_ge(silued, 2 * b + half + 1)
                        dve.tensor_tensor(half_view(k.hT, half), half_view(act_gate, half), bb[half][:, 0:2 * BLOCK],
                                          ALU.mult).then_inc(h_done, 1)
                    dve.wait_ge(y_made, 2 * b + 2)
                    dve.tensor_copy(y[:, HALF:], yb[1][:, :]).then_inc(y_dve, 1)

                listed(dve, body)

            @block.tensor
            def _(pe):
                def body(b):
                    pe.wait_ge(gathered, 16 * (b + 1))
                    for half in range(2):
                        turn_block(pe, k, rows, tb[half], half).then_inc(turned, 1)
                    for part in range(3):
                        pe.wait_ge(k.raw_in[part], 16 * b + 16 * (EXPERTS + 1))
                    pe.wait_ge(x_act, b + 1)
                    pe.wait_ge(x_dve, b + 1)
                    for half in range(2):
                        expert_products(pe, k, ab[half], bb[half], half).then_inc(hidden, 1)
                    pe.wait_ge(h_done, 2 * b + 2)
                    for half in range(2):
                        down_products(pe, k, yb[half], half).then_inc(y_made, 1)

                listed(pe, body)


def combine(k):
    with k.stage() as st:
        flat = k.yT[:, :, :].rearrange("p a b -> p (a b)")
        SLOTS_Y = 4
        space = [part[:, :, :].rearrange("p k n -> p (k n)") for part in k.raw[0:2]]
        rows = [[space[j][:, i * D:(i + 1) * D] for j in range(TOP_K)] for i in range(SLOTS_Y)]
        result = [flat[:, i * D:(i + 1) * D] for i in range(2)]
        gain = flat[:, 2 * D:3 * D]
        square = flat[:, 3 * D:4 * D]
        stat = st.sbuf("final_stat", [P, TT, 4])
        gain_in = st.sem("final_gain_in")
        gathered = [[st.sem(f"y_in{i}_{j}") for j in range(TOP_K)] for i in range(SLOTS_Y)]
        stored = [st.sem(f"out_stored{i}") for i in range(2)]
        added, squared, variance, root, inverse, ready = (
            st.sem("c_" + n) for n in "added squared variance root inverse ready".split())

        with st.block() as block:

            @block.gpsimd
            def _(pool):
                for t in range(TT):
                    if t >= SLOTS_Y:
                        pool.wait_ge(added, 2 * (t - SLOTS_Y) + 2)
                    for j in range(TOP_K):
                        i = j * TT + t
                        pool.indirect_dma_start(rows[t % SLOTS_Y][j], None, k.y_dram,
                                                bass.IndirectOffsetOnAxis(k.dest[:, i:i + 1], 0)).then_inc(
                            gathered[t % SLOTS_Y][j], 16)

            @block.vector
            def _(dve):
                dve.wait_ge(gain_in, 16)
                for t in range(TT + 2):
                    if t < TT:
                        for j in range(TOP_K):
                            dve.wait_ge(gathered[t % SLOTS_Y][j], 16 * (t // SLOTS_Y + 1))
                            if j:
                                dve.wait_ge(added, 2 * t + 1)
                            dve.scalar_tensor_tensor(out=k.x[:, t, :], in0=rows[t % SLOTS_Y][j],
                                                     scalar=k.gate[:, j * TT + t:j * TT + t + 1], in1=k.x[:, t, :],
                                                     op0=ALU.mult, op1=ALU.add).then_inc(added, 1)
                    if 1 <= t <= TT:
                        u = t - 1
                        dve.wait_ge(squared, u + 1)
                        dve.tensor_scalar(stat[:, u, 1:2], stat[:, u, 0:1], 1.0 / D, EPS, ALU.mult,
                                          ALU.add).then_inc(variance, 1)
                    if t >= 2:
                        u = t - 2
                        dve.wait_ge(root, u + 1)
                        dve.reciprocal(stat[:, u, 3:4], stat[:, u, 2:3]).then_inc(inverse, 1)
                        dve.wait_ge(inverse, u + 1)
                        if u >= 2:
                            dve.wait_ge(stored[u % 2], 16 * (u // 2))
                        dve.scalar_tensor_tensor(out=result[u % 2], in0=k.x[:, u, :], scalar=stat[:, u, 3:4], in1=gain,
                                                 op0=ALU.mult, op1=ALU.mult).then_inc(ready, 1)

            @block.scalar
            def _(act):
                for t in range(TT + 1):
                    if t < TT:
                        act.wait_ge(added, 2 * t + 2)
                        if t:
                            act.wait_ge(squared, t)
                        act.activation(square, k.x[:, t, :], ACT.Square, accum_out=stat[:, t, 0:1]).then_inc(squared, 1)
                    if t >= 1:
                        act.wait_ge(variance, t)
                        act.activation(stat[:, t - 1, 2:3], stat[:, t - 1, 1:2], ACT.Sqrt).then_inc(root, 1)

            @block.sync
            def _(sp):
                sp.dma_start(gain, k.w["final_norm"][0:1, :].partition_broadcast(P)).then_inc(gain_in, 16)
                for t in range(TT):
                    sp.wait_ge(ready, t + 1)
                    sp.dma_start(k.out[t * P:(t + 1) * P, :], result[t % 2]).then_inc(stored[t % 2], 16)
                for i in range(2):
                    sp.wait_ge(stored[i], 16 * (TT // 2))


class Core:
    pass


class Stage:

    def __init__(self, nc, ident):
        self.nc, self.ident, self.held, self.sems = nc, ident, ExitStack(), []

    def __enter__(self):
        return self

    def __exit__(self, *what):
        self.held.close()
        self.nc.clear_and_free_semaphores(self.sems)
        self.nc.all_engine_barrier()

    def sbuf(self, name, shape, dt=F32):
        return self.held.enter_context(self.nc.sbuf_tensor(name, shape, dt))

    def psum(self, name, shape, dt=F32):
        return self.held.enter_context(self.nc.psum_tensor(name, shape, dt))

    def sem(self, name):
        self.sems.append(self.nc.alloc_semaphore(name))
        return self.sems[-1]

    def block(self):
        return self.nc.Block()


def build(nc, w, out):
    k = Core()
    k.w, k.out, k.nc = w, out, nc
    with ExitStack() as ctx:
        def sbuf(name, shape, dt=F32):
            return ctx.enter_context(nc.sbuf_tensor(name, shape, dt))

        k.ident = sbuf("ident", [P, P])
        k.vec = sbuf("vec", [P, VEC_N])
        k.stage = lambda: Stage(nc, k.ident)
        w_in = w["w_in"]
        k.chunks = [(w_in[:, COL_UO:COL_GATE], HALF), (w_in[:, COL_GATE:COL_Q], 264), (w_in[:, COL_Q:COL_K], HALF),
                    (w_in[:, COL_K:COL_V], HALF), (w_in[:, COL_V:], HALF)]
        k.chunks += [(w["w_out"][:, h * HALF:(h + 1) * HALF], HALF) for h in range(2)]
        k.chunks += [(w["xattn_w_q"][:, h * 256:(h + 1) * 256], 256) for h in range(4)]
        k.chunks += [(w["xattn_w_kv"][:, h * 256:(h + 1) * 256], 256) for h in range(8)]
        k.chunks += [(w["xattn_w_o"][:, h * HALF:(h + 1) * HALF], HALF) for h in range(2)]
        k.chunk_in = [ctx.enter_context(nc.semaphore(f"chunk_in{i}")) for i in range(len(k.chunks))]

        def large_buffers(held, name, parts):
            return [held.enter_context(nc.sbuf_tensor(f"{name}_{part}", [P, n], F32, side="right")) for part, n in parts]

        def weights_at(i, buffer, at):
            k.place[i] = (buffer, at)

        k.place = {}
        k.chunk = lambda i, n: k.place[i][0][:, k.place[i][1]:k.place[i][1] + KT * n].rearrange("p (k n) -> p k n", k=KT)

        def split_input(held, name, slots, slot, chunks):
            chunk_space, high, low = large_buffers(held, name, (("chunks", slots * slot), ("xn_high", KT * S),
                                                                ("xn_low", KT * S)))
            k.xn = [part[:, :].rearrange("p (k n) -> p k n", k=KT) for part in (high, low)]
            for n, i in enumerate(chunks):
                weights_at(i, chunk_space, (n % slots) * slot)

        k.v_dram = nc.dram_tensor("v_dram", [S, A_W], F32, kind="Internal").ap()
        k.attn_dram = nc.dram_tensor("attn_dram", [3, S, O_W], F32, kind="Internal").ap()
        k.y_dram = nc.dram_tensor("y_dram", [BLOCKS * BLOCK, D], F32, kind="Internal").ap()
        k.yT = sbuf("yT", [P, KT, S])
        mixing = ExitStack()
        with ExitStack() as mixers:
            def mixer(name, shape):
                return mixers.enter_context(nc.sbuf_tensor(name, shape, F32))

            k.qT = mixer("qT", [P, 4, S])
            k.kT = mixer("kT", [P, 4, S])
            with ExitStack() as small:
                def small_mixer(name, shape):
                    return small.enter_context(nc.sbuf_tensor(name, shape, F32))

                k.uP = small_mixer("uP", [P, 2, 3 + S])
                k.oT = small_mixer("oT", [P, 2, S])
                k.s_in = small_mixer("s_in", [P, S5_G, S5_L, S5_C])
                k.gateT = small_mixer("gateT", [2 * M_H, S])
                with ExitStack() as held:
                    split_input(held, "mix", 2, SLOT, range(5))
                    in_projection(k)
                out_weights, = large_buffers(mixing, "mix", (("out_weights", 2 * SLOT),))
                weights_at(5, out_weights, 0)
                weights_at(6, out_weights, SLOT)
                mixer_space = ExitStack()
                k.ring, = large_buffers(mixer_space, "mixers", (("ring", 4 * SLOT),))
                mlstm(k)
                s5(k)
            attention(k)
            join_patterns(k)
            mixer_space.close()
        k.x = sbuf("x_residual", [P, TT, D])
        output_projection(k, "mix_out", k.yT, (5, 6), True)
        mixing.close()
        with ExitStack() as cross:
            k.xqT = k.yT
            k.xkT = cross.enter_context(nc.sbuf_tensor("xkT", [P, KT, MEM], F32))
            k.xv = cross.enter_context(nc.sbuf_tensor("xv", [P, MEM // P, D], F32))
            with ExitStack() as held:
                split_input(held, "xa", 3, KT * 256, range(7, 19))
                memory_projections(k)
            crossing = ExitStack()
            out_weights, mixed = large_buffers(crossing, "xa", (("out_weights", 2 * SLOT), ("mixed", KT * S)))
            weights_at(19, out_weights, 0)
            weights_at(20, out_weights, SLOT)
            k.mixedT = mixed[:, :].rearrange("p (k n) -> p k n", k=KT)
            memory_attention(k)
        output_projection(k, "xa_out", k.mixedT, (19, 20), False)
        crossing.close()
        thirds = (("gate", GU_K, DE), ("up", GU_K, DE), ("down", DN_K, D))
        shaped = lambda tile, n: tile[:, :].rearrange("p (k n) -> p k n", k=n)
        raw = large_buffers(ctx, "raw", [(name, n * cols) for name, n, cols in thirds[0:2]])
        raw.append(k.yT[:, 4:8, :].rearrange("p a b -> p (a b)"))
        k.raw = [shaped(tile, n) for tile, (_, n, _) in zip(raw, thirds)]
        k.raw_in = [ctx.enter_context(nc.semaphore(f"raw_in{i}")) for i in range(3)]
        k.gate = sbuf("gate", [P, TOP_K * TT])
        k.dest = sbuf("dest", [P, TOP_K * TT], U32)
        k.indices = sbuf("indices", [P, BLOCKS], U32)
        k.plan = sbuf("plan", [1, EXTRA + 1], I32)
        k.xn_dram = nc.dram_tensor("xn_dram", [S, D], F32, kind="Internal").ap()
        router(k)
        k.parts = [[shaped(tile, n) for tile in large_buffers(ctx, name, (("high", n * cols), ("low", n * cols)))]
                   for name, n, cols in thirds]
        experts(k)
        combine(k)


def attention_bias(table):
    def bucket(dist):
        large = 16 + (np.log(np.maximum(dist, 1) / 16) / np.log(2048 / 16) * 16).astype(np.int32)
        return np.where(dist < 16, dist, np.minimum(large, 31))

    i, j = np.arange(BLK)[:, None], np.arange(2 * BLK)[None, :]
    off = BLK + i - j
    parts = []
    for window, dil in PATTERNS[:2]:
        band = (off >= 0) & (off <= window // dil)
        parts.append(np.where(band[:, None], table[bucket(np.maximum(off, 0) * dil)].transpose(0, 2, 1), np.float32(NEG)))
    i, j = np.arange(BLK)[:, None], np.arange(BLK)[None, :]
    off = i // 2 - j // 2
    band = (off >= 0) & (i % 2 == j % 2)
    parts.append(np.where(band[:, None], table[bucket(np.maximum(off, 0) * PATTERNS[2][1])].transpose(0, 2, 1), np.float32(NEG)))
    return np.concatenate(parts, axis=2).astype(np.float32)


def kernel(**inputs):
    import concourse.bacc as bacc
    from concourse.bass_utils import run_bass_kernel_spmd as run

    a = {n: np.ascontiguousarray(v) for n, v in inputs.items()}
    data = {"x": a["x"][0], "mem": a["mem"][0], "norm_mix": a["norm_mix"], "w_in": a["w_in"][0]}
    for n in ("w_out", "xattn_w_q", "xattn_w_kv", "xattn_w_o", "s5_w_glu", "expert_w_gu", "expert_w_down"):
        data[n] = a[n][0]
    for n in ("norm_xattn", "norm_mem", "norm_ffn", "s5_b_glu"):
        data[n] = a[n]
    data["final_norm"] = a["final_norm"][None]

    def channels(v, n):
        return v.reshape(n, P).T

    def pairs(v):
        return v.reshape(S5_G // 2, 2, 64).transpose(1, 2, 0).reshape(P, S5_G // 2)

    gate_b = np.zeros((P, 1), np.float32)
    gate_b[0:2 * M_H, 0] = a["mlstm_gate_bias"][0]
    data["vec"] = np.concatenate([
        a["mlstm_conv_w"][0].reshape(4, 2, P).transpose(2, 1, 0).reshape(P, 8), channels(a["mlstm_conv_b"][0], 2),
        channels(a["mlstm_norm"][0], 2), channels(a["mlstm_skip"][0], 2), channels(a["s5_out_norm"][0], 2),
        channels(a["attn_out_norm"][0], 4), gate_b, pairs(a["s5_a_re"][0]), pairs(a["s5_a_im"][0]),
        pairs(np.broadcast_to(a["s5_log_dt"][0][:, None], (S5_G, 64))),
        np.where(np.arange(P) < 64, 1.0, -1.0).astype(np.float32)[:, None]], axis=1)
    mw = np.zeros((2, DH, 2, 3, 2, DH), np.float32)
    for i, n in enumerate(("mlstm_wq", "mlstm_wk", "mlstm_wv")):
        for h in range(M_H):
            mw[h % 2, :, h // 2, i, h % 2, :] = a[n][0, h]
    data["mlstm_w"] = mw.reshape(P, 2, 3, P)

    def pair_rows(v):
        return v.reshape(S5_G // 2, 2, 64, S5_C).transpose(1, 2, 0, 3).reshape(P, S5_G // 2, S5_C)

    data["attn_bias"] = attention_bias(a["rel_bias"])
    data["s5_bc"] = np.stack([pair_rows(a["s5_b_re"][0]), pair_rows(a["s5_b_im"][0]),
                              pair_rows(a["s5_c_re"][0].transpose(0, 2, 1)),
                              pair_rows(a["s5_c_im"][0].transpose(0, 2, 1))], axis=1)
    diag = np.zeros((S5_C, S5_G, S5_C), np.float32)
    for c in range(S5_C):
        diag[c, :, c] = a["s5_d"][0, :, c]
    data["s5_diag"] = diag
    data["router_w"] = np.concatenate([a["router_w_group"][0], a["router_w_expert"][0]], axis=1)
    data["router_b"] = np.concatenate([a["router_b_group"], a["router_b_expert"]], axis=1)
    numbers = np.arange(S, dtype=np.float32)
    data["route_const"] = np.concatenate([np.triu(np.ones((P, P), np.float32), 1), np.broadcast_to(numbers[:P], (P, P)),
                                          numbers.reshape(TT, P).T], axis=1)
    data["ident"] = np.eye(P, dtype=np.float32)
    data = {n: np.ascontiguousarray(v) for n, v in data.items()}
    nc = bacc.Bacc("TRN2", target_bir_lowering=False, num_devices=1)
    w = {n: nc.dram_tensor("in_" + n, v.shape, F32, kind="ExternalInput").ap()
                           for n, v in data.items()}
    out = nc.dram_tensor("out", (S, D), F32, kind="ExternalOutput").ap()
    build(nc, w, out)
    got = run(nc, [{"in_" + n: v for n, v in data.items()}], core_ids=[0])
    return got.results[0]["out"].reshape(1, S, D)
```
